# Optimizing a Trainium2 kernel written in Bass

```python
import jax, jax.numpy as jnp
from jax import lax
import numpy as np
import math

D_MODEL = 1024
BATCH = 1
SEQ = 512
DEPTH = 2

N_MIXERS = 2
N_ML_LAYERS = (DEPTH + 1) // 2
N_NSA_LAYERS = DEPTH // 2
RMS_EPS = 1e-6
LN_EPS = 1e-6
NEG_INF = -1e30

ML_INNER = 2 * D_MODEL
ML_HEADS = 4
ML_DH = ML_INNER // ML_HEADS
ML_CONV = 4
ML_QKV_BLK = 4
ML_NBLK = ML_INNER // ML_QKV_BLK
ML_CHUNK = 64

NSA_HEADS = 16
NSA_GROUPS = 4
NSA_HPG = NSA_HEADS // NSA_GROUPS
NSA_DK = 64
NSA_DV = 64
NSA_INNER = NSA_HEADS * NSA_DV
NSA_PROJ = NSA_HEADS * NSA_DK + 6 * NSA_GROUPS * NSA_DK + NSA_INNER + 3 * NSA_HEADS
ROPE_DIM = NSA_DK // 4
ROPE_THETA = 500000.0
CMP_BLOCK = 32
CMP_STRIDE = 16
CMP_HIDDEN = 2 * NSA_DK
SEL_BLOCK = 64
SEL_TOPK = 16
SEL_LOCAL = 2
SEL_FORCE = 1e9
SEL_Q_BLOCK = 16
WINDOW = 512
WIN_Q_BLOCK = 128


def rmsnorm(x, g):
    xf = x.astype(jnp.float32)
    y = xf * lax.rsqrt(jnp.mean(xf * xf, axis=-1, keepdims=True) + RMS_EPS)
    return y.astype(x.dtype) * g

def rope_partial(t, cos, sin):
    half = ROPE_DIM // 2
    shape = (t.shape[1],) + (1,) * (t.ndim - 3) + (half,)
    c = cos.reshape(shape).astype(t.dtype)
    s = sin.reshape(shape).astype(t.dtype)
    t1, t2, rest = t[..., :half], t[..., half:ROPE_DIM], t[..., ROPE_DIM:]
    return jnp.concatenate([t1 * c - t2 * s, t2 * c + t1 * s, rest], axis=-1)

def masked_softmax(s, mask):
    s = jnp.where(mask, s.astype(jnp.float32), NEG_INF)
    return jax.nn.softmax(s, axis=-1)

def mlstm_chunkwise(q, k, v, i_pre, log_f):
    B, NH, S, DH = q.shape
    nc = S // ML_CHUNK

    def to_chunks(t):
        return jnp.moveaxis(t.reshape(t.shape[:2] + (nc, ML_CHUNK) + t.shape[3:]), 2, 0)

    causal = jnp.tril(jnp.ones((ML_CHUNK, ML_CHUNK), dtype=bool))

    def step(carry, xs):
        C, n, m = carry
        qc, kc, vc, ic, fc = xs
        b = jnp.cumsum(fc, axis=-1)
        dmat = jnp.where(causal, b[..., :, None] - b[..., None, :] + ic[..., None, :], -jnp.inf)
        inter = b + m[..., None]
        m_row = jnp.maximum(inter, dmat.max(-1))
        w_intra = jnp.exp(dmat - m_row[..., None])
        w_inter = jnp.exp(inter - m_row)
        s = jnp.einsum('bhid,bhjd->bhij', qc, kc) * w_intra
        num = jnp.einsum('bhij,bhjd->bhid', s, vc) + w_inter[..., None] * jnp.einsum('bhvk,bhik->bhiv', C, qc)
        den = s.sum(-1) + w_inter * jnp.einsum('bhk,bhik->bhi', n, qc)
        h = num / jnp.maximum(jnp.abs(den), jnp.exp(-m_row))[..., None]
        b_last = b[..., -1]
        a = b_last[..., None] - b + ic
        m_new = jnp.maximum(b_last + m, a.max(-1))
        w_state = jnp.exp(a - m_new[..., None])
        decay = jnp.exp(b_last + m - m_new)
        C = decay[..., None, None] * C + jnp.einsum('bhjv,bhjk->bhvk', vc * w_state[..., None], kc)
        n = decay[..., None] * n + jnp.einsum('bhj,bhjk->bhk', w_state, kc)
        return (C, n, m_new), h

    init = (jnp.zeros((B, NH, DH, DH), jnp.float32),
            jnp.zeros((B, NH, DH), jnp.float32),
            jnp.zeros((B, NH), jnp.float32))
    _, h = lax.scan(step, init, tuple(to_chunks(t) for t in (q, k, v, i_pre, log_f)))
    return jnp.moveaxis(h, 0, 2).reshape(B, NH, S, DH)

def mlstm_mixer(h, w_in, conv_w, conv_b, w_q, w_k, w_v, w_if, b_if, ln_w, skip, w_out):
    B, S, _ = h.shape
    x_in, z = jnp.split(h @ w_in, 2, axis=-1)
    x_pad = jnp.pad(x_in, ((0, 0), (ML_CONV - 1, 0), (0, 0)))
    conv = sum(x_pad[:, tap:tap + S] * conv_w[tap] for tap in range(ML_CONV))
    x_conv = jax.nn.silu(conv + conv_b)

    def headwise(t, w):
        return jnp.einsum('bsnj,nij->bsni', t.reshape(B, S, ML_NBLK, ML_QKV_BLK), w).reshape(B, S, ML_INNER)

    q = headwise(x_conv, w_q)
    k = headwise(x_conv, w_k)
    v = headwise(x_in, w_v)
    gates = (jnp.concatenate([q, k, v], axis=-1) @ w_if + b_if).astype(jnp.float32)
    i_pre, f_pre = jnp.split(gates, 2, axis=-1)

    def heads(t):
        return t.reshape(B, S, ML_HEADS, ML_DH).transpose(0, 2, 1, 3).astype(jnp.float32)

    hh = mlstm_chunkwise(heads(q) * ML_DH ** -0.5, heads(k), heads(v),
                         i_pre.transpose(0, 2, 1), jax.nn.log_sigmoid(f_pre).transpose(0, 2, 1))
    mu = hh.mean(-1, keepdims=True)
    var = jnp.mean(jnp.square(hh - mu), axis=-1, keepdims=True)
    hn = ((hh - mu) * lax.rsqrt(var + LN_EPS)).transpose(0, 2, 1, 3).reshape(B, S, ML_INNER)
    hn = hn.astype(h.dtype) * ln_w
    return ((hn + skip * x_conv) * jax.nn.silu(z)) @ w_out

def nsa_mixer(h, w_in, b_gate, cmp_pe, cmp_w1, cmp_w2, w_out, cos, sin):
    B, S, _ = h.shape
    G, HPG, DK, DV = NSA_GROUPS, NSA_HPG, NSA_DK, NSA_DV
    sizes = [NSA_HEADS * DK] + [G * DK] * 6 + [NSA_INNER]
    q, k_c, v_c, k_s, v_s, k_w, v_w, z, g_logit = jnp.split(h @ w_in, np.cumsum(sizes).tolist(), axis=-1)
    q = q.reshape(B, S, G, HPG, DK)
    k_c, v_c, k_s, v_s, k_w, v_w = (t.reshape(B, S, G, DK) for t in (k_c, v_c, k_s, v_s, k_w, v_w))
    scale = DK ** -0.5
    pos = jnp.arange(S)

    n_cmp = (S - CMP_BLOCK) // CMP_STRIDE + 1
    cmp_start = jnp.arange(n_cmp) * CMP_STRIDE
    tok_idx = cmp_start[:, None] + jnp.arange(CMP_BLOCK)[None, :]

    def compress(t, pe, w1, w2):
        blocks = t[:, tok_idx] + pe[:, None, :]
        flat = blocks.transpose(0, 1, 3, 2, 4).reshape(B, n_cmp, G, CMP_BLOCK * DK)
        return jax.nn.silu(flat @ w1) @ w2

    k_cmp = compress(k_c, cmp_pe[0], cmp_w1[0], cmp_w2[0])
    v_cmp = compress(v_c, cmp_pe[1], cmp_w1[1], cmp_w2[1])
    cmp_mask = (cmp_start + CMP_BLOCK - 1)[None, :] <= pos[:, None]
    p_cmp = masked_softmax(jnp.einsum('bsghd,bcgd->bghsc', q, k_cmp) * scale, cmp_mask)
    p_cmp = p_cmp * cmp_mask.any(-1)[:, None].astype(jnp.float32)
    o_cmp = jnp.einsum('bghsc,bcgd->bsghd', p_cmp.astype(v_cmp.dtype), v_cmp)

    q_r = rope_partial(q, cos, sin)
    k_s = rope_partial(k_s, cos, sin)
    k_w = rope_partial(k_w, cos, sin)

    n_sel = S // SEL_BLOCK
    sel_start = jnp.arange(n_sel) * SEL_BLOCK
    overlap = jnp.clip(jnp.minimum(cmp_start[:, None] + CMP_BLOCK, sel_start[None, :] + SEL_BLOCK)
                       - jnp.maximum(cmp_start[:, None], sel_start[None, :]), 0, None)
    overlap = overlap.astype(jnp.float32) / CMP_STRIDE
    importance = jnp.einsum('bghsc,cn->bgsn', p_cmp, overlap)
    blk = jnp.arange(n_sel)
    dist = (pos // SEL_BLOCK)[:, None] - blk[None, :]
    forced = (blk[None, :] == 0) | ((dist >= 0) & (dist < SEL_LOCAL))
    importance = jnp.where(forced, SEL_FORCE, jnp.where(dist >= 0, importance, -1.0))
    top_k = min(SEL_TOPK, n_sel)
    top_val, top_idx = lax.top_k(importance, top_k)
    ks_blk = k_s.transpose(0, 2, 1, 3).reshape(B, G, n_sel, SEL_BLOCK, DK)
    vs_blk = v_s.transpose(0, 2, 1, 3).reshape(B, G, n_sel, SEL_BLOCK, DV)
    QB = SEL_Q_BLOCK
    n_qb = S // QB
    bi = jnp.arange(B)[:, None, None]
    gi = jnp.arange(G)[None, :, None]

    def sel_step(args):
        qb, idx, ok, qpos = args
        flat = idx.reshape(B, G, QB * top_k)
        kg = ks_blk[bi, gi, flat].reshape(B, G, QB, top_k * SEL_BLOCK, DK)
        vg = vs_blk[bi, gi, flat].reshape(B, G, QB, top_k * SEL_BLOCK, DV)
        kpos = idx[..., None] * SEL_BLOCK + jnp.arange(SEL_BLOCK)
        mask = (ok[..., None] & (kpos <= qpos[:, None, None])).reshape(B, G, 1, QB, top_k * SEL_BLOCK)
        p = masked_softmax(jnp.einsum('bqghd,bgqkd->bghqk', qb, kg) * scale, mask)
        return jnp.einsum('bghqk,bgqkd->bqghd', p.astype(vg.dtype), vg)

    xs = (jnp.moveaxis(q_r.reshape(B, n_qb, QB, G, HPG, DK), 1, 0),
          jnp.moveaxis(top_idx.reshape(B, G, n_qb, QB, top_k), 2, 0),
          jnp.moveaxis((top_val >= 0).reshape(B, G, n_qb, QB, top_k), 2, 0),
          pos.reshape(n_qb, QB))
    o_sel = jnp.moveaxis(lax.map(sel_step, xs), 0, 1).reshape(B, S, G, HPG, DV)

    k_wp = jnp.pad(k_w, ((0, 0), (WINDOW, 0), (0, 0), (0, 0)))
    v_wp = jnp.pad(v_w, ((0, 0), (WINDOW, 0), (0, 0), (0, 0)))
    span = WIN_Q_BLOCK + WINDOW

    def win_step(start):
        qb = lax.dynamic_slice_in_dim(q_r, start, WIN_Q_BLOCK, axis=1)
        kb = lax.dynamic_slice_in_dim(k_wp, start, span, axis=1)
        vb = lax.dynamic_slice_in_dim(v_wp, start, span, axis=1)
        kpos = start - WINDOW + jnp.arange(span)
        diff = (start + jnp.arange(WIN_Q_BLOCK))[:, None] - kpos[None, :]
        mask = (diff >= 0) & (diff < WINDOW) & (kpos >= 0)[None, :]
        p = masked_softmax(jnp.einsum('bqghd,bkgd->bghqk', qb, kb) * scale, mask)
        return jnp.einsum('bghqk,bkgd->bqghd', p.astype(vb.dtype), vb)

    o_win = lax.map(win_step, jnp.arange(S // WIN_Q_BLOCK) * WIN_Q_BLOCK)
    o_win = jnp.moveaxis(o_win, 0, 1).reshape(B, S, G, HPG, DV)

    gate = jax.nn.sigmoid((g_logit + b_gate).astype(jnp.float32)).reshape(B, S, NSA_HEADS, 3).astype(h.dtype)

    def heads(o):
        return o.reshape(B, S, NSA_HEADS, DV)

    o = gate[..., 0:1] * heads(o_cmp) + gate[..., 1:2] * heads(o_sel) + gate[..., 2:3] * heads(o_win)
    return (o.reshape(B, S, NSA_INNER) * jax.nn.silu(z)) @ w_out

def first_inputs(seed: int = 0) -> dict:
    key = jax.random.key(seed)
    ks = jax.random.split(key, 24)
    f32 = jnp.float32

    def nrm(k, shape, fan):
        return jax.random.normal(k, shape, f32) * fan ** -0.5

    def gain(k, shape):
        return 1.0 + 0.02 * jax.random.normal(k, shape, f32)

    def small(k, shape, s=0.02):
        return s * jax.random.normal(k, shape, f32)

    LM, LN = N_ML_LAYERS, N_NSA_LAYERS
    b_if = jnp.concatenate([small(ks[10], (LM, ML_HEADS), 0.1),
                            jnp.linspace(3.0, 6.0, ML_HEADS, dtype=f32)[None, :]
                            + small(ks[11], (LM, ML_HEADS), 0.01)], axis=-1)
    return {
        'x': jax.random.normal(ks[0], (BATCH, SEQ, D_MODEL), f32),
        'ml_norm': gain(ks[1], (LM, D_MODEL)),
        'ml_w_in': nrm(ks[2], (LM, D_MODEL, 2 * ML_INNER), D_MODEL),
        'ml_conv_w': nrm(ks[3], (LM, ML_CONV, ML_INNER), ML_CONV),
        'ml_conv_b': small(ks[4], (LM, ML_INNER)),
        'ml_w_q': nrm(ks[5], (LM, ML_NBLK, ML_QKV_BLK, ML_QKV_BLK), ML_QKV_BLK),
        'ml_w_k': nrm(ks[6], (LM, ML_NBLK, ML_QKV_BLK, ML_QKV_BLK), ML_QKV_BLK),
        'ml_w_v': nrm(ks[7], (LM, ML_NBLK, ML_QKV_BLK, ML_QKV_BLK), ML_QKV_BLK),
        'ml_w_if': nrm(ks[8], (LM, 3 * ML_INNER, 2 * ML_HEADS), 3 * ML_INNER),
        'ml_b_if': b_if,
        'ml_ln_w': gain(ks[12], (LM, ML_INNER)),
        'ml_skip': gain(ks[13], (LM, ML_INNER)),
        'ml_w_out': nrm(ks[14], (LM, ML_INNER, D_MODEL), ML_INNER),
        'nsa_norm': gain(ks[15], (LN, D_MODEL)),
        'nsa_w_in': nrm(ks[16], (LN, D_MODEL, NSA_PROJ), D_MODEL),
        'nsa_b_gate': small(ks[17], (LN, 3 * NSA_HEADS)),
        'nsa_cmp_pe': small(ks[18], (LN, 2, CMP_BLOCK, NSA_DK), 0.1),
        'nsa_cmp_w1': nrm(ks[19], (LN, 2, CMP_BLOCK * NSA_DK, CMP_HIDDEN), CMP_BLOCK * NSA_DK),
        'nsa_cmp_w2': nrm(ks[20], (LN, 2, CMP_HIDDEN, NSA_DK), CMP_HIDDEN),
        'nsa_w_out': nrm(ks[21], (LN, NSA_INNER, D_MODEL), NSA_INNER),
        'final_norm': gain(ks[22], (D_MODEL,)),
    }

def first_block(x, ml_norm, ml_w_in, ml_conv_w, ml_conv_b, ml_w_q, ml_w_k, ml_w_v, ml_w_if, ml_b_if,
              ml_ln_w, ml_skip, ml_w_out, nsa_norm, nsa_w_in, nsa_b_gate, nsa_cmp_pe, nsa_cmp_w1,
              nsa_cmp_w2, nsa_w_out, final_norm):
    S = x.shape[1]
    pos_f = jnp.arange(S, dtype=jnp.float32)
    inv_freq = ROPE_THETA ** (-jnp.arange(0, ROPE_DIM, 2, dtype=jnp.float32) / ROPE_DIM)
    ang = pos_f[:, None] * inv_freq[None, :]
    cos, sin = jnp.cos(ang), jnp.sin(ang)
    for i in range(DEPTH):
        j = i // N_MIXERS
        if i % N_MIXERS == 0:
            x = x + mlstm_mixer(rmsnorm(x, ml_norm[j]), ml_w_in[j], ml_conv_w[j], ml_conv_b[j],
                                ml_w_q[j], ml_w_k[j], ml_w_v[j], ml_w_if[j], ml_b_if[j],
                                ml_ln_w[j], ml_skip[j], ml_w_out[j])
        else:
            x = x + nsa_mixer(rmsnorm(x, nsa_norm[j]), nsa_w_in[j], nsa_b_gate[j], nsa_cmp_pe[j],
                              nsa_cmp_w1[j], nsa_cmp_w2[j], nsa_w_out[j], cos, sin)
    return rmsnorm(x, final_norm)


DEPTH_2 = 1

RWKV_HEAD_DIM = 64
RWKV_HEADS = D_MODEL // (2 * RWKV_HEAD_DIM)
RWKV_WIDTH = RWKV_HEADS * RWKV_HEAD_DIM
DECAY_LORA = 64
ICLR_LORA = 64
GATE_LORA = 128
GN_EPS = 64e-5
N_DIR = 2

DA_HEAD_DIM = 64
DA_HEADS = D_MODEL // (4 * DA_HEAD_DIM)
DA_V_DIM = 2 * DA_HEAD_DIM
DA_QK_WIDTH = DA_HEADS * 2 * DA_HEAD_DIM
DA_V_WIDTH = DA_HEADS * DA_V_DIM
SUBLN_EPS = 1e-5
Q_BLOCK = 128

ROPE_DIM_2 = DA_HEAD_DIM // 4

D_FF = 4 * D_MODEL
PLE_DIM = 256
N_BRANCH = 2

RWKV_COLS = 3 * RWKV_WIDTH + N_DIR * DECAY_LORA + N_DIR * ICLR_LORA + GATE_LORA
DA_COLS = 2 * DA_QK_WIDTH + DA_V_WIDTH
GATE_COLS = N_BRANCH * D_MODEL
IN_COLS = RWKV_COLS + DA_COLS + GATE_COLS


def rmsnorm_2(x, g, eps=RMS_EPS):
    xf = x.astype(jnp.float32)
    y = xf * lax.rsqrt(jnp.mean(xf * xf, axis=-1, keepdims=True) + eps)
    return (y * g.astype(jnp.float32)).astype(x.dtype)

def centred_shift(u, mu_prev, mu_next):
    up = jnp.pad(u, ((0, 0), (1, 1), (0, 0)))
    return u + mu_prev * (up[:, :-2] - u) + mu_next * (up[:, 2:] - u)

def rwkv7_scan(r, w, k, v, kk, a, reverse):
    B, S, H, N = r.shape

    def step(state, inp):
        r_t, w_t, k_t, v_t, kk_t, a_t = inp
        sa = jnp.einsum('bhij,bhj->bhi', state, -kk_t)
        state = (state * w_t[:, :, None, :]
                 + sa[..., None] * (kk_t * a_t)[:, :, None, :]
                 + v_t[..., None] * k_t[:, :, None, :])
        y_t = jnp.einsum('bhij,bhj->bhi', state, r_t)
        return state, y_t

    xs = tuple(jnp.moveaxis(t, 1, 0) for t in (r, w, k, v, kk, a))
    s0 = jnp.zeros((B, H, N, N), jnp.float32)
    _, ys = lax.scan(step, s0, xs, reverse=reverse)
    return jnp.moveaxis(ys, 0, 1)

def rwkv7_branch(u, mu_prev, mu_next, w0, w2, a0, a2, g2, k_k, k_a, r_k, ln_w, ln_b, w_o):
    f32 = jnp.float32
    B, S, _ = u.shape
    H, N, W = RWKV_HEADS, RWKV_HEAD_DIM, RWKV_WIDTH
    u = centred_shift(u, mu_prev, mu_next).astype(f32)
    o1, o2, o3 = W, 2 * W, 3 * W
    o4 = o3 + N_DIR * DECAY_LORA
    o5 = o4 + N_DIR * ICLR_LORA
    r = u[..., :o1]
    k = u[..., o1:o2]
    v = u[..., o2:o3]
    wd = u[..., o3:o4].reshape(B, S, N_DIR, DECAY_LORA)
    ad = u[..., o4:o5].reshape(B, S, N_DIR, ICLR_LORA)
    gd = u[..., o5:]

    w_log = -jax.nn.softplus(-(w0.astype(f32) + jnp.einsum('bsdr,drc->bsdc', jnp.tanh(wd), w2.astype(f32)))) - 0.5
    decay = jnp.exp(-jnp.exp(w_log)).reshape(B, S, N_DIR, H, N)
    a = jax.nn.sigmoid(a0.astype(f32) + jnp.einsum('bsdr,drc->bsdc', ad, a2.astype(f32))).reshape(B, S, N_DIR, H, N)
    g = jax.nn.sigmoid(gd) @ g2.astype(f32)

    kk = (k * k_k.astype(f32)).reshape(B, S, H, N)
    kk = kk / jnp.maximum(jnp.sqrt(jnp.sum(kk * kk, axis=-1, keepdims=True)), 1e-12)
    r_h = r.reshape(B, S, H, N)
    v_h = v.reshape(B, S, H, N)
    k_dir = k.reshape(B, S, 1, H, N) * (1.0 + (a - 1.0) * k_a.astype(f32).reshape(H, N))

    y = (rwkv7_scan(r_h, decay[:, :, 0], k_dir[:, :, 0], v_h, kk, a[:, :, 0], False)
         + rwkv7_scan(r_h, decay[:, :, 1], k_dir[:, :, 1], v_h, kk, a[:, :, 1], True))

    mean = jnp.mean(y, axis=-1, keepdims=True)
    var = jnp.mean(jnp.square(y - mean), axis=-1, keepdims=True)
    y = ((y - mean) * lax.rsqrt(var + GN_EPS)).reshape(B, S, W)
    y = y * ln_w.astype(f32) + ln_b.astype(f32)
    bonus = jnp.sum(jnp.sum(r_h[:, :, None] * k_dir * r_k.astype(f32), axis=-1, keepdims=True), axis=2) * v_h
    y = (y + bonus.reshape(B, S, W)) * g
    return (y @ w_o.astype(f32)).astype(w_o.dtype)

def rope_tables(S):
    pos = jnp.arange(S, dtype=jnp.float32)
    inv_freq = ROPE_THETA ** (-jnp.arange(0, ROPE_DIM_2, 2, dtype=jnp.float32) / ROPE_DIM_2)
    ang = pos[:, None] * inv_freq[None, :]
    return jnp.cos(ang), jnp.sin(ang)

def partial_rope(x, cos, sin):
    half = ROPE_DIM_2 // 2
    c = cos[:, None, None, :]
    s = sin[:, None, None, :]
    x1 = x[..., :half].astype(jnp.float32)
    x2 = x[..., half:ROPE_DIM_2].astype(jnp.float32)
    rot = jnp.concatenate([x1 * c - x2 * s, x2 * c + x1 * s], axis=-1)
    return jnp.concatenate([rot.astype(x.dtype), x[..., ROPE_DIM_2:]], axis=-1)

def diff_attn_branch(u, lq1, lk1, lq2, lk2, subln_w, w_o, lambda_init):
    f32 = jnp.float32
    B, S, _ = u.shape
    H, DH, DV = DA_HEADS, DA_HEAD_DIM, DA_V_DIM
    q = u[..., :DA_QK_WIDTH].reshape(B, S, H, 2, DH)
    k = u[..., DA_QK_WIDTH:2 * DA_QK_WIDTH].reshape(B, S, H, 2, DH)
    v = u[..., 2 * DA_QK_WIDTH:].reshape(B, S, H, DV)
    cos, sin = rope_tables(S)
    q = partial_rope(q, cos, sin) * (DH ** -0.5)
    k = partial_rope(k, cos, sin)
    lam = (jnp.exp(jnp.sum(lq1.astype(f32) * lk1.astype(f32)))
           - jnp.exp(jnp.sum(lq2.astype(f32) * lk2.astype(f32))) + lambda_init)

    kt = k.transpose(0, 2, 3, 1, 4)
    vt = v.transpose(0, 2, 1, 3)
    n_blk = S // Q_BLOCK
    qb = q.reshape(B, n_blk, Q_BLOCK, H, 2, DH).transpose(1, 0, 3, 4, 2, 5)

    def block(q_blk):
        s = jnp.einsum('bhcqd,bhckd->bhcqk', q_blk, kt).astype(f32)
        pr = jax.nn.softmax(s, axis=-1)
        pd = pr[:, :, 0] - lam * pr[:, :, 1]
        return jnp.einsum('bhqk,bhkv->bhqv', pd.astype(vt.dtype), vt)

    o = lax.map(block, qb)
    o = o.transpose(1, 0, 3, 2, 4).reshape(B, S, H, DV).astype(f32)
    o = o * lax.rsqrt(jnp.mean(o * o, axis=-1, keepdims=True) + SUBLN_EPS)
    o = o * subln_w.astype(f32) * (1.0 - lambda_init)
    return o.reshape(B, S, DA_V_WIDTH).astype(w_o.dtype) @ w_o

def second_inputs(seed: int = 0) -> dict:
    key = jax.random.key(seed)
    ks = iter(jax.random.split(key, 40))
    L, D, W = DEPTH_2, D_MODEL, RWKV_WIDTH
    f32 = jnp.float32

    def nrm(shape, scale):
        return jax.random.normal(next(ks), shape, f32) * scale

    def gain(shape):
        return 1.0 + 0.05 * jax.random.normal(next(ks), shape, f32)

    def unif(shape, lo, hi):
        return jax.random.uniform(next(ks), shape, f32, lo, hi)

    return {
        "x": nrm((BATCH, SEQ, D), 1.0),
        "p": nrm((DEPTH_2, BATCH, SEQ, PLE_DIM), 1.0),
        "norm_mix": gain((L, D)),
        "w_in": nrm((L, D, IN_COLS), D ** -0.5),
        "shift_mu_prev": unif((L, RWKV_COLS), 0.0, 0.5),
        "shift_mu_next": unif((L, RWKV_COLS), 0.0, 0.5),
        "rwkv_w0": unif((L, N_DIR, W), -6.0, 1.0),
        "rwkv_w2": nrm((L, N_DIR, DECAY_LORA, W), 0.1 * DECAY_LORA ** -0.5),
        "rwkv_a0": nrm((L, N_DIR, W), 0.5),
        "rwkv_a2": nrm((L, N_DIR, ICLR_LORA, W), 0.1 * ICLR_LORA ** -0.5),
        "rwkv_g2": nrm((L, GATE_LORA, W), GATE_LORA ** -0.5),
        "rwkv_k_k": 0.85 + 0.05 * jax.random.normal(next(ks), (L, W), f32),
        "rwkv_k_a": gain((L, W)),
        "rwkv_r_k": nrm((L, RWKV_HEADS, RWKV_HEAD_DIM), 0.1),
        "rwkv_ln_w": gain((L, W)),
        "rwkv_ln_b": nrm((L, W), 0.01),
        "rwkv_w_o": nrm((L, W, D), W ** -0.5),
        "da_lq1": nrm((L, DA_HEAD_DIM), 0.1),
        "da_lk1": nrm((L, DA_HEAD_DIM), 0.1),
        "da_lq2": nrm((L, DA_HEAD_DIM), 0.1),
        "da_lk2": nrm((L, DA_HEAD_DIM), 0.1),
        "da_subln_w": gain((L, DA_V_DIM)),
        "da_w_o": nrm((L, DA_V_WIDTH, D), DA_V_WIDTH ** -0.5),
        "w_out": nrm((L, D, D), D ** -0.5),
        "norm_ffn": gain((L, D)),
        "w_ff1": nrm((L, D, D_FF), D ** -0.5),
        "w_ff2": nrm((L, D_FF, D), D_FF ** -0.5),
        "norm_ple": gain((L, D)),
        "w_ple_gate": nrm((L, D, D), D ** -0.5),
        "w_ple_proj": nrm((L, PLE_DIM, D), PLE_DIM ** -0.5),
        "norm_final": gain((D,)),
    }

def second_block(x, p, norm_mix, w_in, shift_mu_prev, shift_mu_next, rwkv_w0, rwkv_w2, rwkv_a0,
              rwkv_a2, rwkv_g2, rwkv_k_k, rwkv_k_a, rwkv_r_k, rwkv_ln_w, rwkv_ln_b, rwkv_w_o,
              da_lq1, da_lk1, da_lq2, da_lk2, da_subln_w, da_w_o, w_out, norm_ffn, w_ff1, w_ff2,
              norm_ple, w_ple_gate, w_ple_proj, norm_final):
    B, S, D = x.shape
    for i in range(DEPTH_2):
        lambda_init = 0.8 - 0.6 * math.exp(-0.3 * i)
        h = rmsnorm_2(x, norm_mix[i])
        u = h @ w_in[i]
        u_rwkv = u[..., :RWKV_COLS]
        u_da = u[..., RWKV_COLS:RWKV_COLS + DA_COLS]
        gates = jax.nn.sigmoid(u[..., RWKV_COLS + DA_COLS:].astype(jnp.float32)).reshape(B, S, N_BRANCH, D)
        y_a = rwkv7_branch(u_rwkv, shift_mu_prev[i], shift_mu_next[i], rwkv_w0[i], rwkv_w2[i],
                           rwkv_a0[i], rwkv_a2[i], rwkv_g2[i], rwkv_k_k[i], rwkv_k_a[i], rwkv_r_k[i],
                           rwkv_ln_w[i], rwkv_ln_b[i], rwkv_w_o[i])
        y_b = diff_attn_branch(u_da, da_lq1[i], da_lk1[i], da_lq2[i], da_lk2[i], da_subln_w[i],
                               da_w_o[i], lambda_init)
        merged = (gates[:, :, 0] * y_a.astype(jnp.float32)
                  + gates[:, :, 1] * y_b.astype(jnp.float32)).astype(x.dtype)
        x = x + merged @ w_out[i]
        h = rmsnorm_2(x, norm_ffn[i])
        x = x + jnp.square(jax.nn.relu(h @ w_ff1[i])) @ w_ff2[i]
        h = rmsnorm_2(x, norm_ple[i])
        x = x + jax.nn.sigmoid(h @ w_ple_gate[i]) * (p[i] @ w_ple_proj[i])
    return rmsnorm_2(x, norm_final)


def setup_inputs(seed=0):
    out = dict(first_inputs(seed))
    for name, value in second_inputs(seed + 1).items():
        if name != "x":
            out[name + "_2"] = value
    return out


def reference(
    x, ml_norm, ml_w_in, ml_conv_w, ml_conv_b, ml_w_q, ml_w_k, ml_w_v, ml_w_if, ml_b_if,
    ml_ln_w, ml_skip, ml_w_out, nsa_norm, nsa_w_in, nsa_b_gate, nsa_cmp_pe, nsa_cmp_w1,
    nsa_cmp_w2, nsa_w_out, final_norm, p_2, norm_mix_2, w_in_2, shift_mu_prev_2,
    shift_mu_next_2, rwkv_w0_2, rwkv_w2_2, rwkv_a0_2, rwkv_a2_2, rwkv_g2_2, rwkv_k_k_2,
    rwkv_k_a_2, rwkv_r_k_2, rwkv_ln_w_2, rwkv_ln_b_2, rwkv_w_o_2, da_lq1_2, da_lk1_2, da_lq2_2,
    da_lk2_2, da_subln_w_2, da_w_o_2, w_out_2, norm_ffn_2, w_ff1_2, w_ff2_2, norm_ple_2,
    w_ple_gate_2, w_ple_proj_2, norm_final_2,
):
    x = first_block(
        x, ml_norm, ml_w_in, ml_conv_w, ml_conv_b, ml_w_q, ml_w_k, ml_w_v, ml_w_if, ml_b_if,
        ml_ln_w, ml_skip, ml_w_out, nsa_norm, nsa_w_in, nsa_b_gate, nsa_cmp_pe, nsa_cmp_w1,
        nsa_cmp_w2, nsa_w_out, final_norm,
    )
    return second_block(
        x, p_2, norm_mix_2, w_in_2, shift_mu_prev_2, shift_mu_next_2, rwkv_w0_2, rwkv_w2_2,
        rwkv_a0_2, rwkv_a2_2, rwkv_g2_2, rwkv_k_k_2, rwkv_k_a_2, rwkv_r_k_2, rwkv_ln_w_2,
        rwkv_ln_b_2, rwkv_w_o_2, da_lq1_2, da_lk1_2, da_lq2_2, da_lk2_2, da_subln_w_2, da_w_o_2,
        w_out_2, norm_ffn_2, w_ff1_2, w_ff2_2, norm_ple_2, w_ple_gate_2, w_ple_proj_2,
        norm_final_2,
    )


_drawn_inputs = setup_inputs


def setup_inputs(seed=0):
    import zlib

    import numpy as np

    out = dict(_drawn_inputs(seed))
    spreads = {}
    factors = {'ml_ln_w': 4.722,
     'ml_skip': 7.352,
     'nsa_norm': 8.0,
     'nsa_b_gate': 8.0,
     'rwkv_w2_2': 8.0,
     'rwkv_a2_2': 6.936,
     'rwkv_k_k_2': 4.12,
     'rwkv_k_a_2': 2.784,
     'rwkv_ln_w_2': 4.015,
     'rwkv_ln_b_2': 34.817,
     'da_lk2_2': 5.39,
     'da_subln_w_2': 3.091,
     'norm_ple_2': 30.781}
    for name, (base, spread) in spreads.items():
        noise = np.random.default_rng([zlib.crc32(name.encode()), seed]).standard_normal(out[name].shape)
        drawn = base * np.exp(spread * noise) if base else spread * noise
        out[name] = __import__('jax').numpy.asarray(drawn.astype(out[name].dtype))
    for name, factor in factors.items():
        out[name] = (out[name] * factor).astype(out[name].dtype)
    return out
```

```python
from contextlib import ExitStack

import concourse.bass as bass
from concourse import mybir

F32 = mybir.dt.float32
F32R = mybir.dt.float32r
BF16 = mybir.dt.bfloat16
ALU = mybir.AluOpType
ACT = mybir.ActivationFunctionType
AX = mybir.AxisListType.X

P = 128
S = 512
D = 1024
KD = D // P
TT = S // P

ML_INNER = 2048
ML_T = ML_INNER // P
ML_HEADS = 4
ML_DH = 512
CONV = 4

NSA_HEADS = 16
NSA_GROUPS = 4
DK = 64
CMP_STRIDE = 16
CMP_BLOCK = 32
N_CMP = (S - CMP_BLOCK) // CMP_STRIDE + 1

DA_HEADS = 4
RW_T = 4
CHUNK = 64
N_CHUNK = S // CHUNK
LEVELS = 6
DECAY_SCALE = 0.6065306597126334
LAMBDA_INIT = 0.8 - 0.6

RAW_SLOTS = 3
BLOCK_COLS = 256


def weight_blocks():
    out = []

    def cols(name, r0, rows, c0, c1):
        while c0 < c1:
            n = min(BLOCK_COLS, c1 - c0)
            out.append((name, r0, rows, c0, n))
            c0 += n

    cols("ml_in", 0, D, 0, 2 * ML_INNER)
    for g in range(2):
        cols("ml_out", g * D, D, 0, D)
    cols("nsa_in", 0, D, 0, 29 * P)
    cols("nsa_out", 0, D, 0, D)
    cols("in_2", 0, D, 0, 43 * P)
    cols("mix_o", 0, D, 0, D)
    cols("out_2", 0, D, 0, D)
    for f in range(4):
        cols("ff1", 0, D, f * D, (f + 1) * D)
        cols("ff2", f * D, D, 0, D)
    cols("ple_gate", 0, D, 0, D)
    cols("ple_proj", 0, 256, 0, D)
    return out


BLOCKS = weight_blocks()
BLOCK_AT, TILE_AT = [], []
_at = _t = 0
for _name, _r0, _rows, _c0, _n in BLOCKS:
    BLOCK_AT.append(_at)
    TILE_AT.append(_t)
    _at += _rows // P * _n
    _t += _n // P
STREAM_COLS = _at
BLOCK_AT.append(_at)
TILE_AT.append(_t)


def first_block(name, nth=0):
    starts = [b for b, x in enumerate(BLOCKS) if x[0] == name and (b == 0 or BLOCKS[b - 1][0] != name or
              (x[3] == 0))]
    return starts[nth]


COLS = {}
_c = 0
for _name, _n in (("ml_norm", 8), ("conv_w", 64), ("conv_b", 16), ("ml_ln_w", 16), ("skip", 16),
                  ("nsa_norm", 8), ("final_norm", 8), ("norm_mix", 8), ("norm_ffn", 8), ("norm_ple", 8),
                  ("norm_final", 8), ("mu_prev", 15), ("mu_next", 15), ("w0", 8), ("a0", 8), ("k_k", 4),
                  ("k_a", 4), ("r_k", 4), ("rw_ln_w", 4), ("rw_ln_b", 4), ("subln", 1), ("b_if", 1),
                  ("b_gate", 1), ("lq1", 1), ("lk1", 1), ("lq2", 1), ("lk2", 1),
                  ("eps6", 1), ("eps5", 1), ("eps_gn", 1), ("one", 1), ("cmp_any", 1)):
    COLS[_name] = _c
    _c += _n
N_COLS = _c

CONSTS = {}
_c = 0
for _name, _n in (("ident", 128), ("ones", 128), ("mean_ones", 128), ("block_ones", 128), ("rot", 128),
                  ("same4", 32), ("sel", 512), ("cos", 512), ("sin", 512)):
    CONSTS[_name] = _c
    _c += _n
N_CONSTS = _c
RW_CONSTS = {}
_c = 0
for _name, _n in (("scan", 512), ("score0", 256), ("score1", 256), ("level0", 6 * 64), ("level1", 6 * 64),
                  ("eye64", 64)):
    RW_CONSTS[_name] = _c
    _c += _n
N_RW_CONSTS = _c

KB = 1024
BASE = 17 * KB


class Core:

    def __init__(self, nc, ctx, io):
        self.nc, self.ctx, self.io = nc, ctx, io
        self.stage, self.in_use, self.spent = None, [], []
        at = self.at
        self.consts = at("consts", [P, N_CONSTS], F32, 0)
        self.cols = at("cols", [P, N_COLS], F32, 9)
        self.ident_bf = at("ident_bf", [P, P], BF16, 10.25)
        self.causal_bf = at("causal_bf", [P, P], BF16, 10.5)
        self.cmp_bf = at("cmp_bf", [P, TT * 32], BF16, 10.75)
        self.small = at("small", [P, 256], F32, 11)
        self.xT = at("xT", [P, KD, S], F32, 12)
        self.act_hi = at("act_hi", [P, KD, S], F32R, 28)
        self.act_lo = at("act_lo", [P, KD, S], F32R, 44)
        self.raw = [at(f"raw{i}", [P, KD * BLOCK_COLS], F32, 60 + 8 * i) for i in range(RAW_SLOTS)]
        self.whi = [at(f"whi{i}", [P, KD * BLOCK_COLS], F32R, 84 + 8 * i) for i in range(2)]
        self.wlo = [at(f"wlo{i}", [P, KD * BLOCK_COLS], F32R, 100 + 8 * i) for i in range(2)]
        self.ps = ctx.enter_context(nc.psum_tensor("ps", [P, 8, S], F32))
        self.landed = [self.sem(f"weights_landed{i}") for i in range(RAW_SLOTS)]
        self.hi_done = self.sem("weights_hi_done")
        self.lo_done = self.sem("weights_lo_done")
        self.tile_done = self.sem("tile_done")
        self.evac_done = self.sem("evac_done")
        self.out_stored = self.sem("out_stored")
        self.loaded = 0

    def at(self, name, shape, dtype, kb):
        return self.nc.alloc_sbuf_tensor_at(name, shape, dtype, offset=BASE + int(kb * KB))

    def region(self, name, shape, dtype, kb):
        return self.at(name, shape, dtype, 116 + kb)

    def sem(self, name):
        s = (self.stage or self.ctx).enter_context(self.nc.semaphore(name))
        self.in_use.append(s)
        return s

    def run(self, stage):
        for first, end in self.spent:
            self.nc.sync.sem_clear(range(first, end))
        self.in_use = []
        with ExitStack() as self.stage:
            stage(self)
            numbers = sorted(s.num for s in self.in_use)
            self.spent = []
            for n in numbers:
                if self.spent and self.spent[-1][1] == n:
                    self.spent[-1][1] = n + 1
                else:
                    self.spent.append([n, n + 1])

    def const(self, name, n=P):
        c = CONSTS[name]
        return self.consts[:, c:c + n]

    def col(self, name, i=0, rows=slice(0, P)):
        c = COLS[name] + i
        return self.cols[rows, c:c + 1]


def load_blocks(k, sp, upto):
    while k.loaded < min(upto, len(BLOCKS)):
        b = k.loaded
        if b >= RAW_SLOTS:
            sp.wait_ge(k.lo_done, b - RAW_SLOTS + 1)
        n = BLOCK_AT[b + 1] - BLOCK_AT[b]
        sp.dma_start(k.raw[b % RAW_SLOTS][:, 0:n], k.io["stream"][:, BLOCK_AT[b]:BLOCK_AT[b + 1]]) \
            .then_inc(k.landed[b % RAW_SLOTS], 16)
        k.loaded += 1


def split_hi(k, act, b):
    if b >= len(BLOCKS):
        return
    n = BLOCK_AT[b + 1] - BLOCK_AT[b]
    act.wait_ge(k.landed[b % RAW_SLOTS], 16 * (b // RAW_SLOTS + 1))
    if b >= 2:
        act.wait_ge(k.tile_done, TILE_AT[b - 1])
    act.activation(k.whi[b % 2][:, 0:n], k.raw[b % RAW_SLOTS][:, 0:n], ACT.Copy).then_inc(k.hi_done, 1)


def split_lo(k, dve, b):
    if b >= len(BLOCKS):
        return
    n = BLOCK_AT[b + 1] - BLOCK_AT[b]
    dve.wait_ge(k.hi_done, b + 1)
    dve.tensor_tensor(k.wlo[b % 2][:, 0:n], k.raw[b % RAW_SLOTS][:, 0:n],
                      k.whi[b % 2][:, 0:n].bitcast(F32), ALU.subtract).then_inc(k.lo_done, 1)


def multiply_tile(k, pe, b, j, k0=0):
    _, _, rows, _, n = BLOCKS[b]
    t = TILE_AT[b] + j
    pe.wait_ge(k.lo_done, b + 1)
    if t >= 4:
        pe.wait_ge(k.evac_done, t - 3)
    bank = k.ps[:, t % 4, :]
    for kt in range(rows // P):
        w = slice(kt * n + j * P, kt * n + j * P + P)
        hi, lo = k.whi[b % 2][:, w], k.wlo[b % 2][:, w]
        pe.matmul(bank, hi, k.act_hi[:, k0 + kt, :], start=(kt == 0), stop=False)
        pe.matmul(bank, hi, k.act_lo[:, k0 + kt, :], start=False, stop=False)
        last = pe.matmul(bank, lo, k.act_hi[:, k0 + kt, :], start=False, stop=(kt == rows // P - 1))
    last.then_inc(k.tile_done, 1)


def tiles_of(b0, b1):
    return [(b, j) for b in range(b0, b1) for j in range(BLOCKS[b][4] // P)]


def stage_open(k):
    io, nc = k.io, k.nc
    got = k.sem("open_landed")
    with nc.Block() as block:
        @block.sync
        def _(sp):
            sp.dma_start(k.xT[:], io["xT"]).then_inc(got, 16)
            sp.dma_start(k.consts[:], io["consts"]).then_inc(got, 16)
            sp.dma_start(k.cols[:], io["cols"]).then_inc(got, 16)
            sp.dma_start(k.ident_bf[:], io["masks_bf"][:, 0:P]).then_inc(got, 16)
            sp.dma_start(k.causal_bf[:], io["masks_bf"][:, P:2 * P]).then_inc(got, 16)
            sp.dma_start(k.cmp_bf[:], io["masks_bf"][:, 2 * P:3 * P]).then_inc(got, 16)
            load_blocks(k, sp, RAW_SLOTS)
            sp.wait_ge(got, 96)

        @block.scalar
        def _(act):
            split_hi(k, act, 0)

        @block.vector
        def _(dve):
            split_lo(k, dve, 0)


def stage_norm(k, tag, gain, onto_residual=False):
    nc = k.nc
    sq = k.region(f"{tag}_sq", [P, KD, S], F32, 0)
    root = k.region(f"{tag}_root", [P, S], F32, 16)
    inv = k.region(f"{tag}_inv", [P, S], F32, 18)
    sq_done, ms_done, root_done = k.sem(f"{tag}_sq_done"), k.sem(f"{tag}_ms_done"), k.sem(f"{tag}_root_done")
    h_done, hi_done, inv_done = k.sem(f"{tag}_h_done"), k.sem(f"{tag}_hi_done"), k.sem(f"{tag}_inv_done")
    with nc.Block() as block:
        @block.scalar
        def _(act):
            for i in range(KD):
                act.activation(sq[:, i, :], k.xT[:, i, :], ACT.Square).then_inc(sq_done, 1)
            act.wait_ge(ms_done, 1)
            act.activation(root[:], k.ps[:, 7, :], ACT.Sqrt, bias=k.col("eps6")).then_inc(root_done, 1)
            if not onto_residual:
                for i in range(KD):
                    act.wait_ge(h_done, i + 1)
                    act.activation(k.act_hi[:, i, :], sq[:, i, :], ACT.Copy).then_inc(hi_done, 1)

        @block.tensor
        def _(pe):
            for i in range(KD):
                pe.wait_ge(sq_done, i + 1)
                last = pe.matmul(k.ps[:, 7, :], k.const("mean_ones"), sq[:, i, :], start=(i == 0),
                                 stop=(i == KD - 1))
            last.then_inc(ms_done, 1)

        @block.vector
        def _(dve):
            dve.wait_ge(root_done, 1)
            dve.reciprocal(inv[:], root[:]).then_inc(inv_done, 1)
            dve.wait_ge(inv_done, 1)
            for i in range(KD):
                out = k.xT[:, i, :] if onto_residual else sq[:, i, :]
                dve.scalar_tensor_tensor(out=out, in0=k.xT[:, i, :], scalar=k.col(gain, i), in1=inv[:],
                                         op0=ALU.mult, op1=ALU.mult).then_inc(h_done, 1)
                if not onto_residual and i >= 1:
                    dve.wait_ge(hi_done, i)
                    dve.tensor_tensor(k.act_lo[:, i - 1, :], sq[:, i - 1, :],
                                      k.act_hi[:, i - 1, :].bitcast(F32), ALU.subtract)
            if not onto_residual:
                dve.wait_ge(hi_done, KD)
                dve.tensor_tensor(k.act_lo[:, KD - 1, :], sq[:, KD - 1, :],
                                  k.act_hi[:, KD - 1, :].bitcast(F32), ALU.subtract)


def stage_add(k, tag, b0, b1):
    with k.nc.Block() as block:
        @block.sync
        def _(sp):
            load_blocks(k, sp, b1 + RAW_SLOTS)

        @block.scalar
        def _(act):
            for b in range(b0, b1):
                split_hi(k, act, b + 1)

        @block.tensor
        def _(pe):
            for b, j in tiles_of(b0, b1):
                multiply_tile(k, pe, b, j)

        @block.vector
        def _(dve):
            n = 0
            for b, j in tiles_of(b0, b1):
                if j == 0:
                    split_lo(k, dve, b + 1)
                t = TILE_AT[b] + j
                dve.wait_ge(k.tile_done, t + 1)
                dve.tensor_tensor(k.xT[:, n, :], k.xT[:, n, :], k.ps[:, t % 4, :], ALU.add) \
                    .then_inc(k.evac_done, 1)
                n += 1


def stage_fold(k):
    nc = k.nc
    k.hw = k.region("hw", [P, 3, ML_T, 4], F32, 84)
    hwt = k.region("hwt", [P, 3, ML_T, 4], F32, 60)
    wif = k.region("wif", [P, 3, ML_T, 8], F32, 61)
    wide = k.region("wide", [P, 4, P], F32, 63)
    k.fold = k.region("fold", [P, 2, ML_T, 36], F32, 36)
    got, wide_done, fold_mm, zeroed = k.sem("fold_landed"), k.sem("fold_wide_done"), k.sem("fold_mm"), k.sem("fold_zeroed")
    with nc.Block() as block:
        @block.sync
        def _(sp):
            sp.dma_start(k.hw[:], k.io["hw"]).then_inc(got, 16)
            sp.dma_start(hwt[:], k.io["hwt"]).then_inc(got, 16)
            sp.dma_start(wif[:], k.io["wif"]).then_inc(got, 16)

        @block.gpsimd
        def _(pool):
            pool.wait_ge(got, 48)
            for u in range(3 * ML_T):
                m, t = u % 3, u // 3
                if u >= 4:
                    pool.wait_ge(fold_mm, u - 3)
                widen(k, pool, wide[:, u % 4, :], hwt[:, m, t, :]).then_inc(wide_done, 1)

        @block.tensor
        def _(pe):
            for u in range(3 * ML_T):
                m, t = u % 3, u // 3
                pe.wait_ge(wide_done, u + 1)
                x = 1 if m == 2 else 0
                pe.matmul(k.ps[:, 6 + x, 8 * t:8 * t + 8], wide[:, u % 4, :], wif[:, m, t, :],
                          start=(m != 1), stop=(m != 0)).then_inc(fold_mm, 1)

        @block.vector
        def _(dve):
            dve.memset(k.fold[:], 0.0).then_inc(zeroed, 1)
            dve.wait_ge(zeroed, 1)
            dve.wait_ge(fold_mm, 3 * ML_T)
            for x in range(2):
                sums = k.ps[:, 6 + x, 0:8 * ML_T].rearrange("p (t g) -> p t g", g=8)
                for g in range(2):
                    dve.tensor_copy(k.fold[:, x, :, 32 * g:32 * g + 4], sums[:, :, 4 * g:4 * g + 4])


def widen(k, eng, out, blocks):
    return eng.tensor_tensor(out.rearrange("p (n i) -> p n i", i=4),
                             blocks.rearrange("p (o i) -> p o i", o=1).to_broadcast([P, 32, 4]),
                             k.const("same4", 32).rearrange("p (n o) -> p n o", o=1).to_broadcast([P, 32, 4]),
                             ALU.mult)


def stage_ml_inner(k):
    nc = k.nc
    b0 = first_block("ml_in")
    b1 = b0 + ML_INNER // BLOCK_COLS
    k.xconv = k.region("xconv", [P, ML_T, S], F32, 0)
    xin = k.region("xin", [P, 2, CONV - 1 + S + 1], F32, 42)
    acc = k.region("conv_acc", [P, 2, S], F32, 47)
    wide = k.region("wide_v", [P, 2, P], F32, 51)
    vout = k.region("v_out", [P, 2, TT, P], F32, 52)
    pad_done, xin_ready, conv_done, xconv_ready = (k.sem("pad_done"), k.sem("xin_ready"), k.sem("conv_done"),
                                                   k.sem("xconv_ready"))
    conv_step = k.sem("conv_step")
    wide_done, v_mm, v_copied, gate_mm = k.sem("wide_v_done"), k.sem("v_mm"), k.sem("v_copied"), k.sem("gate_mm")
    k.v_stored = [k.sem(f"v_stored{i}") for i in range(2)]

    def store_v(act, t):
        act.wait_ge(v_copied, t + 1)
        act.dma_start(k.io["v_scratch"][t // 4][:, :, (t % 4) * P:(t % 4 + 1) * P], vout[:, t % 2]) \
            .then_inc(k.v_stored[t % 2], 16)

    def conv_in(t, tap):
        return xin[:, t % 2, tap:tap + S]

    with nc.Block() as block:
        @block.sync
        def _(sp):
            load_blocks(k, sp, b1 + RAW_SLOTS)

        @block.gpsimd
        def _(pool):
            for t in range(ML_T):
                if t >= 2:
                    pool.wait_ge(v_mm, t - 1)
                widen(k, pool, wide[:, t % 2, :], k.hw[:, 2, t, :]).then_inc(wide_done, 1)

        @block.scalar
        def _(act):
            act.wait_ge(pad_done, 1)
            for t in range(ML_T + 1):
                if t < ML_T:
                    if t % 2 == 0:
                        split_hi(k, act, b0 + t // 2 + 1)
                    tile = TILE_AT[b0] + t
                    act.wait_ge(k.tile_done, tile + 1)
                    if t >= 2:
                        act.wait_ge(conv_done, t - 1)
                        act.wait_ge(gate_mm, t - 1)
                    act.activation(xin[:, t % 2, CONV - 1:CONV - 1 + S], k.ps[:, tile % 4, :], ACT.Copy) \
                        .then_inc(xin_ready, 1)
                    act.wait_ge(xin_ready, t + 1)
                    act.sem_inc(k.evac_done, 1)
                if t >= 1:
                    act.wait_ge(conv_done, t)
                    act.activation(k.xconv[:, t - 1, :], acc[:, (t - 1) % 2, :], ACT.Silu).then_inc(xconv_ready, 1)
                if t >= 2:
                    store_v(act, t - 2)
            store_v(act, ML_T - 1)
            for i in range(2):
                act.wait_ge(k.v_stored[i], 16 * ML_T // 2)

        @block.vector
        def _(dve):
            dve.memset(xin[:, :, 0:CONV - 1], 0.0).then_inc(pad_done, 1)
            for t in range(ML_T + 1):
                if t < ML_T:
                    if t % 2 == 0:
                        split_lo(k, dve, b0 + t // 2 + 1)
                    dve.wait_ge(xin_ready, t + 1)
                    if t >= 2:
                        dve.wait_ge(xconv_ready, t - 1)
                    dve.tensor_scalar(acc[:, t % 2, :], conv_in(t, 0), k.col("conv_w", 0 * ML_T + t),
                                      k.col("conv_b", t), ALU.mult, ALU.add).then_inc(conv_step, 1)
                    for tap in range(1, CONV):
                        dve.wait_ge(conv_step, (CONV - 1) * t + tap)
                        dve.scalar_tensor_tensor(out=acc[:, t % 2, :], in0=conv_in(t, tap),
                                                 scalar=k.col("conv_w", tap * ML_T + t), in1=acc[:, t % 2, :],
                                                 op0=ALU.mult, op1=ALU.add) \
                            .then_inc(conv_step if tap < CONV - 1 else conv_done, 1)
                if t >= 1:
                    u = t - 1
                    dve.wait_ge(v_mm, u + 1)
                    if u >= 2:
                        dve.wait_ge(k.v_stored[u % 2], 16 * (u // 2))
                    dve.tensor_copy(vout[:, u % 2].rearrange("p a n -> p (a n)"), k.ps[:, 4 + u % 2, :]) \
                        .then_inc(v_copied, 1)

        @block.tensor
        def _(pe):
            for t in range(ML_T + 1):
                if t < ML_T:
                    multiply_tile(k, pe, b0 + t // 2, t % 2)
                if t >= 1:
                    u = t - 1
                    pe.wait_ge(xin_ready, u + 1)
                    pe.wait_ge(wide_done, u + 1)
                    if u >= 2:
                        pe.wait_ge(v_copied, u - 1)
                    for i in range(TT):
                        last = pe.matmul(k.ps[:, 4 + u % 2, i * P:(i + 1) * P],
                                         xin[:, u % 2, CONV - 1 + i * P:CONV - 1 + (i + 1) * P],
                                         wide[:, u % 2, :], start=True, stop=True)
                    last.then_inc(v_mm, 1)
                    pe.matmul(k.ps[0:36, 6, :], k.fold[:, 1, u, :], xin[:, u % 2, CONV - 1:CONV - 1 + S],
                              start=(u == 0), stop=False)
                    pe.wait_ge(xconv_ready, u + 1)
                    pe.matmul(k.ps[0:36, 6, :], k.fold[:, 0, u, :], k.xconv[:, u, :], start=False,
                              stop=(u == ML_T - 1)).then_inc(gate_mm, 1)


def stage_ml_gate(k):
    nc = k.nc
    b0 = first_block("ml_in") + ML_INNER // BLOCK_COLS
    b1 = b0 + ML_INNER // BLOCK_COLS
    zt = k.region("zt", [P, 4, S], F32, 32)
    rows = k.region("gate_rows", [4, 10, S], F32, 42)
    k.neg_m = k.region("neg_m", [4, S], F32, 86)
    k.g_col = k.small[:, 0:16].rearrange("p (t h) -> p t h", h=4)
    k.floor_col = k.small[:, 16:32].rearrange("p (t h) -> p t h", h=4)
    inp, fg, mag, ex, ln, neg, run, g, top, floor = (rows[:, i, :] for i in range(10))
    k.z_stored = [k.sem(f"z_stored{i}") for i in range(4)]
    z_ready, a_step, d_step, g_tr, g_out = (k.sem("z_ready"), k.sem("gate_act_step"), k.sem("gate_dve_step"),
                                            k.sem("g_transposed"), k.sem("g_out"))
    zeros = k.sem("gate_zeros")
    zero, one = rows[:, 3, :], rows[:, 2, :]
    with nc.Block() as block:
        @block.sync
        def _(sp):
            load_blocks(k, sp, b1 + RAW_SLOTS)

        @block.scalar
        def _(act):
            f32r = slice(32, 36)
            act.activation(inp, k.ps[0:4, 6, :], ACT.Identity, bias=k.col("b_if", rows=slice(0, 4))).then_inc(a_step, 1)
            act.activation(fg, k.ps[f32r, 6, :], ACT.Identity, bias=k.col("b_if", rows=f32r)).then_inc(a_step, 1)
            act.wait_ge(a_step, 2)
            act.activation(mag, fg, ACT.Abs).then_inc(a_step, 1)
            act.wait_ge(a_step, 3)
            act.activation(ex, mag, ACT.Exp, scale=-1.0).then_inc(a_step, 1)
            act.wait_ge(a_step, 4)
            act.activation(ln, ex, ACT.Ln, bias=k.col("one", rows=slice(0, 4))).then_inc(a_step, 1)
            act.wait_ge(d_step, 8)
            act.activation(floor, floor, ACT.Exp, scale=-1.0).then_inc(a_step, 1)
            for t in range(ML_T):
                if t % 2 == 0:
                    split_hi(k, act, b0 + t // 2 + 1)
                tile = TILE_AT[b0] + t
                act.wait_ge(k.tile_done, tile + 1)
                if t >= 4:
                    act.wait_ge(k.z_stored[t % 4], 16 * (t // 4))
                act.activation(zt[:, t % 4, :], k.ps[:, tile % 4, :], ACT.Silu).then_inc(z_ready, 1)
                act.wait_ge(z_ready, t + 1)
                act.sem_inc(k.evac_done, 1)
                act.dma_start(k.io["z_scratch"][t], zt[:, t % 4, :]).then_inc(k.z_stored[t % 4], 16)
            for i in range(4):
                act.wait_ge(k.z_stored[i], 16 * ML_T // 4)

        @block.vector
        def _(dve):
            dve.wait_ge(a_step, 5)
            dve.memset(zero, 0.0).then_inc(d_step, 1)
            dve.memset(one, 1.0).then_inc(d_step, 1)
            dve.tensor_scalar(neg, fg, 0.0, None, ALU.min).then_inc(d_step, 1)
            dve.wait_ge(d_step, 3)
            dve.tensor_tensor(neg, neg, ln, ALU.subtract).then_inc(d_step, 1)
            dve.wait_ge(d_step, 4)
            dve.tensor_tensor_scan(run, one, neg, 0.0, ALU.mult, ALU.add).then_inc(d_step, 1)
            dve.wait_ge(d_step, 5)
            dve.tensor_tensor(g, inp, run, ALU.subtract).then_inc(d_step, 1)
            dve.wait_ge(d_step, 6)
            dve.tensor_tensor_scan(top, g, zero, 0.0, ALU.max, ALU.max).then_inc(d_step, 1)
            dve.wait_ge(d_step, 7)
            dve.tensor_tensor(floor, run, top, ALU.add).then_inc(d_step, 1)
            dve.tensor_scalar(k.neg_m[:], top, -1.0, None, ALU.mult)
            for t in range(0, ML_T, 2):
                split_lo(k, dve, b0 + t // 2 + 1)
                if t == 2:
                    dve.wait_ge(g_tr, 2)
                    dve.tensor_copy(k.small[:, 0:32], k.ps[:, 7, 0:32]).then_inc(g_out, 1)

        @block.tensor
        def _(pe):
            for t in range(ML_T):
                multiply_tile(k, pe, b0 + t // 2, t % 2)
                if t == 1:
                    pe.wait_ge(a_step, 6)
                    pe.wait_ge(d_step, 8)
                    for n, row in enumerate((g, floor)):
                        for i in range(TT):
                            c = 16 * n + 4 * i
                            last = pe.transpose(k.ps[:, 7, c:c + 4], row[:, i * P:(i + 1) * P],
                                                k.const("ident")[0:4, 0:4])
                        last.then_inc(g_tr, 1)


def stage_ml_heads(k, first):
    nc = k.nc
    tag = f"ml{first}"
    v = k.region(f"{tag}_v", [P, TT, S], F32, 32)
    q = k.region(f"{tag}_q", [P, TT, S], F32, 40)
    kk = k.region(f"{tag}_k", [P, TT, S], F32, 48)
    st = k.region(f"{tag}_st", [P, TT, S], F32, 56)
    wexp = k.region(f"{tag}_wexp", [P, 2, S], F32, 64)
    z = k.region(f"{tag}_z", [P, 2, S], F32, 68)
    wide = k.region(f"{tag}_wide", [P, 2, 2, P], F32, 72)
    y = k.region(f"{tag}_y", [P, 2, S], F32, 74)
    sc = k.small
    den, adn, r, sd, scale, shift = (sc[:, 32 + 4 * i:36 + 4 * i] for i in range(6))
    stats = sc[:, 64:64 + 24].rearrange("p (t s) -> p t s", s=6)
    mv = sc[:, 96:104].rearrange("p (t s) -> p t s", s=2)
    r2v = sc[:, 104:108]
    s = {n: k.sem(f"{tag}_{n}") for n in ("v_landed", "wide_done", "qk_mm", "q_copied", "k_copied", "nm_mm", "sc_mm",
                                          "wexp_raw", "wexp_done", "st_done", "h_mm", "hn_done", "tr_mm", "y_read",
                                          "y_done", "y_hi", "y_lo", "step", "r2v_done", "sd_done", "scale_done", "t1")}
    zl = [k.sem(f"{tag}_z_landed{i}") for i in range(2)]
    heads = range(2)

    def lo(dve, u):
        dve.wait_ge(s["y_hi"], u + 1)
        dve.tensor_tensor(k.act_lo[:, u, :], y[:, u % 2, :], k.act_hi[:, u, :].bitcast(F32), ALU.subtract) \
            .then_inc(s["y_lo"], 1)

    with nc.Block() as block:
        @block.sync
        def _(sp):
            for h in heads:
                if h:
                    sp.wait_ge(s["h_mm"], TT * h)
                sp.dma_start(v[:], k.io["v_scratch"][first + h]).then_inc(s["v_landed"], 16)
                for c in range(TT):
                    u = TT * h + c
                    if u >= 2:
                        sp.wait_ge(s["y_done"], u - 1)
                    sp.dma_start(z[:, c % 2, :], k.io["z_scratch"][TT * (first + h) + c]).then_inc(zl[c % 2], 16)

        @block.gpsimd
        def _(pool):
            for h in heads:
                for c in range(TT):
                    u = TT * h + c
                    if u >= 2:
                        pool.wait_ge(s["qk_mm"], u - 1)
                    t = TT * (first + h) + c
                    widen(k, pool, wide[:, c % 2, 0, :], k.hw[:, 0, t, :]).then_inc(s["wide_done"], 1)
                    widen(k, pool, wide[:, c % 2, 1, :], k.hw[:, 1, t, :]).then_inc(s["wide_done"], 1)
                for j in range(TT):
                    pool.wait_ge(s["wexp_raw"], TT * h + j + 1)
                    part = wexp[:, j % 2, j * P:(j + 1) * P]
                    pool.affine_select(out=part, in_=part, compare_op=ALU.is_ge, fill=0.0, base=0,
                                       pattern=[[1, P]], channel_multiplier=-1).then_inc(s["wexp_done"], 1)

        @block.tensor
        def _(pe):
            for h in heads:
                if h:
                    pe.wait_ge(s["y_read"], TT * h)
                for c in range(TT):
                    u = TT * h + c
                    pe.wait_ge(s["wide_done"], 2 * u + 2)
                    if u:
                        pe.wait_ge(s["q_copied"], u)
                        pe.wait_ge(s["k_copied"], u)
                    x = k.xconv[:, TT * (first + h) + c, :]
                    pe.matmul(k.ps[:, 4, :], wide[:, c % 2, 0, :], x, start=True, stop=True)
                    pe.matmul(k.ps[:, 5, :], wide[:, c % 2, 1, :], x, start=True, stop=True).then_inc(s["qk_mm"], 1)
                pe.matmul(k.ps[:, 6, :], k.const("sel", 512)[0:4, (first + h) * P:(first + h + 1) * P], k.neg_m[:],
                          start=True, stop=True).then_inc(s["nm_mm"], 1)
                pe.wait_ge(s["q_copied"], TT * (h + 1))
                pe.wait_ge(s["k_copied"], TT * (h + 1))
                for j in range(TT):
                    if j >= 2:
                        pe.wait_ge(s["st_done"], TT * h + j - 1)
                    for c in range(TT):
                        last = pe.matmul(k.ps[:, 4 + j % 2, j * P:S], kk[:, c, j * P:(j + 1) * P], q[:, c, j * P:S],
                                         start=(c == 0), stop=(c == TT - 1))
                    last.then_inc(s["sc_mm"], 1)
                pe.wait_ge(s["v_landed"], 16 * (h + 1))
                if h:
                    pe.wait_ge(s["hn_done"], TT * h)
                for i in range(TT):
                    pe.wait_ge(s["st_done"], TT * h + i + 1)
                    for j in range(i + 1):
                        lhs = st[:, j, i * P:(i + 1) * P]
                        pe.matmul(k.ps[:, i, :], lhs, v[:, j, :], start=(j == 0), stop=(j == i))
                        last = pe.matmul(k.ps[:, 7, i:i + 1], lhs, k.const("ones")[:, 0:1], start=(j == 0), stop=(j == i))
                    last.then_inc(s["h_mm"], 1)
                pe.wait_ge(s["hn_done"], TT * (h + 1))
                for c in range(TT):
                    if c >= 2:
                        pe.wait_ge(s["y_read"], TT * h + c - 1)
                    for i in range(TT):
                        last = pe.transpose(k.ps[:, 4 + c % 2, i * P:(i + 1) * P], kk[:, i, c * P:(c + 1) * P],
                                            k.const("ident"))
                    last.then_inc(s["tr_mm"], 1)

        @block.scalar
        def _(act):
            for h in heads:
                for c in range(TT):
                    act.wait_ge(s["qk_mm"], TT * h + c + 1)
                    act.activation(q[:, c, :], k.ps[:, 4, :], ACT.Copy).then_inc(s["q_copied"], 1)
                act.wait_ge(s["nm_mm"], h + 1)
                for j in range(TT):
                    u = TT * h + j
                    if u >= 2:
                        act.wait_ge(s["st_done"], u - 1)
                    act.activation(wexp[:, j % 2, j * P:S], k.ps[:, 6, j * P:S], ACT.Exp,
                                   bias=k.g_col[:, j, first + h:first + h + 1]).then_inc(s["wexp_raw"], 1)
                act.wait_ge(s["r2v_done"], h + 1)
                act.activation(sd, r2v, ACT.Sqrt, bias=k.col("eps6")).then_inc(s["sd_done"], 1)
                act.wait_ge(s["scale_done"], h + 1)
                for i in range(TT):
                    act.activation(kk[:, i, :], k.ps[:, i, :], ACT.Identity, scale=scale[:, i:i + 1],
                                   bias=shift[:, i:i + 1]).then_inc(s["hn_done"], 1)
                for c in range(TT):
                    u = TT * h + c
                    act.wait_ge(s["y_done"], u + 1)
                    act.activation(k.act_hi[:, u, :], y[:, c % 2, :], ACT.Copy).then_inc(s["y_hi"], 1)

        @block.vector
        def _(dve):
            step = [0]

            def then_wait(ins):
                step[0] += 1
                ins.then_inc(s["step"], 1)
                dve.wait_ge(s["step"], step[0])

            for h in heads:
                for c in range(TT):
                    dve.wait_ge(s["qk_mm"], TT * h + c + 1)
                    dve.tensor_copy(kk[:, c, :], k.ps[:, 5, :]).then_inc(s["k_copied"], 1)
                for j in range(TT):
                    u = TT * h + j
                    dve.wait_ge(s["sc_mm"], u + 1)
                    dve.wait_ge(s["wexp_done"], u + 1)
                    dve.scalar_tensor_tensor(out=st[:, j, j * P:S], in0=k.ps[:, 4 + j % 2, j * P:S],
                                             scalar=ML_DH ** -0.5, in1=wexp[:, j % 2, j * P:S],
                                             op0=ALU.mult, op1=ALU.mult).then_inc(s["st_done"], 1)
                for i in range(TT):
                    dve.wait_ge(s["h_mm"], TT * h + i + 1)
                    then_wait(dve.bn_stats(stats[:, i, :], k.ps[:, i, :]))
                    then_wait(dve.bn_aggr(mv[:, i, :], stats[:, i, :]))
                floor = k.floor_col[:, :, first + h]
                then_wait(dve.tensor_copy(den, k.ps[:, 7, 0:TT]))
                then_wait(dve.scalar_tensor_tensor(out=adn, in0=den, scalar=-1.0, in1=den, op0=ALU.mult, op1=ALU.max))
                then_wait(dve.tensor_tensor(adn, adn, floor, ALU.max))
                then_wait(dve.reciprocal(r, adn))
                then_wait(dve.tensor_tensor(r2v, mv[:, :, 1], r, ALU.mult))
                dve.tensor_tensor(r2v, r2v, r, ALU.mult).then_inc(s["r2v_done"], 1)
                dve.wait_ge(s["sd_done"], h + 1)
                then_wait(dve.reciprocal(sd, sd))
                then_wait(dve.tensor_tensor(scale, sd, r, ALU.mult))
                dve.scalar_tensor_tensor(out=shift, in0=mv[:, :, 0], scalar=-1.0, in1=scale, op0=ALU.mult,
                                         op1=ALU.mult).then_inc(s["scale_done"], 1)
                for c in range(TT):
                    u = TT * h + c
                    t = TT * (first + h) + c
                    x = k.xconv[:, t, :]
                    if u >= 2:
                        dve.wait_ge(s["y_lo"], u - 1)
                    then_wait(dve.tensor_scalar(y[:, c % 2, :], x, k.col("skip", t), None, ALU.mult))
                    dve.wait_ge(s["tr_mm"], u + 1)
                    dve.scalar_tensor_tensor(out=y[:, c % 2, :], in0=k.ps[:, 4 + c % 2, :], scalar=k.col("ml_ln_w", t),
                                             in1=y[:, c % 2, :], op0=ALU.mult, op1=ALU.add).then_inc(s["y_read"], 1)
                    dve.wait_ge(s["y_read"], u + 1)
                    dve.wait_ge(zl[c % 2], 16 * (u // 2 + 1))
                    dve.tensor_tensor(y[:, c % 2, :], y[:, c % 2, :], z[:, c % 2, :], ALU.mult).then_inc(s["y_done"], 1)
                    if c:
                        lo(dve, u - 1)
                lo(dve, TT * h + TT - 1)


class Steps:

    def __init__(self, sem):
        self.sem, self.n = sem, 0

    def then_wait(self, eng, ins):
        self.n += 1
        ins.then_inc(self.sem, 1)
        eng.wait_ge(self.sem, self.n)


def stage_nsa_in(k):
    nc = k.nc
    b0 = first_block("nsa_in")
    b1 = first_block("nsa_out")
    k.q = k.region("nsa_q", [P, 8, S], F32, 0)
    k.kv = k.region("nsa_kv", [P, 12, S], F32, 16)
    k.gate_rows = k.region("nsa_gates", [48, S], F32, 40)
    k.w1 = [k.region(f"cmp_w1_{i}", [P, CMP_BLOCK, P], F32, 42 + 16 * i) for i in range(2)]
    k.cmp_small = k.region("cmp_small", [P, 2 * 32 + 2 * 64], F32, 74)
    zt = k.region("nsa_zt", [P, 4, S], F32, 76)
    landed = k.sem("nsa_landed")
    z_ready, plain = k.sem("nsa_z_ready"), k.sem("nsa_plain")
    stored = [k.sem(f"nsa_z_stored{i}") for i in range(4)]
    with nc.Block() as block:
        @block.sync
        def _(sp):
            for i in range(2):
                sp.dma_start(k.w1[i][:], k.io["cmp_w1"][:, i]).then_inc(landed, 16)
            sp.dma_start(k.cmp_small[:], k.io["cmp_small"]).then_inc(landed, 16)
            load_blocks(k, sp, b1 + RAW_SLOTS)
            sp.wait_ge(landed, 48)

        @block.scalar
        def _(act):
            for t, (b, j) in enumerate(tiles_of(b0, b1)):
                if j == 0:
                    split_hi(k, act, b + 1)
                tile = TILE_AT[b] + j
                act.wait_ge(k.tile_done, tile + 1)
                bank = k.ps[:, tile % 4, :]
                if t < 20:
                    out = k.q[:, t, :] if t < 8 else k.kv[:, t - 8, :]
                    act.activation(out, bank, ACT.Copy).then_inc(k.evac_done, 1)
                elif t < 28:
                    z = t - 20
                    if z >= 4:
                        act.wait_ge(stored[z % 4], 16)
                    act.activation(zt[:, z % 4, :], bank, ACT.Silu).then_inc(z_ready, 1)
                    act.wait_ge(z_ready, z + 1)
                    act.sem_inc(k.evac_done, 1)
                    act.dma_start(k.io["z_scratch"][z], zt[:, z % 4, :]).then_inc(stored[z % 4], 16)
                else:
                    act.activation(k.gate_rows[:], bank[0:48], ACT.Sigmoid, bias=k.col("b_gate", rows=slice(0, 48))) \
                        .then_inc(k.evac_done, 1)
            for i in range(4):
                act.wait_ge(stored[i], 32)

        @block.tensor
        def _(pe):
            for b, j in tiles_of(b0, b1):
                multiply_tile(k, pe, b, j)

        @block.vector
        def _(dve):
            for b in range(b0, b1):
                split_lo(k, dve, b + 1)


def stage_nsa_prep(k):
    nc = k.nc
    k.vtok = k.region("nsa_vtok", [P, 2, TT, 256], F32, 76)
    k.gtok = k.region("nsa_gtok", [P, TT, 48], F32, 84)
    k.kcmp = k.region("kcmp", [P, 2, 32], F32, 84.75)
    k.vcmp = k.region("vcmp", [P, 4, 4, DK], F32, 85)
    hid = k.region("cmp_hid", [P, 2, 2, 2, 31], F32, 89)
    peb = k.small[:, 0:2]
    k.q_rot = k.at("q_rot", [P, 8, S], F32, 28)
    turned = k.at("turned", [P, 2, S], F32, 44)
    straight = k.at("straight", [P, 2, S], F32, 48)
    s = {n: k.sem(f"prep_{n}") for n in ("rot_mm", "rot_read", "straight", "turned", "done", "tr", "tr_read", "hid_mm",
                                         "pe_mm", "pe_read", "hid_done", "cmp_mm", "cmp_read", "zeroed", "v_mm")}
    pairs = [(k.q, i, k.q_rot, i) for i in range(8)] + [(k.kv, i, k.kv, i) for i in (4, 5, 8, 9)]
    w2 = k.cmp_small[:, 64:192].rearrange("p (x d) -> p x d", d=DK)
    pe_t = k.cmp_small[:, 0:64].rearrange("p (x t) -> p x t", t=CMP_BLOCK)
    with nc.Block() as block:
        @block.tensor
        def _(pe):
            for n in range(5):
                if n >= 2:
                    pe.wait_ge(s["tr_read"], n - 1)
                for i in range(TT):
                    if n < 4:
                        last = pe.transpose(k.ps[:, n % 2, i * P:(i + 1) * P],
                                            k.kv[:, 6 + 4 * (n // 2) + n % 2, i * P:(i + 1) * P], k.const("ident"))
                    else:
                        last = pe.transpose(k.ps[:, 0, i * 48:(i + 1) * 48], k.gate_rows[:, i * P:(i + 1) * P],
                                            k.const("ident")[0:48, 0:48])
                last.then_inc(s["tr"], 1)
            for x in range(2):
                for half in range(2):
                    rows = slice(64 * half, 64 * half + 64)
                    for t in range(CMP_BLOCK):
                        src = k.kv[rows, 2 * x:2 * x + 2, t:t + (N_CMP - 1) * CMP_STRIDE + 1:CMP_STRIDE]
                        c = x * 64
                        last = pe.matmul(k.ps[:, 2 + half, c:c + 2 * N_CMP].rearrange("p (a n) -> p a n", n=N_CMP),
                                         k.w1[x][rows, t, :], src, start=(t == 0), stop=(t == CMP_BLOCK - 1))
                for t in range(CMP_BLOCK):
                    last = pe.matmul(k.ps[:, 2, 128 + x:129 + x], k.w1[x][0:64, t, :], pe_t[0:64, x, t:t + 1],
                                     start=(t == 0), stop=(t == CMP_BLOCK - 1))
                last.then_inc(s["hid_mm"], 1)
            for n, (src, i, _, _) in enumerate(pairs):
                if n >= 2:
                    pe.wait_ge(s["rot_read"], n - 1)
                pe.matmul(k.ps[:, 4 + n % 2, :], k.const("rot"), src[:, i, :], start=True, stop=True) \
                    .then_inc(s["rot_mm"], 1)
            pe.wait_ge(s["hid_done"], 4)
            for half in range(2):
                rows = slice(64 * half, 64 * half + 64)
                for gp in range(2):
                    pe.matmul(k.ps[rows, 6, 32 * gp:32 * gp + N_CMP], w2[:, 0, :], hid[:, 0, half, gp, :],
                              start=True, stop=True)
            for hh in range(4):
                for g in range(4):
                    last = pe.matmul(k.ps[32 * hh:32 * hh + N_CMP, 7, g * DK:(g + 1) * DK], hid[:, 1, g % 2, g // 2, :],
                                     w2[:, 1, :], start=True, stop=True)
            last.then_inc(s["v_mm"], 1)

        @block.scalar
        def _(act):
            act.wait_ge(s["pe_read"], 1)
            for x in range(2):
                for half in range(2):
                    c = x * 64
                    act.activation(hid[:, x, half], k.ps[:, 2 + half, c:c + 2 * N_CMP].rearrange("p (a n) -> p a n", n=N_CMP),
                                   ACT.Silu, bias=peb[:, x:x + 1]).then_inc(s["hid_done"], 1)

        @block.gpsimd
        def _(pool):
            pool.memset(k.vcmp[:], 0.0).then_inc(s["zeroed"], 1)
            for n, (src, i, _, _) in enumerate(pairs):
                if n >= 2:
                    pool.wait_ge(s["done"], n - 1)
                pool.tensor_tensor(straight[:, n % 2, :], src[:, i, :], k.const("cos", S), ALU.mult) \
                    .then_inc(s["straight"], 1)

        @block.vector
        def _(dve):
            for n in range(4):
                dve.wait_ge(s["tr"], n + 1)
                dve.tensor_copy(k.vtok[:, n // 2, :, n % 2 * P:(n % 2 + 1) * P],
                                k.ps[:, n % 2, :].rearrange("p (t c) -> p t c", c=P)).then_inc(s["tr_read"], 1)
            dve.wait_ge(s["tr"], 5)
            dve.tensor_copy(k.gtok[:].rearrange("p t c -> p (t c)"), k.ps[:, 0, 0:192])
            dve.wait_ge(s["hid_mm"], 2)
            dve.tensor_copy(peb, k.ps[:, 2, 128:130]).then_inc(s["pe_read"], 1)
            for n, (src, i, dst, o) in enumerate(pairs):
                dve.wait_ge(s["rot_mm"], n + 1)
                if n >= 2:
                    dve.wait_ge(s["done"], n - 1)
                dve.tensor_tensor(turned[:, n % 2, :], k.ps[:, 4 + n % 2, :], k.const("sin", S), ALU.mult) \
                    .then_inc(s["rot_read"], 1)
                dve.wait_ge(s["rot_read"], n + 1)
                dve.wait_ge(s["straight"], n + 1)
                dve.tensor_tensor(dst[:, o, :], turned[:, n % 2, :], straight[:, n % 2, :], ALU.add) \
                    .then_inc(s["done"], 1)
            dve.wait_ge(s["v_mm"], 1)
            dve.tensor_copy(k.kcmp[:, :, 0:N_CMP], k.ps[:, 6, 0:64].rearrange("p (a n) -> p a n", n=32)[:, :, 0:N_CMP])
            dve.wait_ge(s["zeroed"], 1)
            for hh in range(4):
                rows = slice(32 * hh, 32 * hh + N_CMP)
                dve.tensor_copy(k.vcmp[rows, :, hh, :], k.ps[rows, 7, 0:256].rearrange("p (g d) -> p g d", d=DK))


def stage_nsa_cmp(k):
    nc = k.nc
    k.o = k.region("nsa_o", [P, TT, NSA_HEADS * DK], F32, 42)
    p = k.region("cmp_p", [P, 2, NSA_HEADS, 32], F32, 58)
    pt = k.region("cmp_pt", [P, 2, 4, P], F32, 62)
    top = k.small[:, 8:24]
    total = k.small[:, 24:40]
    weight = k.small[:, 40:56]
    s = {n: k.sem(f"cmp_{n}") for n in ("zeroed", "sc_mm", "p_ready", "exp_done", "tr_mm", "tr_read", "pv_mm", "o_done",
                                        "step")}
    with nc.Block() as block:
        @block.tensor
        def _(pe):
            for i in range(TT):
                if i:
                    pe.wait_ge(s["p_ready"], i)
                mask = k.cmp_bf[:, 32 * i:32 * i + N_CMP].rearrange("p (o c) -> p o c", o=1).to_broadcast([P, 8, N_CMP])
                for par in range(2):
                    bank = k.ps[:, par, 0:256].rearrange("p (h c) -> p h c", c=32)[:, :, 0:N_CMP]
                    pe.matmul(bank, k.ident_bf[:], mask, start=True, stop=False)
                for a in range(8):
                    for par in range(2):
                        rows = slice(64 * par, 64 * par + 64)
                        last = pe.matmul(k.ps[:, par, 32 * a:32 * a + N_CMP], k.q[rows, a, i * P:(i + 1) * P],
                                         k.kcmp[rows, a // 4, 0:N_CMP], start=False, stop=(a == 7))
                last.then_inc(s["sc_mm"], 1)
                pe.wait_ge(s["exp_done"], i + 1)
                if i:
                    pe.wait_ge(s["tr_read"], i)
                for g in range(4):
                    at = 8 * (g % 2) + 4 * (g // 2)
                    last = pe.transpose(k.ps[:, 2, g * P:(g + 1) * P],
                                        p[:, i % 2, at:at + 4, :].rearrange("p h c -> p (h c)"), k.const("ident"))
                last.then_inc(s["tr_mm"], 1)
                pe.wait_ge(s["tr_read"], i + 1)
                if i:
                    pe.wait_ge(s["o_done"], i)
                for g in range(4):
                    last = pe.matmul(k.ps[:, 4 + g // 2, g % 2 * 256:g % 2 * 256 + 256], pt[:, i % 2, g, :],
                                     k.vcmp[:, g].rearrange("p h d -> p (h d)"), start=True, stop=True)
                last.then_inc(s["pv_mm"], 1)

        @block.scalar
        def _(act):
            for i in range(TT):
                act.wait_ge(s["p_ready"], i + 1)
                x = p[:, i % 2, :, 0:N_CMP]
                act.activation(x, x, ACT.Exp, scale=DK ** -0.5).then_inc(s["exp_done"], 1)

        @block.vector
        def _(dve):
            steps = Steps(s["step"])
            steps.then_wait(dve, dve.memset(p[:], 0.0))
            for i in range(TT):
                dve.wait_ge(s["sc_mm"], i + 1)
                sc = k.ps[:, 0:2, 0:256].rearrange("p b (h c) -> p b h c", c=32)[:, :, :, 0:N_CMP]
                steps.then_wait(dve, dve.tensor_reduce(top.rearrange("p (b h) -> p b h", b=2), sc, AX, ALU.max))
                if i >= 2:
                    dve.wait_ge(s["tr_mm"], i - 1)
                dve.tensor_tensor(p[:, i % 2, :, 0:N_CMP].rearrange("p (b h) c -> p b h c", b=2), sc,
                                  top.rearrange("p (b h o) -> p b h o", b=2, o=1).to_broadcast([P, 2, 8, N_CMP]),
                                  ALU.subtract).then_inc(s["p_ready"], 1)
                dve.wait_ge(s["exp_done"], i + 1)
                steps.then_wait(dve, dve.tensor_reduce(total, p[:, i % 2, :, 0:N_CMP], AX, ALU.add))
                steps.then_wait(dve, dve.reciprocal(total, total))
                gates = k.gtok[:, i, :].rearrange("p (a b h c) -> p b a h c", a=2, b=2, c=3)[:, :, :, :, 0]
                v4 = "p (b a h) -> p b a h"
                steps.then_wait(dve, dve.tensor_tensor(weight.rearrange(v4, b=2, a=2), total.rearrange(v4, b=2, a=2),
                                                       gates, ALU.mult))
                if i == 0:
                    steps.then_wait(dve, dve.tensor_scalar(weight, weight, k.col("cmp_any"), None, ALU.mult))
                dve.wait_ge(s["tr_mm"], i + 1)
                dve.tensor_copy(pt[:, i % 2].rearrange("p g t -> p (g t)"), k.ps[:, 2, :]).then_inc(s["tr_read"], 1)
                dve.wait_ge(s["pv_mm"], i + 1)
                for g in range(4):
                    at = 8 * (g % 2) + 4 * (g // 2)
                    last = dve.tensor_tensor(k.o[:, i, 256 * g:256 * g + 256].rearrange("p (h d) -> p h d", d=DK),
                                             k.ps[:, 4 + g // 2, g % 2 * 256:g % 2 * 256 + 256]
                                             .rearrange("p (h d) -> p h d", d=DK),
                                             weight[:, at:at + 4].rearrange("p (h o) -> p h o", o=1)
                                             .to_broadcast([P, 4, DK]), ALU.mult)
                last.then_inc(s["o_done"], 1)


def stage_nsa_attention(k):
    nc = k.nc
    p = k.region("att_p", [P, 2, 2, S], F32, 58)
    pt = k.region("att_pt", [P, 2, 2, S], F32, 66)
    part = k.region("att_part", [P, 2, P], F32, 74)
    s = {n: k.sem(f"att_{n}") for n in ("sc_mm", "nm_done", "exp_done", "tr_mm", "pt0", "pt1", "pv_mm", "part", "o_done",
                                        "step", "w_done")}
    units = [(br, g, i, pr) for br in range(2) for g in range(4) for i in range(TT) for pr in range(2)]
    U = len(units)

    def length(n):
        return (units[n][2] + 1) * P

    def sm(base, n):
        return k.small[:, base + 2 * (n % 4):base + 2 * (n % 4) + 2]

    with nc.Block() as block:
        @block.tensor
        def _(pe):
            for n in range(U + 2):
                if n < U:
                    br, g, i, pr = units[n]
                    rows = slice(64 * (g % 2), 64 * (g % 2) + 64)
                    L = length(n)
                    if n >= 2:
                        pe.wait_ge(s["exp_done"], 2 * (n - 1))
                    for e in range(2):
                        bank = 2 * (n % 2) + e
                        pe.matmul(k.ps[:, bank, 0:L], k.q_rot[rows, g // 2 * 4 + 2 * pr + e, i * P:(i + 1) * P],
                                  k.kv[rows, 4 + 4 * br + g // 2, 0:L], start=True, stop=False)
                        last = pe.matmul(k.ps[:, bank, i * P:L], k.ident_bf[:], k.causal_bf[:], start=False, stop=True)
                    last.then_inc(s["sc_mm"], 1)
                if 1 <= n <= U:
                    m = n - 1
                    i = units[m][2]
                    for e in range(2):
                        pe.wait_ge(s["exp_done"], 2 * m + e + 1)
                        if m:
                            pe.wait_ge(s[f"pt{e}"], m)
                        for j in range(i + 1):
                            last = pe.transpose(k.ps[:, 4 + e, j * P:(j + 1) * P], p[:, m % 2, e, j * P:(j + 1) * P],
                                                k.const("ident"))
                        last.then_inc(s["tr_mm"], 1)
                if n >= 2:
                    m = n - 2
                    br, g, i, pr = units[m]
                    if m >= 2:
                        pe.wait_ge(s["part"], m - 1)
                    for e in range(2):
                        pe.wait_ge(s[f"pt{e}"], m + 1)
                        for j in range(i + 1):
                            last = pe.matmul(k.ps[:, 6 + m % 2, e * DK:(e + 1) * DK], pt[:, m % 2, e, j * P:(j + 1) * P],
                                             k.vtok[:, br, j, g * DK:(g + 1) * DK], start=(j == 0), stop=(j == i))
                    last.then_inc(s["pv_mm"], 1)

        @block.scalar
        def _(act):
            for n in range(U + 1):
                if n < U:
                    L = length(n)
                    act.wait_ge(s["nm_done"], n + 1)
                    if n >= 4:
                        act.wait_ge(s["w_done"], n - 3)
                    for e in range(2):
                        if n >= 2:
                            act.wait_ge(s["tr_mm"], 2 * (n - 2) + e + 1)
                        act.activation(p[:, n % 2, e, 0:L], k.ps[:, 2 * (n % 2) + e, 0:L], ACT.Exp,
                                       bias=sm(0, n)[:, e:e + 1], scale=DK ** -0.5,
                                       accum_out=sm(8, n)[:, e:e + 1]).then_inc(s["exp_done"], 1)
                if n >= 1:
                    m = n - 1
                    L = length(m)
                    act.wait_ge(s["tr_mm"], 2 * m + 2)
                    if m >= 2:
                        act.wait_ge(s["pv_mm"], m - 1)
                    act.activation(pt[:, m % 2, 1, 0:L], k.ps[:, 5, 0:L], ACT.Copy).then_inc(s["pt1"], 1)

        @block.vector
        def _(dve):
            steps = Steps(s["step"])
            for n in range(U + 2):
                if n < U:
                    L = length(n)
                    dve.wait_ge(s["sc_mm"], n + 1)
                    if n >= 4:
                        dve.wait_ge(s["exp_done"], 2 * (n - 3))
                    bank = 2 * (n % 2)
                    steps.then_wait(dve, dve.tensor_reduce(sm(16, n), k.ps[:, bank:bank + 2, 0:L], AX, ALU.max))
                    dve.tensor_scalar(sm(0, n), sm(16, n), -DK ** -0.5, None, ALU.mult).then_inc(s["nm_done"], 1)
                if 1 <= n <= U:
                    m = n - 1
                    L = length(m)
                    dve.wait_ge(s["tr_mm"], 2 * m + 1)
                    if m >= 2:
                        dve.wait_ge(s["pv_mm"], m - 1)
                    dve.tensor_copy(pt[:, m % 2, 0, 0:L], k.ps[:, 4, 0:L]).then_inc(s["pt0"], 1)
                if n >= 2:
                    m = n - 2
                    br, g, i, pr = units[m]
                    h = 4 * g + 2 * pr
                    dve.wait_ge(s["exp_done"], 2 * m + 2)
                    steps.then_wait(dve, dve.reciprocal(sm(24, m), sm(8, m)))
                    gates = k.gtok[:, i, :].rearrange("p (h b) -> p h b", b=3)[:, h:h + 2, 1 + br]
                    dve.tensor_tensor(sm(32, m), sm(24, m), gates, ALU.mult).then_inc(s["w_done"], 1)
                    dve.wait_ge(s["w_done"], m + 1)
                    dve.wait_ge(s["pv_mm"], m + 1)
                    if m >= 2:
                        dve.wait_ge(s["o_done"], m - 1)
                    dve.tensor_tensor(part[:, m % 2, :].rearrange("p (h d) -> p h d", d=DK),
                                      k.ps[:, 6 + m % 2, 0:P].rearrange("p (h d) -> p h d", d=DK),
                                      sm(32, m).rearrange("p (h o) -> p h o", o=1).to_broadcast([P, 2, DK]),
                                      ALU.mult).then_inc(s["part"], 1)
                    dve.wait_ge(s["part"], m + 1)
                    o = k.o[:, i, h * DK:(h + 2) * DK]
                    dve.tensor_tensor(o, o, part[:, m % 2, :], ALU.add).then_inc(s["o_done"], 1)


def stage_nsa_gate(k):
    nc = k.nc
    z = k.region("nsag_z", [P, 4, S], F32, 58)
    y = k.region("nsag_y", [P, 2, S], F32, 66)
    zl = [k.sem(f"nsag_z{i}") for i in range(4)]
    tr, y_done, y_hi, y_lo = k.sem("nsag_tr"), k.sem("nsag_y_done"), k.sem("nsag_y_hi"), k.sem("nsag_y_lo")
    with nc.Block() as block:
        @block.sync
        def _(sp):
            for n in range(8):
                if n >= 4:
                    sp.wait_ge(y_done, n - 3)
                sp.dma_start(z[:, n % 4, :], k.io["z_scratch"][n]).then_inc(zl[n % 4], 16)

        @block.tensor
        def _(pe):
            for n in range(8):
                if n >= 2:
                    pe.wait_ge(y_done, n - 1)
                for i in range(TT):
                    last = pe.transpose(k.ps[:, n % 2, i * P:(i + 1) * P], k.o[:, i, n * P:(n + 1) * P], k.const("ident"))
                last.then_inc(tr, 1)

        @block.scalar
        def _(act):
            for n in range(8):
                act.wait_ge(y_done, n + 1)
                act.activation(k.act_hi[:, n, :], y[:, n % 2, :], ACT.Copy).then_inc(y_hi, 1)

        @block.vector
        def _(dve):
            for n in range(9):
                if n < 8:
                    dve.wait_ge(tr, n + 1)
                    dve.wait_ge(zl[n % 4], 16 * (n // 4 + 1))
                    if n >= 2:
                        dve.wait_ge(y_lo, n - 1)
                    dve.tensor_tensor(y[:, n % 2, :], k.ps[:, n % 2, :], z[:, n % 4, :], ALU.mult).then_inc(y_done, 1)
                if n >= 1:
                    dve.wait_ge(y_hi, n)
                    dve.tensor_tensor(k.act_lo[:, n - 1, :], y[:, (n - 1) % 2, :], k.act_hi[:, n - 1, :].bitcast(F32),
                                      ALU.subtract).then_inc(y_lo, 1)


GATE_T = 16
DA_T = 12
RW_ALL = 15


def stage_in_2(k):
    nc = k.nc
    b0 = first_block("in_2")
    b1 = first_block("mix_o")
    k.rw = k.region("rw", [P, RW_ALL, S], F32, 0)
    k.da = k.region("da", [P, DA_T, S], F32, 30)
    zt = k.region("in2_zt", [P, 4, S], F32, 54)
    u = k.region("in2_u", [P, 2, S + 2], F32, 62)
    t1 = k.region("in2_t1", [P, 2, S], F32, 67)
    k.keep = k.region("mu_keep", [P, RW_ALL], F32, 71)
    z_ready, plain = k.sem("in2_z_ready"), k.sem("in2_plain")
    u_ready, pad, keep_done, step, rw_done = (k.sem("in2_u_ready"), k.sem("in2_pad"), k.sem("in2_keep"),
                                              k.sem("in2_step"), k.sem("in2_rw_done"))
    stored = [k.sem(f"in2_stored{i}") for i in range(4)]
    with nc.Block() as block:
        @block.sync
        def _(sp):
            load_blocks(k, sp, b1)

        @block.scalar
        def _(act):
            for t, (b, j) in enumerate(tiles_of(b0, b1)):
                if j == 0 and b + 1 < b1:
                    split_hi(k, act, b + 1)
                tile = TILE_AT[b] + j
                act.wait_ge(k.tile_done, tile + 1)
                bank = k.ps[:, tile % 4, :]
                if t < GATE_T:
                    if t >= 4:
                        act.wait_ge(stored[t % 4], 16 * (t // 4))
                    act.activation(zt[:, t % 4, :], bank, ACT.Sigmoid).then_inc(z_ready, 1)
                    act.wait_ge(z_ready, t + 1)
                    act.sem_inc(k.evac_done, 1)
                    act.dma_start(k.io["z_scratch"][t], zt[:, t % 4, :]).then_inc(stored[t % 4], 16)
                elif t < GATE_T + DA_T:
                    act.activation(k.da[:, t - GATE_T, :], bank, ACT.Copy).then_inc(k.evac_done, 1)
                else:
                    m = t - GATE_T - DA_T
                    if m == 0:
                        act.wait_ge(pad, 2)
                    if m >= 2:
                        act.wait_ge(rw_done, m - 1)
                    act.activation(u[:, m % 2, 1:1 + S], bank, ACT.Copy).then_inc(u_ready, 1)
                    act.wait_ge(u_ready, m + 1)
                    act.sem_inc(k.evac_done, 1)
            for i in range(4):
                act.wait_ge(stored[i], 16 * GATE_T // 4)

        @block.tensor
        def _(pe):
            for b, j in tiles_of(b0, b1):
                multiply_tile(k, pe, b, j)

        @block.vector
        def _(dve):
            steps = Steps(step)
            dve.memset(u[:, :, 0:1], 0.0).then_inc(pad, 1)
            dve.memset(u[:, :, S + 1:S + 2], 0.0).then_inc(pad, 1)
            mp, mn = COLS["mu_prev"], COLS["mu_next"]
            steps.then_wait(dve, dve.tensor_tensor(k.keep[:], k.cols[:, mp:mp + RW_ALL], k.cols[:, mn:mn + RW_ALL],
                                                   ALU.add))
            steps.then_wait(dve, dve.tensor_scalar(k.keep[:], k.keep[:], -1.0, 1.0, ALU.mult, ALU.add))
            for t, (b, j) in enumerate(tiles_of(b0, b1)):
                if j == 0 and b + 1 < b1:
                    split_lo(k, dve, b + 1)
                m = t - GATE_T - DA_T
                if m >= 0:
                    x = u[:, m % 2]
                    dve.wait_ge(u_ready, m + 1)
                    steps.then_wait(dve, dve.tensor_scalar(t1[:, 0], x[:, 1:1 + S], k.keep[:, m:m + 1], None, ALU.mult))
                    steps.then_wait(dve, dve.scalar_tensor_tensor(out=t1[:, 1], in0=x[:, 0:S], scalar=k.col("mu_prev", m),
                                                                  in1=t1[:, 0], op0=ALU.mult, op1=ALU.add))
                    dve.scalar_tensor_tensor(out=k.rw[:, m, :], in0=x[:, 2:2 + S], scalar=k.col("mu_next", m),
                                             in1=t1[:, 1], op0=ALU.mult, op1=ALU.add).then_inc(rw_done, 1)
                    dve.wait_ge(rw_done, m + 1)


def stage_da_prep(k):
    nc = k.nc
    k.da_v = k.region("da_v", [P, TT, S], F32, 54)
    turned = k.region("da_turned", [P, 2, S], F32, 74)
    straight = k.region("da_straight", [P, 2, S], F32, 78)
    prod = k.region("da_prod", [P, 8], F32, 72)
    k.neg_lam = k.small[:, 255:256]
    s = {n: k.sem(f"dap_{n}") for n in ("rot_mm", "rot_read", "straight", "done", "tr", "tr_read", "prod", "lam_mm", "exp",
                                        "step")}
    with nc.Block() as block:
        @block.tensor
        def _(pe):
            for n in range(8):
                if n >= 2:
                    pe.wait_ge(s["rot_read"], n - 1)
                pe.matmul(k.ps[:, 4 + n % 2, :], k.const("rot"), k.da[:, n, :], start=True, stop=True) \
                    .then_inc(s["rot_mm"], 1)
            for n in range(4):
                if n >= 2:
                    pe.wait_ge(s["tr_read"], n - 1)
                for i in range(TT):
                    last = pe.transpose(k.ps[:, n % 2, i * P:(i + 1) * P], k.da[:, 8 + n, i * P:(i + 1) * P],
                                        k.const("ident"))
                last.then_inc(s["tr"], 1)
            pe.wait_ge(s["prod"], 2)
            pe.matmul(k.ps[:, 7, 0:2], k.const("ones")[0:64, :], prod[0:64, 0:2], start=True, stop=True) \
                .then_inc(s["lam_mm"], 1)

        @block.scalar
        def _(act):
            act.wait_ge(s["lam_mm"], 1)
            act.activation(prod[:, 2:4], k.ps[:, 7, 0:2], ACT.Exp).then_inc(s["exp"], 1)

        @block.gpsimd
        def _(pool):
            for n in range(8):
                if n >= 2:
                    pool.wait_ge(s["done"], n - 1)
                pool.tensor_tensor(straight[:, n % 2, :], k.da[:, n, :], k.const("cos", S), ALU.mult) \
                    .then_inc(s["straight"], 1)

        @block.vector
        def _(dve):
            steps = Steps(s["step"])
            low = slice(0, 64)
            dve.tensor_tensor(prod[low, 0:1], k.col("lq1", rows=low), k.col("lk1", rows=low), ALU.mult) \
                .then_inc(s["prod"], 1)
            dve.tensor_tensor(prod[low, 1:2], k.col("lq2", rows=low), k.col("lk2", rows=low), ALU.mult) \
                .then_inc(s["prod"], 1)
            for n in range(8):
                dve.wait_ge(s["rot_mm"], n + 1)
                if n >= 2:
                    dve.wait_ge(s["done"], n - 1)
                dve.tensor_tensor(turned[:, n % 2, :], k.ps[:, 4 + n % 2, :], k.const("sin", S), ALU.mult) \
                    .then_inc(s["rot_read"], 1)
                dve.wait_ge(s["rot_read"], n + 1)
                dve.wait_ge(s["straight"], n + 1)
                dve.tensor_tensor(k.da[:, n, :], turned[:, n % 2, :], straight[:, n % 2, :], ALU.add) \
                    .then_inc(s["done"], 1)
            for n in range(4):
                dve.wait_ge(s["tr"], n + 1)
                dve.tensor_copy(k.da_v[:, :, n * P:(n + 1) * P], k.ps[:, n % 2, :].rearrange("p (t c) -> p t c", c=P)) \
                    .then_inc(s["tr_read"], 1)
            dve.wait_ge(s["exp"], 1)
            steps.then_wait(dve, dve.tensor_tensor(prod[:, 4:5], prod[:, 3:4], prod[:, 2:3], ALU.subtract))
            dve.tensor_scalar(k.neg_lam, prod[:, 4:5], -LAMBDA_INIT, None, ALU.add)


def stage_da_attention(k):
    nc = k.nc
    k.da_o = k.region("da_o", [P, TT, S], F32, 62)
    p = k.region("da_p", [P, 2, 2, S], F32, 74)
    pt = k.region("da_pt", [P, 2, S], F32, 82)
    junk = k.region("da_junk", [P, 2, P], F32, 71.25)
    s = {n: k.sem(f"daa_{n}") for n in ("sc_mm", "nm_done", "exp_done", "pd_done", "tr_mm", "pt", "pv_mm", "o_done",
                                        "sq_done", "step", "root", "root_read", "y_tr", "y_hi", "y_done", "y_lo", "normed")}
    units = [(h, i) for h in range(DA_HEADS) for i in range(TT)]
    U = len(units)
    sumsq = k.small[:, 64:64 + U]
    y = k.region("da_y", [P, 2, S], F32, 86)

    def sm(base, n):
        return k.small[:, base + 2 * (n % 4):base + 2 * (n % 4) + 2]

    with nc.Block() as block:
        @block.tensor
        def _(pe):
            for n in range(U + 2):
                if n < U:
                    h, i = units[n]
                    if n >= 2:
                        pe.wait_ge(s["exp_done"], 2 * (n - 1))
                    for c in range(2):
                        rows = slice(64 * c, 64 * c + 64)
                        last = pe.matmul(k.ps[:, 2 * (n % 2) + c, :], k.da[rows, h, i * P:(i + 1) * P], k.da[rows, 4 + h, :],
                                         start=True, stop=True)
                    last.then_inc(s["sc_mm"], 1)
                if 1 <= n <= U:
                    m = n - 1
                    pe.wait_ge(s["pd_done"], m + 1)
                    if m >= 2:
                        pe.wait_ge(s["pt"], m - 1)
                    for j in range(TT):
                        last = pe.transpose(k.ps[:, 4 + m % 2, j * P:(j + 1) * P], p[:, m % 2, 0, j * P:(j + 1) * P],
                                            k.const("ident"))
                    last.then_inc(s["tr_mm"], 1)
                if n >= 2:
                    m = n - 2
                    h, i = units[m]
                    pe.wait_ge(s["pt"], m + 1)
                    if m >= 2:
                        pe.wait_ge(s["o_done"], m - 1)
                    for j in range(TT):
                        last = pe.matmul(k.ps[:, 6 + m % 2, 0:P], pt[:, m % 2, j * P:(j + 1) * P],
                                         k.da_v[:, j, h * P:(h + 1) * P], start=(j == 0), stop=(j == TT - 1))
                    last.then_inc(s["pv_mm"], 1)
            for h in range(DA_HEADS):
                pe.wait_ge(s["normed"], TT)
                if h >= 2:
                    pe.wait_ge(s["y_done"], h - 1)
                for i in range(TT):
                    last = pe.transpose(k.ps[:, h % 2, i * P:(i + 1) * P], k.da_o[:, i, h * P:(h + 1) * P],
                                        k.const("ident"))
                last.then_inc(s["y_tr"], 1)

        @block.scalar
        def _(act):
            for n in range(U + 2):
                if n < U:
                    act.wait_ge(s["nm_done"], n + 1)
                    if n >= 2:
                        act.wait_ge(s["tr_mm"], n - 1)
                    for c in range(2):
                        act.activation(p[:, n % 2, c, :], k.ps[:, 2 * (n % 2) + c, :], ACT.Exp, bias=sm(0, n)[:, c:c + 1],
                                       scale=DK ** -0.5, accum_out=sm(8, n)[:, c:c + 1]).then_inc(s["exp_done"], 1)
                if n >= 2:
                    m = n - 2
                    h, i = units[m]
                    act.wait_ge(s["o_done"], m + 1)
                    if m >= 2:
                        act.wait_ge(s["sq_done"], m - 1)
                    act.activation(junk[:, m % 2, :], k.da_o[:, i, h * P:(h + 1) * P], ACT.Square,
                                   accum_out=sumsq[:, 4 * i + h:4 * i + h + 1]).then_inc(s["sq_done"], 1)
            act.wait_ge(s["sq_done"], U)
            act.activation(sumsq, sumsq, ACT.Sqrt, scale=1.0 / P, bias=k.col("eps5")).then_inc(s["root"], 1)
            for h in range(DA_HEADS):
                act.wait_ge(s["y_done"], h + 1)
                act.activation(k.act_hi[:, 4 + h, :], y[:, h % 2, :], ACT.Copy).then_inc(s["y_hi"], 1)

        @block.vector
        def _(dve):
            steps = Steps(s["step"])
            for n in range(U + 2):
                if n < U:
                    bank = 2 * (n % 2)
                    dve.wait_ge(s["sc_mm"], n + 1)
                    if n >= 4:
                        dve.wait_ge(s["exp_done"], 2 * (n - 3))
                    steps.then_wait(dve, dve.tensor_reduce(sm(16, n), k.ps[:, bank:bank + 2, :], AX, ALU.max))
                    dve.tensor_scalar(sm(0, n), sm(16, n), -DK ** -0.5, None, ALU.mult).then_inc(s["nm_done"], 1)
                    dve.wait_ge(s["exp_done"], 2 * n + 2)
                    steps.then_wait(dve, dve.reciprocal(sm(24, n), sm(8, n)))
                    x = p[:, n % 2]
                    w = sm(24, n)
                    dve.tensor_scalar(w[:, 1:2], w[:, 1:2], k.neg_lam, None, ALU.mult)
                    steps.then_wait(dve, dve.tensor_scalar(x[:, 0, :], x[:, 0, :], w[:, 0:1], None, ALU.mult))
                    dve.scalar_tensor_tensor(out=x[:, 0, :], in0=x[:, 1, :], scalar=w[:, 1:2], in1=x[:, 0, :],
                                             op0=ALU.mult, op1=ALU.add).then_inc(s["pd_done"], 1)
                if 1 <= n <= U:
                    m = n - 1
                    dve.wait_ge(s["tr_mm"], m + 1)
                    if m >= 2:
                        dve.wait_ge(s["pv_mm"], m - 1)
                    dve.tensor_copy(pt[:, m % 2, :], k.ps[:, 4 + m % 2, :]).then_inc(s["pt"], 1)
                if n >= 2:
                    m = n - 2
                    h, i = units[m]
                    dve.wait_ge(s["pv_mm"], m + 1)
                    dve.tensor_copy(k.da_o[:, i, h * P:(h + 1) * P], k.ps[:, 6 + m % 2, 0:P]).then_inc(s["o_done"], 1)
            dve.wait_ge(s["root"], 1)
            steps.then_wait(dve, dve.reciprocal(sumsq, sumsq))
            dve.wait_ge(s["o_done"], U)
            for i in range(TT):
                o = k.da_o[:, i, :].rearrange("p (h d) -> p h d", d=P)
                dve.tensor_tensor(o, o, sumsq[:, 4 * i:4 * i + 4].rearrange("p (h o) -> p h o", o=1).to_broadcast([P, 4, P]),
                                  ALU.mult).then_inc(s["normed"], 1)
            for h in range(DA_HEADS):
                dve.wait_ge(s["y_tr"], h + 1)
                if h >= 2:
                    dve.wait_ge(s["y_lo"], h - 1)
                dve.tensor_scalar(y[:, h % 2, :], k.ps[:, h % 2, :], k.col("subln"), 1.0 - LAMBDA_INIT, ALU.mult,
                                  ALU.mult).then_inc(s["y_done"], 1)
                dve.wait_ge(s["y_hi"], h + 1)
                dve.tensor_tensor(k.act_lo[:, 4 + h, :], y[:, h % 2, :], k.act_hi[:, 4 + h, :].bitcast(F32),
                                  ALU.subtract).then_inc(s["y_lo"], 1)


def stage_rw_prep(k):
    nc = k.nc
    k.lora = k.at("rw_lora", [P, 3, S], F32, 28)
    k.rwc = k.at("rw_consts", [P, N_RW_CONSTS], F32, 44)
    got = k.sem("rwp_landed")
    with nc.Block() as block:
        @block.sync
        def _(sp):
            sp.dma_start(k.lora[:], k.io["lora"]).then_inc(got, 16)
            sp.dma_start(k.rwc[:], k.io["rw_consts"]).then_inc(got, 16)
            sp.wait_ge(got, 32)

        @block.scalar
        def _(act):
            act.activation(k.rw[:, 12, :], k.rw[:, 12, :], ACT.Tanh)
            act.activation(k.rw[:, 14, :], k.rw[:, 14, :], ACT.Sigmoid)
    k.ytok = k.region("rw_ytok", [P, TT, S], F32, 74)
    k.bonus = k.region("rw_bonus", [P, RW_T, S], F32, 82)


def halves():
    return [(d, hd, it, par) for d in range(2) for hd in range(2) for it in range(TT) for par in range(2)]


def rows_half(x):
    return slice(64 * x, 64 * x + 64)


def stage_rw_heads(k, c):
    nc = k.nc
    tag = f"rw{c}"
    ar = k.at(f"{tag}_ar", [P, 2, 2, S], F32, 60)
    bt = k.at(f"{tag}_bt", [P, 2, S], F32, 68)
    kt = k.at(f"{tag}_kt", [P, 2, S], F32, 72)
    bh = k.at(f"{tag}_bh", [P, 2, S], F32, 76)
    kh = k.at(f"{tag}_kh", [P, 2, S], F32, 80)
    T = k.at(f"{tag}_T", [P, 16, CHUNK], F32, 68)
    Tt = k.at(f"{tag}_Tt", [P, 16, CHUNK], F32, 72)
    Z = k.at(f"{tag}_Z", [P, 16, CHUNK], F32, 76)
    off = [k.at(f"{tag}_off0", [P, 16, CHUNK], F32, 80), k.region(f"{tag}_off1", [P, 16, CHUNK], F32, 62)]
    tok = k.at(f"{tag}_tok", [P, 2, 3, TT, P], F32, 84)
    vtok = k.at(f"{tag}_vtok", [P, TT, P], F32, 96)
    wu = k.at(f"{tag}_wu", [P, 16, P], F32, 98)
    bb = k.at(f"{tag}_b", [P, 2, S], F32, 98)
    kd = k.at(f"{tag}_kd", [P, 2, S], F32, 102)
    akv = k.at(f"{tag}_akv", [P, 16, CHUNK], F32, 106)
    kkn = k.at(f"{tag}_kkn", [P, S], F32, 106)
    sq = k.at(f"{tag}_sq", [P, S], F32, 108)
    mt = k.at(f"{tag}_mt", [P, 2, N_CHUNK, CHUNK], F32, 110)
    tmp = k.at(f"{tag}_tmp", [P, 2, S], F32, 110)
    pend = k.at(f"{tag}_pend", [P, 2, N_CHUNK], F32, 114)
    sc = k.region(f"{tag}_sc", [P, 16, 4, CHUNK], F32, 30)
    ex = k.region(f"{tag}_ex", [P, 2, 4, S], F32, 30)
    add = k.region(f"{tag}_add", [P, 2, N_CHUNK, CHUNK], F32, 46)
    state = k.region(f"{tag}_state", [P, 2, N_CHUNK, CHUNK], F32, 50)
    sig = k.region(f"{tag}_sig", [P, 2, S], F32, 54)
    X = k.region(f"{tag}_X", [P, 2, S], F32, 58)
    E1 = k.region(f"{tag}_E1", [P, 2, S], F32, 62)
    E2 = k.region(f"{tag}_E2", [P, 2, S], F32, 66)
    rate = k.region(f"{tag}_rate", [P, 2, S], F32, 70)
    ss = {n: k.sem(f"{tag[0:2]}{c}_{n}") for n in
          ("pre", "sigs", "kk", "sqd", "ss", "root", "sums", "exps", "kd", "bonp", "bonm", "feat", "pool_feat", "tr", "tok",
           "scm", "sc", "off", "init", "z", "zc", "tz", "t", "akvm", "akv", "wum", "wu_a", "wu_d", "rm", "rhat", "pcd", "mm",
           "mt", "nm", "add", "stm", "st", "yb", "ybc", "ya", "step", "pstep", "st0")}
    r, kf, v = k.rw[:, c, :], k.rw[:, 4 + c, :], k.rw[:, 8 + c, :]

    def rc(name, n, at=0):
        a = RW_CONSTS[name] + at
        return k.rwc[:, a:a + n]

    eye = rc("eye64", 64).rearrange("p (o n) -> p o n", o=1)

    def chunk(t):
        return slice(t * CHUNK, (t + 1) * CHUNK)

    with nc.Block() as block:
        @block.tensor
        def _(pe):
            for m, rows in ((0, 12), (1, 13)):
                for d in range(2):
                    h = rows_half(d)
                    last = pe.matmul(k.ps[:, 2 * m + d, :], k.lora[h, m, c * P:(c + 1) * P], k.rw[h, rows, :],
                                     start=True, stop=True)
            last.then_inc(ss["pre"], 1)
            pe.wait_ge(ss["sqd"], 1)
            pe.matmul(k.ps[:, 4, :], k.const("block_ones"), sq[:], start=True, stop=True).then_inc(ss["ss"], 1)
            pe.wait_ge(ss["bonp"], 1)
            pe.matmul(k.ps[:, 5, :], k.const("block_ones"), tmp[:, 0, :], start=True, stop=True).then_inc(ss["bonm"], 1)
            pe.wait_ge(ss["feat"], 6)
            pe.wait_ge(ss["pool_feat"], 6)
            jobs = [v] + [x for d in range(2) for x in (ar[:, d, 0, :], bh[:, d, :], kh[:, d, :])]
            for n, src in enumerate(jobs):
                if n >= 2:
                    pe.wait_ge(ss["tok"], n - 1)
                for i in range(TT):
                    last = pe.transpose(k.ps[:, 6 + n % 2, i * P:(i + 1) * P], src[:, i * P:(i + 1) * P], k.const("ident"))
                last.then_inc(ss["tr"], 1)
            n = 0
            for d in range(2):
                for hd in range(2):
                    for q in range(2):
                        if n >= 4:
                            pe.wait_ge(ss["sc"], n - 3)
                        for it in (2 * q, 2 * q + 1):
                            for par in range(2):
                                t = chunk(2 * it + par)
                                for m, lhs in ((0, bt), (1, kt)):
                                    o = 256 * (it % 2) + 128 * m
                                    last = pe.matmul(k.ps[rows_half(par), n % 4, o:o + 128]
                                                     .rearrange("p (x t) -> p x t", x=2),
                                                     lhs[rows_half(hd), d, t], ar[rows_half(hd), d, :, t],
                                                     start=True, stop=True)
                        last.then_inc(ss["scm"], 1)
                        n += 1
            pe.wait_ge(ss["off"], 2)
            for u in range(16):
                for par in range(2):
                    h = rows_half(par)
                    last = pe.matmul(k.ps[h, u // 8, chunk(u % 8)], off[0][h, u, :], rc("eye64", 64)[h], start=True,
                                     stop=True)
            last.then_inc(ss["z"], 1)
            for lv in range(1, LEVELS):
                pe.wait_ge(ss["off"], 2 * lv + 2)
                pe.wait_ge(ss["t"], 4 * lv)
                for u in range(16):
                    for par in range(2):
                        h = rows_half(par)
                        last = pe.matmul(k.ps[h, u // 8, chunk(u % 8)], off[lv % 2][h, u, :], T[h, u, :], start=True,
                                         stop=True)
                    if u % 8 == 7:
                        last.then_inc(ss["z"], 1)
                for d in range(2):
                    pe.wait_ge(ss["zc"], 2 * (lv - 1) + d + 1)
                    for u in range(8 * d, 8 * d + 8):
                        for par in range(2):
                            h = rows_half(par)
                            if lv < LEVELS - 1:
                                pe.matmul(k.ps[h, 2 + d, chunk(u % 8)], Tt[h, u, :], Z[h, u, :], start=True, stop=True)
                            last = pe.matmul(k.ps[h, 4 + d, chunk(u % 8)], Z[h, u, :], Tt[h, u, :], start=True, stop=True)
                    last.then_inc(ss["tz"], 1)
            for d, hd, it, par in halves():
                u, h = 8 * d + 4 * hd + it, rows_half(par)
                last = pe.matmul(k.ps[h, 6 + d, chunk(u % 8)], sc[h, u, 2, :], vtok[h, it, chunk(hd)], start=True, stop=True)
            last.then_inc(ss["akvm"], 1)
            pe.wait_ge(ss["t"], 4 * (LEVELS - 1) + 2)
            pe.wait_ge(ss["akv"], 2)
            for d, hd, it, par in halves():
                u, h = 8 * d + 4 * hd + it, rows_half(par)
                o = u % 4 * P
                pe.matmul(k.ps[h, u // 4, o:o + 64], Tt[h, u, :], tok[h, d, 0, it, chunk(hd)], start=True, stop=True)
                last = pe.matmul(k.ps[h, u // 4, o + 64:o + 128], Tt[h, u, :], akv[h, u, :], start=True, stop=True)
                if it == TT - 1 and par == 1:
                    last.then_inc(ss["wum"], 1)
            pe.wait_ge(ss["wu_a"], 2)
            pe.wait_ge(ss["wu_d"], 2)
            for par in range(2):
                h = rows_half(par)
                for d in range(2):
                    for hd in range(2):
                        for it in range(TT):
                            u = 8 * d + 4 * hd + it
                            last = pe.matmul(k.ps[rows_half(hd), 4 + par, chunk(4 * d + it)], wu[h, u, 0:64], sc[h, u, 1, :],
                                             start=True, stop=True)
            last.then_inc(ss["rm"], 1)
            for par in range(2):
                h = rows_half(par)
                for d in range(2):
                    for hd in range(2):
                        for it in range(TT):
                            u = 8 * d + 4 * hd + it
                            last = pe.matmul(k.ps[rows_half(hd), 6 + par, chunk(4 * d + it)], wu[h, u, 0:64],
                                             tok[h, d, 1, it, chunk(hd)], start=True, stop=True)
            last.then_inc(ss["mm"], 1)
            for par in range(2):
                h = rows_half(par)
                for d in range(2):
                    for hd in range(2):
                        for it in range(TT):
                            u = 8 * d + 4 * hd + it
                            out = k.ps[rows_half(hd), par, chunk(4 * d + it)]
                            pe.matmul(out, tok[h, d, 2, it, chunk(hd)], vtok[h, it, chunk(hd)], start=True, stop=False)
                            last = pe.matmul(out, tok[h, d, 1, it, chunk(hd)], wu[h, u, 64:128], start=False, stop=True)
            last.then_inc(ss["nm"], 1)
            pe.wait_ge(ss["mt"], 2)
            for hd in range(2):
                for it in range(TT):
                    for par in range(2):
                        h = rows_half(par)
                        out = k.ps[h, 6, chunk(4 * hd + it)]
                        for d in range(2):
                            u = 8 * d + 4 * hd + it
                            pe.matmul(out, sc[h, u, 1, :], wu[h, u, 64:128], start=(d == 0), stop=False)
                            last = pe.matmul(out, sc[h, u, 3, :], vtok[h, it, chunk(hd)], start=False, stop=(d == 1))
            last.then_inc(ss["yb"], 1)
            for n in range(1, N_CHUNK - 1):
                pe.wait_ge(ss["st"], n)
                for d in range(2):
                    ch = n if d == 0 else N_CHUNK - 1 - n
                    for hd in range(2):
                        h = rows_half(hd)
                        last = pe.matmul(k.ps[h, 2 + d, chunk(n)], mt[h, d, ch, :], state[h, d, ch, :], start=True, stop=True)
                last.then_inc(ss["stm"], 1)
            pe.wait_ge(ss["st"], N_CHUNK - 1)
            pe.wait_ge(ss["rhat"], 2)
            for hd in range(2):
                h = rows_half(hd)
                for it in range(TT):
                    for par in range(2):
                        t = 2 * it + par
                        for d in range(2):
                            last = pe.matmul(k.ps[rows_half(par), 4 + hd, chunk(it)], ar[h, d, 1, chunk(t)],
                                             state[h, d, t, :], start=(d == 0), stop=(d == 1))
            last.then_inc(ss["ya"], 1)

        @block.scalar
        def _(act):
            act.wait_ge(ss["pre"], 1)
            for m, out, bias in ((0, sig, "w0"), (1, rate, "a0")):
                for d in range(2):
                    act.activation(out[:, d, :], k.ps[:, 2 * m + d, :], ACT.Sigmoid, bias=k.col(bias, 4 * d + c)) \
                        .then_inc(ss["sigs"], 1)
            act.wait_ge(ss["kk"], 1)
            act.activation(sq[:], kkn[:], ACT.Square).then_inc(ss["sqd"], 1)
            act.wait_ge(ss["ss"], 1)
            act.activation(sq[:], k.ps[:, 4, :], ACT.Sqrt).then_inc(ss["root"], 1)
            act.wait_ge(ss["sums"], 1)
            for d in range(2):
                incl, excl, rest = X, (E1, E2)[d], (E2, E1)[d]
                for n, (src, sign) in enumerate(((incl, -1.0), (excl, -1.0), (incl, 1.0), (rest, -1.0))):
                    act.activation(ex[:, d, n, :], src[:, d, :], ACT.Exp, scale=sign * DECAY_SCALE) \
                        .then_inc(ss["exps"], 1)
            for n in range(7):
                act.wait_ge(ss["tr"], n + 1)
                out = vtok[:] if n == 0 else tok[:, (n - 1) // 3, (n - 1) % 3]
                act.activation(out, k.ps[:, 6 + n % 2, :].rearrange("p (t c) -> p t c", c=P), ACT.Copy) \
                    .then_inc(ss["tok"], 1)
            for lv in range(1, LEVELS):
                for d in range(2):
                    act.wait_ge(ss["z"], 1 + 2 * (lv - 1) + d + 1)
                    act.activation(Z[:, 8 * d:8 * d + 8, :].rearrange("p u t -> p (u t)"), k.ps[:, d, :], ACT.Copy) \
                        .then_inc(ss["zc"], 1)
            act.wait_ge(ss["akvm"], 1)
            for d in range(2):
                act.activation(akv[:, 8 * d:8 * d + 8, :].rearrange("p u t -> p (u t)"), k.ps[:, 6 + d, :], ACT.Copy) \
                    .then_inc(ss["akv"], 1)
            for g in (0, 2):
                act.wait_ge(ss["wum"], g + 1)
                act.activation(wu[:, 4 * g:4 * g + 4, :].rearrange("p u t -> p (u t)"), k.ps[:, g, :], ACT.Copy) \
                    .then_inc(ss["wu_a"], 1)
            act.wait_ge(ss["nm"], 1)
            for par in range(2):
                act.activation(add[:].rearrange("p d (i a) t -> p d i a t", a=2)[:, :, :, par, :],
                               k.ps[:, par, :].rearrange("p (d i t) -> p d i t", d=2, t=CHUNK), ACT.Copy) \
                    .then_inc(ss["add"], 1)
            act.wait_ge(ss["yb"], 1)
            for hd in range(2):
                act.activation(k.ytok[:, :, c * P + 64 * hd:c * P + 64 * hd + 64],
                               k.ps[:, 6, 256 * hd:256 * hd + 256].rearrange("p (i t) -> p i t", t=CHUNK), ACT.Copy) \
                    .then_inc(ss["ybc"], 1)

        @block.gpsimd
        def _(pool):
            pool.wait_ge(ss["exps"], 8)
            pool.wait_ge(ss["kd"], 2)
            for d in range(2):
                pool.tensor_tensor(ar[:, d, 1, :], r, ex[:, d, 0, :], ALU.mult).then_inc(ss["pool_feat"], 1)
                pool.tensor_tensor(kt[:, d, :], kd[:, d, :], ex[:, d, 2, :], ALU.mult).then_inc(ss["pool_feat"], 1)
                pool.tensor_tensor(kh[:, d, :], kd[:, d, :], ex[:, d, 3, :], ALU.mult).then_inc(ss["pool_feat"], 1)
            for lv in range(LEVELS):
                if lv == 0:
                    pool.wait_ge(ss["sc"], 8)
                    pool.wait_ge(ss["tok"], 7)
                elif lv >= 2:
                    pool.wait_ge(ss["z"], 1 + 2 * (lv - 2))
                    if lv == 2:
                        pool.wait_ge(ss["init"], 1)
                for d in range(2):
                    u = slice(8 * d, 8 * d + 8)
                    mask = rc(f"level{d}", 64, 64 * lv).rearrange("p (o n) -> p o n", o=1).to_broadcast([P, 8, CHUNK])
                    pool.tensor_tensor(off[lv % 2][:, u, :], sc[:, u, 0, :], mask, ALU.mult).then_inc(ss["off"], 1)
            pool.wait_ge(ss["t"], 4 * (LEVELS - 1) + 2)
            pool.tensor_tensor(mt[:], rc("eye64", 64).rearrange("p (a b n) -> p a b n", a=1, b=1)
                               .to_broadcast([P, 2, N_CHUNK, CHUNK]),
                               pend[:].rearrange("p d (n o) -> p d n o", o=1).to_broadcast([P, 2, N_CHUNK, CHUNK]),
                               ALU.mult).then_inc(ss["pcd"], 1)

        @block.vector
        def _(dve):
            steps = Steps(ss["step"])

            def wait(ins):
                steps.then_wait(dve, ins)

            dve.tensor_scalar(kkn[:], kf, k.col("k_k", c), None, ALU.mult).then_inc(ss["kk"], 1)
            dve.wait_ge(ss["sigs"], 4)
            for d in range(2):
                wait(dve.tensor_tensor_scan(X[:, d, :], rc("scan", S), sig[:, d, :], 0.0, ALU.mult, ALU.add))
            x4 = X[:].rearrange("p d (n t) -> p d n t", t=CHUNK)
            wait(dve.tensor_tensor(E1[:], X[:], sig[:], ALU.subtract))
            for d in range(2):
                x3 = X[:, d, :].rearrange("p (n t) -> p n t", t=CHUNK)
                e3 = E2[:, d, :].rearrange("p (n t) -> p n t", t=CHUNK)
                wait(dve.tensor_tensor(e3, x3[:, :, CHUNK - 1:CHUNK].to_broadcast([P, N_CHUNK, CHUNK]), x3, ALU.subtract))
            dve.tensor_tensor(X[:, 1, :], E2[:, 1, :], sig[:, 1, :], ALU.add).then_inc(ss["sums"], 1)
            for d in range(2):
                wait(dve.tensor_scalar(tmp[:, d, :], rate[:, d, :], -1.0, k.col("k_a", c), ALU.add, ALU.mult))
                dve.scalar_tensor_tensor(out=kd[:, d, :], in0=tmp[:, d, :], scalar=1.0, in1=kf, op0=ALU.add,
                                         op1=ALU.mult).then_inc(ss["kd"], 1)
            dve.wait_ge(ss["kd"], 2)
            wait(dve.tensor_tensor(tmp[:, 1, :], kd[:, 0, :], kd[:, 1, :], ALU.add))
            dve.scalar_tensor_tensor(out=tmp[:, 0, :], in0=tmp[:, 1, :], scalar=k.col("r_k", c), in1=r, op0=ALU.mult,
                                     op1=ALU.mult).then_inc(ss["bonp"], 1)
            dve.wait_ge(ss["root"], 1)
            wait(dve.tensor_scalar(sq[:], sq[:], 1e-12, None, ALU.max))
            wait(dve.reciprocal(sq[:], sq[:]))
            wait(dve.tensor_tensor(kkn[:], kkn[:], sq[:], ALU.mult))
            for d in range(2):
                wait(dve.tensor_tensor(bb[:, d, :], kkn[:], rate[:, d, :], ALU.mult))
            dve.wait_ge(ss["exps"], 8)
            for d in range(2):
                dve.tensor_tensor(ar[:, d, 0, :], kkn[:], ex[:, d, 1, :], ALU.mult).then_inc(ss["feat"], 1)
                dve.tensor_tensor(bt[:, d, :], bb[:, d, :], ex[:, d, 2, :], ALU.mult).then_inc(ss["feat"], 1)
                dve.scalar_tensor_tensor(out=bh[:, d, :], in0=bb[:, d, :], scalar=-1.0, in1=ex[:, d, 3, :], op0=ALU.mult,
                                         op1=ALU.mult).then_inc(ss["feat"], 1)
                end = ex[:, d, 0, :].rearrange("p (n t) -> p n t", t=CHUNK)[:, :, (CHUNK - 1, 0)[d]]
                wait(dve.tensor_copy(pend[:, d, :], end))
            dve.wait_ge(ss["bonm"], 1)
            dve.tensor_tensor(k.bonus[:, c, :], k.ps[:, 5, :], v, ALU.mult)
            dve.wait_ge(ss["pool_feat"], 6)
            for n in range(8):
                d = n // 4
                u = 2 * n
                dve.wait_ge(ss["scm"], n + 1)
                mask = rc(f"score{d}", 256).rearrange("p (o n) -> p o n", o=1).to_broadcast([P, 2, 256])
                dve.tensor_tensor(sc[:, u:u + 2].rearrange("p u m t -> p u (m t)"),
                                  k.ps[:, n % 4, :].rearrange("p (u m) -> p u m", u=2), mask, ALU.mult) \
                    .then_inc(ss["sc"], 1)
            dve.wait_ge(ss["off"], 2)
            wide = eye.to_broadcast([P, 8, CHUNK])
            for d in range(2):
                u = slice(8 * d, 8 * d + 8)
                dve.tensor_tensor(Tt[:, u, :], off[0][:, u, :], wide, ALU.add).then_inc(ss["t"], 1)
            dve.wait_ge(ss["z"], 1)
            for d in range(2):
                u = slice(8 * d, 8 * d + 8)
                dve.tensor_tensor(T[:, u, :], k.ps[:, d, :].rearrange("p (u t) -> p u t", t=CHUNK), wide, ALU.add) \
                    .then_inc(ss["t"], 1)
            dve.wait_ge(ss["t"], 4)
            dve.sem_inc(ss["init"], 1)
            done = 4
            for lv in range(1, LEVELS):
                for d in range(2):
                    u = slice(8 * d, 8 * d + 8)
                    dve.wait_ge(ss["tz"], 2 * (lv - 1) + d + 1)
                    for x, bank in ((Tt, 4), (T, 2)):
                        if x is T and lv == LEVELS - 1:
                            continue
                        dve.tensor_tensor(x[:, u, :], x[:, u, :], k.ps[:, bank + d, :].rearrange("p (u t) -> p u t", t=CHUNK),
                                          ALU.add).then_inc(ss["t"], 1)
                        done += 1
                dve.wait_ge(ss["t"], done)
            for g in (1, 3):
                dve.wait_ge(ss["wum"], g + 1)
                dve.tensor_copy(wu[:, 4 * g:4 * g + 4, :].rearrange("p u t -> p (u t)"), k.ps[:, g, :]) \
                    .then_inc(ss["wu_d"], 1)
            dve.memset(state[:, 0, 0, :], 0.0).then_inc(ss["st0"], 1)
            dve.memset(state[:, 1, N_CHUNK - 1, :], 0.0).then_inc(ss["st0"], 1)
            dve.wait_ge(ss["rm"], 1)
            for par in range(2):
                x = ar[:, :, 1, :].rearrange("p d (i a t) -> p d i a t", a=2, t=CHUNK)[:, :, :, par, :]
                dve.tensor_tensor(x, x, k.ps[:, 4 + par, :].rearrange("p (d i t) -> p d i t", d=2, t=CHUNK), ALU.add) \
                    .then_inc(ss["rhat"], 1)
            dve.wait_ge(ss["mm"], 1)
            dve.wait_ge(ss["pcd"], 1)
            for par in range(2):
                x = mt[:].rearrange("p d (i a) t -> p d i a t", a=2)[:, :, :, par, :]
                dve.tensor_tensor(x, x, k.ps[:, 6 + par, :].rearrange("p (d i t) -> p d i t", d=2, t=CHUNK), ALU.add) \
                    .then_inc(ss["mt"], 1)
            dve.wait_ge(ss["add"], 2)
            dve.wait_ge(ss["st0"], 2)
            dve.tensor_copy(state[:, 0, 1, :], add[:, 0, 0, :])
            dve.tensor_copy(state[:, 1, N_CHUNK - 2, :], add[:, 1, N_CHUNK - 1, :]).then_inc(ss["st"], 1)
            for n in range(1, N_CHUNK - 1):
                dve.wait_ge(ss["stm"], n)
                dve.tensor_tensor(state[:, 0, n + 1, :], k.ps[:, 2, chunk(n)], add[:, 0, n, :], ALU.add)
                m = N_CHUNK - 1 - n
                dve.tensor_tensor(state[:, 1, m - 1, :], k.ps[:, 3, chunk(n)], add[:, 1, m, :], ALU.add) \
                    .then_inc(ss["st"], 1)
            dve.wait_ge(ss["ya"], 1)
            dve.wait_ge(ss["ybc"], 2)
            for hd in range(2):
                x = k.ytok[:, :, c * P + 64 * hd:c * P + 64 * hd + 64]
                dve.tensor_tensor(x, x, k.ps[:, 4 + hd, 0:256].rearrange("p (i t) -> p i t", t=CHUNK), ALU.add)


def stage_rw_out(k):
    nc = k.nc
    sqr = k.region("rwo_sq", [P, TT, S], F32, 30)
    g = k.region("rwo_g", [P, RW_T, S], F32, 38)
    y = k.region("rwo_y", [P, 2, S], F32, 46)
    N = TT * 8
    mean, var = k.small[:, 0:N], k.small[:, N:2 * N]
    s = {n: k.sem(f"rwo_{n}") for n in ("gm", "gc", "step", "vars", "root", "normed", "tr", "aff", "y", "hi", "lo")}
    with nc.Block() as block:
        @block.tensor
        def _(pe):
            for c in range(RW_T):
                last = pe.matmul(k.ps[:, 4 + c, :], k.lora[:, 2, c * P:(c + 1) * P], k.rw[:, 14, :], start=True, stop=True)
            last.then_inc(s["gm"], 1)
            pe.wait_ge(s["normed"], 1)
            for c in range(RW_T):
                for i in range(TT):
                    last = pe.transpose(k.ps[:, c, i * P:(i + 1) * P], k.ytok[:, i, c * P:(c + 1) * P], k.const("ident"))
                last.then_inc(s["tr"], 1)

        @block.scalar
        def _(act):
            act.wait_ge(s["gm"], 1)
            for c in range(RW_T):
                act.activation(g[:, c, :], k.ps[:, 4 + c, :], ACT.Copy).then_inc(s["gc"], 1)
            act.wait_ge(s["vars"], 1)
            act.activation(var, var, ACT.Sqrt, scale=1.0 / DK, bias=k.col("eps_gn")).then_inc(s["root"], 1)
            for c in range(RW_T + 1):
                if c < RW_T:
                    act.wait_ge(s["tr"], c + 1)
                    if c >= 2:
                        act.wait_ge(s["lo"], c - 1)
                    act.activation(y[:, c % 2, :], k.ps[:, c, :], ACT.Identity, scale=k.col("rw_ln_w", c),
                                   bias=k.col("rw_ln_b", c)).then_inc(s["aff"], 1)
                if c >= 1:
                    act.wait_ge(s["y"], c)
                    act.activation(k.act_hi[:, c - 1, :], y[:, (c - 1) % 2, :], ACT.Copy).then_inc(s["hi"], 1)

        @block.vector
        def _(dve):
            steps = Steps(s["step"])
            y3 = k.ytok[:].rearrange("p t (h d) -> p (t h) d", d=DK)
            s3 = sqr[:].rearrange("p t (h d) -> p (t h) d", d=DK)
            steps.then_wait(dve, dve.tensor_reduce(mean, y3, AX, ALU.add))
            steps.then_wait(dve, dve.tensor_scalar(mean, mean, 1.0 / DK, None, ALU.mult))
            steps.then_wait(dve, dve.tensor_tensor(y3, y3, mean.rearrange("p (h o) -> p h o", o=1).to_broadcast([P, N, DK]),
                                                   ALU.subtract))
            steps.then_wait(dve, dve.tensor_tensor(s3, y3, y3, ALU.mult))
            dve.tensor_reduce(var, s3, AX, ALU.add).then_inc(s["vars"], 1)
            dve.wait_ge(s["root"], 1)
            steps.then_wait(dve, dve.reciprocal(var, var))
            dve.tensor_tensor(y3, y3, var.rearrange("p (h o) -> p h o", o=1).to_broadcast([P, N, DK]), ALU.mult) \
                .then_inc(s["normed"], 1)
            dve.wait_ge(s["gc"], RW_T)
            for c in range(RW_T):
                dve.wait_ge(s["aff"], c + 1)
                x = y[:, c % 2, :]
                steps.then_wait(dve, dve.tensor_tensor(x, x, k.bonus[:, c, :], ALU.add))
                dve.tensor_tensor(x, x, g[:, c, :], ALU.mult).then_inc(s["y"], 1)
                dve.wait_ge(s["hi"], c + 1)
                dve.tensor_tensor(k.act_lo[:, c, :], x, k.act_hi[:, c, :].bitcast(F32), ALU.subtract).then_inc(s["lo"], 1)


def stage_mix(k):
    nc = k.nc
    b0 = first_block("mix_o")
    b1 = first_block("out_2")
    g = k.region("mix_g", [P, 4, 2, S], F32, 0)
    merged = k.region("merged", [P, KD, S], F32, 16)
    parts = k.region("mix_parts", [P, 2, 2, S], F32, 32)
    gl = [k.sem(f"mix_g{i}") for i in range(4)]
    pair, read, part, merged_done, hi = (k.sem("mix_pair"), k.sem("mix_read"), k.sem("mix_part"), k.sem("mix_merged"),
                                         k.sem("mix_hi"))
    tiles = tiles_of(b0, b1)
    with nc.Block() as block:
        @block.sync
        def _(sp):
            load_blocks(k, sp, b0 + RAW_SLOTS)
            for n in range(KD):
                if n >= 4:
                    sp.wait_ge(part, 2 * (n - 3))
                for x in range(2):
                    sp.dma_start(g[:, n % 4, x, :], k.io["z_scratch"][KD * x + n]).then_inc(gl[n % 4], 16)
                if n == 3:
                    load_blocks(k, sp, b1 + RAW_SLOTS - 1)
            load_blocks(k, sp, b1 + RAW_SLOTS)

        @block.scalar
        def _(act):
            split_hi(k, act, b0)
            for b in range(b0, b1):
                split_hi(k, act, b + 1)
            for n in range(KD):
                act.wait_ge(merged_done, n + 1)
                if n == 0:
                    act.wait_ge(pair, 2 * KD)
                act.activation(k.act_hi[:, n, :], merged[:, n, :], ACT.Copy).then_inc(hi, 1)

        @block.tensor
        def _(pe):
            for n, (b, j) in enumerate(tiles):
                pe.wait_ge(k.lo_done, b + 1)
                for x in range(2):
                    if n >= 2:
                        pe.wait_ge(read, 2 * (n - 2) + x + 1)
                    for kt in range(4 * x, 4 * x + 4):
                        w = slice(kt * BLOCK_COLS + j * P, kt * BLOCK_COLS + j * P + P)
                        whi, wlo = k.whi[b % 2][:, w], k.wlo[b % 2][:, w]
                        bank = k.ps[:, 2 * (n % 2) + x, :]
                        pe.matmul(bank, whi, k.act_hi[:, kt, :], start=(kt == 4 * x), stop=False)
                        pe.matmul(bank, whi, k.act_lo[:, kt, :], start=False, stop=False)
                        last = pe.matmul(bank, wlo, k.act_hi[:, kt, :], start=False, stop=(kt == 4 * x + 3))
                    last.then_inc(pair, 1)
                pe.wait_ge(pair, 2 * n + 2)
                pe.sem_inc(k.tile_done, 1)

        @block.vector
        def _(dve):
            split_lo(k, dve, b0)
            for n, (b, j) in enumerate(tiles):
                if j == 0:
                    split_lo(k, dve, b + 1)
                dve.wait_ge(gl[n % 4], 32 * (n // 4 + 1))
                for x in range(2):
                    dve.wait_ge(pair, 2 * n + x + 1)
                    if n >= 2:
                        dve.wait_ge(merged_done, n - 1)
                    dve.tensor_tensor(parts[:, n % 2, x, :], k.ps[:, 2 * (n % 2) + x, :], g[:, n % 4, x, :], ALU.mult) \
                        .then_inc(read, 1)
                dve.wait_ge(read, 2 * n + 2)
                dve.sem_inc(part, 2)
                dve.sem_inc(k.evac_done, 1)
                dve.tensor_tensor(merged[:, n, :], parts[:, n % 2, 0, :], parts[:, n % 2, 1, :], ALU.add) \
                    .then_inc(merged_done, 1)
            for n in range(KD):
                dve.wait_ge(hi, n + 1)
                dve.tensor_tensor(k.act_lo[:, n, :], merged[:, n, :], k.act_hi[:, n, :].bitcast(F32), ALU.subtract)


def stage_ffn(k):
    nc = k.nc
    b0 = first_block("ff1")
    f_hi = k.region("f_hi", [P, KD, S], F32R, 0)
    f_lo = k.region("f_lo", [P, KD, S], F32R, 16)
    sq = k.region("ff_sq", [P, 2, S], F32, 32)
    relu = k.region("ff_relu", [P, 2, S], F32, 36)
    relu_done, sq_done, hi, lo = k.sem("ff_relu_done"), k.sem("ff_sq_done"), k.sem("ff_hi"), k.sem("ff_lo")
    with nc.Block() as block:
        @block.sync
        def _(sp):
            load_blocks(k, sp, b0 + 32 + RAW_SLOTS)

        @block.scalar
        def _(act):
            for f in range(4):
                for n, (b, j) in enumerate(tiles_of(b0 + 8 * f, b0 + 8 * f + 4)):
                    if j == 0:
                        split_hi(k, act, b + 1)
                    m = KD * f + n
                    act.wait_ge(sq_done, m + 1)
                    if n == 0 and f:
                        act.wait_ge(k.tile_done, TILE_AT[b0 + 8 * f])
                    act.activation(f_hi[:, n, :], sq[:, m % 2, :], ACT.Copy).then_inc(hi, 1)
                for b in range(b0 + 8 * f + 4, b0 + 8 * f + 8):
                    split_hi(k, act, b + 1)

        @block.tensor
        def _(pe):
            for f in range(4):
                for b, j in tiles_of(b0 + 8 * f, b0 + 8 * f + 4):
                    multiply_tile(k, pe, b, j)
                pe.wait_ge(lo, KD * (f + 1))
                for b, j in tiles_of(b0 + 8 * f + 4, b0 + 8 * f + 8):
                    t = TILE_AT[b] + j
                    pe.wait_ge(k.lo_done, b + 1)
                    pe.wait_ge(k.evac_done, t - 3)
                    for kt in range(KD):
                        w = slice(kt * BLOCK_COLS + j * P, kt * BLOCK_COLS + j * P + P)
                        whi, wlo = k.whi[b % 2][:, w], k.wlo[b % 2][:, w]
                        pe.matmul(k.ps[:, t % 4, :], whi, f_hi[:, kt, :], start=(kt == 0), stop=False)
                        pe.matmul(k.ps[:, t % 4, :], whi, f_lo[:, kt, :], start=False, stop=False)
                        last = pe.matmul(k.ps[:, t % 4, :], wlo, f_hi[:, kt, :], start=False, stop=(kt == KD - 1))
                    last.then_inc(k.tile_done, 1)

        @block.vector
        def _(dve):
            for f in range(4):
                for n, (b, j) in enumerate(tiles_of(b0 + 8 * f, b0 + 8 * f + 4)):
                    if j == 0:
                        split_lo(k, dve, b + 1)
                    m, t = KD * f + n, TILE_AT[b] + j
                    dve.wait_ge(k.tile_done, t + 1)
                    dve.tensor_scalar(relu[:, m % 2, :], k.ps[:, t % 4, :], 0.0, None, ALU.max).then_inc(k.evac_done, 1)
                    dve.wait_ge(k.evac_done, t + 1)
                    if m >= 2:
                        dve.wait_ge(lo, m - 1)
                    dve.tensor_tensor(sq[:, m % 2, :], relu[:, m % 2, :], relu[:, m % 2, :], ALU.mult).then_inc(sq_done, 1)
                    dve.wait_ge(hi, m + 1)
                    dve.tensor_tensor(f_lo[:, n, :], sq[:, m % 2, :], f_hi[:, n, :].bitcast(F32), ALU.subtract) \
                        .then_inc(lo, 1)
                for n, (b, j) in enumerate(tiles_of(b0 + 8 * f + 4, b0 + 8 * f + 8)):
                    if j == 0:
                        split_lo(k, dve, b + 1)
                    t = TILE_AT[b] + j
                    dve.wait_ge(k.tile_done, t + 1)
                    dve.tensor_tensor(k.xT[:, n, :], k.xT[:, n, :], k.ps[:, t % 4, :], ALU.add).then_inc(k.evac_done, 1)


def stage_ple(k):
    nc = k.nc
    b0 = first_block("ple_gate")
    b1 = first_block("ple_proj")
    b2 = b1 + 4
    gate = k.region("ple_gates", [P, KD, S], F32, 20)
    pf = k.region("ple_p", [P, 2, S], F32, 36)
    p_hi = k.region("ple_p_hi", [P, 2, S], F32R, 40)
    p_lo = k.region("ple_p_lo", [P, 2, S], F32R, 44)
    part = k.region("ple_part", [P, 2, S], F32, 48)
    landed, p_hi_done, p_lo_done, gates, part_done, added = (k.sem("ple_landed"), k.sem("ple_p_hi_done"),
                                                             k.sem("ple_p_lo_done"), k.sem("ple_gates_done"),
                                                             k.sem("ple_part_done"), k.sem("ple_added"))
    with nc.Block() as block:
        @block.sync
        def _(sp):
            sp.dma_start(pf[:], k.io["pT"]).then_inc(landed, 16)
            load_blocks(k, sp, b2)

        @block.scalar
        def _(act):
            act.wait_ge(landed, 16)
            act.activation(p_hi[:], pf[:], ACT.Copy).then_inc(p_hi_done, 1)
            for n, (b, j) in enumerate(tiles_of(b0, b1)):
                if j == 0:
                    split_hi(k, act, b + 1)
                t = TILE_AT[b] + j
                act.wait_ge(k.tile_done, t + 1)
                act.activation(gate[:, n, :], k.ps[:, t % 4, :], ACT.Sigmoid).then_inc(k.evac_done, 1)
            for b in range(b1, b2):
                split_hi(k, act, b + 1)

        @block.tensor
        def _(pe):
            for b, j in tiles_of(b0, b1):
                multiply_tile(k, pe, b, j)
            pe.wait_ge(p_lo_done, 1)
            for b, j in tiles_of(b1, b2):
                t = TILE_AT[b] + j
                pe.wait_ge(k.lo_done, b + 1)
                pe.wait_ge(k.evac_done, t - 3)
                for kt in range(2):
                    w = slice(kt * BLOCK_COLS + j * P, kt * BLOCK_COLS + j * P + P)
                    whi, wlo = k.whi[b % 2][:, w], k.wlo[b % 2][:, w]
                    pe.matmul(k.ps[:, t % 4, :], whi, p_hi[:, kt, :], start=(kt == 0), stop=False)
                    pe.matmul(k.ps[:, t % 4, :], whi, p_lo[:, kt, :], start=False, stop=False)
                    last = pe.matmul(k.ps[:, t % 4, :], wlo, p_hi[:, kt, :], start=False, stop=(kt == 1))
                last.then_inc(k.tile_done, 1)

        @block.vector
        def _(dve):
            dve.wait_ge(p_hi_done, 1)
            dve.tensor_tensor(p_lo[:], pf[:], p_hi[:].bitcast(F32), ALU.subtract).then_inc(p_lo_done, 1)
            for b in range(b0, b1):
                split_lo(k, dve, b + 1)
            dve.wait_ge(k.evac_done, TILE_AT[b1])
            for n, (b, j) in enumerate(tiles_of(b1, b2)):
                if j == 0:
                    split_lo(k, dve, b + 1)
                t = TILE_AT[b] + j
                dve.wait_ge(k.tile_done, t + 1)
                if n >= 2:
                    dve.wait_ge(added, n - 1)
                dve.tensor_tensor(part[:, n % 2, :], k.ps[:, t % 4, :], gate[:, n, :], ALU.mult).then_inc(k.evac_done, 1)
                dve.wait_ge(k.evac_done, t + 1)
                dve.tensor_tensor(k.xT[:, n, :], k.xT[:, n, :], part[:, n % 2, :], ALU.add).then_inc(added, 1)


def stage_out(k):
    with k.nc.Block() as block:
        @block.sync
        def _(sp):
            sp.dma_start(k.io["out"], k.xT[:]).then_inc(k.out_stored, 16)
            sp.wait_ge(k.out_stored, 16)


def build(nc, io, stop=None):
    with ExitStack() as ctx:
        k = Core(nc, ctx, io)
        for n, stage in enumerate(program()):
            if stop is not None and n >= stop:
                break
            k.run(stage)
        if stop is not None:
            with nc.Block() as block:
                @block.sync
                def _(sp):
                    for i in range(RAW_SLOTS):
                        n = len(range(i, k.loaded, RAW_SLOTS))
                        if n:
                            sp.wait_ge(k.landed[i], 16 * n)
    return k


def program():
    out0, nsa0, out2 = first_block("ml_out"), first_block("nsa_out"), first_block("out_2")
    return [
        stage_open,
        lambda k: stage_norm(k, "norm_ml", "ml_norm"),
        stage_fold,
        stage_ml_inner,
        stage_ml_gate,
        lambda k: stage_ml_heads(k, 0),
        lambda k: stage_add(k, "ml_out0", out0, out0 + 4),
        lambda k: stage_ml_heads(k, 2),
        lambda k: stage_add(k, "ml_out1", out0 + 4, out0 + 8),
        lambda k: stage_norm(k, "norm_nsa", "nsa_norm"),
        stage_nsa_in,
        stage_nsa_prep,
        stage_nsa_cmp,
        stage_nsa_attention,
        stage_nsa_gate,
        lambda k: stage_add(k, "nsa_out", nsa0, nsa0 + 4),
        lambda k: stage_norm(k, "norm_first", "final_norm", onto_residual=True),
        lambda k: stage_norm(k, "norm_mix", "norm_mix"),
        stage_in_2,
        stage_da_prep,
        stage_da_attention,
        stage_rw_prep,
        *[lambda k, c=c: stage_rw_heads(k, c) for c in range(RW_T)],
        stage_rw_out,
        stage_mix,
        lambda k: stage_add(k, "out_2", out2, out2 + 4),
        lambda k: stage_norm(k, "norm_ffn", "norm_ffn"),
        stage_ffn,
        lambda k: stage_norm(k, "norm_ple", "norm_ple"),
        stage_ple,
        lambda k: stage_norm(k, "norm_final", "norm_final", onto_residual=True),
        stage_out,
    ]


def kernel(**inputs):
    import numpy as np
    import ml_dtypes
    import concourse.bacc as bacc
    from concourse.bass_utils import run_bass_kernel_spmd

    a = {n: np.asarray(x) for n, x in inputs.items()}
    arrays = layout(np, ml_dtypes, a)
    nc = bacc.Bacc("TRN2", target_bir_lowering=False, num_devices=1)
    io, ins = {}, {}
    for n, x in arrays.items():
        x = np.ascontiguousarray(x)
        ins[n + "_in"] = x
        io[n] = nc.dram_tensor(n + "_in", x.shape, mybir.dt.from_np(x.dtype), kind="ExternalInput").ap()
    scratch(nc, io)
    build(nc, io)
    r = run_bass_kernel_spmd(nc, [ins], core_ids=[0])
    got = r.results[0]["out_T"]
    return got.transpose(2, 1, 0).reshape(1, S, D)


def scratch(nc, io):
    io["v_scratch"] = nc.dram_tensor("v_scratch", [ML_HEADS, P, TT, S], F32).ap()
    io["z_scratch"] = nc.dram_tensor("z_scratch", [ML_T, P, S], F32).ap()
    io["out"] = nc.dram_tensor("out_T", [P, KD, S], F32, kind="ExternalOutput").ap()


def rows_of(np, x):
    return x.reshape(-1, P, x.shape[-1]).transpose(1, 0, 2)


def layout(np, ml_dtypes, a):
    f32, bf16 = np.float32, ml_dtypes.bfloat16
    out = {"xT": a["x"][0].T.reshape(KD, P, S).transpose(1, 0, 2)}

    order = [(2 * gp + half) * 4 + hh for gp in range(2) for hh in range(4) for half in range(2)]
    nsa_cols = np.concatenate([np.concatenate([np.arange(h * DK, (h + 1) * DK) for h in order]),
                               np.arange(NSA_HEADS * DK, a["nsa_w_in"].shape[2])])
    nsa_in = a["nsa_w_in"][0][:, nsa_cols]
    nsa_in = np.concatenate([nsa_in, np.zeros((D, 29 * P - nsa_in.shape[1]), f32)], axis=1)
    mix_o = np.concatenate([a["rwkv_w_o_2"][0], a["da_w_o_2"][0]], axis=0)
    w2 = a["w_in_2"][0]
    in_2 = np.concatenate([w2[:, 1920 + 1536:], w2[:, 1920:1920 + 1536], w2[:, :1920]], axis=1)
    weights = {"ml_in": a["ml_w_in"][0], "ml_out": a["ml_w_out"][0], "nsa_in": nsa_in, "nsa_out": a["nsa_w_out"][0],
               "in_2": in_2, "mix_o": mix_o, "out_2": a["w_out_2"][0], "ff1": a["w_ff1_2"][0], "ff2": a["w_ff2_2"][0],
               "ple_gate": a["w_ple_gate_2"][0], "ple_proj": a["w_ple_proj_2"][0]}
    stream = np.empty((P, STREAM_COLS), f32)
    for b, (name, r0, rows, c0, n) in enumerate(BLOCKS):
        stream[:, BLOCK_AT[b]:BLOCK_AT[b + 1]] = rows_of(np, weights[name][r0:r0 + rows, c0:c0 + n]).reshape(P, -1)
    out["stream"] = stream

    cols = np.zeros((P, N_COLS), f32)

    def put(name, x):
        x = x.reshape(-1, P)
        cols[:, COLS[name]:COLS[name] + x.shape[0]] = x.T

    for name, key in (("ml_norm", "ml_norm"), ("conv_w", "ml_conv_w"), ("conv_b", "ml_conv_b"), ("ml_ln_w", "ml_ln_w"),
                      ("skip", "ml_skip"), ("nsa_norm", "nsa_norm"), ("final_norm", "final_norm"),
                      ("norm_mix", "norm_mix_2"), ("norm_ffn", "norm_ffn_2"), ("norm_ple", "norm_ple_2"),
                      ("norm_final", "norm_final_2"), ("mu_prev", "shift_mu_prev_2"), ("mu_next", "shift_mu_next_2"),
                      ("w0", "rwkv_w0_2"), ("a0", "rwkv_a0_2"), ("k_k", "rwkv_k_k_2"), ("k_a", "rwkv_k_a_2"),
                      ("r_k", "rwkv_r_k_2"), ("rw_ln_w", "rwkv_ln_w_2"), ("rw_ln_b", "rwkv_ln_b_2"),
                      ("subln", "da_subln_w_2")):
        put(name, a[key])
    cols[0:4, COLS["b_if"]] = a["ml_b_if"][0, 0:4]
    cols[32:36, COLS["b_if"]] = a["ml_b_if"][0, 4:8]
    cols[0:48, COLS["b_gate"]] = a["nsa_b_gate"][0]
    for n in ("lq1", "lk1", "lq2", "lk2"):
        cols[0:64, COLS[n]] = a[f"da_{n}_2"][0]
    for n, x in (("eps6", 1e-6), ("eps5", 1e-5), ("eps_gn", 64e-5), ("one", 1.0)):
        cols[:, COLS[n]] = x
    cols[:, COLS["cmp_any"]] = np.arange(P) >= CMP_BLOCK - 1
    out["cols"] = cols

    w = np.stack([a["ml_w_q"][0], a["ml_w_k"][0], a["ml_w_v"][0]]).reshape(3, ML_T, 32, 4, 4)
    out["hw"] = w.transpose(2, 4, 0, 1, 3).reshape(P, 3, ML_T, 4)
    out["hwt"] = w.transpose(2, 3, 0, 1, 4).reshape(P, 3, ML_T, 4)
    out["wif"] = a["ml_w_if"][0].reshape(3, ML_T, P, 8).transpose(2, 0, 1, 3)

    w1 = a["nsa_cmp_w1"][0].reshape(2, CMP_BLOCK, DK, P).transpose(2, 0, 1, 3)
    out["cmp_w1"] = np.concatenate([w1, w1], axis=0)
    pe = a["nsa_cmp_pe"][0].transpose(2, 0, 1).reshape(DK, 64)
    w2 = a["nsa_cmp_w2"][0].transpose(1, 0, 2).reshape(P, 2 * DK)
    out["cmp_small"] = np.concatenate([np.concatenate([pe, pe], axis=0), w2], axis=1)

    i = np.arange(P)
    c = np.zeros((P, N_CONSTS), f32)

    def const(name, x):
        c[:x.shape[0], CONSTS[name]:CONSTS[name] + x.shape[1]] = x

    const("ident", np.eye(P))
    const("ones", np.ones((P, P)))
    const("mean_ones", np.full((P, P), 1.0 / D))
    const("block_ones", (i[:, None] // 64 == i[None, :] // 64))
    rot = np.zeros((P, P))
    for m in range(P):
        if m % 64 < 8:
            rot[m + 8, m] = -1.0
        elif m % 64 < 16:
            rot[m - 8, m] = 1.0
    const("rot", rot)
    const("same4", i[:, None] // 4 == np.arange(32)[None, :])
    sel = np.zeros((4, 4, P))
    for h in range(4):
        sel[h, h] = 1.0
    const("sel", sel.reshape(4, 512))
    inv_freq = (f32(500000.0) ** (-np.arange(0, 16, 2, dtype=f32) / f32(16))).astype(f32)
    ang = np.arange(S, dtype=f32)[:, None] * inv_freq[None, :]
    cos, sin = np.ones((P, S)), np.zeros((P, S))
    for m in range(P):
        if m % 64 < 16:
            cos[m], sin[m] = np.cos(ang[:, m % 8]), np.sin(ang[:, m % 8])
    const("cos", cos)
    const("sin", sin)
    out["consts"] = c

    out["pT"] = a["p_2"][0, 0].T.reshape(2, P, S).transpose(1, 0, 2)
    w2, a2 = (a[n][0].reshape(P, S) for n in ("rwkv_w2_2", "rwkv_a2_2"))
    out["lora"] = np.stack([w2, a2, a["rwkv_g2_2"][0]], axis=1)
    rw = np.zeros((P, N_RW_CONSTS), f32)
    rw[:, RW_CONSTS["scan"]:RW_CONSTS["scan"] + S] = np.arange(S) % CHUNK != 0
    src, dst = (i % CHUNK)[:, None], np.arange(CHUNK)[None, :]
    for d in range(2):
        before = src < dst if d == 0 else src > dst
        upto = before | (src == dst)
        at = RW_CONSTS[f"score{d}"]
        rw[:, at:at + 256] = np.concatenate([-1.0 * before, -1.0 * upto, 1.0 * before, 1.0 * upto], axis=1)
        for lv in range(LEVELS):
            b = 1 << lv
            at = RW_CONSTS[f"level{d}"] + CHUNK * lv
            rw[:, at:at + CHUNK] = before & (src // (2 * b) == dst // (2 * b)) & (src // b != dst // b)
    rw[:, RW_CONSTS["eye64"]:RW_CONSTS["eye64"] + CHUNK] = src == dst
    out["rw_consts"] = rw

    masks = np.zeros((P, 3 * P), bf16)
    masks[:, 0:P] = np.eye(P)
    masks[:, P:2 * P] = np.where(i[None, :] <= i[:, None], 0.0, -1e30)
    for t in range(TT):
        pos = t * P + i
        end = np.arange(32) * CMP_STRIDE + CMP_BLOCK - 1
        masks[:, 2 * P + 32 * t:2 * P + 32 * t + 32] = np.where(end[None, :] <= pos[:, None], 0.0, -1e30)
    out["masks_bf"] = masks
    return out
```

```python
from contextlib import ExitStack

import concourse.bass as bass
from concourse import mybir

F32 = mybir.dt.float32
F32R = mybir.dt.float32r
BF16 = mybir.dt.bfloat16
ALU = mybir.AluOpType
ACT = mybir.ActivationFunctionType
AX = mybir.AxisListType.X

P = 128
S = 512
D = 1024
KD = D // P
TT = S // P

ML_INNER = 2048
ML_T = ML_INNER // P
ML_HEADS = 4
ML_DH = 512
CONV = 4

NSA_HEADS = 16
NSA_GROUPS = 4
DK = 64
CMP_STRIDE = 16
CMP_BLOCK = 32
N_CMP = (S - CMP_BLOCK) // CMP_STRIDE + 1

DA_HEADS = 4
RW_T = 4
CHUNK = 64
N_CHUNK = S // CHUNK
LEVELS = 6
DECAY_SCALE = 0.6065306597126334
LAMBDA_INIT = 0.8 - 0.6

RAW_SLOTS = 3
BLOCK_COLS = 256


def weight_blocks():
    out = []

    def cols(name, r0, rows, c0, c1):
        while c0 < c1:
            n = min(BLOCK_COLS, c1 - c0)
            out.append((name, r0, rows, c0, n))
            c0 += n

    cols("ml_in", 0, D, 0, 2 * ML_INNER)
    for g in range(2):
        cols("ml_out", g * D, D, 0, D)
    cols("nsa_in", 0, D, 0, 29 * P)
    cols("nsa_out", 0, D, 0, D)
    cols("in_2", 0, D, 0, 43 * P)
    cols("mix_o", 0, D, 0, D)
    cols("out_2", 0, D, 0, D)
    for f in range(4):
        cols("ff1", 0, D, f * D, (f + 1) * D)
        cols("ff2", f * D, D, 0, D)
    cols("ple_gate", 0, D, 0, D)
    cols("ple_proj", 0, 256, 0, D)
    return out


BLOCKS = weight_blocks()
BLOCK_AT, TILE_AT = [], []
_at = _t = 0
for _name, _r0, _rows, _c0, _n in BLOCKS:
    BLOCK_AT.append(_at)
    TILE_AT.append(_t)
    _at += _rows // P * _n
    _t += _n // P
STREAM_COLS = _at
BLOCK_AT.append(_at)
TILE_AT.append(_t)


def first_block(name, nth=0):
    starts = [b for b, x in enumerate(BLOCKS) if x[0] == name and (b == 0 or BLOCKS[b - 1][0] != name or
              (x[3] == 0))]
    return starts[nth]


COLS = {}
_c = 0
for _name, _n in (("ml_norm", 8), ("conv_w", 64), ("conv_b", 16), ("ml_ln_w", 16), ("skip", 16),
                  ("nsa_norm", 8), ("final_norm", 8), ("norm_mix", 8), ("norm_ffn", 8), ("norm_ple", 8),
                  ("norm_final", 8), ("mu_prev", 15), ("mu_next", 15), ("w0", 8), ("a0", 8), ("k_k", 4),
                  ("k_a", 4), ("r_k", 4), ("rw_ln_w", 4), ("rw_ln_b", 4), ("subln", 1), ("b_if", 1),
                  ("b_gate", 1), ("lq1", 1), ("lk1", 1), ("lq2", 1), ("lk2", 1),
                  ("eps6", 1), ("eps5", 1), ("eps_gn", 1), ("one", 1), ("cmp_any", 1)):
    COLS[_name] = _c
    _c += _n
N_COLS = _c

CONSTS = {}
_c = 0
for _name, _n in (("ident", 128), ("ones", 128), ("mean_ones", 128), ("block_ones", 128), ("rot", 128),
                  ("same4", 32), ("sel", 512), ("cos", 512), ("sin", 512)):
    CONSTS[_name] = _c
    _c += _n
N_CONSTS = _c
RW_CONSTS = {}
_c = 0
for _name, _n in (("scan", 512), ("score0", 256), ("score1", 256), ("level0", 6 * 64), ("level1", 6 * 64),
                  ("eye64", 64)):
    RW_CONSTS[_name] = _c
    _c += _n
N_RW_CONSTS = _c

KB = 1024
BASE = 17 * KB


class Core:

    def __init__(self, nc, ctx, io):
        self.nc, self.ctx, self.io = nc, ctx, io
        self.stage, self.in_use, self.spent = None, [], []
        at = self.at
        self.consts = at("consts", [P, N_CONSTS], F32, 0)
        self.cols = at("cols", [P, N_COLS], F32, 9)
        self.ident_bf = at("ident_bf", [P, P], BF16, 10.25)
        self.causal_bf = at("causal_bf", [P, P], BF16, 10.5)
        self.cmp_bf = at("cmp_bf", [P, TT * 32], BF16, 10.75)
        self.small = at("small", [P, 256], F32, 11)
        self.xT = at("xT", [P, KD, S], F32, 12)
        self.act_hi = at("act_hi", [P, KD, S], F32R, 28)
        self.act_lo = at("act_lo", [P, KD, S], F32R, 44)
        self.raw = [at(f"raw{i}", [P, KD * BLOCK_COLS], F32, 60 + 8 * i) for i in range(RAW_SLOTS)]
        self.whi = [at(f"whi{i}", [P, KD * BLOCK_COLS], F32R, 84 + 8 * i) for i in range(2)]
        self.wlo = [at(f"wlo{i}", [P, KD * BLOCK_COLS], F32R, 100 + 8 * i) for i in range(2)]
        self.ps = ctx.enter_context(nc.psum_tensor("ps", [P, 8, S], F32))
        self.landed = [self.sem(f"weights_landed{i}") for i in range(RAW_SLOTS)]
        self.hi_done = self.sem("weights_hi_done")
        self.lo_done = self.sem("weights_lo_done")
        self.tile_done = self.sem("tile_done")
        self.evac_done = self.sem("evac_done")
        self.out_stored = self.sem("out_stored")
        self.loaded = 0

    def at(self, name, shape, dtype, kb):
        return self.nc.alloc_sbuf_tensor_at(name, shape, dtype, offset=BASE + int(kb * KB))

    def region(self, name, shape, dtype, kb):
        return self.at(name, shape, dtype, 116 + kb)

    def sem(self, name):
        s = (self.stage or self.ctx).enter_context(self.nc.semaphore(name))
        self.in_use.append(s)
        return s

    def run(self, stage):
        for first, end in self.spent:
            self.nc.sync.sem_clear(range(first, end))
        self.in_use = []
        with ExitStack() as self.stage:
            stage(self)
            numbers = sorted(s.num for s in self.in_use)
            self.spent = []
            for n in numbers:
                if self.spent and self.spent[-1][1] == n:
                    self.spent[-1][1] = n + 1
                else:
                    self.spent.append([n, n + 1])

    def const(self, name, n=P):
        c = CONSTS[name]
        return self.consts[:, c:c + n]

    def col(self, name, i=0, rows=slice(0, P)):
        c = COLS[name] + i
        return self.cols[rows, c:c + 1]


def load_blocks(k, sp, upto):
    while k.loaded < min(upto, len(BLOCKS)):
        b = k.loaded
        if b >= RAW_SLOTS:
            sp.wait_ge(k.lo_done, b - RAW_SLOTS + 1)
        n = BLOCK_AT[b + 1] - BLOCK_AT[b]
        sp.dma_start(k.raw[b % RAW_SLOTS][:, 0:n], k.io["stream"][:, BLOCK_AT[b]:BLOCK_AT[b + 1]]) \
            .then_inc(k.landed[b % RAW_SLOTS], 16)
        k.loaded += 1


def split_hi(k, act, b):
    if b >= len(BLOCKS):
        return
    n = BLOCK_AT[b + 1] - BLOCK_AT[b]
    act.wait_ge(k.landed[b % RAW_SLOTS], 16 * (b // RAW_SLOTS + 1))
    if b >= 2:
        act.wait_ge(k.tile_done, TILE_AT[b - 1])
    act.activation(k.whi[b % 2][:, 0:n], k.raw[b % RAW_SLOTS][:, 0:n], ACT.Copy).then_inc(k.hi_done, 1)


def split_lo(k, dve, b):
    if b >= len(BLOCKS):
        return
    n = BLOCK_AT[b + 1] - BLOCK_AT[b]
    dve.wait_ge(k.hi_done, b + 1)
    dve.tensor_tensor(k.wlo[b % 2][:, 0:n], k.raw[b % RAW_SLOTS][:, 0:n],
                      k.whi[b % 2][:, 0:n].bitcast(F32), ALU.subtract).then_inc(k.lo_done, 1)


def multiply_tile(k, pe, b, j, fed=None):
    _, _, rows, _, n = BLOCKS[b]
    t = TILE_AT[b] + j
    pe.wait_ge(k.lo_done, b + 1)
    if t >= 4:
        pe.wait_ge(k.evac_done, t - 3)
    bank = k.ps[:, t % 4, :]
    for kt in range(rows // P):
        w = slice(kt * n + j * P, kt * n + j * P + P)
        hi, lo = k.whi[b % 2][:, w], k.wlo[b % 2][:, w]
        if fed:
            pe.wait_ge(fed, kt + 1)
        pe.matmul(bank, hi, k.act_hi[:, kt, :], start=(kt == 0), stop=False)
        pe.matmul(bank, hi, k.act_lo[:, kt, :], start=False, stop=False)
        last = pe.matmul(bank, lo, k.act_hi[:, kt, :], start=False, stop=(kt == rows // P - 1))
    last.then_inc(k.tile_done, 1)


def tiles_of(b0, b1):
    return [(b, j) for b in range(b0, b1) for j in range(BLOCKS[b][4] // P)]


class Norm:

    def __init__(self, k, tag, gain, kb):
        self.k, self.tag, self.gain = k, tag, gain
        self.sq = k.region(f"{tag}_sq", [P, 2, S], F32, kb)
        self.h = k.region(f"{tag}_h", [P, 2, S], F32, kb)
        self.root = k.region(f"{tag}_root", [P, S], F32, kb + 4)

    def squares_stage(self):
        self.sq_done, self.sq_used = self.k.sem(f"{self.tag}_sq_done"), self.k.sem(f"{self.tag}_sq_used")

    def square(self, act, n):
        if n >= 2:
            act.wait_ge(self.sq_used, n - 1)
        act.activation(self.sq[:, n % 2, :], self.k.xT[:, n, :], ACT.Square).then_inc(self.sq_done, 1)

    def mean(self, pe, n):
        pe.wait_ge(self.sq_done, n + 1)
        return pe.matmul(self.k.ps[:, 7, :], self.k.const("mean_ones"), self.sq[:, n % 2, :], start=(n == 0),
                         stop=(n == KD - 1)).then_inc(self.sq_used, 1)

    def scale_stage(self):
        k, tag = self.k, self.tag
        self.root_done, self.inv_done = k.sem(f"{tag}_root_done"), k.sem(f"{tag}_inv_done")
        self.h_done, self.hi_done, self.fed = k.sem(f"{tag}_h_done"), k.sem(f"{tag}_hi_done"), k.sem(f"{tag}_fed")

    def take_root(self, act):
        act.activation(self.root[:], self.k.ps[:, 7, :], ACT.Sqrt, bias=self.k.col("eps6")).then_inc(self.root_done, 1)

    def scale_act(self, act):
        self.take_root(act)
        for i in range(KD):
            act.wait_ge(self.h_done, i + 1)
            act.activation(self.k.act_hi[:, i, :], self.h[:, i % 2, :], ACT.Copy).then_inc(self.hi_done, 1)

    def invert(self, dve):
        dve.wait_ge(self.root_done, 1)
        dve.reciprocal(self.root[:], self.root[:]).then_inc(self.inv_done, 1)
        dve.wait_ge(self.inv_done, 1)

    def scale_dve(self, dve):
        k = self.k
        self.invert(dve)
        for i in range(KD + 1):
            if i < KD:
                if i >= 2:
                    dve.wait_ge(self.fed, i - 1)
                dve.scalar_tensor_tensor(out=self.h[:, i % 2, :], in0=k.xT[:, i, :], scalar=k.col(self.gain, i),
                                         in1=self.root[:], op0=ALU.mult, op1=ALU.mult).then_inc(self.h_done, 1)
            if i >= 1:
                dve.wait_ge(self.hi_done, i)
                dve.tensor_tensor(k.act_lo[:, i - 1, :], self.h[:, (i - 1) % 2, :],
                                  k.act_hi[:, i - 1, :].bitcast(F32), ALU.subtract).then_inc(self.fed, 1)


def stage_norm_residual(k, norm, then=None):
    nc = k.nc
    norm.scale_stage()
    if then:
        then.squares_stage()
    with nc.Block() as block:
        @block.scalar
        def _(act):
            norm.take_root(act)
            if then:
                for i in range(KD):
                    act.wait_ge(norm.h_done, i + 1)
                    then.square(act, i)

        @block.tensor
        def _(pe):
            if then:
                for i in range(KD):
                    then.mean(pe, i)

        @block.vector
        def _(dve):
            norm.invert(dve)
            for i in range(KD):
                dve.scalar_tensor_tensor(out=k.xT[:, i, :], in0=k.xT[:, i, :], scalar=k.col(norm.gain, i),
                                         in1=norm.root[:], op0=ALU.mult, op1=ALU.mult).then_inc(norm.h_done, 1)

        @block.sync
        def _(sp):
            if not then:
                for i in range(0, KD, 2):
                    sp.wait_ge(norm.h_done, i + 2)
                    sp.dma_start(k.io["out"][:, i:i + 2], k.xT[:, i:i + 2]).then_inc(k.out_stored, 16)
                sp.wait_ge(k.out_stored, 16 * KD // 2)


def stage_add(k, b0, b1, norm=None):
    if norm:
        norm.squares_stage()
    tiles = tiles_of(b0, b1)
    with k.nc.Block() as block:
        @block.sync
        def _(sp):
            load_blocks(k, sp, b1 + RAW_SLOTS)

        @block.scalar
        def _(act):
            for n, (b, j) in enumerate(tiles):
                if j == 0:
                    split_hi(k, act, b + 1)
                if norm:
                    act.wait_ge(k.evac_done, TILE_AT[b] + j + 1)
                    norm.square(act, n)

        @block.tensor
        def _(pe):
            for n, (b, j) in enumerate(tiles):
                multiply_tile(k, pe, b, j)
                if norm and n:
                    norm.mean(pe, n - 1)
            if norm:
                norm.mean(pe, KD - 1)

        @block.vector
        def _(dve):
            for n, (b, j) in enumerate(tiles):
                if j == 0:
                    split_lo(k, dve, b + 1)
                t = TILE_AT[b] + j
                dve.wait_ge(k.tile_done, t + 1)
                dve.tensor_tensor(k.xT[:, n, :], k.xT[:, n, :], k.ps[:, t % 4, :], ALU.add) \
                    .then_inc(k.evac_done, 1)


def stage_open(k, norm):
    k.hw = k.region("hw", [P, 3, ML_T, 4], F32, 84)
    hwt = k.region("hwt", [P, 3, ML_T, 4], F32, 60)
    wif = k.region("wif", [P, 3, ML_T, 8], F32, 61)
    wide = k.region("wide", [P, 4, P], F32, 63)
    k.fold = k.region("fold", [P, 2, ML_T, 36], F32, 36)
    got, got_x, got_rest = k.sem("fold_landed"), [k.sem(f"x_landed{i}") for i in range(4)], k.sem("open_landed")
    wide_pool, wide_dve, fold_mm, zeroed = (k.sem("wide_by_pool"), k.sem("wide_by_dve"), k.sem("fold_mm"),
                                            k.sem("fold_zeroed"))
    norm.squares_stage()
    io = k.io
    with k.nc.Block() as block:
        @block.sync
        def _(sp):
            sp.dma_start(hwt[:], io["hwt"]).then_inc(got, 16)
            sp.dma_start(k.consts[:, 0:CONSTS["sel"]], io["consts"][:, 0:CONSTS["sel"]]).then_inc(got, 16)
            sp.dma_start(wif[:], io["wif"]).then_inc(got, 16)
            for i in range(4):
                sp.dma_start(k.xT[:, 2 * i:2 * i + 2], io["xT"][:, 2 * i:2 * i + 2]).then_inc(got_x[i], 16)
            sp.dma_start(k.cols[:], io["cols"]).then_inc(got_rest, 16)
            load_blocks(k, sp, 1)
            sp.dma_start(k.hw[:], io["hw"]).then_inc(got_rest, 16)
            sp.dma_start(k.consts[:, CONSTS["sel"]:], io["consts"][:, CONSTS["sel"]:]).then_inc(got_rest, 16)
            sp.dma_start(k.ident_bf[:], io["masks_bf"][:, 0:P]).then_inc(got_rest, 16)
            sp.dma_start(k.causal_bf[:], io["masks_bf"][:, P:2 * P]).then_inc(got_rest, 16)
            sp.dma_start(k.cmp_bf[:], io["masks_bf"][:, 2 * P:3 * P]).then_inc(got_rest, 16)
            load_blocks(k, sp, RAW_SLOTS)
            sp.wait_ge(got_rest, 96)

        @block.scalar
        def _(act):
            for n in range(KD):
                if n % 2 == 0:
                    act.wait_ge(got_x[n // 2], 16)
                norm.square(act, n)
            split_hi(k, act, 0)

        def widen_own(eng, first, done):
            eng.wait_ge(got, 48)
            for u in range(first, 3 * ML_T, 2):
                if u >= 4:
                    eng.wait_ge(fold_mm, u - 3)
                widen(k, eng, wide[:, u % 4, :], hwt[:, u % 3, u // 3, :]).then_inc(done, 1)

        @block.gpsimd
        def _(pool):
            widen_own(pool, 0, wide_pool)

        @block.tensor
        def _(pe):
            for u in range(3 * ML_T):
                m, t = u % 3, u // 3
                pe.wait_ge((wide_pool, wide_dve)[u % 2], u // 2 + 1)
                x = 1 if m == 2 else 0
                pe.matmul(k.ps[:, 5 + x, 8 * t:8 * t + 8], wide[:, u % 4, :], wif[:, m, t, :],
                          start=(m != 1), stop=(m != 0)).then_inc(fold_mm, 1)
                if u % 4 == 3 and u >= 16:
                    norm.mean(pe, (u - 16) // 4)

        @block.vector
        def _(dve):
            dve.memset(k.fold[:], 0.0).then_inc(zeroed, 1)
            widen_own(dve, 1, wide_dve)
            dve.wait_ge(zeroed, 1)
            dve.wait_ge(fold_mm, 3 * ML_T)
            for x in range(2):
                sums = k.ps[:, 5 + x, 0:8 * ML_T].rearrange("p (t g) -> p t g", g=8)
                for g in range(2):
                    dve.tensor_copy(k.fold[:, x, :, 32 * g:32 * g + 4], sums[:, :, 4 * g:4 * g + 4])
            split_lo(k, dve, 0)


def widen(k, eng, out, blocks):
    return eng.tensor_tensor(out.rearrange("p (n i) -> p n i", i=4),
                             blocks.rearrange("p (o i) -> p o i", o=1).to_broadcast([P, 32, 4]),
                             k.const("same4", 32).rearrange("p (n o) -> p n o", o=1).to_broadcast([P, 32, 4]),
                             ALU.mult)


def stage_ml_inner(k, norm):
    nc = k.nc
    norm.scale_stage()
    b0 = first_block("ml_in")
    b1 = b0 + ML_INNER // BLOCK_COLS
    k.xconv = k.region("xconv", [P, ML_T, S], F32, 0)
    xin = k.region("xin", [P, 2, CONV - 1 + S + 1], F32, 42)
    acc = k.region("conv_acc", [P, 2, S], F32, 47)
    wide = k.region("wide_v", [P, 2, P], F32, 51)
    vout = k.region("v_out", [P, 2, TT, P], F32, 52)
    pad_done, xin_ready, conv_done, xconv_ready = (k.sem("pad_done"), k.sem("xin_ready"), k.sem("conv_done"),
                                                   k.sem("xconv_ready"))
    conv_step = k.sem("conv_step")
    wide_done, v_mm, v_copied, gate_mm = k.sem("wide_v_done"), k.sem("v_mm"), k.sem("v_copied"), k.sem("gate_mm")
    k.v_stored = [k.sem(f"v_stored{i}") for i in range(2)]

    def store_v(act, t):
        act.wait_ge(v_copied, t + 1)
        act.dma_start(k.io["v_scratch"][t // 4][:, :, (t % 4) * P:(t % 4 + 1) * P], vout[:, t % 2]) \
            .then_inc(k.v_stored[t % 2], 16)

    def conv_in(t, tap):
        return xin[:, t % 2, tap:tap + S]

    with nc.Block() as block:
        @block.sync
        def _(sp):
            load_blocks(k, sp, b1 + RAW_SLOTS)

        @block.gpsimd
        def _(pool):
            for t in range(ML_T):
                if t >= 2:
                    pool.wait_ge(v_mm, t - 1)
                widen(k, pool, wide[:, t % 2, :], k.hw[:, 2, t, :]).then_inc(wide_done, 1)

        @block.scalar
        def _(act):
            norm.scale_act(act)
            act.wait_ge(pad_done, 1)
            for t in range(ML_T + 1):
                if t < ML_T:
                    if t % 2 == 0:
                        split_hi(k, act, b0 + t // 2 + 1)
                    tile = TILE_AT[b0] + t
                    act.wait_ge(k.tile_done, tile + 1)
                    if t >= 2:
                        act.wait_ge(conv_done, t - 1)
                        act.wait_ge(gate_mm, t - 1)
                    act.activation(xin[:, t % 2, CONV - 1:CONV - 1 + S], k.ps[:, tile % 4, :], ACT.Copy) \
                        .then_inc(xin_ready, 1)
                    act.wait_ge(xin_ready, t + 1)
                    act.sem_inc(k.evac_done, 1)
                if t >= 1:
                    act.wait_ge(conv_done, t)
                    act.activation(k.xconv[:, t - 1, :], acc[:, (t - 1) % 2, :], ACT.Silu).then_inc(xconv_ready, 1)
                if t >= 2:
                    store_v(act, t - 2)
            store_v(act, ML_T - 1)
            for i in range(2):
                act.wait_ge(k.v_stored[i], 16 * ML_T // 2)

        @block.vector
        def _(dve):
            dve.memset(xin[:, :, 0:CONV - 1], 0.0).then_inc(pad_done, 1)
            norm.scale_dve(dve)
            for t in range(ML_T + 1):
                if t < ML_T:
                    if t % 2 == 0:
                        split_lo(k, dve, b0 + t // 2 + 1)
                    dve.wait_ge(xin_ready, t + 1)
                    if t >= 2:
                        dve.wait_ge(xconv_ready, t - 1)
                    dve.tensor_scalar(acc[:, t % 2, :], conv_in(t, 0), k.col("conv_w", 0 * ML_T + t),
                                      k.col("conv_b", t), ALU.mult, ALU.add).then_inc(conv_step, 1)
                    for tap in range(1, CONV):
                        dve.wait_ge(conv_step, (CONV - 1) * t + tap)
                        dve.scalar_tensor_tensor(out=acc[:, t % 2, :], in0=conv_in(t, tap),
                                                 scalar=k.col("conv_w", tap * ML_T + t), in1=acc[:, t % 2, :],
                                                 op0=ALU.mult, op1=ALU.add) \
                            .then_inc(conv_step if tap < CONV - 1 else conv_done, 1)
                if t >= 1:
                    u = t - 1
                    dve.wait_ge(v_mm, u + 1)
                    if u >= 2:
                        dve.wait_ge(k.v_stored[u % 2], 16 * (u // 2))
                    dve.tensor_copy(vout[:, u % 2].rearrange("p a n -> p (a n)"), k.ps[:, 4 + u % 2, :]) \
                        .then_inc(v_copied, 1)

        @block.tensor
        def _(pe):
            for t in range(ML_T + 1):
                if t < ML_T:
                    multiply_tile(k, pe, b0 + t // 2, t % 2, norm.fed if t == 0 else None)
                if t >= 1:
                    u = t - 1
                    pe.wait_ge(xin_ready, u + 1)
                    pe.wait_ge(wide_done, u + 1)
                    if u >= 2:
                        pe.wait_ge(v_copied, u - 1)
                    for i in range(TT):
                        last = pe.matmul(k.ps[:, 4 + u % 2, i * P:(i + 1) * P],
                                         xin[:, u % 2, CONV - 1 + i * P:CONV - 1 + (i + 1) * P],
                                         wide[:, u % 2, :], start=True, stop=True)
                    last.then_inc(v_mm, 1)
                    pe.matmul(k.ps[0:36, 6, :], k.fold[:, 1, u, :], xin[:, u % 2, CONV - 1:CONV - 1 + S],
                              start=(u == 0), stop=False)
                    pe.wait_ge(xconv_ready, u + 1)
                    pe.matmul(k.ps[0:36, 6, :], k.fold[:, 0, u, :], k.xconv[:, u, :], start=False,
                              stop=(u == ML_T - 1)).then_inc(gate_mm, 1)


def stage_ml_gate(k):
    nc = k.nc
    b0 = first_block("ml_in") + ML_INNER // BLOCK_COLS
    b1 = b0 + ML_INNER // BLOCK_COLS
    zt = k.region("zt", [P, 4, S], F32, 32)
    rows = k.region("gate_rows", [4, 10, S], F32, 42)
    k.neg_m = k.region("neg_m", [4, S], F32, 86)
    k.g_col = k.small[:, 0:16].rearrange("p (t h) -> p t h", h=4)
    k.floor_col = k.small[:, 16:32].rearrange("p (t h) -> p t h", h=4)
    inp, fg, mag, ex, ln, neg, run, g, top, floor = (rows[:, i, :] for i in range(10))
    k.z_stored = [k.sem(f"z_stored{i}") for i in range(4)]
    z_ready, a_step, d_step, g_tr, g_out = (k.sem("z_ready"), k.sem("gate_act_step"), k.sem("gate_dve_step"),
                                            k.sem("g_transposed"), k.sem("g_out"))
    zeros = k.sem("gate_zeros")
    zero, one = rows[:, 3, :], rows[:, 2, :]
    with nc.Block() as block:
        @block.sync
        def _(sp):
            load_blocks(k, sp, b1 + RAW_SLOTS)

        @block.scalar
        def _(act):
            f32r = slice(32, 36)
            act.activation(inp, k.ps[0:4, 6, :], ACT.Identity, bias=k.col("b_if", rows=slice(0, 4))).then_inc(a_step, 1)
            act.activation(fg, k.ps[f32r, 6, :], ACT.Identity, bias=k.col("b_if", rows=f32r)).then_inc(a_step, 1)
            act.wait_ge(a_step, 2)
            act.activation(mag, fg, ACT.Abs).then_inc(a_step, 1)
            act.wait_ge(a_step, 3)
            act.activation(ex, mag, ACT.Exp, scale=-1.0).then_inc(a_step, 1)
            act.wait_ge(a_step, 4)
            act.activation(ln, ex, ACT.Ln, bias=k.col("one", rows=slice(0, 4))).then_inc(a_step, 1)
            act.wait_ge(d_step, 8)
            act.activation(floor, floor, ACT.Exp, scale=-1.0).then_inc(a_step, 1)
            for t in range(ML_T):
                if t % 2 == 0:
                    split_hi(k, act, b0 + t // 2 + 1)
                tile = TILE_AT[b0] + t
                act.wait_ge(k.tile_done, tile + 1)
                if t >= 4:
                    act.wait_ge(k.z_stored[t % 4], 16 * (t // 4))
                act.activation(zt[:, t % 4, :], k.ps[:, tile % 4, :], ACT.Silu).then_inc(z_ready, 1)
                act.wait_ge(z_ready, t + 1)
                act.sem_inc(k.evac_done, 1)
                act.dma_start(k.io["z_scratch"][t], zt[:, t % 4, :]).then_inc(k.z_stored[t % 4], 16)
            for i in range(4):
                act.wait_ge(k.z_stored[i], 16 * ML_T // 4)

        @block.vector
        def _(dve):
            dve.wait_ge(a_step, 5)
            dve.memset(zero, 0.0).then_inc(d_step, 1)
            dve.memset(one, 1.0).then_inc(d_step, 1)
            dve.tensor_scalar(neg, fg, 0.0, None, ALU.min).then_inc(d_step, 1)
            dve.wait_ge(d_step, 3)
            dve.tensor_tensor(neg, neg, ln, ALU.subtract).then_inc(d_step, 1)
            dve.wait_ge(d_step, 4)
            dve.tensor_tensor_scan(run, one, neg, 0.0, ALU.mult, ALU.add).then_inc(d_step, 1)
            dve.wait_ge(d_step, 5)
            dve.tensor_tensor(g, inp, run, ALU.subtract).then_inc(d_step, 1)
            dve.wait_ge(d_step, 6)
            dve.tensor_tensor_scan(top, g, zero, 0.0, ALU.max, ALU.max).then_inc(d_step, 1)
            dve.wait_ge(d_step, 7)
            dve.tensor_tensor(floor, run, top, ALU.add).then_inc(d_step, 1)
            dve.tensor_scalar(k.neg_m[:], top, -1.0, None, ALU.mult)
            for t in range(0, ML_T, 2):
                split_lo(k, dve, b0 + t // 2 + 1)
                if t == 2:
                    dve.wait_ge(g_tr, 2)
                    dve.tensor_copy(k.small[:, 0:32], k.ps[:, 7, 0:32]).then_inc(g_out, 1)

        @block.tensor
        def _(pe):
            for t in range(ML_T):
                multiply_tile(k, pe, b0 + t // 2, t % 2)
                if t == 1:
                    pe.wait_ge(a_step, 6)
                    pe.wait_ge(d_step, 8)
                    for n, row in enumerate((g, floor)):
                        for i in range(TT):
                            c = 16 * n + 4 * i
                            last = pe.transpose(k.ps[:, 7, c:c + 4], row[:, i * P:(i + 1) * P],
                                                k.const("ident")[0:4, 0:4])
                        last.then_inc(g_tr, 1)


def stage_ml_heads(k, first):
    nc = k.nc
    tag = f"ml{first}"
    v = k.region(f"{tag}_v", [P, TT, S], F32, 32)
    q = k.region(f"{tag}_q", [P, TT, S], F32, 40)
    kk = k.region(f"{tag}_k", [P, TT, S], F32, 48)
    st = k.region(f"{tag}_st", [P, TT, S], F32, 56)
    wexp = k.region(f"{tag}_wexp", [P, 2, S], F32, 64)
    z = k.region(f"{tag}_z", [P, 2, S], F32, 68)
    wide = k.region(f"{tag}_wide", [P, 2, 2, P], F32, 72)
    y = k.region(f"{tag}_y", [P, 2, S], F32, 74)
    sc = k.small
    den, adn, r, sd, scale, shift = (sc[:, 32 + 4 * i:36 + 4 * i] for i in range(6))
    stats = sc[:, 64:64 + 24].rearrange("p (t s) -> p t s", s=6)
    mv = sc[:, 96:104].rearrange("p (t s) -> p t s", s=2)
    r2v = sc[:, 104:108]
    s = {n: k.sem(f"{tag}_{n}") for n in ("v_landed", "wide_done", "qk_mm", "q_copied", "k_copied", "nm_mm", "sc_mm",
                                          "wexp_raw", "wexp_done", "st_done", "h_mm", "hn_done", "tr_mm", "y_read",
                                          "y_done", "y_hi", "y_lo", "step", "r2v_done", "sd_done", "scale_done", "t1")}
    zl = [k.sem(f"{tag}_z_landed{i}") for i in range(2)]
    heads = range(2)

    def lo(dve, u):
        dve.wait_ge(s["y_hi"], u + 1)
        dve.tensor_tensor(k.act_lo[:, u, :], y[:, u % 2, :], k.act_hi[:, u, :].bitcast(F32), ALU.subtract) \
            .then_inc(s["y_lo"], 1)

    with nc.Block() as block:
        @block.sync
        def _(sp):
            for h in heads:
                if h:
                    sp.wait_ge(s["h_mm"], TT * h)
                sp.dma_start(v[:], k.io["v_scratch"][first + h]).then_inc(s["v_landed"], 16)
                for c in range(TT):
                    u = TT * h + c
                    if u >= 2:
                        sp.wait_ge(s["y_done"], u - 1)
                    sp.dma_start(z[:, c % 2, :], k.io["z_scratch"][TT * (first + h) + c]).then_inc(zl[c % 2], 16)

        @block.gpsimd
        def _(pool):
            for h in heads:
                for c in range(TT):
                    u = TT * h + c
                    if u >= 2:
                        pool.wait_ge(s["qk_mm"], u - 1)
                    t = TT * (first + h) + c
                    widen(k, pool, wide[:, c % 2, 0, :], k.hw[:, 0, t, :]).then_inc(s["wide_done"], 1)
                    widen(k, pool, wide[:, c % 2, 1, :], k.hw[:, 1, t, :]).then_inc(s["wide_done"], 1)
                for j in range(TT):
                    pool.wait_ge(s["wexp_raw"], TT * h + j + 1)
                    part = wexp[:, j % 2, j * P:(j + 1) * P]
                    pool.affine_select(out=part, in_=part, compare_op=ALU.is_ge, fill=0.0, base=0,
                                       pattern=[[1, P]], channel_multiplier=-1).then_inc(s["wexp_done"], 1)

        @block.tensor
        def _(pe):
            for h in heads:
                if h:
                    pe.wait_ge(s["y_read"], TT * h)
                for c in range(TT):
                    u = TT * h + c
                    pe.wait_ge(s["wide_done"], 2 * u + 2)
                    if u:
                        pe.wait_ge(s["q_copied"], u)
                        pe.wait_ge(s["k_copied"], u)
                    x = k.xconv[:, TT * (first + h) + c, :]
                    pe.matmul(k.ps[:, 4, :], wide[:, c % 2, 0, :], x, start=True, stop=True)
                    pe.matmul(k.ps[:, 5, :], wide[:, c % 2, 1, :], x, start=True, stop=True).then_inc(s["qk_mm"], 1)
                pe.matmul(k.ps[:, 6, :], k.const("sel", 512)[0:4, (first + h) * P:(first + h + 1) * P], k.neg_m[:],
                          start=True, stop=True).then_inc(s["nm_mm"], 1)
                pe.wait_ge(s["q_copied"], TT * (h + 1))
                pe.wait_ge(s["k_copied"], TT * (h + 1))
                for j in range(TT):
                    if j >= 2:
                        pe.wait_ge(s["st_done"], TT * h + j - 1)
                    for c in range(TT):
                        last = pe.matmul(k.ps[:, 4 + j % 2, j * P:S], kk[:, c, j * P:(j + 1) * P], q[:, c, j * P:S],
                                         start=(c == 0), stop=(c == TT - 1))
                    last.then_inc(s["sc_mm"], 1)
                pe.wait_ge(s["v_landed"], 16 * (h + 1))
                if h:
                    pe.wait_ge(s["hn_done"], TT * h)
                for i in range(TT):
                    pe.wait_ge(s["st_done"], TT * h + i + 1)
                    for j in range(i + 1):
                        lhs = st[:, j, i * P:(i + 1) * P]
                        pe.matmul(k.ps[:, i, :], lhs, v[:, j, :], start=(j == 0), stop=(j == i))
                        last = pe.matmul(k.ps[:, 7, i:i + 1], lhs, k.const("ones")[:, 0:1], start=(j == 0), stop=(j == i))
                    last.then_inc(s["h_mm"], 1)
                pe.wait_ge(s["hn_done"], TT * (h + 1))
                for c in range(TT):
                    if c >= 2:
                        pe.wait_ge(s["y_read"], TT * h + c - 1)
                    for i in range(TT):
                        last = pe.transpose(k.ps[:, 4 + c % 2, i * P:(i + 1) * P], kk[:, i, c * P:(c + 1) * P],
                                            k.const("ident"))
                    last.then_inc(s["tr_mm"], 1)

        @block.scalar
        def _(act):
            for h in heads:
                for c in range(TT):
                    act.wait_ge(s["qk_mm"], TT * h + c + 1)
                    act.activation(q[:, c, :], k.ps[:, 4, :], ACT.Copy).then_inc(s["q_copied"], 1)
                act.wait_ge(s["nm_mm"], h + 1)
                for j in range(TT):
                    u = TT * h + j
                    if u >= 2:
                        act.wait_ge(s["st_done"], u - 1)
                    act.activation(wexp[:, j % 2, j * P:S], k.ps[:, 6, j * P:S], ACT.Exp,
                                   bias=k.g_col[:, j, first + h:first + h + 1]).then_inc(s["wexp_raw"], 1)
                act.wait_ge(s["r2v_done"], h + 1)
                act.activation(sd, r2v, ACT.Sqrt, bias=k.col("eps6")).then_inc(s["sd_done"], 1)
                act.wait_ge(s["scale_done"], h + 1)
                for i in range(TT):
                    act.activation(kk[:, i, :], k.ps[:, i, :], ACT.Identity, scale=scale[:, i:i + 1],
                                   bias=shift[:, i:i + 1]).then_inc(s["hn_done"], 1)
                for c in range(TT):
                    u = TT * h + c
                    act.wait_ge(s["y_done"], u + 1)
                    act.activation(k.act_hi[:, u, :], y[:, c % 2, :], ACT.Copy).then_inc(s["y_hi"], 1)

        @block.vector
        def _(dve):
            step = [0]

            def then_wait(ins):
                step[0] += 1
                ins.then_inc(s["step"], 1)
                dve.wait_ge(s["step"], step[0])

            for h in heads:
                for c in range(TT):
                    dve.wait_ge(s["qk_mm"], TT * h + c + 1)
                    dve.tensor_copy(kk[:, c, :], k.ps[:, 5, :]).then_inc(s["k_copied"], 1)
                for j in range(TT):
                    u = TT * h + j
                    dve.wait_ge(s["sc_mm"], u + 1)
                    dve.wait_ge(s["wexp_done"], u + 1)
                    dve.scalar_tensor_tensor(out=st[:, j, j * P:S], in0=k.ps[:, 4 + j % 2, j * P:S],
                                             scalar=ML_DH ** -0.5, in1=wexp[:, j % 2, j * P:S],
                                             op0=ALU.mult, op1=ALU.mult).then_inc(s["st_done"], 1)
                for i in range(TT):
                    dve.wait_ge(s["h_mm"], TT * h + i + 1)
                    then_wait(dve.bn_stats(stats[:, i, :], k.ps[:, i, :]))
                    then_wait(dve.bn_aggr(mv[:, i, :], stats[:, i, :]))
                floor = k.floor_col[:, :, first + h]
                then_wait(dve.tensor_copy(den, k.ps[:, 7, 0:TT]))
                then_wait(dve.scalar_tensor_tensor(out=adn, in0=den, scalar=-1.0, in1=den, op0=ALU.mult, op1=ALU.max))
                then_wait(dve.tensor_tensor(adn, adn, floor, ALU.max))
                then_wait(dve.reciprocal(r, adn))
                then_wait(dve.tensor_tensor(r2v, mv[:, :, 1], r, ALU.mult))
                dve.tensor_tensor(r2v, r2v, r, ALU.mult).then_inc(s["r2v_done"], 1)
                dve.wait_ge(s["sd_done"], h + 1)
                then_wait(dve.reciprocal(sd, sd))
                then_wait(dve.tensor_tensor(scale, sd, r, ALU.mult))
                dve.scalar_tensor_tensor(out=shift, in0=mv[:, :, 0], scalar=-1.0, in1=scale, op0=ALU.mult,
                                         op1=ALU.mult).then_inc(s["scale_done"], 1)
                for c in range(TT):
                    u = TT * h + c
                    t = TT * (first + h) + c
                    x = k.xconv[:, t, :]
                    if u >= 2:
                        dve.wait_ge(s["y_lo"], u - 1)
                    then_wait(dve.tensor_scalar(y[:, c % 2, :], x, k.col("skip", t), None, ALU.mult))
                    dve.wait_ge(s["tr_mm"], u + 1)
                    dve.scalar_tensor_tensor(out=y[:, c % 2, :], in0=k.ps[:, 4 + c % 2, :], scalar=k.col("ml_ln_w", t),
                                             in1=y[:, c % 2, :], op0=ALU.mult, op1=ALU.add).then_inc(s["y_read"], 1)
                    dve.wait_ge(s["y_read"], u + 1)
                    dve.wait_ge(zl[c % 2], 16 * (u // 2 + 1))
                    dve.tensor_tensor(y[:, c % 2, :], y[:, c % 2, :], z[:, c % 2, :], ALU.mult).then_inc(s["y_done"], 1)
                    if c:
                        lo(dve, u - 1)
                lo(dve, TT * h + TT - 1)


class Steps:

    def __init__(self, sem):
        self.sem, self.n = sem, 0

    def then_wait(self, eng, ins):
        self.n += 1
        ins.then_inc(self.sem, 1)
        eng.wait_ge(self.sem, self.n)


def stage_nsa_in(k, norm):
    nc = k.nc
    norm.scale_stage()
    b0 = first_block("nsa_in")
    b1 = first_block("nsa_out")
    k.q = k.region("nsa_q", [P, 8, S], F32, 0)
    k.kv = k.region("nsa_kv", [P, 8, S], F32, 16)
    k.gate_rows = k.region("nsa_gates", [48, S], F32, 32)
    k.padded = [k.region(f"cmp_in{i}", [P, 4, S + CMP_BLOCK], F32, at) for i, at in enumerate((34, 75.5))]
    k.w1 = [k.region(f"cmp_w1_{i}", [P, CMP_BLOCK, P], F32, 42.5 + 16 * i) for i in range(2)]
    k.cmp_small = k.region("cmp_small", [P, 2 * 32 + 2 * 64], F32, 74.5)
    zt = k.region("nsa_zt", [P, 2, S], F32, 84)
    zeroed = k.sem("nsa_zeroed")
    landed = k.sem("nsa_landed")
    z_ready, copied = k.sem("nsa_z_ready"), k.sem("nsa_copied")
    stored = [k.sem(f"nsa_z_stored{i}") for i in range(2)]
    with nc.Block() as block:
        @block.sync
        def _(sp):
            for i in range(2):
                sp.dma_start(k.w1[i][:], k.io["cmp_w1"][:, i]).then_inc(landed, 16)
            sp.dma_start(k.cmp_small[:], k.io["cmp_small"]).then_inc(landed, 16)
            load_blocks(k, sp, b1 + RAW_SLOTS)
            sp.wait_ge(landed, 48)

        @block.gpsimd
        def _(pool):
            for x in range(2):
                pool.memset(k.padded[x][:], 0.0).then_inc(zeroed, 1)

        @block.scalar
        def _(act):
            norm.scale_act(act)
            for t, (b, j) in enumerate(tiles_of(b0, b1)):
                if j == 0:
                    split_hi(k, act, b + 1)
                tile = TILE_AT[b] + j
                act.wait_ge(k.tile_done, tile + 1)
                bank = k.ps[:, tile % 4, :]
                if 8 <= t < 12:
                    act.wait_ge(zeroed, 2)
                    for half in range(2):
                        rows = slice(64 * half, 64 * half + 64)
                        act.activation(k.padded[(t - 8) // 2][rows, 2 * half + t % 2, 0:S], bank[rows], ACT.Copy) \
                            .then_inc(copied, 1)
                    act.wait_ge(copied, 2 * (t - 7))
                    act.sem_inc(k.evac_done, 1)
                elif t < 20:
                    out = k.q[:, t, :] if t < 8 else k.kv[:, t - 12, :]
                    act.activation(out, bank, ACT.Copy).then_inc(k.evac_done, 1)
                elif t < 28:
                    z = t - 20
                    if z == 0:
                        act.wait_ge(norm.fed, KD)
                    if z >= 2:
                        act.wait_ge(stored[z % 2], 16 * (z // 2))
                    act.activation(zt[:, z % 2, :], bank, ACT.Silu).then_inc(z_ready, 1)
                    act.wait_ge(z_ready, z + 1)
                    act.sem_inc(k.evac_done, 1)
                    act.dma_start(k.io["z_scratch"][z], zt[:, z % 2, :]).then_inc(stored[z % 2], 16)
                else:
                    act.activation(k.gate_rows[:], bank[0:48], ACT.Sigmoid, bias=k.col("b_gate", rows=slice(0, 48))) \
                        .then_inc(k.evac_done, 1)
            for i in range(2):
                act.wait_ge(stored[i], 64)

        @block.tensor
        def _(pe):
            for t, (b, j) in enumerate(tiles_of(b0, b1)):
                multiply_tile(k, pe, b, j, norm.fed if t == 0 else None)

        @block.vector
        def _(dve):
            norm.scale_dve(dve)
            for b in range(b0, b1):
                split_lo(k, dve, b + 1)


def stage_nsa_prep(k):
    nc = k.nc
    k.vtok = k.at("nsa_vtok", [P, 2, TT, 256], F32, 52)
    k.gtok = k.region("nsa_gtok", [P, TT, 48], F32, 84)
    k.kcmp = k.region("kcmp", [P, 2, 32], F32, 84.75)
    k.vcmp = k.region("vcmp", [P, 4, 4, DK], F32, 85)
    hid = k.region("cmp_hid", [P, 2, 2, 2, 31], F32, 89)
    peb = k.small[:, 0:2]
    k.q_rot = k.at("q_rot", [P, 8, S], F32, 28)
    turned = k.at("turned", [P, 2, S], F32, 44)
    straight = k.at("straight", [P, 2, S], F32, 48)
    s = {n: k.sem(f"prep_{n}") for n in ("rot_mm", "rot_read", "straight", "turned", "done", "tr", "tr_read", "hid_mm",
                                         "pe_in", "pe_read", "hid_done", "cmp_mm", "cmp_read", "zeroed", "v_mm")}
    pairs = [(k.q, i, k.q_rot, i) for i in range(8)] + [(k.kv, i, k.kv, i) for i in (0, 1, 4, 5)]
    w2 = k.cmp_small[:, 64:192].rearrange("p (x d) -> p x d", d=DK)
    pe_t = k.cmp_small[:, 0:64].rearrange("p (x t) -> p x t", t=CMP_BLOCK)
    V = N_CMP + 2
    with nc.Block() as block:
        @block.tensor
        def _(pe):
            def turn(n):
                src, i, _, _ = pairs[n]
                if n >= 2:
                    pe.wait_ge(s["rot_read"], n - 1)
                pe.matmul(k.ps[:, 4 + n % 2, :], k.const("rot"), src[:, i, :], start=True, stop=True) \
                    .then_inc(s["rot_mm"], 1)

            for x in range(2):
                for t in range(CMP_BLOCK):
                    u = CMP_BLOCK * x + t
                    if u % 5 == 0 and u // 5 < len(pairs):
                        turn(u // 5)
                    if t == 0:
                        pe.wait_ge(s["pe_in"], x + 1)
                    last = pe.matmul(k.ps[:, 2 + x, 0:4 * V].rearrange("p (a n) -> p a n", n=V), k.w1[x][:, t, :],
                                     k.padded[x][:, :, t:t + (V - 1) * CMP_STRIDE + 1:CMP_STRIDE],
                                     start=(t == 0), stop=(t == CMP_BLOCK - 1))
                last.then_inc(s["hid_mm"], 1)
            for n in range(5):
                if n >= 2:
                    pe.wait_ge(s["tr_read"], n - 1)
                for i in range(TT):
                    if n < 4:
                        last = pe.transpose(k.ps[:, n % 2, i * P:(i + 1) * P],
                                            k.kv[:, 2 + 4 * (n // 2) + n % 2, i * P:(i + 1) * P], k.const("ident"))
                    else:
                        last = pe.transpose(k.ps[:, 0, i * 48:(i + 1) * 48], k.gate_rows[:, i * P:(i + 1) * P],
                                            k.const("ident")[0:48, 0:48])
                last.then_inc(s["tr"], 1)
            pe.wait_ge(s["hid_done"], 2)
            for half in range(2):
                rows = slice(64 * half, 64 * half + 64)
                for gp in range(2):
                    pe.matmul(k.ps[rows, 6, 32 * gp:32 * gp + N_CMP], w2[:, 0, :], hid[:, 0, half, gp, :],
                              start=True, stop=True)
            for hh in range(4):
                for g in range(4):
                    last = pe.matmul(k.ps[32 * hh:32 * hh + N_CMP, 7, g * DK:(g + 1) * DK], hid[:, 1, g % 2, g // 2, :],
                                     w2[:, 1, :], start=True, stop=True)
            last.then_inc(s["v_mm"], 1)

        @block.scalar
        def _(act):
            for x in range(2):
                act.wait_ge(s["hid_mm"], x + 1)
                act.activation(peb[:, x:x + 1], k.ps[:, 2 + x, V - 1:V], ACT.Copy).then_inc(s["pe_read"], 1)
                act.wait_ge(s["pe_read"], x + 1)
                act.activation(hid[:, x].rearrange("p h a n -> p (h a) n"),
                               k.ps[:, 2 + x, 0:4 * V].rearrange("p (a n) -> p a n", n=V)[:, :, 0:N_CMP],
                               ACT.Silu, bias=peb[:, x:x + 1]).then_inc(s["hid_done"], 1)
            for n in range(4):
                act.wait_ge(s["tr"], n + 1)
                act.activation(k.vtok[:, n // 2, :, n % 2 * P:(n % 2 + 1) * P],
                               k.ps[:, n % 2, :].rearrange("p (t c) -> p t c", c=P), ACT.Copy).then_inc(s["tr_read"], 1)
            act.wait_ge(s["tr"], 5)
            act.activation(k.gtok[:].rearrange("p t c -> p (t c)"), k.ps[:, 0, 0:192], ACT.Copy)

        @block.gpsimd
        def _(pool):
            for x in range(2):
                pool.tensor_copy(k.padded[x][0:64, 0, S:S + CMP_BLOCK], pe_t[0:64, x, :]).then_inc(s["pe_in"], 1)
            pool.memset(k.vcmp[:], 0.0).then_inc(s["zeroed"], 1)
            for n, (src, i, _, _) in enumerate(pairs):
                if n >= 2:
                    pool.wait_ge(s["done"], n - 1)
                pool.tensor_tensor(straight[:, n % 2, :], src[:, i, :], k.const("cos", S), ALU.mult) \
                    .then_inc(s["straight"], 1)

        @block.vector
        def _(dve):
            for n, (src, i, dst, o) in enumerate(pairs):
                dve.wait_ge(s["rot_mm"], n + 1)
                if n >= 2:
                    dve.wait_ge(s["done"], n - 1)
                dve.tensor_tensor(turned[:, n % 2, :], k.ps[:, 4 + n % 2, :], k.const("sin", S), ALU.mult) \
                    .then_inc(s["rot_read"], 1)
                dve.wait_ge(s["rot_read"], n + 1)
                dve.wait_ge(s["straight"], n + 1)
                dve.tensor_tensor(dst[:, o, :], turned[:, n % 2, :], straight[:, n % 2, :], ALU.add) \
                    .then_inc(s["done"], 1)
            dve.wait_ge(s["v_mm"], 1)
            dve.tensor_copy(k.kcmp[:, :, 0:N_CMP], k.ps[:, 6, 0:64].rearrange("p (a n) -> p a n", n=32)[:, :, 0:N_CMP])
            dve.wait_ge(s["zeroed"], 1)
            for hh in range(4):
                rows = slice(32 * hh, 32 * hh + N_CMP)
                dve.tensor_copy(k.vcmp[rows, :, hh, :], k.ps[rows, 7, 0:256].rearrange("p (g d) -> p g d", d=DK))


def stage_nsa_cmp(k):
    nc = k.nc
    k.o = k.region("nsa_o", [P, TT, NSA_HEADS * DK], F32, 42)
    p = k.region("cmp_p", [P, 2, NSA_HEADS, 32], F32, 58)
    pt = k.region("cmp_pt", [P, 2, 4, P], F32, 62)
    top = k.small[:, 8:24]
    total = k.small[:, 24:40]
    weight = k.small[:, 40:56]
    s = {n: k.sem(f"cmp_{n}") for n in ("zeroed", "sc_mm", "p_ready", "exp_done", "tr_mm", "tr_read", "pv_mm", "o_done",
                                        "step")}
    with nc.Block() as block:
        @block.tensor
        def _(pe):
            for i in range(TT):
                if i:
                    pe.wait_ge(s["p_ready"], i)
                mask = k.cmp_bf[:, 32 * i:32 * i + N_CMP].rearrange("p (o c) -> p o c", o=1).to_broadcast([P, 8, N_CMP])
                for par in range(2):
                    bank = k.ps[:, par, 0:256].rearrange("p (h c) -> p h c", c=32)[:, :, 0:N_CMP]
                    pe.matmul(bank, k.ident_bf[:], mask, start=True, stop=False)
                for a in range(8):
                    for par in range(2):
                        rows = slice(64 * par, 64 * par + 64)
                        last = pe.matmul(k.ps[:, par, 32 * a:32 * a + N_CMP], k.q[rows, a, i * P:(i + 1) * P],
                                         k.kcmp[rows, a // 4, 0:N_CMP], start=False, stop=(a == 7))
                last.then_inc(s["sc_mm"], 1)
                pe.wait_ge(s["exp_done"], i + 1)
                if i:
                    pe.wait_ge(s["tr_read"], i)
                for g in range(4):
                    at = 8 * (g % 2) + 4 * (g // 2)
                    last = pe.transpose(k.ps[:, 2, g * P:(g + 1) * P],
                                        p[:, i % 2, at:at + 4, :].rearrange("p h c -> p (h c)"), k.const("ident"))
                last.then_inc(s["tr_mm"], 1)
                pe.wait_ge(s["tr_read"], i + 1)
                if i:
                    pe.wait_ge(s["o_done"], i)
                for g in range(4):
                    last = pe.matmul(k.ps[:, 4 + g // 2, g % 2 * 256:g % 2 * 256 + 256], pt[:, i % 2, g, :],
                                     k.vcmp[:, g].rearrange("p h d -> p (h d)"), start=True, stop=True)
                last.then_inc(s["pv_mm"], 1)

        @block.scalar
        def _(act):
            for i in range(TT):
                act.wait_ge(s["p_ready"], i + 1)
                x = p[:, i % 2, :, 0:N_CMP]
                act.activation(x, x, ACT.Exp, scale=DK ** -0.5).then_inc(s["exp_done"], 1)

        @block.vector
        def _(dve):
            steps = Steps(s["step"])
            steps.then_wait(dve, dve.memset(p[:], 0.0))
            for i in range(TT):
                dve.wait_ge(s["sc_mm"], i + 1)
                sc = k.ps[:, 0:2, 0:256].rearrange("p b (h c) -> p b h c", c=32)[:, :, :, 0:N_CMP]
                steps.then_wait(dve, dve.tensor_reduce(top.rearrange("p (b h) -> p b h", b=2), sc, AX, ALU.max))
                if i >= 2:
                    dve.wait_ge(s["tr_mm"], i - 1)
                dve.tensor_tensor(p[:, i % 2, :, 0:N_CMP].rearrange("p (b h) c -> p b h c", b=2), sc,
                                  top.rearrange("p (b h o) -> p b h o", b=2, o=1).to_broadcast([P, 2, 8, N_CMP]),
                                  ALU.subtract).then_inc(s["p_ready"], 1)
                dve.wait_ge(s["exp_done"], i + 1)
                steps.then_wait(dve, dve.tensor_reduce(total, p[:, i % 2, :, 0:N_CMP], AX, ALU.add))
                steps.then_wait(dve, dve.reciprocal(total, total))
                gates = k.gtok[:, i, :].rearrange("p (a b h c) -> p b a h c", a=2, b=2, c=3)[:, :, :, :, 0]
                v4 = "p (b a h) -> p b a h"
                steps.then_wait(dve, dve.tensor_tensor(weight.rearrange(v4, b=2, a=2), total.rearrange(v4, b=2, a=2),
                                                       gates, ALU.mult))
                if i == 0:
                    steps.then_wait(dve, dve.tensor_scalar(weight, weight, k.col("cmp_any"), None, ALU.mult))
                dve.wait_ge(s["tr_mm"], i + 1)
                dve.tensor_copy(pt[:, i % 2].rearrange("p g t -> p (g t)"), k.ps[:, 2, :]).then_inc(s["tr_read"], 1)
                dve.wait_ge(s["pv_mm"], i + 1)
                for g in range(4):
                    at = 8 * (g % 2) + 4 * (g // 2)
                    last = dve.tensor_tensor(k.o[:, i, 256 * g:256 * g + 256].rearrange("p (h d) -> p h d", d=DK),
                                             k.ps[:, 4 + g // 2, g % 2 * 256:g % 2 * 256 + 256]
                                             .rearrange("p (h d) -> p h d", d=DK),
                                             weight[:, at:at + 4].rearrange("p (h o) -> p h o", o=1)
                                             .to_broadcast([P, 4, DK]), ALU.mult)
                last.then_inc(s["o_done"], 1)


def stage_nsa_attention(k):
    nc = k.nc
    p = k.region("att_p", [P, 2, 2, S], F32, 58)
    pt = k.region("att_pt", [P, 2, 2, S], F32, 66)
    part = k.region("att_part", [P, 2, P], F32, 74)
    s = {n: k.sem(f"att_{n}") for n in ("sc_mm", "nm_done", "exp_done", "tr_mm", "pt0", "pt1", "pv_mm", "part", "o_done",
                                        "step", "w_done")}
    units = [(br, g, i, pr) for br in range(2) for g in range(4) for i in range(TT) for pr in range(2)]
    U = len(units)

    def length(n):
        return (units[n][2] + 1) * P

    def sm(base, n):
        return k.small[:, base + 2 * (n % 4):base + 2 * (n % 4) + 2]

    with nc.Block() as block:
        @block.tensor
        def _(pe):
            for n in range(U + 2):
                if n < U:
                    br, g, i, pr = units[n]
                    rows = slice(64 * (g % 2), 64 * (g % 2) + 64)
                    L = length(n)
                    if n >= 2:
                        pe.wait_ge(s["exp_done"], 2 * (n - 1))
                    for e in range(2):
                        bank = 2 * (n % 2) + e
                        pe.matmul(k.ps[:, bank, 0:L], k.q_rot[rows, g // 2 * 4 + 2 * pr + e, i * P:(i + 1) * P],
                                  k.kv[rows, 4 * br + g // 2, 0:L], start=True, stop=False)
                        last = pe.matmul(k.ps[:, bank, i * P:L], k.ident_bf[:], k.causal_bf[:], start=False, stop=True)
                    last.then_inc(s["sc_mm"], 1)
                if 1 <= n <= U:
                    m = n - 1
                    i = units[m][2]
                    for e in range(2):
                        pe.wait_ge(s["exp_done"], 2 * m + e + 1)
                        if m:
                            pe.wait_ge(s[f"pt{e}"], m)
                        for j in range(i + 1):
                            last = pe.transpose(k.ps[:, 4 + e, j * P:(j + 1) * P], p[:, m % 2, e, j * P:(j + 1) * P],
                                                k.const("ident"))
                        last.then_inc(s["tr_mm"], 1)
                if n >= 2:
                    m = n - 2
                    br, g, i, pr = units[m]
                    if m >= 2:
                        pe.wait_ge(s["part"], m - 1)
                    for e in range(2):
                        pe.wait_ge(s[f"pt{e}"], m + 1)
                        for j in range(i + 1):
                            last = pe.matmul(k.ps[:, 6 + m % 2, e * DK:(e + 1) * DK], pt[:, m % 2, e, j * P:(j + 1) * P],
                                             k.vtok[:, br, j, g * DK:(g + 1) * DK], start=(j == 0), stop=(j == i))
                    last.then_inc(s["pv_mm"], 1)

        @block.scalar
        def _(act):
            for n in range(U + 1):
                if n < U:
                    L = length(n)
                    act.wait_ge(s["nm_done"], n + 1)
                    if n >= 4:
                        act.wait_ge(s["w_done"], n - 3)
                    for e in range(2):
                        if n >= 2:
                            act.wait_ge(s["tr_mm"], 2 * (n - 2) + e + 1)
                        act.activation(p[:, n % 2, e, 0:L], k.ps[:, 2 * (n % 2) + e, 0:L], ACT.Exp,
                                       bias=sm(0, n)[:, e:e + 1], scale=DK ** -0.5,
                                       accum_out=sm(8, n)[:, e:e + 1]).then_inc(s["exp_done"], 1)
                if n >= 1:
                    m = n - 1
                    L = length(m)
                    act.wait_ge(s["tr_mm"], 2 * m + 2)
                    if m >= 2:
                        act.wait_ge(s["pv_mm"], m - 1)
                    act.activation(pt[:, m % 2, 1, 0:L], k.ps[:, 5, 0:L], ACT.Copy).then_inc(s["pt1"], 1)

        @block.vector
        def _(dve):
            steps = Steps(s["step"])
            for n in range(U + 2):
                if n < U:
                    L = length(n)
                    dve.wait_ge(s["sc_mm"], n + 1)
                    if n >= 4:
                        dve.wait_ge(s["exp_done"], 2 * (n - 3))
                    bank = 2 * (n % 2)
                    steps.then_wait(dve, dve.tensor_reduce(sm(16, n), k.ps[:, bank:bank + 2, 0:L], AX, ALU.max))
                    dve.tensor_scalar(sm(0, n), sm(16, n), -DK ** -0.5, None, ALU.mult).then_inc(s["nm_done"], 1)
                if 1 <= n <= U:
                    m = n - 1
                    L = length(m)
                    dve.wait_ge(s["tr_mm"], 2 * m + 1)
                    if m >= 2:
                        dve.wait_ge(s["pv_mm"], m - 1)
                    dve.tensor_copy(pt[:, m % 2, 0, 0:L], k.ps[:, 4, 0:L]).then_inc(s["pt0"], 1)
                if n >= 2:
                    m = n - 2
                    br, g, i, pr = units[m]
                    h = 4 * g + 2 * pr
                    dve.wait_ge(s["exp_done"], 2 * m + 2)
                    steps.then_wait(dve, dve.reciprocal(sm(24, m), sm(8, m)))
                    gates = k.gtok[:, i, :].rearrange("p (h b) -> p h b", b=3)[:, h:h + 2, 1 + br]
                    dve.tensor_tensor(sm(32, m), sm(24, m), gates, ALU.mult).then_inc(s["w_done"], 1)
                    dve.wait_ge(s["w_done"], m + 1)
                    dve.wait_ge(s["pv_mm"], m + 1)
                    if m >= 2:
                        dve.wait_ge(s["o_done"], m - 1)
                    dve.tensor_tensor(part[:, m % 2, :].rearrange("p (h d) -> p h d", d=DK),
                                      k.ps[:, 6 + m % 2, 0:P].rearrange("p (h d) -> p h d", d=DK),
                                      sm(32, m).rearrange("p (h o) -> p h o", o=1).to_broadcast([P, 2, DK]),
                                      ALU.mult).then_inc(s["part"], 1)
                    dve.wait_ge(s["part"], m + 1)
                    o = k.o[:, i, h * DK:(h + 2) * DK]
                    dve.tensor_tensor(o, o, part[:, m % 2, :], ALU.add).then_inc(s["o_done"], 1)


def stage_nsa_gate(k):
    nc = k.nc
    z = k.region("nsag_z", [P, 4, S], F32, 58)
    y = k.region("nsag_y", [P, 2, S], F32, 66)
    zl = [k.sem(f"nsag_z{i}") for i in range(4)]
    tr, y_done, y_hi, y_lo = k.sem("nsag_tr"), k.sem("nsag_y_done"), k.sem("nsag_y_hi"), k.sem("nsag_y_lo")
    with nc.Block() as block:
        @block.sync
        def _(sp):
            for n in range(8):
                if n >= 4:
                    sp.wait_ge(y_done, n - 3)
                sp.dma_start(z[:, n % 4, :], k.io["z_scratch"][n]).then_inc(zl[n % 4], 16)

        @block.tensor
        def _(pe):
            for n in range(8):
                if n >= 2:
                    pe.wait_ge(y_done, n - 1)
                for i in range(TT):
                    last = pe.transpose(k.ps[:, n % 2, i * P:(i + 1) * P], k.o[:, i, n * P:(n + 1) * P], k.const("ident"))
                last.then_inc(tr, 1)

        @block.scalar
        def _(act):
            for n in range(8):
                act.wait_ge(y_done, n + 1)
                act.activation(k.act_hi[:, n, :], y[:, n % 2, :], ACT.Copy).then_inc(y_hi, 1)

        @block.vector
        def _(dve):
            for n in range(9):
                if n < 8:
                    dve.wait_ge(tr, n + 1)
                    dve.wait_ge(zl[n % 4], 16 * (n // 4 + 1))
                    if n >= 2:
                        dve.wait_ge(y_lo, n - 1)
                    dve.tensor_tensor(y[:, n % 2, :], k.ps[:, n % 2, :], z[:, n % 4, :], ALU.mult).then_inc(y_done, 1)
                if n >= 1:
                    dve.wait_ge(y_hi, n)
                    dve.tensor_tensor(k.act_lo[:, n - 1, :], y[:, (n - 1) % 2, :], k.act_hi[:, n - 1, :].bitcast(F32),
                                      ALU.subtract).then_inc(y_lo, 1)


GATE_T = 16
DA_T = 12
RW_ALL = 15


def stage_in_2(k, norm):
    nc = k.nc
    norm.scale_stage()
    b0 = first_block("in_2")
    b1 = first_block("mix_o")
    k.rw = k.region("rw", [P, RW_ALL, S], F32, 0)
    k.da = k.region("da", [P, DA_T, S], F32, 30)
    zt = k.region("in2_zt", [P, 4, S], F32, 54)
    u = k.region("in2_u", [P, 2, S + 2], F32, 62)
    t1 = k.region("in2_t1", [P, 2, S], F32, 67)
    k.keep = k.region("mu_keep", [P, RW_ALL], F32, 71)
    z_ready, plain = k.sem("in2_z_ready"), k.sem("in2_plain")
    u_ready, pad, keep_done, step, rw_done = (k.sem("in2_u_ready"), k.sem("in2_pad"), k.sem("in2_keep"),
                                              k.sem("in2_step"), k.sem("in2_rw_done"))
    stored = [k.sem(f"in2_stored{i}") for i in range(4)]
    with nc.Block() as block:
        @block.sync
        def _(sp):
            load_blocks(k, sp, b1)

        @block.scalar
        def _(act):
            norm.scale_act(act)
            for t, (b, j) in enumerate(tiles_of(b0, b1)):
                if j == 0 and b + 1 < b1:
                    split_hi(k, act, b + 1)
                tile = TILE_AT[b] + j
                act.wait_ge(k.tile_done, tile + 1)
                bank = k.ps[:, tile % 4, :]
                if t < GATE_T:
                    if t >= 4:
                        act.wait_ge(stored[t % 4], 16 * (t // 4))
                    act.activation(zt[:, t % 4, :], bank, ACT.Sigmoid).then_inc(z_ready, 1)
                    act.wait_ge(z_ready, t + 1)
                    act.sem_inc(k.evac_done, 1)
                    act.dma_start(k.io["z_scratch"][t], zt[:, t % 4, :]).then_inc(stored[t % 4], 16)
                elif t < GATE_T + DA_T:
                    act.activation(k.da[:, t - GATE_T, :], bank, ACT.Copy).then_inc(k.evac_done, 1)
                else:
                    m = t - GATE_T - DA_T
                    if m == 0:
                        act.wait_ge(pad, 2)
                    if m >= 2:
                        act.wait_ge(rw_done, m - 1)
                    act.activation(u[:, m % 2, 1:1 + S], bank, ACT.Copy).then_inc(u_ready, 1)
                    act.wait_ge(u_ready, m + 1)
                    act.sem_inc(k.evac_done, 1)
            for i in range(4):
                act.wait_ge(stored[i], 16 * GATE_T // 4)

        @block.tensor
        def _(pe):
            for t, (b, j) in enumerate(tiles_of(b0, b1)):
                multiply_tile(k, pe, b, j, norm.fed if t == 0 else None)

        @block.vector
        def _(dve):
            steps = Steps(step)
            dve.memset(u[:, :, 0:1], 0.0).then_inc(pad, 1)
            dve.memset(u[:, :, S + 1:S + 2], 0.0).then_inc(pad, 1)
            mp, mn = COLS["mu_prev"], COLS["mu_next"]
            steps.then_wait(dve, dve.tensor_tensor(k.keep[:], k.cols[:, mp:mp + RW_ALL], k.cols[:, mn:mn + RW_ALL],
                                                   ALU.add))
            steps.then_wait(dve, dve.tensor_scalar(k.keep[:], k.keep[:], -1.0, 1.0, ALU.mult, ALU.add))
            norm.scale_dve(dve)
            for t, (b, j) in enumerate(tiles_of(b0, b1)):
                if j == 0 and b + 1 < b1:
                    split_lo(k, dve, b + 1)
                m = t - GATE_T - DA_T
                if m >= 0:
                    x = u[:, m % 2]
                    dve.wait_ge(u_ready, m + 1)
                    steps.then_wait(dve, dve.tensor_scalar(t1[:, 0], x[:, 1:1 + S], k.keep[:, m:m + 1], None, ALU.mult))
                    steps.then_wait(dve, dve.scalar_tensor_tensor(out=t1[:, 1], in0=x[:, 0:S], scalar=k.col("mu_prev", m),
                                                                  in1=t1[:, 0], op0=ALU.mult, op1=ALU.add))
                    dve.scalar_tensor_tensor(out=k.rw[:, m, :], in0=x[:, 2:2 + S], scalar=k.col("mu_next", m),
                                             in1=t1[:, 1], op0=ALU.mult, op1=ALU.add).then_inc(rw_done, 1)
                    dve.wait_ge(rw_done, m + 1)


def stage_da_prep(k):
    nc = k.nc
    k.da_v = k.region("da_v", [P, TT, S], F32, 54)
    turned = k.region("da_turned", [P, 2, S], F32, 74)
    straight = k.region("da_straight", [P, 2, S], F32, 78)
    prod = k.region("da_prod", [P, 8], F32, 72)
    k.neg_lam = k.small[:, 255:256]
    s = {n: k.sem(f"dap_{n}") for n in ("rot_mm", "rot_read", "straight", "done", "tr", "tr_read", "prod", "lam_mm", "exp",
                                        "step")}
    with nc.Block() as block:
        @block.tensor
        def _(pe):
            for n in range(8):
                if n >= 2:
                    pe.wait_ge(s["rot_read"], n - 1)
                pe.matmul(k.ps[:, 4 + n % 2, :], k.const("rot"), k.da[:, n, :], start=True, stop=True) \
                    .then_inc(s["rot_mm"], 1)
            for n in range(4):
                if n >= 2:
                    pe.wait_ge(s["tr_read"], n - 1)
                for i in range(TT):
                    last = pe.transpose(k.ps[:, n % 2, i * P:(i + 1) * P], k.da[:, 8 + n, i * P:(i + 1) * P],
                                        k.const("ident"))
                last.then_inc(s["tr"], 1)
            pe.wait_ge(s["prod"], 2)
            pe.matmul(k.ps[:, 7, 0:2], k.const("ones")[0:64, :], prod[0:64, 0:2], start=True, stop=True) \
                .then_inc(s["lam_mm"], 1)

        @block.scalar
        def _(act):
            act.wait_ge(s["lam_mm"], 1)
            act.activation(prod[:, 2:4], k.ps[:, 7, 0:2], ACT.Exp).then_inc(s["exp"], 1)

        @block.gpsimd
        def _(pool):
            for n in range(8):
                if n >= 2:
                    pool.wait_ge(s["done"], n - 1)
                pool.tensor_tensor(straight[:, n % 2, :], k.da[:, n, :], k.const("cos", S), ALU.mult) \
                    .then_inc(s["straight"], 1)

        @block.vector
        def _(dve):
            steps = Steps(s["step"])
            low = slice(0, 64)
            dve.tensor_tensor(prod[low, 0:1], k.col("lq1", rows=low), k.col("lk1", rows=low), ALU.mult) \
                .then_inc(s["prod"], 1)
            dve.tensor_tensor(prod[low, 1:2], k.col("lq2", rows=low), k.col("lk2", rows=low), ALU.mult) \
                .then_inc(s["prod"], 1)
            for n in range(8):
                dve.wait_ge(s["rot_mm"], n + 1)
                if n >= 2:
                    dve.wait_ge(s["done"], n - 1)
                dve.tensor_tensor(turned[:, n % 2, :], k.ps[:, 4 + n % 2, :], k.const("sin", S), ALU.mult) \
                    .then_inc(s["rot_read"], 1)
                dve.wait_ge(s["rot_read"], n + 1)
                dve.wait_ge(s["straight"], n + 1)
                dve.tensor_tensor(k.da[:, n, :], turned[:, n % 2, :], straight[:, n % 2, :], ALU.add) \
                    .then_inc(s["done"], 1)
            for n in range(4):
                dve.wait_ge(s["tr"], n + 1)
                dve.tensor_copy(k.da_v[:, :, n * P:(n + 1) * P], k.ps[:, n % 2, :].rearrange("p (t c) -> p t c", c=P)) \
                    .then_inc(s["tr_read"], 1)
            dve.wait_ge(s["exp"], 1)
            steps.then_wait(dve, dve.tensor_tensor(prod[:, 4:5], prod[:, 3:4], prod[:, 2:3], ALU.subtract))
            dve.tensor_scalar(k.neg_lam, prod[:, 4:5], -LAMBDA_INIT, None, ALU.add)


def stage_da_attention(k):
    nc = k.nc
    k.da_o = k.region("da_o", [P, TT, S], F32, 62)
    p = k.region("da_p", [P, 2, 2, S], F32, 74)
    pt = k.region("da_pt", [P, 2, S], F32, 82)
    junk = k.region("da_junk", [P, 2, P], F32, 71.25)
    s = {n: k.sem(f"daa_{n}") for n in ("sc_mm", "nm_done", "exp_done", "pd_done", "tr_mm", "pt", "pv_mm", "o_done",
                                        "sq_done", "step", "root", "root_read", "y_tr", "y_hi", "y_done", "y_lo", "normed")}
    units = [(h, i) for h in range(DA_HEADS) for i in range(TT)]
    U = len(units)
    sumsq = k.small[:, 64:64 + U]
    y = k.region("da_y", [P, 2, S], F32, 86)

    def sm(base, n):
        return k.small[:, base + 2 * (n % 4):base + 2 * (n % 4) + 2]

    with nc.Block() as block:
        @block.tensor
        def _(pe):
            for n in range(U + 2):
                if n < U:
                    h, i = units[n]
                    if n >= 2:
                        pe.wait_ge(s["exp_done"], 2 * (n - 1))
                    for c in range(2):
                        rows = slice(64 * c, 64 * c + 64)
                        last = pe.matmul(k.ps[:, 2 * (n % 2) + c, :], k.da[rows, h, i * P:(i + 1) * P], k.da[rows, 4 + h, :],
                                         start=True, stop=True)
                    last.then_inc(s["sc_mm"], 1)
                if 1 <= n <= U:
                    m = n - 1
                    pe.wait_ge(s["pd_done"], m + 1)
                    if m >= 2:
                        pe.wait_ge(s["pt"], m - 1)
                    for j in range(TT):
                        last = pe.transpose(k.ps[:, 4 + m % 2, j * P:(j + 1) * P], p[:, m % 2, 0, j * P:(j + 1) * P],
                                            k.const("ident"))
                    last.then_inc(s["tr_mm"], 1)
                if n >= 2:
                    m = n - 2
                    h, i = units[m]
                    pe.wait_ge(s["pt"], m + 1)
                    if m >= 2:
                        pe.wait_ge(s["o_done"], m - 1)
                    for j in range(TT):
                        last = pe.matmul(k.ps[:, 6 + m % 2, 0:P], pt[:, m % 2, j * P:(j + 1) * P],
                                         k.da_v[:, j, h * P:(h + 1) * P], start=(j == 0), stop=(j == TT - 1))
                    last.then_inc(s["pv_mm"], 1)
            for h in range(DA_HEADS):
                pe.wait_ge(s["normed"], TT)
                if h >= 2:
                    pe.wait_ge(s["y_done"], h - 1)
                for i in range(TT):
                    last = pe.transpose(k.ps[:, h % 2, i * P:(i + 1) * P], k.da_o[:, i, h * P:(h + 1) * P],
                                        k.const("ident"))
                last.then_inc(s["y_tr"], 1)

        @block.scalar
        def _(act):
            for n in range(U + 2):
                if n < U:
                    act.wait_ge(s["nm_done"], n + 1)
                    if n >= 2:
                        act.wait_ge(s["tr_mm"], n - 1)
                    for c in range(2):
                        act.activation(p[:, n % 2, c, :], k.ps[:, 2 * (n % 2) + c, :], ACT.Exp, bias=sm(0, n)[:, c:c + 1],
                                       scale=DK ** -0.5, accum_out=sm(8, n)[:, c:c + 1]).then_inc(s["exp_done"], 1)
                if n >= 2:
                    m = n - 2
                    h, i = units[m]
                    act.wait_ge(s["o_done"], m + 1)
                    if m >= 2:
                        act.wait_ge(s["sq_done"], m - 1)
                    act.activation(junk[:, m % 2, :], k.da_o[:, i, h * P:(h + 1) * P], ACT.Square,
                                   accum_out=sumsq[:, 4 * i + h:4 * i + h + 1]).then_inc(s["sq_done"], 1)
            act.wait_ge(s["sq_done"], U)
            act.activation(sumsq, sumsq, ACT.Sqrt, scale=1.0 / P, bias=k.col("eps5")).then_inc(s["root"], 1)
            for h in range(DA_HEADS):
                act.wait_ge(s["y_done"], h + 1)
                act.activation(k.act_hi[:, 4 + h, :], y[:, h % 2, :], ACT.Copy).then_inc(s["y_hi"], 1)

        @block.vector
        def _(dve):
            steps = Steps(s["step"])
            for n in range(U + 2):
                if n < U:
                    bank = 2 * (n % 2)
                    dve.wait_ge(s["sc_mm"], n + 1)
                    if n >= 4:
                        dve.wait_ge(s["exp_done"], 2 * (n - 3))
                    steps.then_wait(dve, dve.tensor_reduce(sm(16, n), k.ps[:, bank:bank + 2, :], AX, ALU.max))
                    dve.tensor_scalar(sm(0, n), sm(16, n), -DK ** -0.5, None, ALU.mult).then_inc(s["nm_done"], 1)
                    dve.wait_ge(s["exp_done"], 2 * n + 2)
                    steps.then_wait(dve, dve.reciprocal(sm(24, n), sm(8, n)))
                    x = p[:, n % 2]
                    w = sm(24, n)
                    dve.tensor_scalar(w[:, 1:2], w[:, 1:2], k.neg_lam, None, ALU.mult)
                    steps.then_wait(dve, dve.tensor_scalar(x[:, 0, :], x[:, 0, :], w[:, 0:1], None, ALU.mult))
                    dve.scalar_tensor_tensor(out=x[:, 0, :], in0=x[:, 1, :], scalar=w[:, 1:2], in1=x[:, 0, :],
                                             op0=ALU.mult, op1=ALU.add).then_inc(s["pd_done"], 1)
                if 1 <= n <= U:
                    m = n - 1
                    dve.wait_ge(s["tr_mm"], m + 1)
                    if m >= 2:
                        dve.wait_ge(s["pv_mm"], m - 1)
                    dve.tensor_copy(pt[:, m % 2, :], k.ps[:, 4 + m % 2, :]).then_inc(s["pt"], 1)
                if n >= 2:
                    m = n - 2
                    h, i = units[m]
                    dve.wait_ge(s["pv_mm"], m + 1)
                    dve.tensor_copy(k.da_o[:, i, h * P:(h + 1) * P], k.ps[:, 6 + m % 2, 0:P]).then_inc(s["o_done"], 1)
            dve.wait_ge(s["root"], 1)
            steps.then_wait(dve, dve.reciprocal(sumsq, sumsq))
            dve.wait_ge(s["o_done"], U)
            for i in range(TT):
                o = k.da_o[:, i, :].rearrange("p (h d) -> p h d", d=P)
                dve.tensor_tensor(o, o, sumsq[:, 4 * i:4 * i + 4].rearrange("p (h o) -> p h o", o=1).to_broadcast([P, 4, P]),
                                  ALU.mult).then_inc(s["normed"], 1)
            for h in range(DA_HEADS):
                dve.wait_ge(s["y_tr"], h + 1)
                if h >= 2:
                    dve.wait_ge(s["y_lo"], h - 1)
                dve.tensor_scalar(y[:, h % 2, :], k.ps[:, h % 2, :], k.col("subln"), 1.0 - LAMBDA_INIT, ALU.mult,
                                  ALU.mult).then_inc(s["y_done"], 1)
                dve.wait_ge(s["y_hi"], h + 1)
                dve.tensor_tensor(k.act_lo[:, 4 + h, :], y[:, h % 2, :], k.act_hi[:, 4 + h, :].bitcast(F32),
                                  ALU.subtract).then_inc(s["y_lo"], 1)


def stage_rw_prep(k):
    nc = k.nc
    k.lora = k.at("rw_lora", [P, 3, S], F32, 28)
    k.rwc = k.at("rw_consts", [P, N_RW_CONSTS], F32, 44)
    got = k.sem("rwp_landed")
    with nc.Block() as block:
        @block.sync
        def _(sp):
            sp.dma_start(k.lora[:], k.io["lora"]).then_inc(got, 16)
            sp.dma_start(k.rwc[:], k.io["rw_consts"]).then_inc(got, 16)
            sp.wait_ge(got, 32)

        @block.scalar
        def _(act):
            act.activation(k.rw[:, 12, :], k.rw[:, 12, :], ACT.Tanh)
            act.activation(k.rw[:, 14, :], k.rw[:, 14, :], ACT.Sigmoid)
    k.ytok = k.region("rw_ytok", [P, TT, S], F32, 74)
    k.bonus = k.region("rw_bonus", [P, RW_T, S], F32, 82)


def halves():
    return [(d, hd, it, par) for d in range(2) for hd in range(2) for it in range(TT) for par in range(2)]


def rows_half(x):
    return slice(64 * x, 64 * x + 64)


def chunk2(a):
    return slice(P * a, P * a + P)


def stage_rw_heads(k, c):
    nc = k.nc
    tag = f"rw{c}"
    ar = k.at(f"{tag}_ar", [P, 2, 2, S], F32, 60)
    bt = k.at(f"{tag}_bt", [P, 2, S], F32, 68)
    kt = k.at(f"{tag}_kt", [P, 2, S], F32, 72)
    bh = k.at(f"{tag}_bh", [P, 2, S], F32, 76)
    kh = k.at(f"{tag}_kh", [P, 2, S], F32, 80)
    T = k.at(f"{tag}_T", [P, 16, P], F32, 68)
    off = [k.at(f"{tag}_off0", [P, 16, P], F32, 76), k.region(f"{tag}_off1", [P, 16, P], F32, 54)]
    Tt = k.region(f"{tag}_Tt", [P, 16, P], F32, 62)
    Z = k.at(f"{tag}_Z", [P, 16, P], F32, 98)
    tok = k.at(f"{tag}_tok", [P, 2, 2, TT, P], F32, 84)
    vtok = k.at(f"{tag}_vtok", [P, TT, P], F32, 92)
    wu = k.at(f"{tag}_wu", [P, 16, P], F32, 98)
    rhs = k.at(f"{tag}_rhs", [P, 16, P], F32, 106)
    bb = k.at(f"{tag}_b", [P, 2, S], F32, 98)
    kd = k.at(f"{tag}_kd", [P, 2, S], F32, 102)
    kkn = k.at(f"{tag}_kkn", [P, S], F32, 106)
    sq = k.at(f"{tag}_sq", [P, S], F32, 108)
    mt = k.at(f"{tag}_mt", [P, 2, N_CHUNK, CHUNK], F32, 110)
    tmp = k.at(f"{tag}_tmp", [P, 2, S], F32, 110)
    pend = k.at(f"{tag}_pend", [P, 2, N_CHUNK], F32, 114)
    sc = k.region(f"{tag}_sc", [P, 16, 4, CHUNK], F32, 30)
    ex = k.region(f"{tag}_ex", [P, 2, 4, S], F32, 30)
    add = k.region(f"{tag}_add", [P, 2, N_CHUNK, CHUNK], F32, 46)
    state = k.region(f"{tag}_state", [P, 2, N_CHUNK, CHUNK], F32, 50)
    sig = k.region(f"{tag}_sig", [P, 2, S], F32, 54)
    X = k.region(f"{tag}_X", [P, 2, S], F32, 58)
    E1 = k.region(f"{tag}_E1", [P, 2, S], F32, 62)
    E2 = k.region(f"{tag}_E2", [P, 2, S], F32, 66)
    rate = k.region(f"{tag}_rate", [P, 2, S], F32, 70)
    ss = {n: k.sem(f"{tag[0:2]}{c}_{n}") for n in
          ("pre", "sigs", "kk", "sqd", "ss", "root", "sums", "exps", "kd", "bonp", "bonm", "feat", "pool_feat", "tr", "tok",
           "scm", "sc", "off", "zero", "off0", "z", "zc", "tz", "t", "akvm", "akv", "wum", "wu_a", "wu_d", "rm", "rhat", "pcd", "mm",
           "mt", "nm", "add", "stm", "st", "yb", "ybc", "ya", "step", "pstep", "st0")}
    r, kf, v = k.rw[:, c, :], k.rw[:, 4 + c, :], k.rw[:, 8 + c, :]

    def rc(name, n, at=0):
        a = RW_CONSTS[name] + at
        return k.rwc[:, a:a + n]

    def off_blocks(eng, lv, d, par):
        h, u = rows_half(par), slice(8 * d, 8 * d + 8)
        mask = rc(f"level{d}", 64, 64 * lv)[h].rearrange("p (o n) -> p o n", o=1).to_broadcast([64, 8, CHUNK])
        return eng.tensor_tensor(off[lv % 2][h, u, chunk(par)], sc[h, u, 0, :], mask, ALU.mult)

    eye = k.const("ident").rearrange("p (o n) -> p o n", o=1).to_broadcast([P, 4, P])

    def pair(op, d, part):
        return k.ps[:, 2 * (op % 4) + part, :]

    def four(x, d, part):
        return x[:, 8 * d + 4 * part:8 * d + 4 * part + 4, :]

    def ops(lv):
        return [("Z", 0), ("Z", 1)] + ([("T", 0), ("Tt", 0), ("T", 1), ("Tt", 1)] if lv < LEVELS - 1 else
                                       [("Tt", 0), ("Tt", 1)])

    def chunk(t):
        return slice(t * CHUNK, (t + 1) * CHUNK)

    with nc.Block() as block:
        @block.tensor
        def _(pe):
            for m, rows in ((0, 12), (1, 13)):
                for d in range(2):
                    h = rows_half(d)
                    last = pe.matmul(k.ps[:, 2 * m + d, :], k.lora[h, m, c * P:(c + 1) * P], k.rw[h, rows, :],
                                     start=True, stop=True)
            last.then_inc(ss["pre"], 1)
            pe.wait_ge(ss["sqd"], 1)
            pe.matmul(k.ps[:, 4, :], k.const("block_ones"), sq[:], start=True, stop=True).then_inc(ss["ss"], 1)
            pe.wait_ge(ss["bonp"], 1)
            pe.matmul(k.ps[:, 5, :], k.const("block_ones"), tmp[:, 0, :], start=True, stop=True).then_inc(ss["bonm"], 1)
            pe.wait_ge(ss["feat"], 6)
            pe.wait_ge(ss["pool_feat"], 6)
            jobs = [v] + [x for d in range(2) for x in (ar[:, d, 0, :], bh[:, d, :], kh[:, d, :])]
            for n, src in enumerate(jobs):
                if n >= 2:
                    pe.wait_ge(ss["tok"], n - 1)
                for i in range(TT):
                    last = pe.transpose(k.ps[:, 6 + n % 2, i * P:(i + 1) * P], src[:, i * P:(i + 1) * P], k.const("ident"))
                last.then_inc(ss["tr"], 1)
            for n in range(4):
                d, q = n // 2, n % 2
                if n >= 2:
                    pe.wait_ge(ss["sc"], 2 * (n - 1))
                for it in (2 * q, 2 * q + 1):
                    for par in range(2):
                        t = chunk(2 * it + par)
                        for m, lhs in ((0, bt), (1, kt)):
                            for hd in range(2):
                                o = 256 * (it % 2) + 128 * m
                                last = pe.matmul(k.ps[rows_half(par), 2 * (n % 2) + hd, o:o + 128]
                                                 .rearrange("p (x t) -> p x t", x=2),
                                                 lhs[rows_half(hd), d, t], ar[rows_half(hd), d, :, t],
                                                 start=True, stop=True)
                last.then_inc(ss["scm"], 1)
            pe.wait_ge(ss["sc"], 8)
            for d, hd, it, par in halves():
                u, h = 8 * d + 4 * hd + it, rows_half(par)
                last = pe.matmul(k.ps[h, 4 + d, chunk(u % 8)], sc[h, u, 2, :], vtok[h, it, chunk(hd)], start=True, stop=True)
            last.then_inc(ss["akvm"], 1)
            pe.wait_ge(ss["off0"], 4)
            pe.wait_ge(ss["akv"], 2)
            for u in range(16):
                last = pe.transpose(k.ps[:, 4 + u // 4, chunk2(u % 4)], off[0][:, u, :], k.const("ident"))
            last.then_inc(ss["z"], 1)
            op = 0
            for lv in range(1, LEVELS):
                for name, d in ops(lv):
                    if name == "Z":
                        pe.wait_ge(ss["off"], 4 * (lv - 1) + 2 * d + 2)
                        pe.wait_ge(ss["t"], 4 if lv == 1 else 4 * (lv - 1) + 1 + 2 * d)
                        lhs, x = off[lv % 2], T
                    else:
                        pe.wait_ge(ss["zc"], 2 * (lv - 1) + d + 1)
                        if name == "Tt" or lv == LEVELS - 1:
                            pe.wait_ge(ss["t"], 4 * lv)
                        lhs, x = (Tt, Z) if name == "T" else (Z, Tt)
                    for part in range(2):
                        for a in range(4):
                            u = 8 * d + 4 * part + a
                            last = pe.matmul(pair(op, d, part)[:, chunk2(a)], lhs[:, u, :], x[:, u, :], start=True,
                                             stop=True)
                    last.then_inc(ss["z"] if name == "Z" else ss["tz"], 1)
                    op += 1
            pe.wait_ge(ss["t"], 4 * (LEVELS - 1) + 2)
            for u in range(16):
                last = pe.matmul(k.ps[:, u // 4, chunk2(u % 4)], Tt[:, u, :], rhs[:, u, :], start=True, stop=True)
                if u % 4 == 3:
                    last.then_inc(ss["wum"], 1)
            pe.wait_ge(ss["wu_a"], 2)
            pe.wait_ge(ss["wu_d"], 2)
            places = [(d, hd, it, 8 * d + 4 * hd + it) for d in range(2) for hd in range(2) for it in range(TT)]
            for d, hd, it, u in places:
                for par in range(2):
                    h = rows_half(par)
                    last = pe.matmul(k.ps[rows_half(hd), 4 + par, chunk(4 * d + it)], wu[h, u, 0:64], sc[h, u, 1, :],
                                     start=True, stop=True)
            last.then_inc(ss["rm"], 1)
            for d, hd, it, u in places:
                for par in range(2):
                    h = rows_half(par)
                    last = pe.matmul(k.ps[rows_half(hd), 6 + par, chunk(4 * d + it)], wu[h, u, 0:64],
                                     tok[h, d, 0, it, chunk(hd)], start=True, stop=True)
            last.then_inc(ss["mm"], 1)
            for d, hd, it, u in places:
                for x in range(2):
                    for par in range(2):
                        h = rows_half(par)
                        lhs, y = ((tok[h, d, 1, it, chunk(hd)], vtok[h, it, chunk(hd)]),
                                  (tok[h, d, 0, it, chunk(hd)], wu[h, u, 64:128]))[x]
                        last = pe.matmul(k.ps[rows_half(hd), par, chunk(4 * d + it)], lhs, y, start=(x == 0), stop=(x == 1))
            last.then_inc(ss["nm"], 1)
            pe.wait_ge(ss["mt"], 2)
            for hd in range(2):
                for it in range(TT):
                    for d in range(2):
                        u = 8 * d + 4 * hd + it
                        for x in range(2):
                            for par in range(2):
                                h = rows_half(par)
                                lhs, y = ((sc[h, u, 1, :], wu[h, u, 64:128]), (sc[h, u, 3, :], vtok[h, it, chunk(hd)]))[x]
                                last = pe.matmul(k.ps[h, 6, chunk(4 * hd + it)], lhs, y, start=(d == x == 0),
                                                 stop=(d == x == 1))
            last.then_inc(ss["yb"], 1)
            for n in range(1, N_CHUNK - 1):
                pe.wait_ge(ss["st"], n)
                for d in range(2):
                    ch = n if d == 0 else N_CHUNK - 1 - n
                    for hd in range(2):
                        h = rows_half(hd)
                        last = pe.matmul(k.ps[h, 2 + d, chunk(n)], mt[h, d, ch, :], state[h, d, ch, :], start=True, stop=True)
                last.then_inc(ss["stm"], 1)
            pe.wait_ge(ss["st"], N_CHUNK - 1)
            pe.wait_ge(ss["rhat"], 2)
            for it in range(TT):
                for par in range(2):
                    t = 2 * it + par
                    for d in range(2):
                        for hd in range(2):
                            h = rows_half(hd)
                            last = pe.matmul(k.ps[rows_half(par), 4 + hd, chunk(it)], ar[h, d, 1, chunk(t)],
                                             state[h, d, t, :], start=(d == 0), stop=(d == 1))
            last.then_inc(ss["ya"], 1)

        @block.scalar
        def _(act):
            act.wait_ge(ss["pre"], 1)
            for m, out, bias in ((0, sig, "w0"), (1, rate, "a0")):
                for d in range(2):
                    act.activation(out[:, d, :], k.ps[:, 2 * m + d, :], ACT.Sigmoid, bias=k.col(bias, 4 * d + c)) \
                        .then_inc(ss["sigs"], 1)
            act.wait_ge(ss["kk"], 1)
            act.activation(sq[:], kkn[:], ACT.Square).then_inc(ss["sqd"], 1)
            act.wait_ge(ss["ss"], 1)
            act.activation(sq[:], k.ps[:, 4, :], ACT.Sqrt).then_inc(ss["root"], 1)
            act.wait_ge(ss["sums"], 1)
            for d in range(2):
                incl, excl, rest = X, (E1, E2)[d], (E2, E1)[d]
                for n, (src, sign) in enumerate(((incl, -1.0), (excl, -1.0), (incl, 1.0), (rest, -1.0))):
                    act.activation(ex[:, d, n, :], src[:, d, :], ACT.Exp, scale=sign * DECAY_SCALE) \
                        .then_inc(ss["exps"], 1)
            for n in range(7):
                act.wait_ge(ss["tr"], n + 1)
                bank = k.ps[:, 6 + n % 2, :].rearrange("p (t c) -> p t c", c=P)
                if n in (1, 4):
                    u = 8 * (n // 4)
                    out = rhs[:, u:u + 8, 0:64].rearrange("p (h t) c -> p t h c", h=2)
                    bank = bank.rearrange("p t (h c) -> p t h c", h=2)
                else:
                    out = vtok[:] if n == 0 else tok[:, (n - 1) // 3, (n - 1) % 3 - 1]
                act.activation(out, bank, ACT.Copy).then_inc(ss["tok"], 1)
            act.wait_ge(ss["akvm"], 1)
            for d in range(2):
                act.activation(rhs[:, 8 * d:8 * d + 8, 64:128], k.ps[:, 4 + d, :].rearrange("p (u t) -> p u t", t=CHUNK),
                               ACT.Copy).then_inc(ss["akv"], 1)
            op = 0
            for lv in range(1, LEVELS):
                for name, d in ops(lv):
                    if name == "Z":
                        act.wait_ge(ss["z"], 1 + 2 * (lv - 1) + d + 1)
                        for part in range(2):
                            last = act.activation(four(Z, d, part).rearrange("p u t -> p (u t)"), pair(op, d, part), ACT.Copy)
                        last.then_inc(ss["zc"], 1)
                    op += 1
            for g in (0, 2):
                act.wait_ge(ss["wum"], g + 1)
                act.activation(wu[:, 4 * g:4 * g + 4, :].rearrange("p u t -> p (u t)"), k.ps[:, g, :], ACT.Copy) \
                    .then_inc(ss["wu_a"], 1)
            act.wait_ge(ss["nm"], 1)
            for par in range(2):
                act.activation(add[:].rearrange("p d (i a) t -> p d i a t", a=2)[:, :, :, par, :],
                               k.ps[:, par, :].rearrange("p (d i t) -> p d i t", d=2, t=CHUNK), ACT.Copy) \
                    .then_inc(ss["add"], 1)
            act.wait_ge(ss["yb"], 1)
            for hd in range(2):
                act.activation(k.ytok[:, :, c * P + 64 * hd:c * P + 64 * hd + 64],
                               k.ps[:, 6, 256 * hd:256 * hd + 256].rearrange("p (i t) -> p i t", t=CHUNK), ACT.Copy) \
                    .then_inc(ss["ybc"], 1)

        @block.gpsimd
        def _(pool):
            pool.wait_ge(ss["exps"], 8)
            pool.wait_ge(ss["kd"], 2)
            for d in range(2):
                pool.tensor_tensor(ar[:, d, 1, :], r, ex[:, d, 0, :], ALU.mult).then_inc(ss["pool_feat"], 1)
                pool.tensor_tensor(kt[:, d, :], kd[:, d, :], ex[:, d, 2, :], ALU.mult).then_inc(ss["pool_feat"], 1)
                pool.tensor_tensor(kh[:, d, :], kd[:, d, :], ex[:, d, 3, :], ALU.mult).then_inc(ss["pool_feat"], 1)
            pool.wait_ge(ss["sc"], 8)
            pool.wait_ge(ss["zero"], 4)
            for lv in range(1, LEVELS):
                if lv >= 2:
                    pool.wait_ge(ss["z"], 1 + 2 * (lv - 2))
                if lv == 2:
                    pool.wait_ge(ss["t"], 4)
                for d in range(2):
                    for par in range(2):
                        off_blocks(pool, lv, d, par).then_inc(ss["off"], 1)
            pool.wait_ge(ss["wum"], 4)
            pool.tensor_tensor(mt[:], rc("eye64", 64).rearrange("p (a b n) -> p a b n", a=1, b=1)
                               .to_broadcast([P, 2, N_CHUNK, CHUNK]),
                               pend[:].rearrange("p d (n o) -> p d n o", o=1).to_broadcast([P, 2, N_CHUNK, CHUNK]),
                               ALU.mult).then_inc(ss["pcd"], 1)

        @block.vector
        def _(dve):
            steps = Steps(ss["step"])

            def wait(ins):
                steps.then_wait(dve, ins)

            dve.tensor_scalar(kkn[:], kf, k.col("k_k", c), None, ALU.mult).then_inc(ss["kk"], 1)
            dve.wait_ge(ss["sigs"], 4)
            for d in range(2):
                wait(dve.tensor_tensor_scan(X[:, d, :], rc("scan", S), sig[:, d, :], 0.0, ALU.mult, ALU.add))
            x4 = X[:].rearrange("p d (n t) -> p d n t", t=CHUNK)
            wait(dve.tensor_tensor(E1[:], X[:], sig[:], ALU.subtract))
            for d in range(2):
                x3 = X[:, d, :].rearrange("p (n t) -> p n t", t=CHUNK)
                e3 = E2[:, d, :].rearrange("p (n t) -> p n t", t=CHUNK)
                wait(dve.tensor_tensor(e3, x3[:, :, CHUNK - 1:CHUNK].to_broadcast([P, N_CHUNK, CHUNK]), x3, ALU.subtract))
            dve.tensor_tensor(X[:, 1, :], E2[:, 1, :], sig[:, 1, :], ALU.add).then_inc(ss["sums"], 1)
            for d in range(2):
                wait(dve.tensor_scalar(tmp[:, d, :], rate[:, d, :], -1.0, k.col("k_a", c), ALU.add, ALU.mult))
                dve.scalar_tensor_tensor(out=kd[:, d, :], in0=tmp[:, d, :], scalar=1.0, in1=kf, op0=ALU.add,
                                         op1=ALU.mult).then_inc(ss["kd"], 1)
            dve.wait_ge(ss["kd"], 2)
            wait(dve.tensor_tensor(tmp[:, 1, :], kd[:, 0, :], kd[:, 1, :], ALU.add))
            dve.scalar_tensor_tensor(out=tmp[:, 0, :], in0=tmp[:, 1, :], scalar=k.col("r_k", c), in1=r, op0=ALU.mult,
                                     op1=ALU.mult).then_inc(ss["bonp"], 1)
            dve.wait_ge(ss["root"], 1)
            wait(dve.tensor_scalar(sq[:], sq[:], 1e-12, None, ALU.max))
            wait(dve.reciprocal(sq[:], sq[:]))
            wait(dve.tensor_tensor(kkn[:], kkn[:], sq[:], ALU.mult))
            for d in range(2):
                wait(dve.tensor_tensor(bb[:, d, :], kkn[:], rate[:, d, :], ALU.mult))
            dve.wait_ge(ss["exps"], 8)
            for d in range(2):
                dve.tensor_tensor(ar[:, d, 0, :], kkn[:], ex[:, d, 1, :], ALU.mult).then_inc(ss["feat"], 1)
                dve.tensor_tensor(bt[:, d, :], bb[:, d, :], ex[:, d, 2, :], ALU.mult).then_inc(ss["feat"], 1)
                dve.scalar_tensor_tensor(out=bh[:, d, :], in0=bb[:, d, :], scalar=-1.0, in1=ex[:, d, 3, :], op0=ALU.mult,
                                         op1=ALU.mult).then_inc(ss["feat"], 1)
                end = ex[:, d, 0, :].rearrange("p (n t) -> p n t", t=CHUNK)[:, :, (CHUNK - 1, 0)[d]]
                wait(dve.tensor_copy(pend[:, d, :], end))
            dve.wait_ge(ss["bonm"], 1)
            dve.tensor_tensor(k.bonus[:, c, :], k.ps[:, 5, :], v, ALU.mult)
            dve.wait_ge(ss["pool_feat"], 6)
            dve.wait_ge(ss["tok"], 7)
            for x in off:
                for par in range(2):
                    dve.memset(x[rows_half(par), :, chunk(1 - par)], 0.0).then_inc(ss["zero"], 1)
            for n in range(8):
                d, q, hd = n // 4, n // 2 % 2, n % 2
                u = 8 * d + 4 * hd + 2 * q
                dve.wait_ge(ss["scm"], n // 2 + 1)
                mask = rc(f"score{d}", 256).rearrange("p (o n) -> p o n", o=1).to_broadcast([P, 2, 256])
                dve.tensor_tensor(sc[:, u:u + 2].rearrange("p u m t -> p u (m t)"),
                                  k.ps[:, 2 * (n // 2 % 2) + hd, :].rearrange("p (u m) -> p u m", u=2), mask, ALU.mult) \
                    .then_inc(ss["sc"], 1)
            dve.wait_ge(ss["sc"], 8)
            for d in range(2):
                for par in range(2):
                    off_blocks(dve, 0, d, par).then_inc(ss["off0"], 1)
            dve.wait_ge(ss["off0"], 4)
            dve.wait_ge(ss["zero"], 4)
            for d in range(2):
                for part in range(2):
                    last = dve.tensor_tensor(four(Tt, d, part), four(off[0], d, part), eye, ALU.add)
                last.then_inc(ss["t"], 1)
            dve.wait_ge(ss["z"], 1)
            for d in range(2):
                for part in range(2):
                    last = dve.tensor_tensor(four(T, d, part),
                                             k.ps[:, 4 + 2 * d + part, :].rearrange("p (u t) -> p u t", t=P), eye, ALU.add)
                last.then_inc(ss["t"], 1)
            done, op, n = 4, 0, 0
            for lv in range(1, LEVELS):
                for name, d in ops(lv):
                    if name != "Z":
                        n += 1
                        dve.wait_ge(ss["tz"], n)
                        if done % 4 == 0 or lv == LEVELS - 1:
                            dve.wait_ge(ss["t"], done)
                        x = T if name == "T" else Tt
                        for part in range(2):
                            last = dve.tensor_tensor(four(x, d, part), four(x, d, part),
                                                     pair(op, d, part).rearrange("p (u t) -> p u t", t=P), ALU.add)
                        last.then_inc(ss["t"], 1)
                        done += 1
                    op += 1
            for g in (1, 3):
                dve.wait_ge(ss["wum"], g + 1)
                dve.tensor_copy(wu[:, 4 * g:4 * g + 4, :].rearrange("p u t -> p (u t)"), k.ps[:, g, :]) \
                    .then_inc(ss["wu_d"], 1)
            dve.memset(state[:, 0, 0, :], 0.0).then_inc(ss["st0"], 1)
            dve.memset(state[:, 1, N_CHUNK - 1, :], 0.0).then_inc(ss["st0"], 1)
            dve.wait_ge(ss["rm"], 1)
            for par in range(2):
                x = ar[:, :, 1, :].rearrange("p d (i a t) -> p d i a t", a=2, t=CHUNK)[:, :, :, par, :]
                dve.tensor_tensor(x, x, k.ps[:, 4 + par, :].rearrange("p (d i t) -> p d i t", d=2, t=CHUNK), ALU.add) \
                    .then_inc(ss["rhat"], 1)
            dve.wait_ge(ss["mm"], 1)
            dve.wait_ge(ss["pcd"], 1)
            for par in range(2):
                x = mt[:].rearrange("p d (i a) t -> p d i a t", a=2)[:, :, :, par, :]
                dve.tensor_tensor(x, x, k.ps[:, 6 + par, :].rearrange("p (d i t) -> p d i t", d=2, t=CHUNK), ALU.add) \
                    .then_inc(ss["mt"], 1)
            dve.wait_ge(ss["add"], 2)
            dve.wait_ge(ss["st0"], 2)
            dve.tensor_copy(state[:, 0, 1, :], add[:, 0, 0, :])
            dve.tensor_copy(state[:, 1, N_CHUNK - 2, :], add[:, 1, N_CHUNK - 1, :]).then_inc(ss["st"], 1)
            for n in range(1, N_CHUNK - 1):
                dve.wait_ge(ss["stm"], n)
                dve.tensor_tensor(state[:, 0, n + 1, :], k.ps[:, 2, chunk(n)], add[:, 0, n, :], ALU.add)
                m = N_CHUNK - 1 - n
                dve.tensor_tensor(state[:, 1, m - 1, :], k.ps[:, 3, chunk(n)], add[:, 1, m, :], ALU.add) \
                    .then_inc(ss["st"], 1)
            dve.wait_ge(ss["ya"], 1)
            dve.wait_ge(ss["ybc"], 2)
            for hd in range(2):
                x = k.ytok[:, :, c * P + 64 * hd:c * P + 64 * hd + 64]
                dve.tensor_tensor(x, x, k.ps[:, 4 + hd, 0:256].rearrange("p (i t) -> p i t", t=CHUNK), ALU.add)


def stage_rw_out(k):
    nc = k.nc
    sqr = k.region("rwo_sq", [P, TT, S], F32, 30)
    g = k.region("rwo_g", [P, RW_T, S], F32, 38)
    y = k.region("rwo_y", [P, 2, S], F32, 46)
    N = TT * 8
    mean, var = k.small[:, 0:N], k.small[:, N:2 * N]
    s = {n: k.sem(f"rwo_{n}") for n in ("gm", "gc", "step", "vars", "root", "normed", "tr", "aff", "y", "hi", "lo")}
    with nc.Block() as block:
        @block.tensor
        def _(pe):
            for c in range(RW_T):
                last = pe.matmul(k.ps[:, 4 + c, :], k.lora[:, 2, c * P:(c + 1) * P], k.rw[:, 14, :], start=True, stop=True)
            last.then_inc(s["gm"], 1)
            pe.wait_ge(s["normed"], 1)
            for c in range(RW_T):
                for i in range(TT):
                    last = pe.transpose(k.ps[:, c, i * P:(i + 1) * P], k.ytok[:, i, c * P:(c + 1) * P], k.const("ident"))
                last.then_inc(s["tr"], 1)

        @block.scalar
        def _(act):
            act.wait_ge(s["gm"], 1)
            for c in range(RW_T):
                act.activation(g[:, c, :], k.ps[:, 4 + c, :], ACT.Copy).then_inc(s["gc"], 1)
            act.wait_ge(s["vars"], 1)
            act.activation(var, var, ACT.Sqrt, scale=1.0 / DK, bias=k.col("eps_gn")).then_inc(s["root"], 1)
            for c in range(RW_T + 1):
                if c < RW_T:
                    act.wait_ge(s["tr"], c + 1)
                    if c >= 2:
                        act.wait_ge(s["lo"], c - 1)
                    act.activation(y[:, c % 2, :], k.ps[:, c, :], ACT.Identity, scale=k.col("rw_ln_w", c),
                                   bias=k.col("rw_ln_b", c)).then_inc(s["aff"], 1)
                if c >= 1:
                    act.wait_ge(s["y"], c)
                    act.activation(k.act_hi[:, c - 1, :], y[:, (c - 1) % 2, :], ACT.Copy).then_inc(s["hi"], 1)

        @block.vector
        def _(dve):
            steps = Steps(s["step"])
            y3 = k.ytok[:].rearrange("p t (h d) -> p (t h) d", d=DK)
            s3 = sqr[:].rearrange("p t (h d) -> p (t h) d", d=DK)
            steps.then_wait(dve, dve.tensor_reduce(mean, y3, AX, ALU.add))
            steps.then_wait(dve, dve.tensor_scalar(mean, mean, 1.0 / DK, None, ALU.mult))
            steps.then_wait(dve, dve.tensor_tensor(y3, y3, mean.rearrange("p (h o) -> p h o", o=1).to_broadcast([P, N, DK]),
                                                   ALU.subtract))
            steps.then_wait(dve, dve.tensor_tensor(s3, y3, y3, ALU.mult))
            dve.tensor_reduce(var, s3, AX, ALU.add).then_inc(s["vars"], 1)
            dve.wait_ge(s["root"], 1)
            steps.then_wait(dve, dve.reciprocal(var, var))
            dve.tensor_tensor(y3, y3, var.rearrange("p (h o) -> p h o", o=1).to_broadcast([P, N, DK]), ALU.mult) \
                .then_inc(s["normed"], 1)
            dve.wait_ge(s["gc"], RW_T)
            for c in range(RW_T):
                dve.wait_ge(s["aff"], c + 1)
                x = y[:, c % 2, :]
                steps.then_wait(dve, dve.tensor_tensor(x, x, k.bonus[:, c, :], ALU.add))
                dve.tensor_tensor(x, x, g[:, c, :], ALU.mult).then_inc(s["y"], 1)
                dve.wait_ge(s["hi"], c + 1)
                dve.tensor_tensor(k.act_lo[:, c, :], x, k.act_hi[:, c, :].bitcast(F32), ALU.subtract).then_inc(s["lo"], 1)


def stage_mix(k):
    nc = k.nc
    b0 = first_block("mix_o")
    b1 = first_block("out_2")
    g = k.region("mix_g", [P, 4, 2, S], F32, 0)
    merged = k.region("merged", [P, KD, S], F32, 16)
    parts = k.region("mix_parts", [P, 2, 2, S], F32, 32)
    gl = [k.sem(f"mix_g{i}") for i in range(4)]
    pair, read, part, merged_done, hi = (k.sem("mix_pair"), k.sem("mix_read"), k.sem("mix_part"), k.sem("mix_merged"),
                                         k.sem("mix_hi"))
    tiles = tiles_of(b0, b1)
    with nc.Block() as block:
        @block.sync
        def _(sp):
            load_blocks(k, sp, b0 + RAW_SLOTS)
            for n in range(KD):
                if n >= 4:
                    sp.wait_ge(part, 2 * (n - 3))
                for x in range(2):
                    sp.dma_start(g[:, n % 4, x, :], k.io["z_scratch"][KD * x + n]).then_inc(gl[n % 4], 16)
                if n == 3:
                    load_blocks(k, sp, b1 + RAW_SLOTS - 1)
            load_blocks(k, sp, b1 + RAW_SLOTS)

        @block.scalar
        def _(act):
            split_hi(k, act, b0)
            for b in range(b0, b1):
                split_hi(k, act, b + 1)
            for n in range(KD):
                act.wait_ge(merged_done, n + 1)
                if n == 0:
                    act.wait_ge(pair, 2 * KD)
                act.activation(k.act_hi[:, n, :], merged[:, n, :], ACT.Copy).then_inc(hi, 1)

        @block.tensor
        def _(pe):
            for n, (b, j) in enumerate(tiles):
                pe.wait_ge(k.lo_done, b + 1)
                for x in range(2):
                    if n >= 2:
                        pe.wait_ge(read, 2 * (n - 2) + x + 1)
                    for kt in range(4 * x, 4 * x + 4):
                        w = slice(kt * BLOCK_COLS + j * P, kt * BLOCK_COLS + j * P + P)
                        whi, wlo = k.whi[b % 2][:, w], k.wlo[b % 2][:, w]
                        bank = k.ps[:, 2 * (n % 2) + x, :]
                        pe.matmul(bank, whi, k.act_hi[:, kt, :], start=(kt == 4 * x), stop=False)
                        pe.matmul(bank, whi, k.act_lo[:, kt, :], start=False, stop=False)
                        last = pe.matmul(bank, wlo, k.act_hi[:, kt, :], start=False, stop=(kt == 4 * x + 3))
                    last.then_inc(pair, 1)
                pe.wait_ge(pair, 2 * n + 2)
                pe.sem_inc(k.tile_done, 1)

        @block.vector
        def _(dve):
            split_lo(k, dve, b0)
            for n, (b, j) in enumerate(tiles):
                if j == 0:
                    split_lo(k, dve, b + 1)
                dve.wait_ge(gl[n % 4], 32 * (n // 4 + 1))
                for x in range(2):
                    dve.wait_ge(pair, 2 * n + x + 1)
                    if n >= 2:
                        dve.wait_ge(merged_done, n - 1)
                    dve.tensor_tensor(parts[:, n % 2, x, :], k.ps[:, 2 * (n % 2) + x, :], g[:, n % 4, x, :], ALU.mult) \
                        .then_inc(read, 1)
                dve.wait_ge(read, 2 * n + 2)
                dve.sem_inc(part, 2)
                dve.sem_inc(k.evac_done, 1)
                dve.tensor_tensor(merged[:, n, :], parts[:, n % 2, 0, :], parts[:, n % 2, 1, :], ALU.add) \
                    .then_inc(merged_done, 1)
            for n in range(KD):
                dve.wait_ge(hi, n + 1)
                dve.tensor_tensor(k.act_lo[:, n, :], merged[:, n, :], k.act_hi[:, n, :].bitcast(F32), ALU.subtract)


def stage_ffn(k, norm, then):
    norm.scale_stage()
    then.squares_stage()
    b0 = first_block("ff1")
    f_hi = k.region("f_hi", [P, KD, S], F32R, 0)
    f_lo = k.region("f_lo", [P, KD, S], F32R, 16)
    sq = k.region("ff_sq", [P, 2, S], F32, 32)
    relu = k.region("ff_relu", [P, 2, S], F32, 36)
    relu_done, sq_done, hi, lo = k.sem("ff_relu_done"), k.sem("ff_sq_done"), k.sem("ff_hi"), k.sem("ff_lo")
    with k.nc.Block() as block:
        @block.sync
        def _(sp):
            load_blocks(k, sp, b0 + 32 + RAW_SLOTS)

        @block.scalar
        def _(act):
            norm.scale_act(act)
            for f in range(4):
                for n, (b, j) in enumerate(tiles_of(b0 + 8 * f, b0 + 8 * f + 4)):
                    if j == 0:
                        split_hi(k, act, b + 1)
                    m = KD * f + n
                    act.wait_ge(sq_done, m + 1)
                    if n == 0 and f:
                        act.wait_ge(k.tile_done, TILE_AT[b0 + 8 * f])
                    act.activation(f_hi[:, n, :], sq[:, m % 2, :], ACT.Copy).then_inc(hi, 1)
                for n, (b, j) in enumerate(tiles_of(b0 + 8 * f + 4, b0 + 8 * f + 8)):
                    if j == 0:
                        split_hi(k, act, b + 1)
                    if f == 3:
                        act.wait_ge(k.evac_done, TILE_AT[b] + j + 1)
                        then.square(act, n)

        @block.tensor
        def _(pe):
            for f in range(4):
                for n, (b, j) in enumerate(tiles_of(b0 + 8 * f, b0 + 8 * f + 4)):
                    multiply_tile(k, pe, b, j, norm.fed if n == f == 0 else None)
                pe.wait_ge(lo, KD * (f + 1))
                for n, (b, j) in enumerate(tiles_of(b0 + 8 * f + 4, b0 + 8 * f + 8)):
                    t = TILE_AT[b] + j
                    pe.wait_ge(k.lo_done, b + 1)
                    pe.wait_ge(k.evac_done, t - 3)
                    for kt in range(KD):
                        w = slice(kt * BLOCK_COLS + j * P, kt * BLOCK_COLS + j * P + P)
                        whi, wlo = k.whi[b % 2][:, w], k.wlo[b % 2][:, w]
                        pe.matmul(k.ps[:, t % 4, :], whi, f_hi[:, kt, :], start=(kt == 0), stop=False)
                        pe.matmul(k.ps[:, t % 4, :], whi, f_lo[:, kt, :], start=False, stop=False)
                        last = pe.matmul(k.ps[:, t % 4, :], wlo, f_hi[:, kt, :], start=False, stop=(kt == KD - 1))
                    last.then_inc(k.tile_done, 1)
                    if f == 3 and n:
                        then.mean(pe, n - 1)
            then.mean(pe, KD - 1)

        @block.vector
        def _(dve):
            norm.scale_dve(dve)
            for f in range(4):
                for n, (b, j) in enumerate(tiles_of(b0 + 8 * f, b0 + 8 * f + 4)):
                    if j == 0:
                        split_lo(k, dve, b + 1)
                    m, t = KD * f + n, TILE_AT[b] + j
                    dve.wait_ge(k.tile_done, t + 1)
                    dve.tensor_scalar(relu[:, m % 2, :], k.ps[:, t % 4, :], 0.0, None, ALU.max).then_inc(k.evac_done, 1)
                    dve.wait_ge(k.evac_done, t + 1)
                    if m >= 2:
                        dve.wait_ge(lo, m - 1)
                    dve.tensor_tensor(sq[:, m % 2, :], relu[:, m % 2, :], relu[:, m % 2, :], ALU.mult).then_inc(sq_done, 1)
                    dve.wait_ge(hi, m + 1)
                    dve.tensor_tensor(f_lo[:, n, :], sq[:, m % 2, :], f_hi[:, n, :].bitcast(F32), ALU.subtract) \
                        .then_inc(lo, 1)
                for n, (b, j) in enumerate(tiles_of(b0 + 8 * f + 4, b0 + 8 * f + 8)):
                    if j == 0:
                        split_lo(k, dve, b + 1)
                    t = TILE_AT[b] + j
                    dve.wait_ge(k.tile_done, t + 1)
                    dve.tensor_tensor(k.xT[:, n, :], k.xT[:, n, :], k.ps[:, t % 4, :], ALU.add).then_inc(k.evac_done, 1)


def stage_ple(k, norm, then):
    nc = k.nc
    norm.scale_stage()
    then.squares_stage()
    b0 = first_block("ple_gate")
    b1 = first_block("ple_proj")
    b2 = b1 + 4
    gate = k.region("ple_gates", [P, KD, S], F32, 20)
    pf = k.region("ple_p", [P, 2, S], F32, 36)
    p_hi = k.region("ple_p_hi", [P, 2, S], F32R, 40)
    p_lo = k.region("ple_p_lo", [P, 2, S], F32R, 44)
    part = k.region("ple_part", [P, 2, S], F32, 48)
    landed, p_hi_done, p_lo_done, gates, part_done, added = (k.sem("ple_landed"), k.sem("ple_p_hi_done"),
                                                             k.sem("ple_p_lo_done"), k.sem("ple_gates_done"),
                                                             k.sem("ple_part_done"), k.sem("ple_added"))
    with nc.Block() as block:
        @block.sync
        def _(sp):
            sp.dma_start(pf[:], k.io["pT"]).then_inc(landed, 16)
            load_blocks(k, sp, b2)

        @block.scalar
        def _(act):
            act.wait_ge(landed, 16)
            act.activation(p_hi[:], pf[:], ACT.Copy).then_inc(p_hi_done, 1)
            norm.scale_act(act)
            for n, (b, j) in enumerate(tiles_of(b0, b1)):
                if j == 0:
                    split_hi(k, act, b + 1)
                t = TILE_AT[b] + j
                act.wait_ge(k.tile_done, t + 1)
                act.activation(gate[:, n, :], k.ps[:, t % 4, :], ACT.Sigmoid).then_inc(k.evac_done, 1)
            for n, (b, j) in enumerate(tiles_of(b1, b2)):
                if j == 0:
                    split_hi(k, act, b + 1)
                act.wait_ge(added, n + 1)
                then.square(act, n)

        @block.tensor
        def _(pe):
            for n, (b, j) in enumerate(tiles_of(b0, b1)):
                multiply_tile(k, pe, b, j, norm.fed if n == 0 else None)
            pe.wait_ge(p_lo_done, 1)
            for n, (b, j) in enumerate(tiles_of(b1, b2)):
                t = TILE_AT[b] + j
                pe.wait_ge(k.lo_done, b + 1)
                pe.wait_ge(k.evac_done, t - 3)
                for kt in range(2):
                    w = slice(kt * BLOCK_COLS + j * P, kt * BLOCK_COLS + j * P + P)
                    whi, wlo = k.whi[b % 2][:, w], k.wlo[b % 2][:, w]
                    pe.matmul(k.ps[:, t % 4, :], whi, p_hi[:, kt, :], start=(kt == 0), stop=False)
                    pe.matmul(k.ps[:, t % 4, :], whi, p_lo[:, kt, :], start=False, stop=False)
                    last = pe.matmul(k.ps[:, t % 4, :], wlo, p_hi[:, kt, :], start=False, stop=(kt == 1))
                last.then_inc(k.tile_done, 1)
                if n >= 2:
                    then.mean(pe, n - 2)
            then.mean(pe, KD - 2)
            then.mean(pe, KD - 1)

        @block.vector
        def _(dve):
            dve.wait_ge(p_hi_done, 1)
            dve.tensor_tensor(p_lo[:], pf[:], p_hi[:].bitcast(F32), ALU.subtract).then_inc(p_lo_done, 1)
            norm.scale_dve(dve)
            for b in range(b0, b1):
                split_lo(k, dve, b + 1)
            dve.wait_ge(k.evac_done, TILE_AT[b1])
            for n, (b, j) in enumerate(tiles_of(b1, b2)):
                if j == 0:
                    split_lo(k, dve, b + 1)
                t = TILE_AT[b] + j
                dve.wait_ge(k.tile_done, t + 1)
                if n >= 2:
                    dve.wait_ge(added, n - 1)
                dve.tensor_tensor(part[:, n % 2, :], k.ps[:, t % 4, :], gate[:, n, :], ALU.mult).then_inc(k.evac_done, 1)
                dve.wait_ge(k.evac_done, t + 1)
                dve.tensor_tensor(k.xT[:, n, :], k.xT[:, n, :], part[:, n % 2, :], ALU.add).then_inc(added, 1)


def build(nc, io, stop=None):
    with ExitStack() as ctx:
        k = Core(nc, ctx, io)
        for n, stage in enumerate(program(k)):
            if stop is not None and n >= stop:
                break
            k.run(stage)
        if stop is not None:
            with nc.Block() as block:
                @block.sync
                def _(sp):
                    for i in range(RAW_SLOTS):
                        n = len(range(i, k.loaded, RAW_SLOTS))
                        if n:
                            sp.wait_ge(k.landed[i], 16 * n)
    return k


def program(k):
    out0, nsa0, out2 = first_block("ml_out"), first_block("nsa_out"), first_block("out_2")
    norm_ml, norm_nsa = Norm(k, "norm_ml", "ml_norm", 66), Norm(k, "norm_nsa", "nsa_norm", 84)
    norm_first, norm_mix = Norm(k, "norm_first", "final_norm", 78), Norm(k, "norm_mix", "norm_mix", 84)
    norm_ffn, norm_ple = Norm(k, "norm_ffn", "norm_ffn", 78), Norm(k, "norm_ple", "norm_ple", 84)
    norm_final = Norm(k, "norm_final", "norm_final", 78)
    return [
        lambda k: stage_open(k, norm_ml),
        lambda k: stage_ml_inner(k, norm_ml),
        stage_ml_gate,
        lambda k: stage_ml_heads(k, 0),
        lambda k: stage_add(k, out0, out0 + 4),
        lambda k: stage_ml_heads(k, 2),
        lambda k: stage_add(k, out0 + 4, out0 + 8, norm_nsa),
        lambda k: stage_nsa_in(k, norm_nsa),
        stage_nsa_prep,
        stage_nsa_cmp,
        stage_nsa_attention,
        stage_nsa_gate,
        lambda k: stage_add(k, nsa0, nsa0 + 4, norm_first),
        lambda k: stage_norm_residual(k, norm_first, norm_mix),
        lambda k: stage_in_2(k, norm_mix),
        stage_da_prep,
        stage_da_attention,
        stage_rw_prep,
        *[lambda k, c=c: stage_rw_heads(k, c) for c in range(RW_T)],
        stage_rw_out,
        stage_mix,
        lambda k: stage_add(k, out2, out2 + 4, norm_ffn),
        lambda k: stage_ffn(k, norm_ffn, norm_ple),
        lambda k: stage_ple(k, norm_ple, norm_final),
        lambda k: stage_norm_residual(k, norm_final),
    ]


def kernel(**inputs):
    import numpy as np
    import ml_dtypes
    import concourse.bacc as bacc
    from concourse.bass_utils import run_bass_kernel_spmd

    a = {n: np.asarray(x) for n, x in inputs.items()}
    arrays = layout(np, ml_dtypes, a)
    nc = bacc.Bacc("TRN2", target_bir_lowering=False, num_devices=1)
    io, ins = {}, {}
    for n, x in arrays.items():
        x = np.ascontiguousarray(x)
        ins[n + "_in"] = x
        io[n] = nc.dram_tensor(n + "_in", x.shape, mybir.dt.from_np(x.dtype), kind="ExternalInput").ap()
    scratch(nc, io)
    build(nc, io)
    r = run_bass_kernel_spmd(nc, [ins], core_ids=[0])
    got = r.results[0]["out_T"]
    return got.transpose(2, 1, 0).reshape(1, S, D)


def scratch(nc, io):
    io["v_scratch"] = nc.dram_tensor("v_scratch", [ML_HEADS, P, TT, S], F32).ap()
    io["z_scratch"] = nc.dram_tensor("z_scratch", [ML_T, P, S], F32).ap()
    io["out"] = nc.dram_tensor("out_T", [P, KD, S], F32, kind="ExternalOutput").ap()


def rows_of(np, x):
    return x.reshape(-1, P, x.shape[-1]).transpose(1, 0, 2)


def layout(np, ml_dtypes, a):
    f32, bf16 = np.float32, ml_dtypes.bfloat16
    out = {"xT": a["x"][0].T.reshape(KD, P, S).transpose(1, 0, 2)}

    order = [(2 * gp + half) * 4 + hh for gp in range(2) for hh in range(4) for half in range(2)]
    nsa_cols = np.concatenate([np.concatenate([np.arange(h * DK, (h + 1) * DK) for h in order]),
                               np.arange(NSA_HEADS * DK, a["nsa_w_in"].shape[2])])
    nsa_in = a["nsa_w_in"][0][:, nsa_cols]
    nsa_in = np.concatenate([nsa_in, np.zeros((D, 29 * P - nsa_in.shape[1]), f32)], axis=1)
    mix_o = np.concatenate([a["rwkv_w_o_2"][0], a["da_w_o_2"][0]], axis=0)
    w2 = a["w_in_2"][0]
    in_2 = np.concatenate([w2[:, 1920 + 1536:], w2[:, 1920:1920 + 1536], w2[:, :1920]], axis=1)
    weights = {"ml_in": a["ml_w_in"][0], "ml_out": a["ml_w_out"][0], "nsa_in": nsa_in, "nsa_out": a["nsa_w_out"][0],
               "in_2": in_2, "mix_o": mix_o, "out_2": a["w_out_2"][0], "ff1": a["w_ff1_2"][0], "ff2": a["w_ff2_2"][0],
               "ple_gate": a["w_ple_gate_2"][0], "ple_proj": a["w_ple_proj_2"][0]}
    stream = np.empty((P, STREAM_COLS), f32)
    for b, (name, r0, rows, c0, n) in enumerate(BLOCKS):
        stream[:, BLOCK_AT[b]:BLOCK_AT[b + 1]] = rows_of(np, weights[name][r0:r0 + rows, c0:c0 + n]).reshape(P, -1)
    out["stream"] = stream

    cols = np.zeros((P, N_COLS), f32)

    def put(name, x):
        x = x.reshape(-1, P)
        cols[:, COLS[name]:COLS[name] + x.shape[0]] = x.T

    for name, key in (("ml_norm", "ml_norm"), ("conv_w", "ml_conv_w"), ("conv_b", "ml_conv_b"), ("ml_ln_w", "ml_ln_w"),
                      ("skip", "ml_skip"), ("nsa_norm", "nsa_norm"), ("final_norm", "final_norm"),
                      ("norm_mix", "norm_mix_2"), ("norm_ffn", "norm_ffn_2"), ("norm_ple", "norm_ple_2"),
                      ("norm_final", "norm_final_2"), ("mu_prev", "shift_mu_prev_2"), ("mu_next", "shift_mu_next_2"),
                      ("w0", "rwkv_w0_2"), ("a0", "rwkv_a0_2"), ("k_k", "rwkv_k_k_2"), ("k_a", "rwkv_k_a_2"),
                      ("r_k", "rwkv_r_k_2"), ("rw_ln_w", "rwkv_ln_w_2"), ("rw_ln_b", "rwkv_ln_b_2"),
                      ("subln", "da_subln_w_2")):
        put(name, a[key])
    cols[0:4, COLS["b_if"]] = a["ml_b_if"][0, 0:4]
    cols[32:36, COLS["b_if"]] = a["ml_b_if"][0, 4:8]
    cols[0:48, COLS["b_gate"]] = a["nsa_b_gate"][0]
    for n in ("lq1", "lk1", "lq2", "lk2"):
        cols[0:64, COLS[n]] = a[f"da_{n}_2"][0]
    for n, x in (("eps6", 1e-6), ("eps5", 1e-5), ("eps_gn", 64e-5), ("one", 1.0)):
        cols[:, COLS[n]] = x
    cols[:, COLS["cmp_any"]] = np.arange(P) >= CMP_BLOCK - 1
    out["cols"] = cols

    w = np.stack([a["ml_w_q"][0], a["ml_w_k"][0], a["ml_w_v"][0]]).reshape(3, ML_T, 32, 4, 4)
    out["hw"] = w.transpose(2, 4, 0, 1, 3).reshape(P, 3, ML_T, 4)
    out["hwt"] = w.transpose(2, 3, 0, 1, 4).reshape(P, 3, ML_T, 4)
    out["wif"] = a["ml_w_if"][0].reshape(3, ML_T, P, 8).transpose(2, 0, 1, 3)

    w1 = a["nsa_cmp_w1"][0].reshape(2, CMP_BLOCK, DK, P).transpose(2, 0, 1, 3)
    out["cmp_w1"] = np.concatenate([w1, w1], axis=0)
    pe = a["nsa_cmp_pe"][0].transpose(2, 0, 1).reshape(DK, 64)
    w2 = a["nsa_cmp_w2"][0].transpose(1, 0, 2).reshape(P, 2 * DK)
    out["cmp_small"] = np.concatenate([np.concatenate([pe, pe], axis=0), w2], axis=1)

    i = np.arange(P)
    c = np.zeros((P, N_CONSTS), f32)

    def const(name, x):
        c[:x.shape[0], CONSTS[name]:CONSTS[name] + x.shape[1]] = x

    const("ident", np.eye(P))
    const("ones", np.ones((P, P)))
    const("mean_ones", np.full((P, P), 1.0 / D))
    const("block_ones", (i[:, None] // 64 == i[None, :] // 64))
    rot = np.zeros((P, P))
    for m in range(P):
        if m % 64 < 8:
            rot[m + 8, m] = -1.0
        elif m % 64 < 16:
            rot[m - 8, m] = 1.0
    const("rot", rot)
    const("same4", i[:, None] // 4 == np.arange(32)[None, :])
    sel = np.zeros((4, 4, P))
    for h in range(4):
        sel[h, h] = 1.0
    const("sel", sel.reshape(4, 512))
    inv_freq = (f32(500000.0) ** (-np.arange(0, 16, 2, dtype=f32) / f32(16))).astype(f32)
    ang = np.arange(S, dtype=f32)[:, None] * inv_freq[None, :]
    cos, sin = np.ones((P, S)), np.zeros((P, S))
    for m in range(P):
        if m % 64 < 16:
            cos[m], sin[m] = np.cos(ang[:, m % 8]), np.sin(ang[:, m % 8])
    const("cos", cos)
    const("sin", sin)
    out["consts"] = c

    out["pT"] = a["p_2"][0, 0].T.reshape(2, P, S).transpose(1, 0, 2)
    w2, a2 = (a[n][0].reshape(P, S) for n in ("rwkv_w2_2", "rwkv_a2_2"))
    out["lora"] = np.stack([w2, a2, a["rwkv_g2_2"][0]], axis=1)
    rw = np.zeros((P, N_RW_CONSTS), f32)
    rw[:, RW_CONSTS["scan"]:RW_CONSTS["scan"] + S] = np.arange(S) % CHUNK != 0
    src, dst = (i % CHUNK)[:, None], np.arange(CHUNK)[None, :]
    for d in range(2):
        before = src < dst if d == 0 else src > dst
        upto = before | (src == dst)
        at = RW_CONSTS[f"score{d}"]
        rw[:, at:at + 256] = np.concatenate([-1.0 * before, -1.0 * upto, 1.0 * before, 1.0 * upto], axis=1)
        for lv in range(LEVELS):
            b = 1 << lv
            at = RW_CONSTS[f"level{d}"] + CHUNK * lv
            rw[:, at:at + CHUNK] = before & (src // (2 * b) == dst // (2 * b)) & (src // b != dst // b)
    rw[:, RW_CONSTS["eye64"]:RW_CONSTS["eye64"] + CHUNK] = src == dst
    out["rw_consts"] = rw

    masks = np.zeros((P, 3 * P), bf16)
    masks[:, 0:P] = np.eye(P)
    masks[:, P:2 * P] = np.where(i[None, :] <= i[:, None], 0.0, -1e30)
    for t in range(TT):
        pos = t * P + i
        end = np.arange(32) * CMP_STRIDE + CMP_BLOCK - 1
        masks[:, 2 * P + 32 * t:2 * P + 32 * t + 32] = np.where(end[None, :] <= pos[:, None], 0.0, -1e30)
    out["masks_bf"] = masks
    return out
```

```python
from contextlib import ExitStack

import concourse.bass as bass
from concourse import mybir

F32 = mybir.dt.float32
F32R = mybir.dt.float32r
BF16 = mybir.dt.bfloat16
ALU = mybir.AluOpType
ACT = mybir.ActivationFunctionType
AX = mybir.AxisListType.X

P = 128
S = 512
D = 1024
KD = D // P
TT = S // P

ML_INNER = 2048
ML_T = ML_INNER // P
ML_HEADS = 4
ML_DH = 512
CONV = 4

NSA_HEADS = 16
NSA_GROUPS = 4
DK = 64
CMP_STRIDE = 16
CMP_BLOCK = 32
N_CMP = (S - CMP_BLOCK) // CMP_STRIDE + 1

DA_HEADS = 4
RW_T = 4
CHUNK = 64
N_CHUNK = S // CHUNK
LEVELS = 6
DECAY_SCALE = 0.6065306597126334
LAMBDA_INIT = 0.8 - 0.6

RAW_SLOTS = 3
BLOCK_COLS = 256


def weight_blocks():
    out = []

    def cols(name, r0, rows, c0, c1):
        while c0 < c1:
            n = min(BLOCK_COLS, c1 - c0)
            out.append((name, r0, rows, c0, n))
            c0 += n

    cols("ml_in", 0, D, 0, 2 * ML_INNER)
    for g in range(2):
        cols("ml_out", g * D, D, 0, D)
    cols("nsa_in", 0, D, 0, 29 * P)
    cols("nsa_out", 0, D, 0, D)
    cols("in_2", 0, D, 0, 43 * P)
    cols("mix_o", 0, D, 0, D)
    cols("out_2", 0, D, 0, D)
    for f in range(4):
        cols("ff1", 0, D, f * D, (f + 1) * D)
        cols("ff2", f * D, D, 0, D)
    cols("ple_gate", 0, D, 0, D)
    cols("ple_proj", 0, 256, 0, D)
    return out


BLOCKS = weight_blocks()
BLOCK_AT, TILE_AT = [], []
_at = _t = 0
for _name, _r0, _rows, _c0, _n in BLOCKS:
    BLOCK_AT.append(_at)
    TILE_AT.append(_t)
    _at += _rows // P * _n
    _t += _n // P
STREAM_COLS = _at
BLOCK_AT.append(_at)
TILE_AT.append(_t)


def first_block(name, nth=0):
    starts = [b for b, x in enumerate(BLOCKS) if x[0] == name and (b == 0 or BLOCKS[b - 1][0] != name or
              (x[3] == 0))]
    return starts[nth]


COLS = {}
_c = 0
for _name, _n in (("ml_norm", 8), ("conv_w", 64), ("conv_b", 16), ("ml_ln_w", 16), ("skip", 16),
                  ("nsa_norm", 8), ("final_norm", 8), ("norm_mix", 8), ("norm_ffn", 8), ("norm_ple", 8),
                  ("norm_final", 8), ("mu_prev", 15), ("mu_next", 15), ("w0", 8), ("a0", 8), ("k_k", 4),
                  ("k_a", 4), ("r_k", 4), ("rw_ln_w", 4), ("rw_ln_b", 4), ("subln", 1), ("b_if", 1),
                  ("b_gate", 1), ("lq1", 1), ("lk1", 1), ("lq2", 1), ("lk2", 1),
                  ("eps6", 1), ("eps5", 1), ("eps_gn", 1), ("one", 1), ("cmp_any", 1)):
    COLS[_name] = _c
    _c += _n
N_COLS = _c

CONSTS = {}
_c = 0
for _name, _n in (("ident", 128), ("ones", 128), ("mean_ones", 128), ("block_ones", 128), ("rot", 128),
                  ("same4", 32), ("sel", 512), ("cos", 512), ("sin", 512)):
    CONSTS[_name] = _c
    _c += _n
N_CONSTS = _c
RW_CONSTS = {}
_c = 0
for _name, _n in (("scan", 512), ("score0", 256), ("score1", 256), ("level0", 6 * 64), ("level1", 6 * 64),
                  ("eye64", 64)):
    RW_CONSTS[_name] = _c
    _c += _n
N_RW_CONSTS = _c

KB = 1024
BASE = 17 * KB


class Core:

    def __init__(self, nc, ctx, io):
        self.nc, self.ctx, self.io = nc, ctx, io
        self.stage, self.in_use, self.spent = None, [], []
        at = self.at
        self.consts = at("consts", [P, N_CONSTS], F32, 0)
        self.cols = at("cols", [P, N_COLS], F32, 9)
        self.ident_bf = at("ident_bf", [P, P], BF16, 10.25)
        self.causal_bf = at("causal_bf", [P, P], BF16, 10.5)
        self.cmp_bf = at("cmp_bf", [P, TT * 32], BF16, 10.75)
        self.small = at("small", [P, 256], F32, 11)
        self.xT = at("xT", [P, KD, S], F32, 12)
        self.act_hi = at("act_hi", [P, KD, S], F32R, 28)
        self.act_lo = at("act_lo", [P, KD, S], F32R, 44)
        self.raw = [at(f"raw{i}", [P, KD * BLOCK_COLS], F32, 60 + 8 * i) for i in range(RAW_SLOTS)]
        self.whi = [at(f"whi{i}", [P, KD * BLOCK_COLS], F32R, 84 + 8 * i) for i in range(2)]
        self.wlo = [at(f"wlo{i}", [P, KD * BLOCK_COLS], F32R, 100 + 8 * i) for i in range(2)]
        self.ps = ctx.enter_context(nc.psum_tensor("ps", [P, 8, S], F32))
        self.landed = [self.sem(f"weights_landed{i}") for i in range(RAW_SLOTS)]
        self.hi_done = self.sem("weights_hi_done")
        self.lo_done = self.sem("weights_lo_done")
        self.tile_done = self.sem("tile_done")
        self.evac_done = self.sem("evac_done")
        self.out_stored = self.sem("out_stored")
        self.loaded = 0

    def at(self, name, shape, dtype, kb):
        return self.nc.alloc_sbuf_tensor_at(name, shape, dtype, offset=BASE + int(kb * KB))

    def region(self, name, shape, dtype, kb):
        return self.at(name, shape, dtype, 116 + kb)

    def sem(self, name):
        s = (self.stage or self.ctx).enter_context(self.nc.semaphore(name))
        self.in_use.append(s)
        return s

    def run(self, stage):
        for first, end in self.spent:
            self.nc.sync.sem_clear(range(first, end))
        self.in_use = []
        with ExitStack() as self.stage:
            stage(self)
            numbers = sorted(s.num for s in self.in_use)
            self.spent = []
            for n in numbers:
                if self.spent and self.spent[-1][1] == n:
                    self.spent[-1][1] = n + 1
                else:
                    self.spent.append([n, n + 1])

    def const(self, name, n=P):
        c = CONSTS[name]
        return self.consts[:, c:c + n]

    def col(self, name, i=0, rows=slice(0, P)):
        c = COLS[name] + i
        return self.cols[rows, c:c + 1]


def load_blocks(k, sp, upto):
    while k.loaded < min(upto, len(BLOCKS)):
        b = k.loaded
        if b >= RAW_SLOTS:
            sp.wait_ge(k.lo_done, b - RAW_SLOTS + 1)
        n = BLOCK_AT[b + 1] - BLOCK_AT[b]
        sp.dma_start(k.raw[b % RAW_SLOTS][:, 0:n], k.io["stream"][:, BLOCK_AT[b]:BLOCK_AT[b + 1]]) \
            .then_inc(k.landed[b % RAW_SLOTS], 16)
        k.loaded += 1


def split_hi(k, act, b):
    if b >= len(BLOCKS):
        return
    n = BLOCK_AT[b + 1] - BLOCK_AT[b]
    act.wait_ge(k.landed[b % RAW_SLOTS], 16 * (b // RAW_SLOTS + 1))
    if b >= 2:
        act.wait_ge(k.tile_done, TILE_AT[b - 1])
    act.activation(k.whi[b % 2][:, 0:n], k.raw[b % RAW_SLOTS][:, 0:n], ACT.Copy).then_inc(k.hi_done, 1)


def split_lo(k, dve, b):
    if b >= len(BLOCKS):
        return
    n = BLOCK_AT[b + 1] - BLOCK_AT[b]
    dve.wait_ge(k.hi_done, b + 1)
    dve.tensor_tensor(k.wlo[b % 2][:, 0:n], k.raw[b % RAW_SLOTS][:, 0:n],
                      k.whi[b % 2][:, 0:n].bitcast(F32), ALU.subtract).then_inc(k.lo_done, 1)


def multiply_tile(k, pe, b, j, fed=None):
    _, _, rows, _, n = BLOCKS[b]
    t = TILE_AT[b] + j
    pe.wait_ge(k.lo_done, b + 1)
    if t >= 4:
        pe.wait_ge(k.evac_done, t - 3)
    bank = k.ps[:, t % 4, :]
    for kt in range(rows // P):
        w = slice(kt * n + j * P, kt * n + j * P + P)
        hi, lo = k.whi[b % 2][:, w], k.wlo[b % 2][:, w]
        if fed:
            pe.wait_ge(fed, kt + 1)
        pe.matmul(bank, hi, k.act_hi[:, kt, :], start=(kt == 0), stop=False)
        pe.matmul(bank, hi, k.act_lo[:, kt, :], start=False, stop=False)
        last = pe.matmul(bank, lo, k.act_hi[:, kt, :], start=False, stop=(kt == rows // P - 1))
    last.then_inc(k.tile_done, 1)


def tiles_of(b0, b1):
    return [(b, j) for b in range(b0, b1) for j in range(BLOCKS[b][4] // P)]


class Norm:

    def __init__(self, k, tag, gain, kb):
        self.k, self.tag, self.gain = k, tag, gain
        self.sq = k.region(f"{tag}_sq", [P, 2, S], F32, kb)
        self.h = k.region(f"{tag}_h", [P, 2, S], F32, kb)
        self.root = k.region(f"{tag}_root", [P, S], F32, kb + 4)

    def squares_stage(self):
        self.sq_done, self.sq_used = self.k.sem(f"{self.tag}_sq_done"), self.k.sem(f"{self.tag}_sq_used")

    def square(self, act, n):
        if n >= 2:
            act.wait_ge(self.sq_used, n - 1)
        act.activation(self.sq[:, n % 2, :], self.k.xT[:, n, :], ACT.Square).then_inc(self.sq_done, 1)

    def mean(self, pe, n):
        pe.wait_ge(self.sq_done, n + 1)
        return pe.matmul(self.k.ps[:, 7, :], self.k.const("mean_ones"), self.sq[:, n % 2, :], start=(n == 0),
                         stop=(n == KD - 1)).then_inc(self.sq_used, 1)

    def scale_stage(self):
        k, tag = self.k, self.tag
        self.root_done, self.inv_done = k.sem(f"{tag}_root_done"), k.sem(f"{tag}_inv_done")
        self.h_done, self.hi_done, self.fed = k.sem(f"{tag}_h_done"), k.sem(f"{tag}_hi_done"), k.sem(f"{tag}_fed")

    def take_root(self, act):
        act.activation(self.root[:], self.k.ps[:, 7, :], ACT.Sqrt, bias=self.k.col("eps6")).then_inc(self.root_done, 1)

    def scale_act(self, act):
        self.take_root(act)
        for i in range(KD):
            act.wait_ge(self.h_done, i + 1)
            act.activation(self.k.act_hi[:, i, :], self.h[:, i % 2, :], ACT.Copy).then_inc(self.hi_done, 1)

    def invert(self, dve):
        dve.wait_ge(self.root_done, 1)
        dve.reciprocal(self.root[:], self.root[:]).then_inc(self.inv_done, 1)
        dve.wait_ge(self.inv_done, 1)

    def scale_dve(self, dve):
        k = self.k
        self.invert(dve)
        for i in range(KD + 1):
            if i < KD:
                if i >= 2:
                    dve.wait_ge(self.fed, i - 1)
                dve.scalar_tensor_tensor(out=self.h[:, i % 2, :], in0=k.xT[:, i, :], scalar=k.col(self.gain, i),
                                         in1=self.root[:], op0=ALU.mult, op1=ALU.mult).then_inc(self.h_done, 1)
            if i >= 1:
                dve.wait_ge(self.hi_done, i)
                dve.tensor_tensor(k.act_lo[:, i - 1, :], self.h[:, (i - 1) % 2, :],
                                  k.act_hi[:, i - 1, :].bitcast(F32), ALU.subtract).then_inc(self.fed, 1)


def stage_norm_residual(k, norm, then=None):
    nc = k.nc
    norm.scale_stage()
    if then:
        then.squares_stage()
    with nc.Block() as block:
        @block.scalar
        def _(act):
            norm.take_root(act)
            if then:
                for i in range(KD):
                    act.wait_ge(norm.h_done, i + 1)
                    then.square(act, i)

        @block.tensor
        def _(pe):
            if then:
                for i in range(KD):
                    then.mean(pe, i)

        @block.vector
        def _(dve):
            norm.invert(dve)
            for i in range(KD):
                dve.scalar_tensor_tensor(out=k.xT[:, i, :], in0=k.xT[:, i, :], scalar=k.col(norm.gain, i),
                                         in1=norm.root[:], op0=ALU.mult, op1=ALU.mult).then_inc(norm.h_done, 1)

        @block.sync
        def _(sp):
            if not then:
                for i in range(0, KD, 2):
                    sp.wait_ge(norm.h_done, i + 2)
                    sp.dma_start(k.io["out"][:, i:i + 2], k.xT[:, i:i + 2]).then_inc(k.out_stored, 16)
                sp.wait_ge(k.out_stored, 16 * KD // 2)


def stage_add(k, b0, b1, norm=None):
    if norm:
        norm.squares_stage()
    tiles = tiles_of(b0, b1)
    with k.nc.Block() as block:
        @block.sync
        def _(sp):
            load_blocks(k, sp, b1 + RAW_SLOTS)

        @block.scalar
        def _(act):
            for n, (b, j) in enumerate(tiles):
                if j == 0:
                    split_hi(k, act, b + 1)
                if norm:
                    act.wait_ge(k.evac_done, TILE_AT[b] + j + 1)
                    norm.square(act, n)

        @block.tensor
        def _(pe):
            for n, (b, j) in enumerate(tiles):
                multiply_tile(k, pe, b, j)
                if norm and n:
                    norm.mean(pe, n - 1)
            if norm:
                norm.mean(pe, KD - 1)

        @block.vector
        def _(dve):
            for n, (b, j) in enumerate(tiles):
                if j == 0:
                    split_lo(k, dve, b + 1)
                t = TILE_AT[b] + j
                dve.wait_ge(k.tile_done, t + 1)
                dve.tensor_tensor(k.xT[:, n, :], k.xT[:, n, :], k.ps[:, t % 4, :], ALU.add) \
                    .then_inc(k.evac_done, 1)


def stage_open(k, norm):
    k.hw = k.region("hw", [P, 3, ML_T, 4], F32, 84)
    hwt = k.region("hwt", [P, 3, ML_T, 4], F32, 60)
    wif = k.region("wif", [P, 3, ML_T, 8], F32, 61)
    W = 8
    wide = k.region("wide", [P, W, P], F32, 63)
    k.fold = k.region("fold", [P, 2, ML_T, 36], F32, 36)
    got, got_x, got_rest = k.sem("fold_landed"), [k.sem(f"x_landed{i}") for i in range(4)], k.sem("open_landed")
    wide_pool, wide_dve, fold_mm, zeroed = (k.sem("wide_by_pool"), k.sem("wide_by_dve"), k.sem("fold_mm"),
                                            k.sem("fold_zeroed"))
    norm.squares_stage()
    io = k.io
    with k.nc.Block() as block:
        @block.sync
        def _(sp):
            sp.dma_start(hwt[:], io["hwt"]).then_inc(got, 16)
            sp.dma_start(k.consts[:, 0:CONSTS["sel"]], io["consts"][:, 0:CONSTS["sel"]]).then_inc(got, 16)
            sp.dma_start(wif[:], io["wif"]).then_inc(got, 16)
            for i in range(4):
                sp.dma_start(k.xT[:, 2 * i:2 * i + 2], io["xT"][:, 2 * i:2 * i + 2]).then_inc(got_x[i], 16)
            sp.dma_start(k.cols[:], io["cols"]).then_inc(got_rest, 16)
            load_blocks(k, sp, 1)
            sp.dma_start(k.hw[:], io["hw"]).then_inc(got_rest, 16)
            sp.dma_start(k.consts[:, CONSTS["sel"]:], io["consts"][:, CONSTS["sel"]:]).then_inc(got_rest, 16)
            sp.dma_start(k.ident_bf[:], io["masks_bf"][:, 0:P]).then_inc(got_rest, 16)
            sp.dma_start(k.causal_bf[:], io["masks_bf"][:, P:2 * P]).then_inc(got_rest, 16)
            sp.dma_start(k.cmp_bf[:], io["masks_bf"][:, 2 * P:3 * P]).then_inc(got_rest, 16)
            load_blocks(k, sp, RAW_SLOTS)
            sp.wait_ge(got_rest, 96)

        @block.scalar
        def _(act):
            for n in range(KD):
                if n % 2 == 0:
                    act.wait_ge(got_x[n // 2], 16)
                norm.square(act, n)
                if n == 1:
                    split_hi(k, act, 0)

        def widen_own(eng, first, done):
            eng.wait_ge(got, 48)
            for u in range(first, 3 * ML_T, 2):
                if u >= W:
                    eng.wait_ge(fold_mm, u - W + 1)
                widen(k, eng, wide[:, u % W, :], hwt[:, u % 3, u // 3, :]).then_inc(done, 1)

        @block.gpsimd
        def _(pool):
            widen_own(pool, 0, wide_pool)

        @block.tensor
        def _(pe):
            for u in range(3 * ML_T):
                m, t = u % 3, u // 3
                pe.wait_ge((wide_pool, wide_dve)[u % 2], u // 2 + 1)
                x = 1 if m == 2 else 0
                pe.matmul(k.ps[:, 5 + x, 8 * t:8 * t + 8], wide[:, u % W, :], wif[:, m, t, :],
                          start=(m != 1), stop=(m != 0)).then_inc(fold_mm, 1)
            for n in range(KD):
                norm.mean(pe, n)

        @block.vector
        def _(dve):
            dve.memset(k.fold[:], 0.0).then_inc(zeroed, 1)
            widen_own(dve, 1, wide_dve)
            split_lo(k, dve, 0)
            dve.wait_ge(zeroed, 1)
            dve.wait_ge(fold_mm, 3 * ML_T)
            for x in range(2):
                sums = k.ps[:, 5 + x, 0:8 * ML_T].rearrange("p (t g) -> p t g", g=8)
                for g in range(2):
                    dve.tensor_copy(k.fold[:, x, :, 32 * g:32 * g + 4], sums[:, :, 4 * g:4 * g + 4])


def widen(k, eng, out, blocks):
    return eng.tensor_tensor(out.rearrange("p (n i) -> p n i", i=4),
                             blocks.rearrange("p (o i) -> p o i", o=1).to_broadcast([P, 32, 4]),
                             k.const("same4", 32).rearrange("p (n o) -> p n o", o=1).to_broadcast([P, 32, 4]),
                             ALU.mult)


def stage_ml_inner(k, norm):
    nc = k.nc
    norm.scale_stage()
    b0 = first_block("ml_in")
    b1 = b0 + ML_INNER // BLOCK_COLS
    k.xconv = k.region("xconv", [P, ML_T, S], F32, 0)
    xin = k.region("xin", [P, 2, CONV - 1 + S + 1], F32, 42)
    acc = k.region("conv_acc", [P, 2, S], F32, 47)
    wide = k.region("wide_v", [P, 2, P], F32, 51)
    vout = k.region("v_out", [P, 2, TT, P], F32, 52)
    pad_done, xin_ready, conv_done, xconv_ready = (k.sem("pad_done"), k.sem("xin_ready"), k.sem("conv_done"),
                                                   k.sem("xconv_ready"))
    conv_step = k.sem("conv_step")
    wide_done, v_mm, v_copied, gate_mm = k.sem("wide_v_done"), k.sem("v_mm"), k.sem("v_copied"), k.sem("gate_mm")
    k.v_stored = [k.sem(f"v_stored{i}") for i in range(2)]

    def store_v(act, t):
        act.wait_ge(v_copied, t + 1)
        act.dma_start(k.io["v_scratch"][t // 4][:, :, (t % 4) * P:(t % 4 + 1) * P], vout[:, t % 2]) \
            .then_inc(k.v_stored[t % 2], 16)

    def conv_in(t, tap):
        return xin[:, t % 2, tap:tap + S]

    with nc.Block() as block:
        @block.sync
        def _(sp):
            load_blocks(k, sp, b1 + RAW_SLOTS)

        @block.gpsimd
        def _(pool):
            for t in range(ML_T):
                if t >= 2:
                    pool.wait_ge(v_mm, t - 1)
                widen(k, pool, wide[:, t % 2, :], k.hw[:, 2, t, :]).then_inc(wide_done, 1)

        @block.scalar
        def _(act):
            norm.scale_act(act)
            act.wait_ge(pad_done, 1)
            for t in range(ML_T + 1):
                if t < ML_T:
                    if t % 2 == 0:
                        split_hi(k, act, b0 + t // 2 + 1)
                    tile = TILE_AT[b0] + t
                    act.wait_ge(k.tile_done, tile + 1)
                    if t >= 2:
                        act.wait_ge(conv_done, t - 1)
                        act.wait_ge(gate_mm, t - 1)
                    act.activation(xin[:, t % 2, CONV - 1:CONV - 1 + S], k.ps[:, tile % 4, :], ACT.Copy) \
                        .then_inc(xin_ready, 1)
                    act.wait_ge(xin_ready, t + 1)
                    act.sem_inc(k.evac_done, 1)
                if t >= 1:
                    act.wait_ge(conv_done, t)
                    act.activation(k.xconv[:, t - 1, :], acc[:, (t - 1) % 2, :], ACT.Silu).then_inc(xconv_ready, 1)
                if t >= 2:
                    store_v(act, t - 2)
            store_v(act, ML_T - 1)
            for i in range(2):
                act.wait_ge(k.v_stored[i], 16 * ML_T // 2)

        @block.vector
        def _(dve):
            dve.memset(xin[:, :, 0:CONV - 1], 0.0).then_inc(pad_done, 1)
            norm.scale_dve(dve)
            for t in range(ML_T + 1):
                if t < ML_T:
                    if t % 2 == 0:
                        split_lo(k, dve, b0 + t // 2 + 1)
                    dve.wait_ge(xin_ready, t + 1)
                    if t >= 2:
                        dve.wait_ge(xconv_ready, t - 1)
                    dve.tensor_scalar(acc[:, t % 2, :], conv_in(t, 0), k.col("conv_w", 0 * ML_T + t),
                                      k.col("conv_b", t), ALU.mult, ALU.add).then_inc(conv_step, 1)
                    for tap in range(1, CONV):
                        dve.wait_ge(conv_step, (CONV - 1) * t + tap)
                        dve.scalar_tensor_tensor(out=acc[:, t % 2, :], in0=conv_in(t, tap),
                                                 scalar=k.col("conv_w", tap * ML_T + t), in1=acc[:, t % 2, :],
                                                 op0=ALU.mult, op1=ALU.add) \
                            .then_inc(conv_step if tap < CONV - 1 else conv_done, 1)
                if t >= 1:
                    u = t - 1
                    dve.wait_ge(v_mm, u + 1)
                    if u >= 2:
                        dve.wait_ge(k.v_stored[u % 2], 16 * (u // 2))
                    dve.tensor_copy(vout[:, u % 2].rearrange("p a n -> p (a n)"), k.ps[:, 4 + u % 2, :]) \
                        .then_inc(v_copied, 1)

        @block.tensor
        def _(pe):
            for t in range(ML_T + 1):
                if t < ML_T:
                    multiply_tile(k, pe, b0 + t // 2, t % 2, norm.fed if t == 0 else None)
                if t >= 1:
                    u = t - 1
                    pe.wait_ge(xin_ready, u + 1)
                    pe.wait_ge(wide_done, u + 1)
                    if u >= 2:
                        pe.wait_ge(v_copied, u - 1)
                    for i in range(TT):
                        last = pe.matmul(k.ps[:, 4 + u % 2, i * P:(i + 1) * P],
                                         xin[:, u % 2, CONV - 1 + i * P:CONV - 1 + (i + 1) * P],
                                         wide[:, u % 2, :], start=True, stop=True)
                    last.then_inc(v_mm, 1)
                    pe.matmul(k.ps[0:36, 6, :], k.fold[:, 1, u, :], xin[:, u % 2, CONV - 1:CONV - 1 + S],
                              start=(u == 0), stop=False)
                    pe.wait_ge(xconv_ready, u + 1)
                    pe.matmul(k.ps[0:36, 6, :], k.fold[:, 0, u, :], k.xconv[:, u, :], start=False,
                              stop=(u == ML_T - 1)).then_inc(gate_mm, 1)


def stage_ml_gate(k):
    nc = k.nc
    b0 = first_block("ml_in") + ML_INNER // BLOCK_COLS
    b1 = b0 + ML_INNER // BLOCK_COLS
    zt = k.region("zt", [P, 4, S], F32, 32)
    rows = k.region("gate_rows", [4, 10, S], F32, 42)
    k.neg_m = k.region("neg_m", [4, S], F32, 86)
    k.g_col = k.small[:, 0:16].rearrange("p (t h) -> p t h", h=4)
    k.floor_col = k.small[:, 16:32].rearrange("p (t h) -> p t h", h=4)
    inp, fg, mag, ex, ln, neg, run, g, top, floor = (rows[:, i, :] for i in range(10))
    k.z_stored = [k.sem(f"z_stored{i}") for i in range(4)]
    z_ready, a_step, d_step, g_tr, g_out = (k.sem("z_ready"), k.sem("gate_act_step"), k.sem("gate_dve_step"),
                                            k.sem("g_transposed"), k.sem("g_out"))
    zeros = k.sem("gate_zeros")
    zero, one = rows[:, 3, :], rows[:, 2, :]
    with nc.Block() as block:
        @block.sync
        def _(sp):
            load_blocks(k, sp, b1 + RAW_SLOTS)

        @block.scalar
        def _(act):
            f32r = slice(32, 36)
            act.activation(inp, k.ps[0:4, 6, :], ACT.Identity, bias=k.col("b_if", rows=slice(0, 4))).then_inc(a_step, 1)
            act.activation(fg, k.ps[f32r, 6, :], ACT.Identity, bias=k.col("b_if", rows=f32r)).then_inc(a_step, 1)
            act.wait_ge(a_step, 2)
            act.activation(mag, fg, ACT.Abs).then_inc(a_step, 1)
            act.wait_ge(a_step, 3)
            act.activation(ex, mag, ACT.Exp, scale=-1.0).then_inc(a_step, 1)
            act.wait_ge(a_step, 4)
            act.activation(ln, ex, ACT.Ln, bias=k.col("one", rows=slice(0, 4))).then_inc(a_step, 1)
            act.wait_ge(d_step, 8)
            act.activation(floor, floor, ACT.Exp, scale=-1.0).then_inc(a_step, 1)
            for t in range(ML_T):
                if t % 2 == 0:
                    split_hi(k, act, b0 + t // 2 + 1)
                tile = TILE_AT[b0] + t
                act.wait_ge(k.tile_done, tile + 1)
                if t >= 4:
                    act.wait_ge(k.z_stored[t % 4], 16 * (t // 4))
                act.activation(zt[:, t % 4, :], k.ps[:, tile % 4, :], ACT.Silu).then_inc(z_ready, 1)
                act.wait_ge(z_ready, t + 1)
                act.sem_inc(k.evac_done, 1)
                act.dma_start(k.io["z_scratch"][t], zt[:, t % 4, :]).then_inc(k.z_stored[t % 4], 16)
            for i in range(4):
                act.wait_ge(k.z_stored[i], 16 * ML_T // 4)

        @block.vector
        def _(dve):
            dve.wait_ge(a_step, 5)
            dve.memset(zero, 0.0).then_inc(d_step, 1)
            dve.memset(one, 1.0).then_inc(d_step, 1)
            dve.tensor_scalar(neg, fg, 0.0, None, ALU.min).then_inc(d_step, 1)
            dve.wait_ge(d_step, 3)
            dve.tensor_tensor(neg, neg, ln, ALU.subtract).then_inc(d_step, 1)
            dve.wait_ge(d_step, 4)
            dve.tensor_tensor_scan(run, one, neg, 0.0, ALU.mult, ALU.add).then_inc(d_step, 1)
            dve.wait_ge(d_step, 5)
            dve.tensor_tensor(g, inp, run, ALU.subtract).then_inc(d_step, 1)
            dve.wait_ge(d_step, 6)
            dve.tensor_tensor_scan(top, g, zero, 0.0, ALU.max, ALU.max).then_inc(d_step, 1)
            dve.wait_ge(d_step, 7)
            dve.tensor_tensor(floor, run, top, ALU.add).then_inc(d_step, 1)
            dve.tensor_scalar(k.neg_m[:], top, -1.0, None, ALU.mult)
            for t in range(0, ML_T, 2):
                split_lo(k, dve, b0 + t // 2 + 1)
                if t == 2:
                    dve.wait_ge(g_tr, 2)
                    dve.tensor_copy(k.small[:, 0:32], k.ps[:, 7, 0:32]).then_inc(g_out, 1)

        @block.tensor
        def _(pe):
            for t in range(ML_T):
                multiply_tile(k, pe, b0 + t // 2, t % 2)
                if t == 1:
                    pe.wait_ge(a_step, 6)
                    pe.wait_ge(d_step, 8)
                    for n, row in enumerate((g, floor)):
                        for i in range(TT):
                            c = 16 * n + 4 * i
                            last = pe.transpose(k.ps[:, 7, c:c + 4], row[:, i * P:(i + 1) * P],
                                                k.const("ident")[0:4, 0:4])
                        last.then_inc(g_tr, 1)


def stage_ml_heads(k, first):
    nc = k.nc
    tag = f"ml{first}"
    v = k.region(f"{tag}_v", [P, TT, S], F32, 32)
    q = k.region(f"{tag}_q", [P, TT, S], F32, 40)
    kk = k.region(f"{tag}_k", [P, TT, S], F32, 48)
    st = k.region(f"{tag}_st", [P, TT, S], F32, 56)
    wexp = k.region(f"{tag}_wexp", [P, 2, S], F32, 64)
    z = k.region(f"{tag}_z", [P, 2, S], F32, 68)
    wide = k.region(f"{tag}_wide", [P, 2, 2, P], F32, 72)
    y = k.region(f"{tag}_y", [P, 2, S], F32, 74)
    sc = k.small
    den, adn, r, sd, scale, shift = (sc[:, 32 + 4 * i:36 + 4 * i] for i in range(6))
    stats = sc[:, 64:64 + 24].rearrange("p (t s) -> p t s", s=6)
    mv = sc[:, 96:104].rearrange("p (t s) -> p t s", s=2)
    r2v = sc[:, 104:108]
    s = {n: k.sem(f"{tag}_{n}") for n in (
          "v_landed", "wide_done", "qk_mm", "q_copied", "k_copied", "nm_mm",
          "sc_mm", "wexp_raw", "wexp_done", "st_done", "h_mm", "hn_done", "hn_dve",
          "tr_mm", "y_read", "y_done", "y_hi", "y_lo", "step", "r2v_done",
          "sd_done", "scale_done")}
    zl = [k.sem(f"{tag}_z_landed{i}") for i in range(2)]
    heads = range(2)

    def lo(pool, u):
        pool.wait_ge(s["y_hi"], u + 1)
        pool.tensor_tensor(k.act_lo[:, u, :], y[:, u % 2, :], k.act_hi[:, u, :].bitcast(F32), ALU.subtract) \
            .then_inc(s["y_lo"], 1)

    with nc.Block() as block:
        @block.sync
        def _(sp):
            for h in heads:
                if h:
                    sp.wait_ge(s["h_mm"], TT * h)
                sp.dma_start(v[:], k.io["v_scratch"][first + h]).then_inc(s["v_landed"], 16)
                for c in range(TT):
                    u = TT * h + c
                    if u >= 2:
                        sp.wait_ge(s["y_done"], u - 1)
                    sp.dma_start(z[:, c % 2, :], k.io["z_scratch"][TT * (first + h) + c]).then_inc(zl[c % 2], 16)

        @block.gpsimd
        def _(pool):
            for h in heads:
                for c in range(TT):
                    u = TT * h + c
                    if u >= 2:
                        pool.wait_ge(s["qk_mm"], u - 1)
                    t = TT * (first + h) + c
                    widen(k, pool, wide[:, c % 2, 0, :], k.hw[:, 0, t, :]).then_inc(s["wide_done"], 1)
                    widen(k, pool, wide[:, c % 2, 1, :], k.hw[:, 1, t, :]).then_inc(s["wide_done"], 1)
                for j in range(TT):
                    pool.wait_ge(s["wexp_raw"], TT * h + j + 1)
                    part = wexp[:, j % 2, j * P:(j + 1) * P]
                    pool.affine_select(out=part, in_=part, compare_op=ALU.is_ge, fill=0.0, base=0,
                                       pattern=[[1, P]], channel_multiplier=-1).then_inc(s["wexp_done"], 1)
                for c in range(TT):
                    lo(pool, TT * h + c)

        @block.tensor
        def _(pe):
            for h in heads:
                for c in range(TT):
                    u = TT * h + c
                    pe.wait_ge(s["wide_done"], 2 * u + 2)
                    if c >= 2:
                        pe.wait_ge(s["q_copied"], u - 1)
                        pe.wait_ge(s["k_copied"], u - 1)
                    x = k.xconv[:, TT * (first + h) + c, :]
                    b = 2 * (c % 2)
                    pe.matmul(k.ps[:, b, :], wide[:, c % 2, 0, :], x, start=True, stop=True)
                    pe.matmul(k.ps[:, b + 1, :], wide[:, c % 2, 1, :], x, start=True, stop=True).then_inc(s["qk_mm"], 1)
                pe.matmul(k.ps[:, 6, :], k.const("sel", 512)[0:4, (first + h) * P:(first + h + 1) * P], k.neg_m[:],
                          start=True, stop=True).then_inc(s["nm_mm"], 1)
                pe.wait_ge(s["q_copied"], TT * (h + 1))
                pe.wait_ge(s["k_copied"], TT * (h + 1))
                if h:
                    pe.wait_ge(s["y_read"], TT * h)
                for j in range(TT):
                    if j >= 2:
                        pe.wait_ge(s["st_done"], TT * h + j - 1)
                    for c in range(TT):
                        last = pe.matmul(k.ps[:, 4 + j % 2, j * P:S], kk[:, c, j * P:(j + 1) * P], q[:, c, j * P:S],
                                         start=(c == 0), stop=(c == TT - 1))
                    last.then_inc(s["sc_mm"], 1)
                pe.wait_ge(s["v_landed"], 16 * (h + 1))
                for i in range(TT):
                    pe.wait_ge(s["st_done"], TT * h + i + 1)
                    for j in range(i + 1):
                        lhs = st[:, j, i * P:(i + 1) * P]
                        pe.matmul(k.ps[:, i, :], lhs, v[:, j, :], start=(j == 0), stop=(j == i))
                        last = pe.matmul(k.ps[:, 7, i:i + 1], lhs, k.const("ones")[:, 0:1], start=(j == 0), stop=(j == i))
                    last.then_inc(s["h_mm"], 1)
                pe.wait_ge(s["hn_done"], TT // 2 * (h + 1))
                pe.wait_ge(s["hn_dve"], TT // 2 * (h + 1))
                for c in range(TT):
                    if c >= 2:
                        pe.wait_ge(s["y_read"], TT * h + c - 1)
                    for i in range(TT):
                        last = pe.transpose(k.ps[:, 4 + c % 2, i * P:(i + 1) * P], kk[:, i, c * P:(c + 1) * P],
                                            k.const("ident"))
                    last.then_inc(s["tr_mm"], 1)

        @block.scalar
        def _(act):
            for h in heads:
                for c in range(TT):
                    act.wait_ge(s["qk_mm"], TT * h + c + 1)
                    act.activation(q[:, c, :], k.ps[:, 2 * (c % 2), :], ACT.Copy).then_inc(s["q_copied"], 1)
                act.wait_ge(s["nm_mm"], h + 1)
                for j in range(TT):
                    u = TT * h + j
                    if u >= 2:
                        act.wait_ge(s["st_done"], u - 1)
                    act.activation(wexp[:, j % 2, j * P:S], k.ps[:, 6, j * P:S], ACT.Exp,
                                   bias=k.g_col[:, j, first + h:first + h + 1]).then_inc(s["wexp_raw"], 1)
                act.wait_ge(s["r2v_done"], h + 1)
                act.activation(sd, r2v, ACT.Sqrt, bias=k.col("eps6")).then_inc(s["sd_done"], 1)
                act.wait_ge(s["scale_done"], h + 1)
                for i in range(0, TT, 2):
                    act.activation(kk[:, i, :], k.ps[:, i, :], ACT.Identity, scale=scale[:, i:i + 1],
                                   bias=shift[:, i:i + 1]).then_inc(s["hn_done"], 1)
                for c in range(TT):
                    u = TT * h + c
                    act.wait_ge(s["y_done"], u + 1)
                    act.activation(k.act_hi[:, u, :], y[:, c % 2, :], ACT.Copy).then_inc(s["y_hi"], 1)

        @block.vector
        def _(dve):
            step = [0]

            def then_wait(ins):
                step[0] += 1
                ins.then_inc(s["step"], 1)
                dve.wait_ge(s["step"], step[0])

            for h in heads:
                for c in range(TT):
                    dve.wait_ge(s["qk_mm"], TT * h + c + 1)
                    dve.tensor_copy(kk[:, c, :], k.ps[:, 2 * (c % 2) + 1, :]).then_inc(s["k_copied"], 1)
                for j in range(TT):
                    u = TT * h + j
                    dve.wait_ge(s["sc_mm"], u + 1)
                    dve.wait_ge(s["wexp_done"], u + 1)
                    dve.scalar_tensor_tensor(out=st[:, j, j * P:S], in0=k.ps[:, 4 + j % 2, j * P:S],
                                             scalar=ML_DH ** -0.5, in1=wexp[:, j % 2, j * P:S],
                                             op0=ALU.mult, op1=ALU.mult).then_inc(s["st_done"], 1)
                for i in range(TT):
                    dve.wait_ge(s["h_mm"], TT * h + i + 1)
                    then_wait(dve.bn_stats(stats[:, i, :], k.ps[:, i, :]))
                    then_wait(dve.bn_aggr(mv[:, i, :], stats[:, i, :]))
                floor = k.floor_col[:, :, first + h]
                then_wait(dve.tensor_copy(den, k.ps[:, 7, 0:TT]))
                then_wait(dve.scalar_tensor_tensor(out=adn, in0=den, scalar=-1.0, in1=den, op0=ALU.mult, op1=ALU.max))
                then_wait(dve.tensor_tensor(adn, adn, floor, ALU.max))
                then_wait(dve.reciprocal(r, adn))
                then_wait(dve.tensor_tensor(r2v, mv[:, :, 1], r, ALU.mult))
                dve.tensor_tensor(r2v, r2v, r, ALU.mult).then_inc(s["r2v_done"], 1)
                dve.wait_ge(s["sd_done"], h + 1)
                then_wait(dve.reciprocal(sd, sd))
                then_wait(dve.tensor_tensor(scale, sd, r, ALU.mult))
                dve.scalar_tensor_tensor(out=shift, in0=mv[:, :, 0], scalar=-1.0, in1=scale, op0=ALU.mult,
                                         op1=ALU.mult).then_inc(s["scale_done"], 1)
                dve.wait_ge(s["scale_done"], h + 1)
                for i in range(1, TT, 2):
                    dve.tensor_scalar(kk[:, i, :], k.ps[:, i, :], scale[:, i:i + 1], shift[:, i:i + 1], ALU.mult,
                                      ALU.add).then_inc(s["hn_dve"], 1)
                for c in range(TT):
                    u = TT * h + c
                    t = TT * (first + h) + c
                    x = k.xconv[:, t, :]
                    if u >= 2:
                        dve.wait_ge(s["y_lo"], u - 1)
                    then_wait(dve.tensor_scalar(y[:, c % 2, :], x, k.col("skip", t), None, ALU.mult))
                    dve.wait_ge(s["tr_mm"], u + 1)
                    dve.scalar_tensor_tensor(out=y[:, c % 2, :], in0=k.ps[:, 4 + c % 2, :], scalar=k.col("ml_ln_w", t),
                                             in1=y[:, c % 2, :], op0=ALU.mult, op1=ALU.add).then_inc(s["y_read"], 1)
                    dve.wait_ge(s["y_read"], u + 1)
                    dve.wait_ge(zl[c % 2], 16 * (u // 2 + 1))
                    dve.tensor_tensor(y[:, c % 2, :], y[:, c % 2, :], z[:, c % 2, :], ALU.mult).then_inc(s["y_done"], 1)


class Steps:

    def __init__(self, sem):
        self.sem, self.n = sem, 0

    def then_wait(self, eng, ins):
        self.n += 1
        ins.then_inc(self.sem, 1)
        eng.wait_ge(self.sem, self.n)


def stage_nsa_in(k, norm):
    nc = k.nc
    norm.scale_stage()
    b0 = first_block("nsa_in")
    b1 = first_block("nsa_out")
    k.q = k.region("nsa_q", [P, 8, S], F32, 0)
    k.kv = k.region("nsa_kv", [P, 8, S], F32, 16)
    k.gate_rows = k.region("nsa_gates", [48, S], F32, 32)
    k.padded = [k.region(f"cmp_in{i}", [P, 4, S + CMP_BLOCK], F32, at) for i, at in enumerate((34, 75.5))]
    k.w1 = [k.region(f"cmp_w1_{i}", [P, CMP_BLOCK, P], F32, 42.5 + 16 * i) for i in range(2)]
    k.cmp_small = k.region("cmp_small", [P, 2 * 32 + 2 * 64], F32, 74.5)
    zt = k.region("nsa_zt", [P, 2, S], F32, 84)
    zeroed = k.sem("nsa_zeroed")
    landed = k.sem("nsa_landed")
    z_ready, copied = k.sem("nsa_z_ready"), k.sem("nsa_copied")
    stored = [k.sem(f"nsa_z_stored{i}") for i in range(2)]
    with nc.Block() as block:
        @block.sync
        def _(sp):
            for i in range(2):
                sp.dma_start(k.w1[i][:], k.io["cmp_w1"][:, i]).then_inc(landed, 16)
            sp.dma_start(k.cmp_small[:], k.io["cmp_small"]).then_inc(landed, 16)
            load_blocks(k, sp, b1 + RAW_SLOTS)
            sp.wait_ge(landed, 48)

        @block.gpsimd
        def _(pool):
            for x in range(2):
                pool.memset(k.padded[x][:], 0.0).then_inc(zeroed, 1)

        @block.scalar
        def _(act):
            norm.scale_act(act)
            for t, (b, j) in enumerate(tiles_of(b0, b1)):
                if j == 0:
                    split_hi(k, act, b + 1)
                tile = TILE_AT[b] + j
                act.wait_ge(k.tile_done, tile + 1)
                bank = k.ps[:, tile % 4, :]
                if 8 <= t < 12:
                    act.wait_ge(zeroed, 2)
                    for half in range(2):
                        rows = slice(64 * half, 64 * half + 64)
                        act.activation(k.padded[(t - 8) // 2][rows, 2 * half + t % 2, 0:S], bank[rows], ACT.Copy) \
                            .then_inc(copied, 1)
                    act.wait_ge(copied, 2 * (t - 7))
                    act.sem_inc(k.evac_done, 1)
                elif t < 20:
                    out = k.q[:, t, :] if t < 8 else k.kv[:, t - 12, :]
                    act.activation(out, bank, ACT.Copy).then_inc(k.evac_done, 1)
                elif t < 28:
                    z = t - 20
                    if z == 0:
                        act.wait_ge(norm.fed, KD)
                    if z >= 2:
                        act.wait_ge(stored[z % 2], 16 * (z // 2))
                    act.activation(zt[:, z % 2, :], bank, ACT.Silu).then_inc(z_ready, 1)
                    act.wait_ge(z_ready, z + 1)
                    act.sem_inc(k.evac_done, 1)
                    act.dma_start(k.io["z_scratch"][z], zt[:, z % 2, :]).then_inc(stored[z % 2], 16)
                else:
                    act.activation(k.gate_rows[:], bank[0:48], ACT.Sigmoid, bias=k.col("b_gate", rows=slice(0, 48))) \
                        .then_inc(k.evac_done, 1)
            for i in range(2):
                act.wait_ge(stored[i], 64)

        @block.tensor
        def _(pe):
            for t, (b, j) in enumerate(tiles_of(b0, b1)):
                multiply_tile(k, pe, b, j, norm.fed if t == 0 else None)

        @block.vector
        def _(dve):
            norm.scale_dve(dve)
            for b in range(b0, b1):
                split_lo(k, dve, b + 1)


def stage_nsa_prep(k):
    nc = k.nc
    k.vtok = k.at("nsa_vtok", [P, 2, TT, 256], F32, 52)
    k.gtok = k.region("nsa_gtok", [P, TT, 48], F32, 84)
    k.kcmp = k.small[:, 128:256].rearrange("p (t x c) -> p t x c", t=2, x=2)
    k.vcmp = k.region("vcmp", [P, 4, 4, DK], F32, 85)
    hid = k.region("cmp_hid", [P, 2, 2, 2, 31], F32, 89)
    peb = k.small[:, 0:2]
    k.q_rot = k.at("q_rot", [P, 8, S], F32, 28)
    turned = k.at("turned", [P, 2, S], F32, 44)
    straight = k.at("straight", [P, 2, S], F32, 48)
    s = {n: k.sem(f"prep_{n}") for n in (
          "rot_mm", "rot_read", "straight", "turned", "done", "tr", "tr_read",
          "hid_mm", "pe_in", "pe_read", "hid_done", "zeroed", "v_mm")}
    pairs = [(k.q, i, k.q_rot, i) for i in range(8)] + [(k.kv, 4 * br + i, k.padded[br], i) for br in range(2)
                                                        for i in range(2)]
    w2 = k.cmp_small[:, 64:192].rearrange("p (x d) -> p x d", d=DK)
    pe_t = k.cmp_small[:, 0:64].rearrange("p (x t) -> p x t", t=CMP_BLOCK)
    V = N_CMP + 2
    with nc.Block() as block:
        @block.tensor
        def _(pe):
            def turn(n):
                src, i, _, _ = pairs[n]
                if n >= 2:
                    pe.wait_ge(s["rot_read"], n - 1)
                pe.matmul(k.ps[:, 4 + n % 2, :], k.const("rot"), src[:, i, :], start=True, stop=True) \
                    .then_inc(s["rot_mm"], 1)

            for x in range(2):
                for t in range(CMP_BLOCK):
                    u = CMP_BLOCK * x + t
                    if u % 5 == 0 and u // 5 < len(pairs):
                        turn(u // 5)
                    if t == 0:
                        pe.wait_ge(s["pe_in"], x + 1)
                    last = pe.matmul(k.ps[:, 2 + x, 0:4 * V].rearrange("p (a n) -> p a n", n=V), k.w1[x][:, t, :],
                                     k.padded[x][:, :, t:t + (V - 1) * CMP_STRIDE + 1:CMP_STRIDE],
                                     start=(t == 0), stop=(t == CMP_BLOCK - 1))
                last.then_inc(s["hid_mm"], 1)
            for n in range(5):
                if n >= 2:
                    pe.wait_ge(s["tr_read"], n - 1)
                for i in range(TT):
                    if n < 4:
                        last = pe.transpose(k.ps[:, n % 2, i * P:(i + 1) * P],
                                            k.kv[:, 2 + 4 * (n // 2) + n % 2, i * P:(i + 1) * P], k.const("ident"))
                    else:
                        last = pe.transpose(k.ps[:, 0, i * 48:(i + 1) * 48], k.gate_rows[:, i * P:(i + 1) * P],
                                            k.const("ident")[0:48, 0:48])
                last.then_inc(s["tr"], 1)
            pe.wait_ge(s["hid_done"], 2)
            for half in range(2):
                rows = slice(64 * half, 64 * half + 64)
                for gp in range(2):
                    pe.matmul(k.ps[rows, 6, 32 * gp:32 * gp + N_CMP], w2[:, 0, :], hid[:, 0, half, gp, :],
                              start=True, stop=True)
            for hh in range(4):
                for g in range(4):
                    last = pe.matmul(k.ps[32 * hh:32 * hh + N_CMP, 7, g * DK:(g + 1) * DK], hid[:, 1, g % 2, g // 2, :],
                                     w2[:, 1, :], start=True, stop=True)
            last.then_inc(s["v_mm"], 1)

        @block.scalar
        def _(act):
            for x in range(2):
                act.wait_ge(s["hid_mm"], x + 1)
                act.activation(peb[:, x:x + 1], k.ps[:, 2 + x, V - 1:V], ACT.Copy).then_inc(s["pe_read"], 1)
                act.wait_ge(s["pe_read"], x + 1)
                act.activation(hid[:, x].rearrange("p h a n -> p (h a) n"),
                               k.ps[:, 2 + x, 0:4 * V].rearrange("p (a n) -> p a n", n=V)[:, :, 0:N_CMP],
                               ACT.Silu, bias=peb[:, x:x + 1]).then_inc(s["hid_done"], 1)
            for n in range(4):
                act.wait_ge(s["tr"], n + 1)
                act.activation(k.vtok[:, n // 2, :, n % 2 * P:(n % 2 + 1) * P],
                               k.ps[:, n % 2, :].rearrange("p (t c) -> p t c", c=P), ACT.Copy).then_inc(s["tr_read"], 1)
            act.wait_ge(s["tr"], 5)
            act.activation(k.gtok[:].rearrange("p t c -> p (t c)"), k.ps[:, 0, 0:192], ACT.Copy)

        @block.gpsimd
        def _(pool):
            for x in range(2):
                pool.tensor_copy(k.padded[x][0:64, 0, S:S + CMP_BLOCK], pe_t[0:64, x, :]).then_inc(s["pe_in"], 1)
            pool.memset(k.vcmp[:], 0.0).then_inc(s["zeroed"], 1)
            pool.memset(k.small[:, 128:256], 0.0).then_inc(s["zeroed"], 1)
            for n, (src, i, _, _) in enumerate(pairs):
                if n >= 2:
                    pool.wait_ge(s["done"], n - 1)
                pool.tensor_tensor(straight[:, n % 2, :], src[:, i, :], k.const("cos", S), ALU.mult) \
                    .then_inc(s["straight"], 1)

        @block.vector
        def _(dve):
            for n, (src, i, dst, o) in enumerate(pairs):
                dve.wait_ge(s["rot_mm"], n + 1)
                if n >= 2:
                    dve.wait_ge(s["done"], n - 1)
                dve.tensor_tensor(turned[:, n % 2, :], k.ps[:, 4 + n % 2, :], k.const("sin", S), ALU.mult) \
                    .then_inc(s["rot_read"], 1)
                dve.wait_ge(s["rot_read"], n + 1)
                dve.wait_ge(s["straight"], n + 1)
                if n < 8:
                    dve.tensor_tensor(dst[:, o, :], turned[:, n % 2, :], straight[:, n % 2, :], ALU.add) \
                        .then_inc(s["done"], 1)
                else:
                    dve.wait_ge(s["hid_mm"], n // 2 - 3)
                    for half in range(2):
                        rows = slice(64 * half, 64 * half + 64)
                        last = dve.tensor_tensor(dst[rows, 2 * half + o, 0:S], turned[rows, n % 2, :],
                                                 straight[rows, n % 2, :], ALU.add)
                    last.then_inc(s["done"], 1)
            dve.wait_ge(s["v_mm"], 1)
            dve.wait_ge(s["zeroed"], 2)
            for half in range(2):
                rows = slice(64 * half, 64 * half + 64)
                dve.tensor_copy(k.kcmp[rows, :, half, 0:N_CMP],
                                k.ps[rows, 6, 0:64].rearrange("p (a n) -> p a n", n=32)[:, :, 0:N_CMP])
            for hh in range(4):
                rows = slice(32 * hh, 32 * hh + N_CMP)
                dve.tensor_copy(k.vcmp[rows, :, hh, :], k.ps[rows, 7, 0:256].rearrange("p (g d) -> p g d", d=DK))


def stage_nsa_cmp(k):
    nc = k.nc
    k.o = k.region("nsa_o", [P, 8, S], F32, 42.5)
    p = k.region("cmp_p", [P, 2, NSA_HEADS, 32], F32, 58.5)
    pt = k.region("cmp_pt", [P, 2, 4, P], F32, 62.5)
    top = k.small[:, 8:24]
    total = k.small[:, 24:40]
    weight = k.small[:, 40:56]
    s = {n: k.sem(f"cmp_{n}") for n in (
          "sc_mm", "p_ready", "exp_done", "tr_mm", "tr_read", "pv_mm", "o_done",
          "scaled", "step")}
    with nc.Block() as block:
        @block.tensor
        def _(pe):
            def scores(i):
                if i >= 2:
                    pe.wait_ge(s["p_ready"], i - 1)
                bank = k.ps[:, i % 2, :].rearrange("p (b h c) -> p b h c", b=2, c=32)[:, :, :, 0:N_CMP]
                mask = k.cmp_bf[:, 32 * i:32 * i + N_CMP].rearrange("p (o c) -> p o c", o=1).to_broadcast([P, 16, N_CMP])
                pe.matmul(k.ps[:, i % 2, :].rearrange("p (h c) -> p h c", c=32)[:, :, 0:N_CMP], k.ident_bf[:], mask,
                          start=True, stop=False)
                for a in range(8):
                    last = pe.matmul(bank[:, :, a, :], k.q[:, a, i * P:(i + 1) * P], k.kcmp[:, a // 4, :, 0:N_CMP],
                                     start=False, stop=(a == 7))
                last.then_inc(s["sc_mm"], 1)

            scores(0)
            for i in range(TT):
                if i + 1 < TT:
                    scores(i + 1)
                pe.wait_ge(s["scaled"], i + 1)
                if i:
                    pe.wait_ge(s["tr_read"], i)
                for g in range(4):
                    at = 8 * (g % 2) + 4 * (g // 2)
                    last = pe.transpose(k.ps[:, 2, g * P:(g + 1) * P],
                                        p[:, i % 2, at:at + 4, :].rearrange("p h c -> p (h c)"), k.const("ident"))
                last.then_inc(s["tr_mm"], 1)
                pe.wait_ge(s["tr_read"], i + 1)
                if i:
                    pe.wait_ge(s["o_done"], i)
                for t in range(8):
                    pair = k.vcmp[:, t // 2, 2 * (t % 2):2 * (t % 2) + 2, :].rearrange("p h d -> p (h d)")
                    last = pe.matmul(k.ps[:, 4 + t // 4, t % 4 * P:(t % 4 + 1) * P], pair, pt[:, i % 2, t // 2, :],
                                     start=True, stop=True)
                last.then_inc(s["pv_mm"], 1)

        @block.scalar
        def _(act):
            def store(i):
                act.wait_ge(s["pv_mm"], i + 1)
                for x in range(2):
                    last = act.activation(k.o[:, 4 * x:4 * x + 4, i * P:(i + 1) * P],
                                          k.ps[:, 4 + x, :].rearrange("p (t c) -> p t c", c=P), ACT.Copy)
                last.then_inc(s["o_done"], 1)

            for i in range(TT):
                act.wait_ge(s["p_ready"], i + 1)
                x = p[:, i % 2, :, 0:N_CMP]
                act.activation(x, x, ACT.Exp, scale=DK ** -0.5).then_inc(s["exp_done"], 1)
                if i:
                    store(i - 1)
            store(TT - 1)

        @block.vector
        def _(dve):
            steps = Steps(s["step"])
            steps.then_wait(dve, dve.memset(p[:], 0.0))

            def subtract_top(i):
                dve.wait_ge(s["sc_mm"], i + 1)
                if i:
                    dve.wait_ge(s["p_ready"], i)
                sc = k.ps[:, i % 2, :].rearrange("p (b h c) -> p b h c", b=2, c=32)[:, :, :, 0:N_CMP]
                steps.then_wait(dve, dve.tensor_reduce(top.rearrange("p (b h) -> p b h", b=2), sc, AX, ALU.max))
                if i >= 2:
                    dve.wait_ge(s["tr_mm"], i - 1)
                dve.tensor_tensor(p[:, i % 2, :, 0:N_CMP].rearrange("p (b h) c -> p b h c", b=2), sc,
                                  top.rearrange("p (b h o) -> p b h o", b=2, o=1).to_broadcast([P, 2, 8, N_CMP]),
                                  ALU.subtract).then_inc(s["p_ready"], 1)

            subtract_top(0)
            for i in range(TT):
                if i + 1 < TT:
                    subtract_top(i + 1)
                dve.wait_ge(s["exp_done"], i + 1)
                steps.then_wait(dve, dve.tensor_reduce(total, p[:, i % 2, :, 0:N_CMP], AX, ALU.add))
                steps.then_wait(dve, dve.reciprocal(total, total))
                gates = k.gtok[:, i, :].rearrange("p (a b h c) -> p b a h c", a=2, b=2, c=3)[:, :, :, :, 0]
                v4 = "p (b a h) -> p b a h"
                steps.then_wait(dve, dve.tensor_tensor(weight.rearrange(v4, b=2, a=2), total.rearrange(v4, b=2, a=2),
                                                       gates, ALU.mult))
                if i == 0:
                    steps.then_wait(dve, dve.tensor_scalar(weight, weight, k.col("cmp_any"), None, ALU.mult))
                x = p[:, i % 2, :, 0:N_CMP]
                dve.tensor_tensor(x, x, weight.rearrange("p (h o) -> p h o", o=1).to_broadcast([P, 16, N_CMP]), ALU.mult) \
                    .then_inc(s["scaled"], 1)
                dve.wait_ge(s["tr_mm"], i + 1)
                dve.tensor_copy(pt[:, i % 2].rearrange("p g t -> p (g t)"), k.ps[:, 2, :]).then_inc(s["tr_read"], 1)


def stage_nsa_attention(k):
    nc = k.nc
    p = k.region("att_p", [P, 3, 2, S], F32, 0)
    pt = k.region("att_pt", [P, 2, 2, S], F32, 12)
    s = {n: k.sem(f"att_{n}") for n in (
          "sc_mm", "nm_done", "exp_done", "tr_mm", "pt0", "pt1", "pv_mm", "o_done",
          "step", "w_done", "scaled0", "scaled1")}
    units = [(br, g, i, pr) for br in range(2) for g in range(4) for pr in range(2) for i in (3, 2, 1, 0)]
    U = len(units)

    def length(n):
        return (units[n][2] + 1) * P

    def sm(base, n):
        return k.small[:, base + 2 * (n % 4):base + 2 * (n % 4) + 2]

    with nc.Block() as block:
        @block.tensor
        def _(pe):
            def scores(n):
                br, g, i, pr = units[n]
                L = length(n)
                if n >= 2:
                    pe.wait_ge(s["exp_done"], 2 * (n - 1))
                for e in range(2):
                    bank = 2 * (n % 2) + e
                    pe.matmul(k.ps[:, bank, 0:L], k.q_rot[:, g // 2 * 4 + 2 * pr + e, i * P:(i + 1) * P],
                              k.padded[br][:, 2 * (g % 2) + g // 2, 0:L], start=True, stop=False)
                    last = pe.matmul(k.ps[:, bank, i * P:L], k.ident_bf[:], k.causal_bf[:], start=False, stop=True)
                last.then_inc(s["sc_mm"], 1)

            scores(0)
            for n in range(U + 3):
                if n + 1 < U:
                    scores(n + 1)
                if 2 <= n < U + 2:
                    m = n - 2
                    i = units[m][2]
                    for e in range(2):
                        pe.wait_ge(s[f"scaled{e}"], m + 1)
                        if m:
                            pe.wait_ge(s[f"pt{e}"], m)
                        for j in range(i + 1):
                            last = pe.transpose(k.ps[:, 4 + e, j * P:(j + 1) * P], p[:, m % 3, e, j * P:(j + 1) * P],
                                                k.const("ident"))
                        last.then_inc(s["tr_mm"], 1)
                if n >= 3:
                    m = n - 3
                    br, g, i, pr = units[m]
                    if m >= 2:
                        pe.wait_ge(s["o_done"], m - 1)
                    for e in range(2):
                        pe.wait_ge(s[f"pt{e}"], m + 1)
                        for j in range(i + 1):
                            last = pe.matmul(k.ps[e * DK:(e + 1) * DK, 6 + m % 2, 0:P], k.vtok[:, br, j, g * DK:(g + 1) * DK],
                                             pt[:, m % 2, e, j * P:(j + 1) * P], start=(j == 0), stop=(j == i))
                    last.then_inc(s["pv_mm"], 1)

        @block.scalar
        def _(act):
            for n in range(U + 2):
                if n < U:
                    L = length(n)
                    act.wait_ge(s["nm_done"], n + 1)
                    if n >= 4:
                        act.wait_ge(s["w_done"], n - 3)
                    for e in range(2):
                        if n >= 3:
                            act.wait_ge(s["tr_mm"], 2 * (n - 3) + e + 1)
                        act.activation(p[:, n % 3, e, 0:L], k.ps[:, 2 * (n % 2) + e, 0:L], ACT.Exp,
                                       bias=sm(0, n)[:, e:e + 1], scale=DK ** -0.5,
                                       accum_out=sm(8, n)[:, e:e + 1]).then_inc(s["exp_done"], 1)
                if n >= 2:
                    m = n - 2
                    L = length(m)
                    act.wait_ge(s["tr_mm"], 2 * m + 2)
                    if m >= 2:
                        act.wait_ge(s["pv_mm"], m - 1)
                    act.activation(pt[:, m % 2, 1, 0:L], k.ps[:, 5, 0:L], ACT.Copy).then_inc(s["pt1"], 1)

        @block.gpsimd
        def _(pool):
            for n in range(U):
                L = length(n)
                pool.wait_ge(s["w_done"], n + 1)
                pool.tensor_scalar(p[:, n % 3, 0, 0:L], p[:, n % 3, 0, 0:L], sm(32, n)[:, 0:1], None, ALU.mult) \
                    .then_inc(s["scaled0"], 1)

        @block.vector
        def _(dve):
            steps = Steps(s["step"])
            for n in range(U + 4):
                if n < U:
                    L = length(n)
                    dve.wait_ge(s["sc_mm"], n + 1)
                    if n >= 4:
                        dve.wait_ge(s["exp_done"], 2 * (n - 3))
                    bank = 2 * (n % 2)
                    steps.then_wait(dve, dve.tensor_reduce(sm(16, n), k.ps[:, bank:bank + 2, 0:L], AX, ALU.max))
                    dve.tensor_scalar(sm(0, n), sm(16, n), -DK ** -0.5, None, ALU.mult).then_inc(s["nm_done"], 1)
                if n >= 4:
                    m = n - 4
                    br, g, i, pr = units[m]
                    dve.wait_ge(s["pv_mm"], m + 1)
                    if m >= 1:
                        dve.wait_ge(s["o_done"], m)
                    o = k.o[:, 2 * g + pr, i * P:(i + 1) * P]
                    dve.tensor_tensor(o, o, k.ps[:, 6 + m % 2, 0:P], ALU.add).then_inc(s["o_done"], 1)
                if 1 <= n <= U:
                    m = n - 1
                    br, g, i, pr = units[m]
                    h = 4 * g + 2 * pr
                    dve.wait_ge(s["exp_done"], 2 * m + 2)
                    steps.then_wait(dve, dve.reciprocal(sm(24, m), sm(8, m)))
                    if m >= 4:
                        dve.wait_ge(s["scaled0"], m - 3)
                        dve.wait_ge(s["scaled1"], m - 3)
                    gates = k.gtok[:, i, :].rearrange("p (h b) -> p h b", b=3)[:, h:h + 2, 1 + br]
                    dve.tensor_tensor(sm(32, m), sm(24, m), gates, ALU.mult).then_inc(s["w_done"], 1)
                    dve.wait_ge(s["w_done"], m + 1)
                    L = length(m)
                    dve.tensor_scalar(p[:, m % 3, 1, 0:L], p[:, m % 3, 1, 0:L], sm(32, m)[:, 1:2], None, ALU.mult) \
                        .then_inc(s["scaled1"], 1)
                if 2 <= n < U + 2:
                    m = n - 2
                    L = length(m)
                    dve.wait_ge(s["tr_mm"], 2 * m + 1)
                    if m >= 2:
                        dve.wait_ge(s["pv_mm"], m - 1)
                    dve.tensor_copy(pt[:, m % 2, 0, 0:L], k.ps[:, 4, 0:L]).then_inc(s["pt0"], 1)


def stage_nsa_gate(k):
    nc = k.nc
    z = k.region("nsag_z", [P, 4, S], F32, 58.5)
    y = k.region("nsag_y", [P, 2, S], F32, 66.5)
    zl = [k.sem(f"nsag_z{i}") for i in range(4)]
    y_done, y_hi, y_lo = k.sem("nsag_y_done"), k.sem("nsag_y_hi"), k.sem("nsag_y_lo")
    with nc.Block() as block:
        @block.sync
        def _(sp):
            for n in range(8):
                if n >= 4:
                    sp.wait_ge(y_done, n - 3)
                sp.dma_start(z[:, n % 4, :], k.io["z_scratch"][n]).then_inc(zl[n % 4], 16)

        @block.scalar
        def _(act):
            for n in range(8):
                act.wait_ge(y_done, n + 1)
                act.activation(k.act_hi[:, n, :], y[:, n % 2, :], ACT.Copy).then_inc(y_hi, 1)

        @block.vector
        def _(dve):
            for n in range(9):
                if n < 8:
                    dve.wait_ge(zl[n % 4], 16 * (n // 4 + 1))
                    if n >= 2:
                        dve.wait_ge(y_lo, n - 1)
                    dve.tensor_tensor(y[:, n % 2, :], k.o[:, n, :], z[:, n % 4, :], ALU.mult).then_inc(y_done, 1)
                if n >= 1:
                    dve.wait_ge(y_hi, n)
                    dve.tensor_tensor(k.act_lo[:, n - 1, :], y[:, (n - 1) % 2, :], k.act_hi[:, n - 1, :].bitcast(F32),
                                      ALU.subtract).then_inc(y_lo, 1)


GATE_T = 16
DA_T = 12
RW_ALL = 15


def stage_in_2(k, norm):
    nc = k.nc
    norm.scale_stage()
    b0 = first_block("in_2")
    b1 = first_block("mix_o")
    k.rw = k.region("rw", [P, RW_ALL, S], F32, 0)
    k.da = k.region("da", [P, DA_T, S], F32, 30)
    zt = k.region("in2_zt", [P, 4, S], F32, 54)
    u = k.region("in2_u", [P, 2, S + 2], F32, 62)
    t1 = k.region("in2_t1", [P, 2, S], F32, 67)
    k.keep = k.region("mu_keep", [P, RW_ALL], F32, 71)
    z_ready = k.sem("in2_z_ready")
    u_ready, pad, keep_done, step, rw_done = (k.sem("in2_u_ready"), k.sem("in2_pad"), k.sem("in2_keep"),
                                              k.sem("in2_step"), k.sem("in2_rw_done"))
    stored = [k.sem(f"in2_stored{i}") for i in range(4)]
    with nc.Block() as block:
        @block.sync
        def _(sp):
            load_blocks(k, sp, b1)

        @block.scalar
        def _(act):
            norm.scale_act(act)
            for t, (b, j) in enumerate(tiles_of(b0, b1)):
                if j == 0 and b + 1 < b1:
                    split_hi(k, act, b + 1)
                tile = TILE_AT[b] + j
                act.wait_ge(k.tile_done, tile + 1)
                bank = k.ps[:, tile % 4, :]
                if t < GATE_T:
                    if t >= 4:
                        act.wait_ge(stored[t % 4], 16 * (t // 4))
                    act.activation(zt[:, t % 4, :], bank, ACT.Sigmoid).then_inc(z_ready, 1)
                    act.wait_ge(z_ready, t + 1)
                    act.sem_inc(k.evac_done, 1)
                    act.dma_start(k.io["z_scratch"][t], zt[:, t % 4, :]).then_inc(stored[t % 4], 16)
                elif t < GATE_T + DA_T:
                    act.activation(k.da[:, t - GATE_T, :], bank, ACT.Copy).then_inc(k.evac_done, 1)
                else:
                    m = t - GATE_T - DA_T
                    if m == 0:
                        act.wait_ge(pad, 2)
                    if m >= 2:
                        act.wait_ge(rw_done, m - 1)
                    act.activation(u[:, m % 2, 1:1 + S], bank, ACT.Copy).then_inc(u_ready, 1)
                    act.wait_ge(u_ready, m + 1)
                    act.sem_inc(k.evac_done, 1)
            for i in range(4):
                act.wait_ge(stored[i], 16 * GATE_T // 4)

        @block.tensor
        def _(pe):
            for t, (b, j) in enumerate(tiles_of(b0, b1)):
                multiply_tile(k, pe, b, j, norm.fed if t == 0 else None)

        @block.vector
        def _(dve):
            steps = Steps(step)
            dve.memset(u[:, :, 0:1], 0.0).then_inc(pad, 1)
            dve.memset(u[:, :, S + 1:S + 2], 0.0).then_inc(pad, 1)
            mp, mn = COLS["mu_prev"], COLS["mu_next"]
            steps.then_wait(dve, dve.tensor_tensor(k.keep[:], k.cols[:, mp:mp + RW_ALL], k.cols[:, mn:mn + RW_ALL],
                                                   ALU.add))
            steps.then_wait(dve, dve.tensor_scalar(k.keep[:], k.keep[:], -1.0, 1.0, ALU.mult, ALU.add))
            norm.scale_dve(dve)
            for t, (b, j) in enumerate(tiles_of(b0, b1)):
                if j == 0 and b + 1 < b1:
                    split_lo(k, dve, b + 1)
                m = t - GATE_T - DA_T
                if m >= 0:
                    x = u[:, m % 2]
                    dve.wait_ge(u_ready, m + 1)
                    steps.then_wait(dve, dve.tensor_scalar(t1[:, 0], x[:, 1:1 + S], k.keep[:, m:m + 1], None, ALU.mult))
                    steps.then_wait(dve, dve.scalar_tensor_tensor(out=t1[:, 1], in0=x[:, 0:S], scalar=k.col("mu_prev", m),
                                                                  in1=t1[:, 0], op0=ALU.mult, op1=ALU.add))
                    dve.scalar_tensor_tensor(out=k.rw[:, m, :], in0=x[:, 2:2 + S], scalar=k.col("mu_next", m),
                                             in1=t1[:, 1], op0=ALU.mult, op1=ALU.add).then_inc(rw_done, 1)
                    dve.wait_ge(rw_done, m + 1)


def stage_da_prep(k):
    nc = k.nc
    k.da_v = k.region("da_v", [P, TT, S], F32, 54)
    k.da_k = k.at("da_k", [P, DA_HEADS, 2, S], F32, 60)
    turned = k.region("da_turned", [P, 2, S], F32, 74)
    straight = k.region("da_straight", [P, 2, S], F32, 78)
    prod = k.region("da_prod", [P, 8], F32, 72)
    k.neg_lam = k.small[:, 255:256]
    s = {n: k.sem(f"dap_{n}") for n in (
          "rot_mm", "rot_read", "straight", "done", "tr", "tr_read", "prod",
          "lam_mm", "exp", "zeroed", "step")}
    with nc.Block() as block:
        @block.tensor
        def _(pe):
            for n in range(8):
                if n >= 2:
                    pe.wait_ge(s["rot_read"], n - 1)
                pe.matmul(k.ps[:, 4 + n % 2, :], k.const("rot"), k.da[:, n, :], start=True, stop=True) \
                    .then_inc(s["rot_mm"], 1)
            for n in range(4):
                if n >= 2:
                    pe.wait_ge(s["tr_read"], n - 1)
                for i in range(TT):
                    last = pe.transpose(k.ps[:, n % 2, i * P:(i + 1) * P], k.da[:, 8 + n, i * P:(i + 1) * P],
                                        k.const("ident"))
                last.then_inc(s["tr"], 1)
            pe.wait_ge(s["prod"], 2)
            pe.matmul(k.ps[:, 7, 0:2], k.const("ones")[0:64, :], prod[0:64, 0:2], start=True, stop=True) \
                .then_inc(s["lam_mm"], 1)

        @block.scalar
        def _(act):
            act.wait_ge(s["lam_mm"], 1)
            act.activation(prod[:, 2:4], k.ps[:, 7, 0:2], ACT.Exp).then_inc(s["exp"], 1)

        @block.gpsimd
        def _(pool):
            for c in range(2):
                pool.memset(k.da_k[64 * c:64 * c + 64, :, 1 - c, :], 0.0).then_inc(s["zeroed"], 1)
                pool.wait_ge(s["zeroed"], c + 1)
            for n in range(8):
                if n >= 2:
                    pool.wait_ge(s["done"], n - 1)
                pool.tensor_tensor(straight[:, n % 2, :], k.da[:, n, :], k.const("cos", S), ALU.mult) \
                    .then_inc(s["straight"], 1)

        @block.vector
        def _(dve):
            steps = Steps(s["step"])
            low = slice(0, 64)
            dve.tensor_tensor(prod[low, 0:1], k.col("lq1", rows=low), k.col("lk1", rows=low), ALU.mult) \
                .then_inc(s["prod"], 1)
            dve.tensor_tensor(prod[low, 1:2], k.col("lq2", rows=low), k.col("lk2", rows=low), ALU.mult) \
                .then_inc(s["prod"], 1)
            for n in range(8):
                dve.wait_ge(s["rot_mm"], n + 1)
                if n >= 2:
                    dve.wait_ge(s["done"], n - 1)
                dve.tensor_tensor(turned[:, n % 2, :], k.ps[:, 4 + n % 2, :], k.const("sin", S), ALU.mult) \
                    .then_inc(s["rot_read"], 1)
                dve.wait_ge(s["rot_read"], n + 1)
                dve.wait_ge(s["straight"], n + 1)
                if n < DA_HEADS:
                    last = dve.tensor_tensor(k.da[:, n, :], turned[:, n % 2, :], straight[:, n % 2, :], ALU.add)
                else:
                    for c in range(2):
                        rows = slice(64 * c, 64 * c + 64)
                        last = dve.tensor_tensor(k.da_k[rows, n - DA_HEADS, c, :], turned[rows, n % 2, :],
                                                 straight[rows, n % 2, :], ALU.add)
                last.then_inc(s["done"], 1)
            for n in range(4):
                dve.wait_ge(s["tr"], n + 1)
                dve.tensor_copy(k.da_v[:, :, n * P:(n + 1) * P], k.ps[:, n % 2, :].rearrange("p (t c) -> p t c", c=P)) \
                    .then_inc(s["tr_read"], 1)
            dve.wait_ge(s["exp"], 1)
            steps.then_wait(dve, dve.tensor_tensor(prod[:, 4:5], prod[:, 3:4], prod[:, 2:3], ALU.subtract))
            dve.tensor_scalar(k.neg_lam, prod[:, 4:5], -LAMBDA_INIT, None, ALU.add)


def stage_da_attention(k):
    nc = k.nc
    k.da_o = k.region("da_o", [P, TT, S], F32, 62)
    p = k.region("da_p", [P, 3, 2, S], F32, 74)
    pt = k.region("da_pt", [P, 2, S], F32, 86)
    junk = k.region("da_junk", [P, 2, P], F32, 71.25)
    s = {n: k.sem(f"daa_{n}") for n in (
          "sc_mm", "nm_done", "exp_done", "pd_done", "tr_mm", "pt", "pv_mm",
          "o_done", "sq_done", "step", "rw_landed", "root", "y_tr", "y_hi",
          "y_done", "y_lo", "normed")}
    units = [(h, i) for h in range(DA_HEADS) for i in range(TT)]
    U = len(units)
    sumsq = k.small[:, 64:64 + U]
    y = k.at("da_y", [P, 2, S], F32, 76)
    k.lora = k.at("rw_lora", [P, 4, S], F32, 28)
    k.gate_lora = k.at("rw_gate_lora", [P, S], F32, 96)
    k.rwc = k.at("rw_consts", [P, N_RW_CONSTS], F32, 44)

    def sm(base, n):
        return k.small[:, base + 2 * (n % 4):base + 2 * (n % 4) + 2]

    with nc.Block() as block:
        @block.sync
        def _(sp):
            sp.dma_start(k.lora[:], k.io["lora"][:, 0:4]).then_inc(s["rw_landed"], 16)
            sp.dma_start(k.gate_lora[:], k.io["lora"][:, 4]).then_inc(s["rw_landed"], 16)
            sp.dma_start(k.rwc[:], k.io["rw_consts"]).then_inc(s["rw_landed"], 16)
            sp.wait_ge(s["rw_landed"], 48)

        @block.tensor
        def _(pe):
            def scores(n):
                h, i = units[n]
                if n >= 2:
                    pe.wait_ge(s["exp_done"], 2 * (n - 1))
                for c in range(2):
                    last = pe.matmul(k.ps[:, 2 * (n % 2) + c, :], k.da[:, h, i * P:(i + 1) * P], k.da_k[:, h, c, :],
                                     start=True, stop=True)
                last.then_inc(s["sc_mm"], 1)

            scores(0)
            for n in range(U + 3):
                if n + 1 < U:
                    scores(n + 1)
                if 2 <= n < U + 2:
                    m = n - 2
                    pe.wait_ge(s["pd_done"], m + 1)
                    if m >= 2:
                        pe.wait_ge(s["pt"], m - 1)
                    for j in range(TT):
                        last = pe.transpose(k.ps[:, 4 + m % 2, j * P:(j + 1) * P], p[:, m % 3, 0, j * P:(j + 1) * P],
                                            k.const("ident"))
                    last.then_inc(s["tr_mm"], 1)
                if n >= 3:
                    m = n - 3
                    h, i = units[m]
                    pe.wait_ge(s["pt"], m + 1)
                    if m >= 2:
                        pe.wait_ge(s["o_done"], m - 1)
                    for j in range(TT):
                        last = pe.matmul(k.ps[:, 6 + m % 2, 0:P], pt[:, m % 2, j * P:(j + 1) * P],
                                         k.da_v[:, j, h * P:(h + 1) * P], start=(j == 0), stop=(j == TT - 1))
                    last.then_inc(s["pv_mm"], 1)
            for h in range(DA_HEADS):
                pe.wait_ge(s["normed"], TT)
                if h >= 2:
                    pe.wait_ge(s["y_done"], h - 1)
                for i in range(TT):
                    last = pe.transpose(k.ps[:, h % 2, i * P:(i + 1) * P], k.da_o[:, i, h * P:(h + 1) * P],
                                        k.const("ident"))
                last.then_inc(s["y_tr"], 1)

        @block.scalar
        def _(act):
            for n in range(U + 4):
                if n < U:
                    act.wait_ge(s["nm_done"], n + 1)
                    if n >= 3:
                        act.wait_ge(s["tr_mm"], n - 2)
                    for c in range(2):
                        act.activation(p[:, n % 3, c, :], k.ps[:, 2 * (n % 2) + c, :], ACT.Exp, bias=sm(0, n)[:, c:c + 1],
                                       scale=DK ** -0.5, accum_out=sm(8, n)[:, c:c + 1]).then_inc(s["exp_done"], 1)
                if n >= 4:
                    m = n - 4
                    h, i = units[m]
                    act.wait_ge(s["o_done"], m + 1)
                    if m >= 2:
                        act.wait_ge(s["sq_done"], m - 1)
                    act.activation(junk[:, m % 2, :], k.da_o[:, i, h * P:(h + 1) * P], ACT.Square,
                                   accum_out=sumsq[:, 4 * i + h:4 * i + h + 1]).then_inc(s["sq_done"], 1)
            act.wait_ge(s["sq_done"], U)
            act.activation(sumsq, sumsq, ACT.Sqrt, scale=1.0 / P, bias=k.col("eps5")).then_inc(s["root"], 1)
            for h in range(DA_HEADS):
                act.wait_ge(s["y_done"], h + 1)
                act.activation(k.act_hi[:, 4 + h, :], y[:, h % 2, :], ACT.Copy).then_inc(s["y_hi"], 1)
            act.activation(k.rw[:, 12, :], k.rw[:, 12, :], ACT.Tanh)
            act.activation(k.rw[:, 14, :], k.rw[:, 14, :], ACT.Sigmoid)

        @block.vector
        def _(dve):
            steps = Steps(s["step"])
            for n in range(U + 4):
                if n < U:
                    bank = 2 * (n % 2)
                    dve.wait_ge(s["sc_mm"], n + 1)
                    if n >= 4:
                        dve.wait_ge(s["exp_done"], 2 * (n - 3))
                    steps.then_wait(dve, dve.tensor_reduce(sm(16, n), k.ps[:, bank:bank + 2, :], AX, ALU.max))
                    dve.tensor_scalar(sm(0, n), sm(16, n), -DK ** -0.5, None, ALU.mult).then_inc(s["nm_done"], 1)
                if n >= 4:
                    m = n - 4
                    h, i = units[m]
                    dve.wait_ge(s["pv_mm"], m + 1)
                    dve.tensor_copy(k.da_o[:, i, h * P:(h + 1) * P], k.ps[:, 6 + m % 2, 0:P]).then_inc(s["o_done"], 1)
                if 1 <= n <= U:
                    m = n - 1
                    dve.wait_ge(s["exp_done"], 2 * m + 2)
                    x, w = p[:, m % 3], sm(24, m)
                    steps.then_wait(dve, dve.reciprocal(w, sm(8, m)))
                    dve.tensor_scalar(w[:, 1:2], w[:, 1:2], k.neg_lam, None, ALU.mult)
                    steps.then_wait(dve, dve.tensor_scalar(x[:, 0, :], x[:, 0, :], w[:, 0:1], None, ALU.mult))
                    dve.scalar_tensor_tensor(out=x[:, 0, :], in0=x[:, 1, :], scalar=w[:, 1:2], in1=x[:, 0, :],
                                             op0=ALU.mult, op1=ALU.add).then_inc(s["pd_done"], 1)
                if 2 <= n < U + 2:
                    m = n - 2
                    dve.wait_ge(s["tr_mm"], m + 1)
                    if m >= 2:
                        dve.wait_ge(s["pv_mm"], m - 1)
                    dve.tensor_copy(pt[:, m % 2, :], k.ps[:, 4 + m % 2, :]).then_inc(s["pt"], 1)
            dve.wait_ge(s["root"], 1)
            steps.then_wait(dve, dve.reciprocal(sumsq, sumsq))
            dve.wait_ge(s["o_done"], U)
            for i in range(TT):
                o = k.da_o[:, i, :].rearrange("p (h d) -> p h d", d=P)
                dve.tensor_tensor(o, o, sumsq[:, 4 * i:4 * i + 4].rearrange("p (h o) -> p h o", o=1).to_broadcast([P, 4, P]),
                                  ALU.mult).then_inc(s["normed"], 1)
            for h in range(DA_HEADS):
                dve.wait_ge(s["y_tr"], h + 1)
                if h >= 2:
                    dve.wait_ge(s["y_lo"], h - 1)
                dve.tensor_scalar(y[:, h % 2, :], k.ps[:, h % 2, :], k.col("subln"), 1.0 - LAMBDA_INIT, ALU.mult,
                                  ALU.mult).then_inc(s["y_done"], 1)
                dve.wait_ge(s["y_hi"], h + 1)
                dve.tensor_tensor(k.act_lo[:, 4 + h, :], y[:, h % 2, :], k.act_hi[:, 4 + h, :].bitcast(F32),
                                  ALU.subtract).then_inc(s["y_lo"], 1)


def halves():
    return [(d, hd, it, par) for d in range(2) for hd in range(2) for it in range(TT) for par in range(2)]


def rows_half(x):
    return slice(64 * x, 64 * x + 64)


def chunk2(a):
    return slice(P * a, P * a + P)


def stage_rw_heads(k, c):
    nc = k.nc
    tag = f"rw{c}"
    ar = k.at(f"{tag}_ar", [P, 2, 2, S], F32, 60)
    bt = k.at(f"{tag}_bt", [P, 2, S], F32, 68)
    kt = k.at(f"{tag}_kt", [P, 2, S], F32, 72)
    bh = k.at(f"{tag}_bh", [P, 2, S], F32, 76)
    kh = k.at(f"{tag}_kh", [P, 2, S], F32, 80)
    T = k.at(f"{tag}_T", [P, 16, P], F32, 68)
    off = [k.region(f"{tag}_off0", [P, 16, P], F32, 54), k.at(f"{tag}_off1", [P, 16, P], F32, 76)]
    Tt = k.region(f"{tag}_Tt", [P, 16, P], F32, 62)
    Z = k.at(f"{tag}_Z", [P, 16, P], F32, 98)
    tok = k.at(f"{tag}_tok", [P, 2, 2, TT, P], F32, 84)
    vtok = k.at(f"{tag}_vtok", [P, TT, P], F32, 92)
    wu = k.at(f"{tag}_wu", [P, 16, P], F32, 98)
    rhs = k.at(f"{tag}_rhs", [P, 16, P], F32, 106)
    bb = k.at(f"{tag}_b", [P, 2, S], F32, 98)
    kd = k.at(f"{tag}_kd", [P, 2, S], F32, 102)
    kkn = k.at(f"{tag}_kkn", [P, S], F32, 94)
    sq = k.at(f"{tag}_sq", [P, S], F32, 108)
    mt = k.at(f"{tag}_mt", [P, 2, N_CHUNK, CHUNK], F32, 110)
    tmp = k.at(f"{tag}_tmp", [P, 2, S], F32, 110)
    pend = k.at(f"{tag}_pend", [P, 2, N_CHUNK], F32, 114)
    sc = k.region(f"{tag}_sc", [P, 16, 4, CHUNK], F32, 30)
    ex = k.region(f"{tag}_ex", [P, 2, 4, S], F32, 30)
    add = k.region(f"{tag}_add", [P, 2, N_CHUNK, CHUNK], F32, 46)
    state = k.region(f"{tag}_state", [P, 2, N_CHUNK, CHUNK], F32, 50)
    sig = k.region(f"{tag}_sig", [P, 2, S], F32, 54)
    X = k.region(f"{tag}_X", [P, 2, S], F32, 58)
    E1 = k.region(f"{tag}_E1", [P, 2, S], F32, 62)
    E2 = k.region(f"{tag}_E2", [P, 2, S], F32, 66)
    rate = k.region(f"{tag}_rate", [P, 2, S], F32, 70)
    ss = {n: k.sem(f"{tag[0:2]}{c}_{n}") for n in
          (
          "pre", "sigs", "kk", "sqd", "ss", "root", "sums", "exps", "kd", "bonp",
          "bonm", "feat", "pool_feat", "tr", "tok", "scm", "sc", "off", "zero",
          "off0", "off0_pool", "z", "zc", "tz", "t", "akvm", "akv", "wum", "wu_a",
          "wu_d", "rm", "rhat", "pcd", "mm", "mt", "nm", "add", "stm", "st", "yb",
          "ybc", "ya", "step", "st0")}
    if c == 0:
        k.ytok = k.region("rw_ytok", [P, TT, S], F32, 74)
        k.bonus = k.region("rw_bonus", [P, RW_T, S], F32, 82)
    r, kf, v = k.rw[:, c, :], k.rw[:, 4 + c, :], k.rw[:, 8 + c, :]

    def rc(name, n, at=0):
        a = RW_CONSTS[name] + at
        return k.rwc[:, a:a + n]

    def off_blocks(eng, lv, d, par):
        h, u = rows_half(par), slice(8 * d, 8 * d + 8)
        mask = rc(f"level{d}", 64, 64 * lv)[h].rearrange("p (o n) -> p o n", o=1).to_broadcast([64, 8, CHUNK])
        return eng.tensor_tensor(off[lv % 2][h, u, chunk(par)], sc[h, u, 0, :], mask, ALU.mult)

    eye = k.const("ident").rearrange("p (o n) -> p o n", o=1).to_broadcast([P, 4, P])

    def pair(op, part):
        return k.ps[:, 2 * (op % 4) + part, :]

    def four(x, d, part):
        return x[:, 8 * d + 4 * part:8 * d + 4 * part + 4, :]

    final = LEVELS - 1
    ops = []
    for lv in range(1, LEVELS):
        for d in range(2):
            ops += [("Z", lv, d)] + ([("Tt", lv - 1, d)] if lv > 1 else [])
        ops += [("T" if lv < final else "Tt", lv, d) for d in range(2)]
    made = {("Tt", 0, 0): 1, ("Tt", 0, 1): 2, ("T", 0, 0): 3, ("T", 0, 1): 4}
    for x in ops:
        if x[0] == "Z":
            made[x] = 2 * (x[1] - 1) + x[2] + 1
        else:
            made[x] = 5 + sum(y in made and y[0] != "Z" for y in ops)
    all_made = made["Tt", final, 1]

    def chunk(t):
        return slice(t * CHUNK, (t + 1) * CHUNK)

    with nc.Block() as block:
        @block.tensor
        def _(pe):
            pe.wait_ge(ss["sqd"], 1)
            pe.matmul(k.ps[:, 4, :], k.const("block_ones"), sq[:], start=True, stop=True).then_inc(ss["ss"], 1)
            for m, rows in ((0, 12), (1, 13)):
                for d in range(2):
                    pe.matmul(k.ps[:, 2 * m + d, :], k.lora[:, 2 * m + d, c * P:(c + 1) * P], k.rw[:, rows, :],
                              start=True, stop=True).then_inc(ss["pre"], 1)
            pe.wait_ge(ss["bonp"], 1)
            pe.matmul(k.ps[:, 5, :], k.const("block_ones"), tmp[:, 0, :], start=True, stop=True).then_inc(ss["bonm"], 1)
            for n in range(4):
                d, q = n // 2, n % 2
                if q == 0:
                    pe.wait_ge(ss["feat"], 3 * (d + 1))
                    pe.wait_ge(ss["pool_feat"], 3 * (d + 1))
                if n >= 2:
                    pe.wait_ge(ss["sc"], 2 * (n - 1))
                for it in (2 * q, 2 * q + 1):
                    for par in range(2):
                        t = chunk(2 * it + par)
                        for m, lhs in ((0, bt), (1, kt)):
                            for hd in range(2):
                                o = 256 * (it % 2) + 128 * m
                                last = pe.matmul(k.ps[rows_half(par), 2 * (n % 2) + hd, o:o + 128]
                                                 .rearrange("p (x t) -> p x t", x=2),
                                                 lhs[rows_half(hd), d, t], ar[rows_half(hd), d, :, t],
                                                 start=True, stop=True)
                last.then_inc(ss["scm"], 1)
            jobs = [v] + [x for d in range(2) for x in (ar[:, d, 0, :], bh[:, d, :], kh[:, d, :])]
            for n, src in enumerate(jobs):
                if n >= 2:
                    pe.wait_ge(ss["tok"], n - 1)
                for i in range(TT):
                    last = pe.transpose(k.ps[:, 6 + n % 2, i * P:(i + 1) * P], src[:, i * P:(i + 1) * P], k.const("ident"))
                last.then_inc(ss["tr"], 1)
            pe.wait_ge(ss["tok"], 7)
            pe.wait_ge(ss["zero"], 2)
            for u in range(16):
                if u % 8 == 0:
                    pe.wait_ge((ss["off0_pool"], ss["off0"])[u // 8], 2)
                last = pe.transpose(k.ps[:, 4 + u // 4, chunk2(u % 4)], off[0][:, u, :], k.const("ident"))
            last.then_inc(ss["z"], 1)
            pe.wait_ge(ss["sc"], 8)
            for d, hd, it, par in halves():
                u, h = 8 * d + 4 * hd + it, rows_half(par)
                last = pe.matmul(k.ps[h, d, chunk(u % 8)], sc[h, u, 2, :], vtok[h, it, chunk(hd)], start=True, stop=True)
            last.then_inc(ss["akvm"], 1)
            pe.wait_ge(ss["akv"], 2)
            for op, (name, lv, d) in enumerate(ops):
                if name == "Z":
                    pe.wait_ge(ss["zero"], 4)
                    pe.wait_ge(ss["off"], 4 * (lv - 1) + 2 * d + 2)
                    pe.wait_ge(ss["t"], made["T", lv - 1, d])
                elif name == "T" or lv == final:
                    pe.wait_ge(ss["zc"], made["Z", lv, d])
                    pe.wait_ge(ss["t"], made["Tt", lv - 1, d])
                if op < 4:
                    pe.wait_ge(ss["t"], 4)
                else:
                    pe.wait_ge(ss["zc" if ops[op - 4][0] == "Z" else "t"], made[ops[op - 4]])
                for u in range(8 * d, 8 * d + 8):
                    out = pair(op, u // 4 % 2)[:, chunk2(u % 4)]
                    if name == "Tt" and lv < final:
                        done = pe.transpose(out, T[:, u, :], k.const("ident"))
                    else:
                        lhs, x = {"Z": (off[lv % 2], T), "T": (Tt, Z), "Tt": (Z, Tt)}[name]
                        done = pe.matmul(out, lhs[:, u, :], x[:, u, :], start=True, stop=True)
                done.then_inc(ss["z"] if name == "Z" else ss["tz"], 1)
            pe.wait_ge(ss["t"], all_made)
            for u in range(16):
                last = pe.matmul(k.ps[:, u // 4, chunk2(u % 4)], Tt[:, u, :], rhs[:, u, :], start=True, stop=True)
                if u % 4 == 3:
                    last.then_inc(ss["wum"], 1)
            pe.wait_ge(ss["wu_a"], 2)
            pe.wait_ge(ss["wu_d"], 2)
            places = [(d, hd, it, 8 * d + 4 * hd + it) for d in range(2) for hd in range(2) for it in range(TT)]
            for d, hd, it, u in places:
                for par in range(2):
                    h = rows_half(par)
                    last = pe.matmul(k.ps[rows_half(hd), 4 + par, chunk(4 * d + it)], wu[h, u, 0:64], sc[h, u, 1, :],
                                     start=True, stop=True)
            last.then_inc(ss["rm"], 1)
            for d, hd, it, u in places:
                for par in range(2):
                    h = rows_half(par)
                    last = pe.matmul(k.ps[rows_half(hd), 6 + par, chunk(4 * d + it)], wu[h, u, 0:64],
                                     tok[h, d, 0, it, chunk(hd)], start=True, stop=True)
            last.then_inc(ss["mm"], 1)
            for d, hd, it, u in places:
                for x in range(2):
                    for par in range(2):
                        h = rows_half(par)
                        lhs, y = ((tok[h, d, 1, it, chunk(hd)], vtok[h, it, chunk(hd)]),
                                  (tok[h, d, 0, it, chunk(hd)], wu[h, u, 64:128]))[x]
                        last = pe.matmul(k.ps[rows_half(hd), par, chunk(4 * d + it)], lhs, y, start=(x == 0), stop=(x == 1))
            last.then_inc(ss["nm"], 1)
            pe.wait_ge(ss["mt"], 2)
            for hd in range(2):
                for it in range(TT):
                    for d in range(2):
                        u = 8 * d + 4 * hd + it
                        for x in range(2):
                            for par in range(2):
                                h = rows_half(par)
                                lhs, y = ((sc[h, u, 1, :], wu[h, u, 64:128]), (sc[h, u, 3, :], vtok[h, it, chunk(hd)]))[x]
                                last = pe.matmul(k.ps[h, 6, chunk(4 * hd + it)], lhs, y, start=(d == x == 0),
                                                 stop=(d == x == 1))
            last.then_inc(ss["yb"], 1)
            for n in range(1, N_CHUNK - 1):
                pe.wait_ge(ss["st"], n)
                for d in range(2):
                    ch = n if d == 0 else N_CHUNK - 1 - n
                    for hd in range(2):
                        h = rows_half(hd)
                        last = pe.matmul(k.ps[h, 2 + d, chunk(n)], mt[h, d, ch, :], state[h, d, ch, :], start=True, stop=True)
                last.then_inc(ss["stm"], 1)
            pe.wait_ge(ss["st"], N_CHUNK - 1)
            pe.wait_ge(ss["rhat"], 2)
            for it in range(TT):
                for par in range(2):
                    t = 2 * it + par
                    for d in range(2):
                        for hd in range(2):
                            h = rows_half(hd)
                            last = pe.matmul(k.ps[rows_half(par), 4 + hd, chunk(it)], ar[h, d, 1, chunk(t)],
                                             state[h, d, t, :], start=(d == 0), stop=(d == 1))
            last.then_inc(ss["ya"], 1)

        @block.scalar
        def _(act):
            act.wait_ge(ss["kk"], 1)
            act.activation(sq[:], kkn[:], ACT.Square).then_inc(ss["sqd"], 1)
            act.wait_ge(ss["ss"], 1)
            act.activation(sq[:], k.ps[:, 4, :], ACT.Sqrt).then_inc(ss["root"], 1)
            for m, out, bias in ((0, sig, "w0"), (1, rate, "a0")):
                for d in range(2):
                    act.wait_ge(ss["pre"], 2 * m + d + 1)
                    act.activation(out[:, d, :], k.ps[:, 2 * m + d, :], ACT.Sigmoid, bias=k.col(bias, 4 * d + c)) \
                        .then_inc(ss["sigs"], 1)
            act.wait_ge(ss["sums"], 1)
            for d in range(2):
                incl, excl, rest = X, (E1, E2)[d], (E2, E1)[d]
                for n, (src, sign) in enumerate(((incl, -1.0), (excl, -1.0), (incl, 1.0), (rest, -1.0))):
                    act.activation(ex[:, d, n, :], src[:, d, :], ACT.Exp, scale=sign * DECAY_SCALE) \
                        .then_inc(ss["exps"], 1)
            for n in range(7):
                act.wait_ge(ss["tr"], n + 1)
                bank = k.ps[:, 6 + n % 2, :].rearrange("p (t c) -> p t c", c=P)
                if n in (1, 4):
                    u = 8 * (n // 4)
                    out = rhs[:, u:u + 8, 0:64].rearrange("p (h t) c -> p t h c", h=2)
                    bank = bank.rearrange("p t (h c) -> p t h c", h=2)
                else:
                    out = vtok[:] if n == 0 else tok[:, (n - 1) // 3, (n - 1) % 3 - 1]
                act.activation(out, bank, ACT.Copy).then_inc(ss["tok"], 1)
            act.wait_ge(ss["akvm"], 1)
            for d in range(2):
                act.activation(rhs[:, 8 * d:8 * d + 8, 64:128], k.ps[:, d, :].rearrange("p (u t) -> p u t", t=CHUNK),
                               ACT.Copy).then_inc(ss["akv"], 1)
            for op, (name, lv, d) in enumerate(ops):
                if name == "Z":
                    act.wait_ge(ss["z"], made[name, lv, d] + 1)
                    for part in range(2):
                        copied = act.activation(four(Z, d, part).rearrange("p u t -> p (u t)"), pair(op, part), ACT.Copy)
                    copied.then_inc(ss["zc"], 1)
            for g in (0, 2):
                act.wait_ge(ss["wum"], g + 1)
                act.activation(wu[:, 4 * g:4 * g + 4, :].rearrange("p u t -> p (u t)"), k.ps[:, g, :], ACT.Copy) \
                    .then_inc(ss["wu_a"], 1)
            act.wait_ge(ss["nm"], 1)
            for par in range(2):
                act.activation(add[:].rearrange("p d (i a) t -> p d i a t", a=2)[:, :, :, par, :],
                               k.ps[:, par, :].rearrange("p (d i t) -> p d i t", d=2, t=CHUNK), ACT.Copy) \
                    .then_inc(ss["add"], 1)
            act.wait_ge(ss["yb"], 1)
            for hd in range(2):
                act.activation(k.ytok[:, :, c * P + 64 * hd:c * P + 64 * hd + 64],
                               k.ps[:, 6, 256 * hd:256 * hd + 256].rearrange("p (i t) -> p i t", t=CHUNK), ACT.Copy) \
                    .then_inc(ss["ybc"], 1)

        @block.gpsimd
        def _(pool):
            pool.wait_ge(ss["exps"], 8)
            pool.wait_ge(ss["kd"], 2)
            for d in range(2):
                pool.tensor_tensor(ar[:, d, 1, :], r, ex[:, d, 0, :], ALU.mult).then_inc(ss["pool_feat"], 1)
                pool.tensor_tensor(kt[:, d, :], kd[:, d, :], ex[:, d, 2, :], ALU.mult).then_inc(ss["pool_feat"], 1)
                pool.tensor_tensor(kh[:, d, :], kd[:, d, :], ex[:, d, 3, :], ALU.mult).then_inc(ss["pool_feat"], 1)
            pool.wait_ge(ss["sc"], 4)
            for par in range(2):
                off_blocks(pool, 0, 0, par).then_inc(ss["off0_pool"], 1)
            pool.wait_ge(ss["tok"], 7)
            for lv in range(1, LEVELS):
                if lv >= 2:
                    pool.wait_ge(ss["z"], 1 + 2 * (lv - 2))
                if lv == 2:
                    pool.wait_ge(ss["t"], 4)
                if lv == 1:
                    pool.wait_ge(ss["sc"], 8)
                for d in range(2):
                    for par in range(2):
                        off_blocks(pool, lv, d, par).then_inc(ss["off"], 1)
            pool.wait_ge(ss["wum"], 4)
            pool.tensor_tensor(mt[:], rc("eye64", 64).rearrange("p (a b n) -> p a b n", a=1, b=1)
                               .to_broadcast([P, 2, N_CHUNK, CHUNK]),
                               pend[:].rearrange("p d (n o) -> p d n o", o=1).to_broadcast([P, 2, N_CHUNK, CHUNK]),
                               ALU.mult).then_inc(ss["pcd"], 1)

        @block.vector
        def _(dve):
            steps = Steps(ss["step"])

            def wait(ins):
                steps.then_wait(dve, ins)

            dve.tensor_scalar(kkn[:], kf, k.col("k_k", c), None, ALU.mult).then_inc(ss["kk"], 1)
            dve.wait_ge(ss["root"], 1)
            wait(dve.tensor_scalar(sq[:], sq[:], 1e-12, None, ALU.max))
            wait(dve.reciprocal(sq[:], sq[:]))
            wait(dve.tensor_tensor(kkn[:], kkn[:], sq[:], ALU.mult))
            dve.wait_ge(ss["sigs"], 2)
            for d in range(2):
                wait(dve.tensor_tensor_scan(X[:, d, :], rc("scan", S), sig[:, d, :], 0.0, ALU.mult, ALU.add))
            x4 = X[:].rearrange("p d (n t) -> p d n t", t=CHUNK)
            wait(dve.tensor_tensor(E1[:], X[:], sig[:], ALU.subtract))
            for d in range(2):
                x3 = X[:, d, :].rearrange("p (n t) -> p n t", t=CHUNK)
                e3 = E2[:, d, :].rearrange("p (n t) -> p n t", t=CHUNK)
                wait(dve.tensor_tensor(e3, x3[:, :, CHUNK - 1:CHUNK].to_broadcast([P, N_CHUNK, CHUNK]), x3, ALU.subtract))
            dve.tensor_tensor(X[:, 1, :], E2[:, 1, :], sig[:, 1, :], ALU.add).then_inc(ss["sums"], 1)
            for d in range(2):
                if d == 0:
                    dve.wait_ge(ss["sigs"], 4)
                wait(dve.tensor_scalar(tmp[:, d, :], rate[:, d, :], -1.0, k.col("k_a", c), ALU.add, ALU.mult))
                dve.scalar_tensor_tensor(out=kd[:, d, :], in0=tmp[:, d, :], scalar=1.0, in1=kf, op0=ALU.add,
                                         op1=ALU.mult).then_inc(ss["kd"], 1)
            dve.wait_ge(ss["kd"], 2)
            wait(dve.tensor_tensor(tmp[:, 1, :], kd[:, 0, :], kd[:, 1, :], ALU.add))
            dve.scalar_tensor_tensor(out=tmp[:, 0, :], in0=tmp[:, 1, :], scalar=k.col("r_k", c), in1=r, op0=ALU.mult,
                                     op1=ALU.mult).then_inc(ss["bonp"], 1)
            for d in range(2):
                wait(dve.tensor_tensor(bb[:, d, :], kkn[:], rate[:, d, :], ALU.mult))
            dve.wait_ge(ss["exps"], 8)
            for d in range(2):
                dve.tensor_tensor(ar[:, d, 0, :], kkn[:], ex[:, d, 1, :], ALU.mult).then_inc(ss["feat"], 1)
                dve.tensor_tensor(bt[:, d, :], bb[:, d, :], ex[:, d, 2, :], ALU.mult).then_inc(ss["feat"], 1)
                dve.scalar_tensor_tensor(out=bh[:, d, :], in0=bb[:, d, :], scalar=-1.0, in1=ex[:, d, 3, :], op0=ALU.mult,
                                         op1=ALU.mult).then_inc(ss["feat"], 1)
                end = ex[:, d, 0, :].rearrange("p (n t) -> p n t", t=CHUNK)[:, :, (CHUNK - 1, 0)[d]]
                wait(dve.tensor_copy(pend[:, d, :], end))
            dve.wait_ge(ss["bonm"], 1)
            dve.tensor_tensor(k.bonus[:, c, :], k.ps[:, 5, :], v, ALU.mult)
            dve.wait_ge(ss["pool_feat"], 6)
            for n in range(8):
                d, q, hd = n // 4, n // 2 % 2, n % 2
                u = 8 * d + 4 * hd + 2 * q
                dve.wait_ge(ss["scm"], n // 2 + 1)
                mask = rc(f"score{d}", 256).rearrange("p (o n) -> p o n", o=1).to_broadcast([P, 2, 256])
                dve.tensor_tensor(sc[:, u:u + 2].rearrange("p u m t -> p u (m t)"),
                                  k.ps[:, 2 * (n // 2 % 2) + hd, :].rearrange("p (u m) -> p u m", u=2), mask, ALU.mult) \
                    .then_inc(ss["sc"], 1)
                if n == 3:
                    for par in range(2):
                        dve.memset(off[0][rows_half(par), :, chunk(1 - par)], 0.0).then_inc(ss["zero"], 1)
            dve.wait_ge(ss["sc"], 8)
            for par in range(2):
                off_blocks(dve, 0, 1, par).then_inc(ss["off0"], 1)
            dve.wait_ge(ss["off0"], 2)
            dve.wait_ge(ss["zero"], 2)
            dve.wait_ge(ss["off0_pool"], 2)
            for d in range(2):
                for part in range(2):
                    last = dve.tensor_tensor(four(Tt, d, part), four(off[0], d, part), eye, ALU.add)
                last.then_inc(ss["t"], 1)
            dve.wait_ge(ss["tok"], 7)
            for par in range(2):
                dve.memset(off[1][rows_half(par), :, chunk(1 - par)], 0.0).then_inc(ss["zero"], 1)
            dve.wait_ge(ss["z"], 1)
            for d in range(2):
                for part in range(2):
                    last = dve.tensor_tensor(four(T, d, part),
                                             k.ps[:, 4 + 2 * d + part, :].rearrange("p (u t) -> p u t", t=P), eye, ALU.add)
                last.then_inc(ss["t"], 1)
            n = 0
            for op, (name, lv, d) in enumerate(ops):
                if name == "Z":
                    continue
                n += 1
                dve.wait_ge(ss["tz"], n)
                for part in range(2):
                    bank = pair(op, part).rearrange("p (u t) -> p u t", t=P)
                    if name == "Tt" and lv < final:
                        made_now = dve.tensor_copy(four(Tt, d, part), bank)
                    else:
                        x = T if name == "T" else Tt
                        if part == 0:
                            dve.wait_ge(ss["t"], made[name, lv - 1, d])
                        made_now = dve.tensor_tensor(four(x, d, part), four(x, d, part), bank, ALU.add)
                made_now.then_inc(ss["t"], 1)
            for g in (1, 3):
                dve.wait_ge(ss["wum"], g + 1)
                dve.tensor_copy(wu[:, 4 * g:4 * g + 4, :].rearrange("p u t -> p (u t)"), k.ps[:, g, :]) \
                    .then_inc(ss["wu_d"], 1)
            dve.memset(state[:, 0, 0, :], 0.0).then_inc(ss["st0"], 1)
            dve.memset(state[:, 1, N_CHUNK - 1, :], 0.0).then_inc(ss["st0"], 1)
            dve.wait_ge(ss["rm"], 1)
            for par in range(2):
                x = ar[:, :, 1, :].rearrange("p d (i a t) -> p d i a t", a=2, t=CHUNK)[:, :, :, par, :]
                dve.tensor_tensor(x, x, k.ps[:, 4 + par, :].rearrange("p (d i t) -> p d i t", d=2, t=CHUNK), ALU.add) \
                    .then_inc(ss["rhat"], 1)
            dve.wait_ge(ss["mm"], 1)
            dve.wait_ge(ss["pcd"], 1)
            for par in range(2):
                x = mt[:].rearrange("p d (i a) t -> p d i a t", a=2)[:, :, :, par, :]
                dve.tensor_tensor(x, x, k.ps[:, 6 + par, :].rearrange("p (d i t) -> p d i t", d=2, t=CHUNK), ALU.add) \
                    .then_inc(ss["mt"], 1)
            dve.wait_ge(ss["add"], 2)
            dve.wait_ge(ss["st0"], 2)
            dve.tensor_copy(state[:, 0, 1, :], add[:, 0, 0, :])
            dve.tensor_copy(state[:, 1, N_CHUNK - 2, :], add[:, 1, N_CHUNK - 1, :]).then_inc(ss["st"], 1)
            for n in range(1, N_CHUNK - 1):
                dve.wait_ge(ss["stm"], n)
                dve.tensor_tensor(state[:, 0, n + 1, :], k.ps[:, 2, chunk(n)], add[:, 0, n, :], ALU.add)
                m = N_CHUNK - 1 - n
                dve.tensor_tensor(state[:, 1, m - 1, :], k.ps[:, 3, chunk(n)], add[:, 1, m, :], ALU.add) \
                    .then_inc(ss["st"], 1)
            dve.wait_ge(ss["ya"], 1)
            dve.wait_ge(ss["ybc"], 2)
            for hd in range(2):
                x = k.ytok[:, :, c * P + 64 * hd:c * P + 64 * hd + 64]
                dve.tensor_tensor(x, x, k.ps[:, 4 + hd, 0:256].rearrange("p (i t) -> p i t", t=CHUNK), ALU.add)


def stage_rw_out(k):
    nc = k.nc
    sqr = k.region("rwo_sq", [P, TT, S], F32, 30)
    g = k.region("rwo_g", [P, RW_T, S], F32, 38)
    y = k.region("rwo_y", [P, 2, S], F32, 46)
    N = TT * 8
    mean, var = k.small[:, 0:N], k.small[:, N:2 * N]
    s = {n: k.sem(f"rwo_{n}") for n in (
          "gm", "gc", "step", "vars", "root", "normed", "tr", "aff", "y", "hi",
          "lo")}
    b0 = first_block("mix_o")
    with nc.Block() as block:
        @block.sync
        def _(sp):
            load_blocks(k, sp, b0 + RAW_SLOTS)

        @block.tensor
        def _(pe):
            for c in range(RW_T):
                last = pe.matmul(k.ps[:, 4 + c, :], k.gate_lora[:, c * P:(c + 1) * P], k.rw[:, 14, :], start=True, stop=True)
            last.then_inc(s["gm"], 1)
            pe.wait_ge(s["normed"], 1)
            for c in range(RW_T):
                for i in range(TT):
                    last = pe.transpose(k.ps[:, c, i * P:(i + 1) * P], k.ytok[:, i, c * P:(c + 1) * P], k.const("ident"))
                last.then_inc(s["tr"], 1)

        @block.scalar
        def _(act):
            act.wait_ge(s["gm"], 1)
            for c in range(RW_T):
                act.activation(g[:, c, :], k.ps[:, 4 + c, :], ACT.Copy).then_inc(s["gc"], 1)
            act.wait_ge(s["vars"], 1)
            act.activation(var, var, ACT.Sqrt, scale=1.0 / DK, bias=k.col("eps_gn")).then_inc(s["root"], 1)
            for c in range(RW_T + 1):
                if c < RW_T:
                    act.wait_ge(s["tr"], c + 1)
                    if c >= 2:
                        act.wait_ge(s["lo"], c - 1)
                    act.activation(y[:, c % 2, :], k.ps[:, c, :], ACT.Identity, scale=k.col("rw_ln_w", c),
                                   bias=k.col("rw_ln_b", c)).then_inc(s["aff"], 1)
                if c >= 1:
                    act.wait_ge(s["y"], c)
                    act.activation(k.act_hi[:, c - 1, :], y[:, (c - 1) % 2, :], ACT.Copy).then_inc(s["hi"], 1)
            split_hi(k, act, b0)

        @block.vector
        def _(dve):
            steps = Steps(s["step"])
            y3 = k.ytok[:].rearrange("p t (h d) -> p (t h) d", d=DK)
            s3 = sqr[:].rearrange("p t (h d) -> p (t h) d", d=DK)
            steps.then_wait(dve, dve.tensor_reduce(mean, y3, AX, ALU.add))
            steps.then_wait(dve, dve.tensor_scalar(mean, mean, 1.0 / DK, None, ALU.mult))
            steps.then_wait(dve, dve.tensor_tensor(y3, y3, mean.rearrange("p (h o) -> p h o", o=1).to_broadcast([P, N, DK]),
                                                   ALU.subtract))
            steps.then_wait(dve, dve.tensor_tensor(s3, y3, y3, ALU.mult))
            dve.tensor_reduce(var, s3, AX, ALU.add).then_inc(s["vars"], 1)
            dve.wait_ge(s["root"], 1)
            steps.then_wait(dve, dve.reciprocal(var, var))
            dve.tensor_tensor(y3, y3, var.rearrange("p (h o) -> p h o", o=1).to_broadcast([P, N, DK]), ALU.mult) \
                .then_inc(s["normed"], 1)
            dve.wait_ge(s["gc"], RW_T)
            for c in range(RW_T):
                dve.wait_ge(s["aff"], c + 1)
                x = y[:, c % 2, :]
                steps.then_wait(dve, dve.tensor_tensor(x, x, k.bonus[:, c, :], ALU.add))
                dve.tensor_tensor(x, x, g[:, c, :], ALU.mult).then_inc(s["y"], 1)
                dve.wait_ge(s["hi"], c + 1)
                dve.tensor_tensor(k.act_lo[:, c, :], x, k.act_hi[:, c, :].bitcast(F32), ALU.subtract).then_inc(s["lo"], 1)
            split_lo(k, dve, b0)


def stage_mix(k):
    nc = k.nc
    b0 = first_block("mix_o")
    b1 = first_block("out_2")
    g = k.region("mix_g", [P, 4, 2, S], F32, 0)
    merged = k.region("merged", [P, KD, S], F32, 16)
    parts = k.region("mix_parts", [P, 2, 2, S], F32, 32)
    gl = [k.sem(f"mix_g{i}") for i in range(4)]
    pair, read, part, merged_done, hi = (k.sem("mix_pair"), k.sem("mix_read"), k.sem("mix_part"), k.sem("mix_merged"),
                                         k.sem("mix_hi"))
    tiles = tiles_of(b0, b1)
    with nc.Block() as block:
        @block.sync
        def _(sp):
            for n in range(KD):
                if n >= 4:
                    sp.wait_ge(part, 2 * (n - 3))
                for x in range(2):
                    sp.dma_start(g[:, n % 4, x, :], k.io["z_scratch"][KD * x + n]).then_inc(gl[n % 4], 16)
                if n == 3:
                    load_blocks(k, sp, b1 + RAW_SLOTS - 1)
            load_blocks(k, sp, b1 + RAW_SLOTS)

        @block.scalar
        def _(act):
            for b in range(b0, b1):
                split_hi(k, act, b + 1)
            for n in range(KD):
                act.wait_ge(merged_done, n + 1)
                if n == 0:
                    act.wait_ge(pair, 2 * KD)
                act.activation(k.act_hi[:, n, :], merged[:, n, :], ACT.Copy).then_inc(hi, 1)

        @block.tensor
        def _(pe):
            for n, (b, j) in enumerate(tiles):
                pe.wait_ge(k.lo_done, b + 1)
                for x in range(2):
                    if n >= 2:
                        pe.wait_ge(read, 2 * (n - 2) + x + 1)
                    for kt in range(4 * x, 4 * x + 4):
                        w = slice(kt * BLOCK_COLS + j * P, kt * BLOCK_COLS + j * P + P)
                        whi, wlo = k.whi[b % 2][:, w], k.wlo[b % 2][:, w]
                        bank = k.ps[:, 2 * (n % 2) + x, :]
                        pe.matmul(bank, whi, k.act_hi[:, kt, :], start=(kt == 4 * x), stop=False)
                        pe.matmul(bank, whi, k.act_lo[:, kt, :], start=False, stop=False)
                        last = pe.matmul(bank, wlo, k.act_hi[:, kt, :], start=False, stop=(kt == 4 * x + 3))
                    last.then_inc(pair, 1)
                pe.wait_ge(pair, 2 * n + 2)
                pe.sem_inc(k.tile_done, 1)

        @block.vector
        def _(dve):
            for n, (b, j) in enumerate(tiles):
                if j == 0:
                    split_lo(k, dve, b + 1)
                dve.wait_ge(gl[n % 4], 32 * (n // 4 + 1))
                for x in range(2):
                    dve.wait_ge(pair, 2 * n + x + 1)
                    if n >= 2:
                        dve.wait_ge(merged_done, n - 1)
                    dve.tensor_tensor(parts[:, n % 2, x, :], k.ps[:, 2 * (n % 2) + x, :], g[:, n % 4, x, :], ALU.mult) \
                        .then_inc(read, 1)
                dve.wait_ge(read, 2 * n + 2)
                dve.sem_inc(part, 2)
                dve.sem_inc(k.evac_done, 1)
                dve.tensor_tensor(merged[:, n, :], parts[:, n % 2, 0, :], parts[:, n % 2, 1, :], ALU.add) \
                    .then_inc(merged_done, 1)
            for n in range(KD):
                dve.wait_ge(hi, n + 1)
                dve.tensor_tensor(k.act_lo[:, n, :], merged[:, n, :], k.act_hi[:, n, :].bitcast(F32), ALU.subtract)


def stage_ffn(k, norm, then):
    norm.scale_stage()
    then.squares_stage()
    b0 = first_block("ff1")
    f_hi = k.region("f_hi", [P, KD, S], F32R, 0)
    f_lo = k.region("f_lo", [P, KD, S], F32R, 16)
    sq = k.region("ff_sq", [P, 2, S], F32, 32)
    relu = k.region("ff_relu", [P, 2, S], F32, 36)
    relu_done, sq_done, hi, lo = k.sem("ff_relu_done"), k.sem("ff_sq_done"), k.sem("ff_hi"), k.sem("ff_lo")
    with k.nc.Block() as block:
        @block.sync
        def _(sp):
            load_blocks(k, sp, b0 + 32 + RAW_SLOTS)

        @block.scalar
        def _(act):
            norm.scale_act(act)
            for f in range(4):
                for n, (b, j) in enumerate(tiles_of(b0 + 8 * f, b0 + 8 * f + 4)):
                    if j == 0:
                        split_hi(k, act, b + 1)
                    m = KD * f + n
                    act.wait_ge(sq_done, m + 1)
                    if n == 0 and f:
                        act.wait_ge(k.tile_done, TILE_AT[b0 + 8 * f])
                    act.activation(f_hi[:, n, :], sq[:, m % 2, :], ACT.Copy).then_inc(hi, 1)
                for n, (b, j) in enumerate(tiles_of(b0 + 8 * f + 4, b0 + 8 * f + 8)):
                    if j == 0:
                        split_hi(k, act, b + 1)
                    if f == 3:
                        act.wait_ge(k.evac_done, TILE_AT[b] + j + 1)
                        then.square(act, n)

        @block.tensor
        def _(pe):
            for f in range(4):
                for n, (b, j) in enumerate(tiles_of(b0 + 8 * f, b0 + 8 * f + 4)):
                    multiply_tile(k, pe, b, j, norm.fed if n == f == 0 else None)
                for n, (b, j) in enumerate(tiles_of(b0 + 8 * f + 4, b0 + 8 * f + 8)):
                    t = TILE_AT[b] + j
                    pe.wait_ge(k.lo_done, b + 1)
                    pe.wait_ge(k.evac_done, t - 3)
                    for kt in range(KD):
                        w = slice(kt * BLOCK_COLS + j * P, kt * BLOCK_COLS + j * P + P)
                        whi, wlo = k.whi[b % 2][:, w], k.wlo[b % 2][:, w]
                        if n == 0:
                            pe.wait_ge(lo, KD * f + kt + 1)
                        pe.matmul(k.ps[:, t % 4, :], whi, f_hi[:, kt, :], start=(kt == 0), stop=False)
                        pe.matmul(k.ps[:, t % 4, :], whi, f_lo[:, kt, :], start=False, stop=False)
                        last = pe.matmul(k.ps[:, t % 4, :], wlo, f_hi[:, kt, :], start=False, stop=(kt == KD - 1))
                    last.then_inc(k.tile_done, 1)
                    if f == 3 and n:
                        then.mean(pe, n - 1)
            then.mean(pe, KD - 1)

        @block.vector
        def _(dve):
            norm.scale_dve(dve)
            for f in range(4):
                for n, (b, j) in enumerate(tiles_of(b0 + 8 * f, b0 + 8 * f + 4)):
                    if j == 0:
                        split_lo(k, dve, b + 1)
                    m, t = KD * f + n, TILE_AT[b] + j
                    dve.wait_ge(k.tile_done, t + 1)
                    dve.tensor_scalar(relu[:, m % 2, :], k.ps[:, t % 4, :], 0.0, None, ALU.max).then_inc(k.evac_done, 1)
                    dve.wait_ge(k.evac_done, t + 1)
                    if m >= 2:
                        dve.wait_ge(lo, m - 1)
                    dve.tensor_tensor(sq[:, m % 2, :], relu[:, m % 2, :], relu[:, m % 2, :], ALU.mult).then_inc(sq_done, 1)
                    dve.wait_ge(hi, m + 1)
                    dve.tensor_tensor(f_lo[:, n, :], sq[:, m % 2, :], f_hi[:, n, :].bitcast(F32), ALU.subtract) \
                        .then_inc(lo, 1)
                for n, (b, j) in enumerate(tiles_of(b0 + 8 * f + 4, b0 + 8 * f + 8)):
                    if j == 0:
                        split_lo(k, dve, b + 1)
                    t = TILE_AT[b] + j
                    dve.wait_ge(k.tile_done, t + 1)
                    dve.tensor_tensor(k.xT[:, n, :], k.xT[:, n, :], k.ps[:, t % 4, :], ALU.add).then_inc(k.evac_done, 1)


def stage_ple(k, norm, then):
    nc = k.nc
    norm.scale_stage()
    then.squares_stage()
    b0 = first_block("ple_gate")
    b1 = first_block("ple_proj")
    b2 = b1 + 4
    gate = k.region("ple_gates", [P, KD, S], F32, 20)
    pf = k.region("ple_p", [P, 2, S], F32, 36)
    p_hi = k.region("ple_p_hi", [P, 2, S], F32R, 40)
    p_lo = k.region("ple_p_lo", [P, 2, S], F32R, 44)
    part = k.region("ple_part", [P, 2, S], F32, 48)
    landed, p_hi_done, p_lo_done, gates, part_done, added = (k.sem("ple_landed"), k.sem("ple_p_hi_done"),
                                                             k.sem("ple_p_lo_done"), k.sem("ple_gates_done"),
                                                             k.sem("ple_part_done"), k.sem("ple_added"))
    with nc.Block() as block:
        @block.sync
        def _(sp):
            sp.dma_start(pf[:], k.io["pT"]).then_inc(landed, 16)
            load_blocks(k, sp, b2)

        @block.scalar
        def _(act):
            norm.scale_act(act)
            act.wait_ge(landed, 16)
            act.activation(p_hi[:], pf[:], ACT.Copy).then_inc(p_hi_done, 1)
            for n, (b, j) in enumerate(tiles_of(b0, b1)):
                if j == 0:
                    split_hi(k, act, b + 1)
                t = TILE_AT[b] + j
                act.wait_ge(k.tile_done, t + 1)
                act.activation(gate[:, n, :], k.ps[:, t % 4, :], ACT.Sigmoid).then_inc(k.evac_done, 1)
            for n, (b, j) in enumerate(tiles_of(b1, b2)):
                if j == 0:
                    split_hi(k, act, b + 1)
                act.wait_ge(added, n + 1)
                then.square(act, n)

        @block.tensor
        def _(pe):
            for n, (b, j) in enumerate(tiles_of(b0, b1)):
                multiply_tile(k, pe, b, j, norm.fed if n == 0 else None)
            pe.wait_ge(p_lo_done, 1)
            for n, (b, j) in enumerate(tiles_of(b1, b2)):
                t = TILE_AT[b] + j
                pe.wait_ge(k.lo_done, b + 1)
                pe.wait_ge(k.evac_done, t - 3)
                for kt in range(2):
                    w = slice(kt * BLOCK_COLS + j * P, kt * BLOCK_COLS + j * P + P)
                    whi, wlo = k.whi[b % 2][:, w], k.wlo[b % 2][:, w]
                    pe.matmul(k.ps[:, t % 4, :], whi, p_hi[:, kt, :], start=(kt == 0), stop=False)
                    pe.matmul(k.ps[:, t % 4, :], whi, p_lo[:, kt, :], start=False, stop=False)
                    last = pe.matmul(k.ps[:, t % 4, :], wlo, p_hi[:, kt, :], start=False, stop=(kt == 1))
                last.then_inc(k.tile_done, 1)
                if n >= 2:
                    then.mean(pe, n - 2)
            then.mean(pe, KD - 2)
            then.mean(pe, KD - 1)

        @block.vector
        def _(dve):
            norm.scale_dve(dve)
            dve.wait_ge(p_hi_done, 1)
            dve.tensor_tensor(p_lo[:], pf[:], p_hi[:].bitcast(F32), ALU.subtract).then_inc(p_lo_done, 1)
            for b in range(b0, b1):
                split_lo(k, dve, b + 1)
            dve.wait_ge(k.evac_done, TILE_AT[b1])
            for n, (b, j) in enumerate(tiles_of(b1, b2)):
                if j == 0:
                    split_lo(k, dve, b + 1)
                t = TILE_AT[b] + j
                dve.wait_ge(k.tile_done, t + 1)
                if n >= 2:
                    dve.wait_ge(added, n - 1)
                dve.tensor_tensor(part[:, n % 2, :], k.ps[:, t % 4, :], gate[:, n, :], ALU.mult).then_inc(k.evac_done, 1)
                dve.wait_ge(k.evac_done, t + 1)
                dve.tensor_tensor(k.xT[:, n, :], k.xT[:, n, :], part[:, n % 2, :], ALU.add).then_inc(added, 1)


def build(nc, io, stop=None):
    with ExitStack() as ctx:
        k = Core(nc, ctx, io)
        for n, stage in enumerate(program(k)):
            if stop is not None and n >= stop:
                break
            k.run(stage)
        if stop is not None:
            with nc.Block() as block:
                @block.sync
                def _(sp):
                    for i in range(RAW_SLOTS):
                        n = len(range(i, k.loaded, RAW_SLOTS))
                        if n:
                            sp.wait_ge(k.landed[i], 16 * n)
    return k


def program(k):
    out0, nsa0, out2 = first_block("ml_out"), first_block("nsa_out"), first_block("out_2")
    norm_ml, norm_nsa = Norm(k, "norm_ml", "ml_norm", 68), Norm(k, "norm_nsa", "nsa_norm", 84)
    norm_first, norm_mix = Norm(k, "norm_first", "final_norm", 78), Norm(k, "norm_mix", "norm_mix", 84)
    norm_ffn, norm_ple = Norm(k, "norm_ffn", "norm_ffn", 78), Norm(k, "norm_ple", "norm_ple", 84)
    norm_final = Norm(k, "norm_final", "norm_final", 78)
    return [
        lambda k: stage_open(k, norm_ml),
        lambda k: stage_ml_inner(k, norm_ml),
        stage_ml_gate,
        lambda k: stage_ml_heads(k, 0),
        lambda k: stage_add(k, out0, out0 + 4),
        lambda k: stage_ml_heads(k, 2),
        lambda k: stage_add(k, out0 + 4, out0 + 8, norm_nsa),
        lambda k: stage_nsa_in(k, norm_nsa),
        stage_nsa_prep,
        stage_nsa_cmp,
        stage_nsa_attention,
        stage_nsa_gate,
        lambda k: stage_add(k, nsa0, nsa0 + 4, norm_first),
        lambda k: stage_norm_residual(k, norm_first, norm_mix),
        lambda k: stage_in_2(k, norm_mix),
        stage_da_prep,
        stage_da_attention,
        *[lambda k, c=c: stage_rw_heads(k, c) for c in range(RW_T)],
        stage_rw_out,
        stage_mix,
        lambda k: stage_add(k, out2, out2 + 4, norm_ffn),
        lambda k: stage_ffn(k, norm_ffn, norm_ple),
        lambda k: stage_ple(k, norm_ple, norm_final),
        lambda k: stage_norm_residual(k, norm_final),
    ]


def kernel(**inputs):
    import numpy as np
    import ml_dtypes
    import concourse.bacc as bacc
    from concourse.bass_utils import run_bass_kernel_spmd

    a = {n: np.asarray(x) for n, x in inputs.items()}
    arrays = layout(np, ml_dtypes, a)
    nc = bacc.Bacc("TRN2", target_bir_lowering=False, num_devices=1)
    io, ins = {}, {}
    for n, x in arrays.items():
        x = np.ascontiguousarray(x)
        ins[n + "_in"] = x
        io[n] = nc.dram_tensor(n + "_in", x.shape, mybir.dt.from_np(x.dtype), kind="ExternalInput").ap()
    scratch(nc, io)
    build(nc, io)
    r = run_bass_kernel_spmd(nc, [ins], core_ids=[0])
    got = r.results[0]["out_T"]
    return got.transpose(2, 1, 0).reshape(1, S, D)


def scratch(nc, io):
    io["v_scratch"] = nc.dram_tensor("v_scratch", [ML_HEADS, P, TT, S], F32).ap()
    io["z_scratch"] = nc.dram_tensor("z_scratch", [ML_T, P, S], F32).ap()
    io["out"] = nc.dram_tensor("out_T", [P, KD, S], F32, kind="ExternalOutput").ap()


def rows_of(np, x):
    return x.reshape(-1, P, x.shape[-1]).transpose(1, 0, 2)


def layout(np, ml_dtypes, a):
    f32, bf16 = np.float32, ml_dtypes.bfloat16
    out = {"xT": a["x"][0].T.reshape(KD, P, S).transpose(1, 0, 2)}

    order = [(2 * gp + half) * 4 + hh for gp in range(2) for hh in range(4) for half in range(2)]
    nsa_cols = np.concatenate([np.concatenate([np.arange(h * DK, (h + 1) * DK) for h in order]),
                               np.arange(NSA_HEADS * DK, a["nsa_w_in"].shape[2])])
    nsa_in = a["nsa_w_in"][0][:, nsa_cols]
    nsa_in = np.concatenate([nsa_in, np.zeros((D, 29 * P - nsa_in.shape[1]), f32)], axis=1)
    mix_o = np.concatenate([a["rwkv_w_o_2"][0], a["da_w_o_2"][0]], axis=0)
    w2 = a["w_in_2"][0]
    in_2 = np.concatenate([w2[:, 1920 + 1536:], w2[:, 1920:1920 + 1536], w2[:, :1920]], axis=1)
    weights = {"ml_in": a["ml_w_in"][0], "ml_out": a["ml_w_out"][0], "nsa_in": nsa_in, "nsa_out": a["nsa_w_out"][0],
               "in_2": in_2, "mix_o": mix_o, "out_2": a["w_out_2"][0], "ff1": a["w_ff1_2"][0], "ff2": a["w_ff2_2"][0],
               "ple_gate": a["w_ple_gate_2"][0], "ple_proj": a["w_ple_proj_2"][0]}
    stream = np.empty((P, STREAM_COLS), f32)
    for b, (name, r0, rows, c0, n) in enumerate(BLOCKS):
        stream[:, BLOCK_AT[b]:BLOCK_AT[b + 1]] = rows_of(np, weights[name][r0:r0 + rows, c0:c0 + n]).reshape(P, -1)
    out["stream"] = stream

    cols = np.zeros((P, N_COLS), f32)

    def put(name, x):
        x = x.reshape(-1, P)
        cols[:, COLS[name]:COLS[name] + x.shape[0]] = x.T

    for name, key in (("ml_norm", "ml_norm"), ("conv_w", "ml_conv_w"), ("conv_b", "ml_conv_b"), ("ml_ln_w", "ml_ln_w"),
                      ("skip", "ml_skip"), ("nsa_norm", "nsa_norm"), ("final_norm", "final_norm"),
                      ("norm_mix", "norm_mix_2"), ("norm_ffn", "norm_ffn_2"), ("norm_ple", "norm_ple_2"),
                      ("norm_final", "norm_final_2"), ("mu_prev", "shift_mu_prev_2"), ("mu_next", "shift_mu_next_2"),
                      ("w0", "rwkv_w0_2"), ("a0", "rwkv_a0_2"), ("k_k", "rwkv_k_k_2"), ("k_a", "rwkv_k_a_2"),
                      ("r_k", "rwkv_r_k_2"), ("rw_ln_w", "rwkv_ln_w_2"), ("rw_ln_b", "rwkv_ln_b_2"),
                      ("subln", "da_subln_w_2")):
        put(name, a[key])
    cols[0:4, COLS["b_if"]] = a["ml_b_if"][0, 0:4]
    cols[32:36, COLS["b_if"]] = a["ml_b_if"][0, 4:8]
    cols[0:48, COLS["b_gate"]] = a["nsa_b_gate"][0]
    for n in ("lq1", "lk1", "lq2", "lk2"):
        cols[0:64, COLS[n]] = a[f"da_{n}_2"][0]
    for n, x in (("eps6", 1e-6), ("eps5", 1e-5), ("eps_gn", 64e-5), ("one", 1.0)):
        cols[:, COLS[n]] = x
    cols[:, COLS["cmp_any"]] = np.arange(P) >= CMP_BLOCK - 1
    out["cols"] = cols

    w = np.stack([a["ml_w_q"][0], a["ml_w_k"][0], a["ml_w_v"][0]]).reshape(3, ML_T, 32, 4, 4)
    out["hw"] = w.transpose(2, 4, 0, 1, 3).reshape(P, 3, ML_T, 4)
    out["hwt"] = w.transpose(2, 3, 0, 1, 4).reshape(P, 3, ML_T, 4)
    out["wif"] = a["ml_w_if"][0].reshape(3, ML_T, P, 8).transpose(2, 0, 1, 3)

    w1 = a["nsa_cmp_w1"][0].reshape(2, CMP_BLOCK, DK, P).transpose(2, 0, 1, 3)
    out["cmp_w1"] = np.concatenate([w1, w1], axis=0)
    pe = a["nsa_cmp_pe"][0].transpose(2, 0, 1).reshape(DK, 64)
    w2 = a["nsa_cmp_w2"][0].transpose(1, 0, 2).reshape(P, 2 * DK)
    out["cmp_small"] = np.concatenate([np.concatenate([pe, pe], axis=0), w2], axis=1)

    i = np.arange(P)
    c = np.zeros((P, N_CONSTS), f32)

    def const(name, x):
        c[:x.shape[0], CONSTS[name]:CONSTS[name] + x.shape[1]] = x

    const("ident", np.eye(P))
    const("ones", np.ones((P, P)))
    const("mean_ones", np.full((P, P), 1.0 / D))
    const("block_ones", (i[:, None] // 64 == i[None, :] // 64))
    rot = np.zeros((P, P))
    for m in range(P):
        if m % 64 < 8:
            rot[m + 8, m] = -1.0
        elif m % 64 < 16:
            rot[m - 8, m] = 1.0
    const("rot", rot)
    const("same4", i[:, None] // 4 == np.arange(32)[None, :])
    sel = np.zeros((4, 4, P))
    for h in range(4):
        sel[h, h] = 1.0
    const("sel", sel.reshape(4, 512))
    inv_freq = (f32(500000.0) ** (-np.arange(0, 16, 2, dtype=f32) / f32(16))).astype(f32)
    ang = np.arange(S, dtype=f32)[:, None] * inv_freq[None, :]
    cos, sin = np.ones((P, S)), np.zeros((P, S))
    for m in range(P):
        if m % 64 < 16:
            cos[m], sin[m] = np.cos(ang[:, m % 8]), np.sin(ang[:, m % 8])
    const("cos", cos)
    const("sin", sin)
    out["consts"] = c

    out["pT"] = a["p_2"][0, 0].T.reshape(2, P, S).transpose(1, 0, 2)
    w2, a2 = (a[n][0].reshape(P, S) for n in ("rwkv_w2_2", "rwkv_a2_2"))
    lora = np.zeros((P, 5, S), f32)
    for d in range(2):
        h = slice(64 * d, 64 * d + 64)
        lora[h, d], lora[h, 2 + d] = w2[h], a2[h]
    lora[:, 4] = a["rwkv_g2_2"][0]
    out["lora"] = lora
    rw = np.zeros((P, N_RW_CONSTS), f32)
    rw[:, RW_CONSTS["scan"]:RW_CONSTS["scan"] + S] = np.arange(S) % CHUNK != 0
    src, dst = (i % CHUNK)[:, None], np.arange(CHUNK)[None, :]
    for d in range(2):
        before = src < dst if d == 0 else src > dst
        upto = before | (src == dst)
        at = RW_CONSTS[f"score{d}"]
        rw[:, at:at + 256] = np.concatenate([-1.0 * before, -1.0 * upto, 1.0 * before, 1.0 * upto], axis=1)
        for lv in range(LEVELS):
            b = 1 << lv
            at = RW_CONSTS[f"level{d}"] + CHUNK * lv
            rw[:, at:at + CHUNK] = before & (src // (2 * b) == dst // (2 * b)) & (src // b != dst // b)
    rw[:, RW_CONSTS["eye64"]:RW_CONSTS["eye64"] + CHUNK] = src == dst
    out["rw_consts"] = rw

    masks = np.zeros((P, 3 * P), bf16)
    masks[:, 0:P] = np.eye(P)
    masks[:, P:2 * P] = np.where(i[None, :] <= i[:, None], 0.0, -1e30)
    for t in range(TT):
        pos = t * P + i
        end = np.arange(32) * CMP_STRIDE + CMP_BLOCK - 1
        masks[:, 2 * P + 32 * t:2 * P + 32 * t + 32] = np.where(end[None, :] <= pos[:, None], 0.0, -1e30)
    out["masks_bf"] = masks
    return out
```
